# Optimizing a Trainium2 kernel written in Bass

```python
import math
import jax, jax.numpy as jnp
from jax import lax
import numpy as np

D_MODEL = 1024
BATCH = 1
SEQ = 512
DEPTH = 2

PLE_DIM = 256
N_EVEN = (DEPTH + 1) // 2
N_ODD = DEPTH // 2

DA_HEADS = 4
DA_HEAD_DIM = 64
DA_V_DIM = 2 * DA_HEAD_DIM
DA_QK_WIDTH = DA_HEADS * 2 * DA_HEAD_DIM
DA_WIDTH = DA_HEADS * DA_V_DIM

HG_HEADS = 4
HG_KDIM = 128
HG_VDIM = 128
HG_KWIDTH = HG_HEADS * HG_KDIM
HG_WIDTH = HG_HEADS * HG_VDIM
HG_CHUNK = 64

DL_HEADS = 16
DL_HEAD_DIM = D_MODEL // DL_HEADS
DL_PAIRS = ((128, 1), (512, 4), (2048, 16))

FFN_DIM = 4 * D_MODEL
ROPE_THETA = 500000.0
ROT_DIM = 64 // 4
ALPHA = (2 * DEPTH) ** 0.25
BETA = (8 * DEPTH) ** -0.25
LN_EPS = 1e-5
Q_BLOCK = 128


def layer_norm(x, g, b):
    xf = x.astype(jnp.float32)
    mu = jnp.mean(xf, -1, keepdims=True)
    var = jnp.mean(jnp.square(xf - mu), -1, keepdims=True)
    return ((xf - mu) * lax.rsqrt(var + LN_EPS) * g + b).astype(x.dtype)

def rms_norm(x, g):
    xf = x.astype(jnp.float32)
    return (xf * lax.rsqrt(jnp.mean(xf * xf, -1, keepdims=True) + LN_EPS) * g).astype(x.dtype)

def rope_tables(seq):
    inv = ROPE_THETA ** (-jnp.arange(0, ROT_DIM, 2, dtype=jnp.float32) / ROT_DIM)
    ang = jnp.arange(seq, dtype=jnp.float32)[:, None] * inv[None, :]
    return jnp.cos(ang), jnp.sin(ang)

def partial_rope(x, cos, sin):
    half = ROT_DIM // 2
    x1, x2, xp = x[..., :half], x[..., half:ROT_DIM], x[..., ROT_DIM:]
    c, s = cos.astype(x.dtype), sin.astype(x.dtype)
    return jnp.concatenate([x1 * c - x2 * s, x1 * s + x2 * c, xp], axis=-1)

def diff_attention(qa, ka, va, lam_params, sub_g, lam_init, cos, sin):
    B, S = qa.shape[:2]
    q = partial_rope(qa.transpose(0, 2, 3, 1, 4), cos, sin) * (DA_HEAD_DIM ** -0.5)
    k = partial_rope(ka.transpose(0, 2, 3, 1, 4), cos, sin)
    v = va.transpose(0, 2, 1, 3)
    lp = lam_params.astype(jnp.float32)
    lam = jnp.exp(jnp.sum(lp[0] * lp[1])) - jnp.exp(jnp.sum(lp[2] * lp[3])) + lam_init
    nb = S // Q_BLOCK
    qb = q.reshape(B, DA_HEADS, 2, nb, Q_BLOCK, DA_HEAD_DIM).transpose(3, 0, 1, 2, 4, 5)
    kpos = jnp.arange(S)

    def block(args):
        qi, i = args
        s = jnp.einsum('bhcqd,bhckd->bhcqk', qi, k).astype(jnp.float32)
        qpos = i * Q_BLOCK + jnp.arange(Q_BLOCK)
        s = jnp.where(kpos[None, :] <= qpos[:, None], s, -jnp.inf)
        pr = jax.nn.softmax(s, axis=-1)
        a = pr[:, :, 0] - lam * pr[:, :, 1]
        return jnp.einsum('bhqk,bhkd->bhqd', a.astype(v.dtype), v)

    o = lax.map(block, (qb, jnp.arange(nb)))
    o = o.transpose(1, 2, 0, 3, 4).reshape(B, DA_HEADS, S, DA_V_DIM)
    o = rms_norm(o, sub_g) * (1.0 - lam_init)
    return o.transpose(0, 2, 1, 3).reshape(B, S, DA_WIDTH)

def hgrn2(hq, hf, hi, hg, lb, out_g):
    B, S, H, dk = hq.shape
    dv = hi.shape[-1]
    f32 = jnp.float32
    q = jax.nn.silu(hq.astype(f32))
    f = lb + (1.0 - lb) * jax.nn.sigmoid(hf.astype(f32))
    kk = 1.0 - f
    logf = jnp.log(f)
    C = HG_CHUNK
    n = S // C

    def chunks(t):
        return t.reshape(B, n, C, H, t.shape[-1]).transpose(1, 0, 3, 2, 4)

    qc, kc, lc, vc = chunks(q), chunks(kk), chunks(logf), chunks(hi.astype(f32))
    b = jnp.cumsum(lc, axis=-2)
    b_last = b[..., C - 1:C, :]
    b_mid = b[..., C // 2 - 1:C // 2, :]
    a = jnp.einsum('nbhtk,nbhsk->nbhts', qc * jnp.exp(b - b_mid), kc * jnp.exp(b_mid - b))
    a = jnp.where(jnp.tril(jnp.ones((C, C), bool)), a, 0.0)
    o_intra = jnp.einsum('nbhts,nbhsv->nbhtv', a, vc)
    q_out = qc * jnp.exp(b)
    k_st = kc * jnp.exp(b_last - b)
    decay = jnp.exp(b_last[..., 0, :])

    def step(state, xs):
        qo, ks, vv, dc = xs
        o_inter = jnp.einsum('bhtk,bhkv->bhtv', qo, state)
        state = dc[..., None] * state + jnp.einsum('bhsk,bhsv->bhkv', ks, vv)
        return state, o_inter

    s0 = jnp.zeros((B, H, dk, dv), f32)
    _, o_inter = lax.scan(step, s0, (q_out, k_st, vc, decay))
    o = (o_intra + o_inter).transpose(1, 0, 3, 2, 4).reshape(B, S, H, dv)
    o = rms_norm(o, out_g) * jax.nn.silu(hg.astype(f32))
    return o.reshape(B, S, H * dv).astype(hi.dtype)

def even_mixer(x, w_in, w_out, lam_params, sub_g, lb, hg_g, lam_init, cos, sin):
    B, S, _ = x.shape
    h = x @ w_in
    sizes = (DA_QK_WIDTH, DA_QK_WIDTH, DA_WIDTH, HG_KWIDTH, HG_KWIDTH, HG_WIDTH, HG_WIDTH)
    cuts = [sum(sizes[:i + 1]) for i in range(len(sizes) - 1)]
    qa, ka, va, hq, hf, hi, hg = jnp.split(h, cuts, axis=-1)
    o_a = diff_attention(qa.reshape(B, S, DA_HEADS, 2, DA_HEAD_DIM),
                         ka.reshape(B, S, DA_HEADS, 2, DA_HEAD_DIM),
                         va.reshape(B, S, DA_HEADS, DA_V_DIM),
                         lam_params, sub_g, lam_init, cos, sin)
    o_b = hgrn2(hq.reshape(B, S, HG_HEADS, HG_KDIM), hf.reshape(B, S, HG_HEADS, HG_KDIM),
                hi.reshape(B, S, HG_HEADS, HG_VDIM), hg.reshape(B, S, HG_HEADS, HG_VDIM),
                lb.reshape(HG_HEADS, HG_KDIM), hg_g)
    return jnp.concatenate([o_a.astype(x.dtype), o_b.astype(x.dtype)], axis=-1) @ w_out

def dilated_branch(q, k, v, dil, span):
    B, H, S, hd = q.shape
    L = S // dil

    def to_res(t):
        return t.reshape(B, H, L, dil, hd).transpose(0, 1, 3, 2, 4)

    blk = span
    nb = -(-L // blk)
    pad = nb * blk - L

    def padl(t, front):
        return jnp.pad(t, ((0, 0), (0, 0), (0, 0), (front, pad), (0, 0)))

    qp = padl(to_res(q), 0).reshape(B, H, dil, nb, blk, hd)
    kp = padl(to_res(k), blk).reshape(B, H, dil, nb + 1, blk, hd)
    vp = padl(to_res(v), blk).reshape(B, H, dil, nb + 1, blk, hd)
    kw = jnp.concatenate([kp[:, :, :, :-1], kp[:, :, :, 1:]], axis=-2)
    vw = jnp.concatenate([vp[:, :, :, :-1], vp[:, :, :, 1:]], axis=-2)
    s = jnp.einsum('bhrnqd,bhrnkd->bhrnqk', qp, kw).astype(jnp.float32)
    a_idx = jnp.arange(blk)[:, None]
    c_idx = jnp.arange(2 * blk)[None, :]
    dist = blk + a_idx - c_idx
    key_idx = (jnp.arange(nb)[:, None, None] - 1) * blk + c_idx[None]
    valid = (dist >= 0)[None] & (dist <= span)[None] & (key_idx >= 0)
    s = jnp.where(valid, s, -jnp.inf)
    m = jnp.max(s, axis=-1, keepdims=True)
    e = jnp.exp(s - m)
    den = jnp.sum(e, axis=-1)
    o = jnp.einsum('bhrnqk,bhrnkd->bhrnqd', e.astype(v.dtype), vw) / den[..., None].astype(v.dtype)
    lse = m[..., 0] + jnp.log(den)
    o = o.reshape(B, H, dil, nb * blk, hd)[:, :, :, :L].transpose(0, 1, 3, 2, 4).reshape(B, H, S, hd)
    lse = lse.reshape(B, H, dil, nb * blk)[..., :L].transpose(0, 1, 3, 2).reshape(B, H, S)
    return o, lse

def odd_mixer(x, w_in, w_out, cos, sin):
    B, S, D = x.shape
    q, k, v = jnp.split(x @ w_in, 3, axis=-1)

    def heads(t):
        return t.reshape(B, S, DL_HEADS, DL_HEAD_DIM).transpose(0, 2, 1, 3)

    q = partial_rope(heads(q), cos, sin) * (DL_HEAD_DIM ** -0.5)
    k = partial_rope(heads(k), cos, sin)
    v = heads(v)
    outs, lses = [], []
    for (w, d) in DL_PAIRS:
        o, lse = dilated_branch(q, k, v, d, w // d)
        outs.append(o)
        lses.append(lse)
    wts = jax.nn.softmax(jnp.stack(lses, axis=0), axis=0)
    o = jnp.einsum('gbhs,gbhsd->bhsd', wts.astype(v.dtype), jnp.stack(outs, axis=0))
    return o.transpose(0, 2, 1, 3).reshape(B, S, D) @ w_out

def first_inputs(seed: int = 0) -> dict:
    key = jax.random.key(seed)
    ks = jax.random.split(key, 20)
    f32 = jnp.float32

    def nrm(k, shape, s):
        return jax.random.normal(k, shape, f32) * s

    def gain(k, shape):
        return 1.0 + 0.02 * jax.random.normal(k, shape, f32)

    even_in = 2 * DA_QK_WIDTH + DA_WIDTH + 2 * HG_KWIDTH + 2 * HG_WIDTH
    return {
        "x": nrm(ks[0], (BATCH, SEQ, D_MODEL), 1.0),
        "p": nrm(ks[1], (DEPTH, BATCH, SEQ, PLE_DIM), 1.0),
        "ev_w_in": nrm(ks[2], (N_EVEN, D_MODEL, even_in), D_MODEL ** -0.5),
        "ev_w_out": nrm(ks[3], (N_EVEN, DA_WIDTH + HG_WIDTH, D_MODEL), BETA * (DA_WIDTH + HG_WIDTH) ** -0.5),
        "da_lambda": nrm(ks[4], (N_EVEN, 4, DA_HEAD_DIM), 0.1),
        "da_subln_g": gain(ks[5], (N_EVEN, DA_V_DIM)),
        "hg_lb_logits": nrm(ks[6], (N_EVEN + 1, HG_KWIDTH), 0.1),
        "hg_norm_g": gain(ks[7], (N_EVEN, HG_VDIM)),
        "od_w_in": nrm(ks[8], (N_ODD, D_MODEL, 3 * D_MODEL), D_MODEL ** -0.5),
        "od_w_out": nrm(ks[9], (N_ODD, D_MODEL, D_MODEL), BETA * D_MODEL ** -0.5),
        "ln1_g": gain(ks[10], (DEPTH, D_MODEL)),
        "ln1_b": nrm(ks[11], (DEPTH, D_MODEL), 0.02),
        "ffn_w1": nrm(ks[12], (DEPTH, D_MODEL, FFN_DIM), D_MODEL ** -0.5),
        "ffn_w2": nrm(ks[13], (DEPTH, FFN_DIM, D_MODEL), BETA * FFN_DIM ** -0.5),
        "ln2_g": gain(ks[14], (DEPTH, D_MODEL)),
        "ln2_b": nrm(ks[15], (DEPTH, D_MODEL), 0.02),
        "ple_w_proj": nrm(ks[16], (DEPTH, PLE_DIM, D_MODEL), PLE_DIM ** -0.5),
        "ple_w_gate": nrm(ks[17], (DEPTH, D_MODEL, D_MODEL), D_MODEL ** -0.5),
        "ple_norm_g": gain(ks[18], (DEPTH, D_MODEL)),
    }

def first_block(x, p, ev_w_in, ev_w_out, da_lambda, da_subln_g, hg_lb_logits, hg_norm_g,
              od_w_in, od_w_out, ln1_g, ln1_b, ffn_w1, ffn_w2, ln2_g, ln2_b,
              ple_w_proj, ple_w_gate, ple_norm_g):
    S = x.shape[1]
    cos, sin = rope_tables(S)
    lb_all = jnp.cumsum(jax.nn.softmax(hg_lb_logits.astype(jnp.float32), axis=0), axis=0)
    for l in range(DEPTH):
        j = l // 2
        if l % 2 == 0:
            lam_init = 0.8 - 0.6 * math.exp(-0.3 * l)
            mix = even_mixer(x, ev_w_in[j], ev_w_out[j], da_lambda[j], da_subln_g[j],
                             lb_all[j], hg_norm_g[j], lam_init, cos, sin)
        else:
            mix = odd_mixer(x, od_w_in[j], od_w_out[j], cos, sin)
        x = layer_norm(ALPHA * x + mix, ln1_g[l], ln1_b[l])
        hdn = jnp.square(jax.nn.relu(x @ ffn_w1[l]))
        x = layer_norm(ALPHA * x + hdn @ ffn_w2[l], ln2_g[l], ln2_b[l])
        e = rms_norm(p[l] @ ple_w_proj[l], ple_norm_g[l])
        x = x + jax.nn.sigmoid(x @ ple_w_gate[l]) * e
    return x


DEPTH_2 = 1

GRID_W = 64
N_MEM = 256
EPS = 1e-6

ATT_HEADS = 8
ATT_KV_HEADS = 2
ATT_HEAD_DIM = 64
ATT_WIDTH = ATT_HEADS * ATT_HEAD_DIM
KV_WIDTH = ATT_KV_HEADS * ATT_HEAD_DIM
ROPE_THETA_2 = 10000.0

SGU_GROUPS = 4
SGU_WIDTH = 512
SGU_GROUP_CH = SGU_WIDTH // SGU_GROUPS
SGU_CHUNK = 128

IN_COLS = ATT_WIDTH + 2 * KV_WIDTH + 2 * SGU_WIDTH + 2 * D_MODEL

X_HEADS = 4
X_HEAD_DIM = 128
X_WIDTH = X_HEADS * X_HEAD_DIM

N_GROUPS = 4
EXPERTS_PER_GROUP = 4
N_EXPERTS = N_GROUPS * EXPERTS_PER_GROUP
TOP_K = 2
D_EXPERT = 512


def rms_norm_2(x, g):
    xf = x.astype(jnp.float32)
    y = xf * lax.rsqrt(jnp.mean(xf * xf, axis=-1, keepdims=True) + EPS)
    return y.astype(x.dtype) * g

def layer_norm_2(x, g, b):
    xf = x.astype(jnp.float32)
    mu = jnp.mean(xf, axis=-1, keepdims=True)
    xc = xf - mu
    var = jnp.mean(xc * xc, axis=-1, keepdims=True)
    return (xc * lax.rsqrt(var + EPS)).astype(x.dtype) * g + b

def axial_rope_tables(seq_len):
    rows = seq_len // GRID_W
    row_ids = jnp.repeat(jnp.arange(rows), GRID_W).astype(jnp.float32)
    col_ids = jnp.tile(jnp.arange(GRID_W), rows).astype(jnp.float32)
    pairs_per_axis = ATT_HEAD_DIM // 4
    inv_freq = ROPE_THETA_2 ** (-jnp.arange(pairs_per_axis, dtype=jnp.float32) / pairs_per_axis)
    ang = jnp.concatenate([row_ids[:, None] * inv_freq[None, :],
                           col_ids[:, None] * inv_freq[None, :]], axis=-1)
    return jnp.cos(ang), jnp.sin(ang)

def apply_rope(x, cos, sin):
    xf = x.astype(jnp.float32).reshape(*x.shape[:-1], x.shape[-1] // 2, 2)
    x0, x1 = xf[..., 0], xf[..., 1]
    c = cos[None, :, None, :]
    s = sin[None, :, None, :]
    out = jnp.stack([x0 * c - x1 * s, x0 * s + x1 * c], axis=-1).reshape(x.shape)
    return out.astype(x.dtype)

def gqa_attention(q, k, v):
    B, S, _, HD = q.shape
    G = ATT_HEADS // ATT_KV_HEADS
    nb = S // Q_BLOCK
    qb = q.reshape(B, nb, Q_BLOCK, ATT_KV_HEADS, G, HD).transpose(1, 0, 2, 3, 4, 5)
    scale = HD ** -0.5

    def block(q_blk):
        s = jnp.einsum('bqhgd,bkhd->bhgqk', q_blk, k, preferred_element_type=jnp.float32) * scale
        p = jax.nn.softmax(s, axis=-1).astype(v.dtype)
        return jnp.einsum('bhgqk,bkhd->bqhgd', p, v)

    o = lax.map(block, qb)
    return o.transpose(1, 0, 2, 3, 4, 5).reshape(B, S, ATT_WIDTH)

def spatial_gating(u, v, w_s, b_s, ln_g, ln_b):
    B, S, _ = v.shape
    nc = S // SGU_CHUNK
    vn = layer_norm_2(v, ln_g, ln_b).reshape(B, nc, SGU_CHUNK, SGU_GROUPS, SGU_GROUP_CH)
    vm = jnp.einsum('gpq,bnqgc->bnpgc', w_s, vn) + b_s.T[:, :, None]
    return u * vm.reshape(B, S, SGU_WIDTH)

def memory_cross_attention(h, mem_n, w_cq, w_ckv, w_co):
    B, S, _ = h.shape
    M = mem_n.shape[1]
    q = (h @ w_cq).reshape(B, S, X_HEADS, X_HEAD_DIM)
    kv = mem_n @ w_ckv
    k = kv[..., :X_WIDTH].reshape(B, M, X_HEADS, X_HEAD_DIM)
    v = kv[..., X_WIDTH:].reshape(B, M, X_HEADS, X_HEAD_DIM)
    s = jnp.einsum('bshd,bmhd->bhsm', q, k, preferred_element_type=jnp.float32) * (X_HEAD_DIM ** -0.5)
    p = jax.nn.softmax(s, axis=-1).astype(v.dtype)
    o = jnp.einsum('bhsm,bmhd->bshd', p, v).reshape(B, S, X_WIDTH)
    return o @ w_co

def hierarchical_moe(h, w_rg, b_rg, w_re, b_re, w_gate, w_up, w_down):
    B, S, D = h.shape
    t = h.reshape(B * S, D)
    glog = (t @ w_rg + b_rg).astype(jnp.float32)
    gprob = jax.nn.softmax(glog, axis=-1)
    gval, gidx = lax.top_k(gprob, 1)
    elog = (t @ w_re + b_re).astype(jnp.float32).reshape(-1, N_GROUPS, EXPERTS_PER_GROUP)
    elog_sel = jnp.take_along_axis(elog, gidx[:, :, None], axis=1)[:, 0]
    evals, eidx = lax.top_k(elog_sel, TOP_K)
    ew = jax.nn.softmax(evals, axis=-1) * gval
    expert_id = gidx * EXPERTS_PER_GROUP + eidx
    combine = jnp.sum(jax.nn.one_hot(expert_id, N_EXPERTS, dtype=jnp.float32) * ew[..., None], axis=1)
    combine = combine.astype(t.dtype)
    y = jnp.zeros_like(t)
    for e in range(N_EXPERTS):
        he = jax.nn.silu(t @ w_gate[e]) * (t @ w_up[e])
        y = y + combine[:, e:e + 1] * (he @ w_down[e])
    return y.reshape(B, S, D)

def second_inputs(seed: int = 0) -> dict:
    key = jax.random.key(seed)
    ks = iter(jax.random.split(key, 40))
    L = DEPTH_2
    f32 = jnp.float32

    def nrm(shape, scale):
        return jax.random.normal(next(ks), shape, f32) * scale

    def gain(shape):
        return 1.0 + 0.1 * jax.random.normal(next(ks), shape, f32)

    return {
        'x': nrm((BATCH, SEQ, D_MODEL), 1.0),
        'mem': nrm((BATCH, N_MEM, D_MODEL), 1.0),
        'g_mix': gain((L, D_MODEL)),
        'w_in': nrm((L, D_MODEL, IN_COLS), D_MODEL ** -0.5),
        'g_q': gain((L, ATT_HEAD_DIM)),
        'g_k': gain((L, ATT_HEAD_DIM)),
        'w_att_out': nrm((L, ATT_WIDTH, D_MODEL), ATT_WIDTH ** -0.5),
        'sgu_ln_g': gain((L, SGU_WIDTH)),
        'sgu_ln_b': nrm((L, SGU_WIDTH), 0.02),
        'w_s': nrm((L, SGU_GROUPS, SGU_CHUNK, SGU_CHUNK), 0.5 * SGU_CHUNK ** -0.5),
        'b_s': 1.0 + nrm((L, SGU_GROUPS, SGU_CHUNK), 0.1),
        'w_sgu_out': nrm((L, SGU_WIDTH, D_MODEL), SGU_WIDTH ** -0.5),
        'w_out': nrm((L, D_MODEL, D_MODEL), D_MODEL ** -0.5),
        'g_cross': gain((L, D_MODEL)),
        'g_mem': gain((L, D_MODEL)),
        'w_cq': nrm((L, D_MODEL, X_WIDTH), D_MODEL ** -0.5),
        'w_ckv': nrm((L, D_MODEL, 2 * X_WIDTH), D_MODEL ** -0.5),
        'w_co': nrm((L, X_WIDTH, D_MODEL), X_WIDTH ** -0.5),
        'g_moe': gain((L, D_MODEL)),
        'w_rg': nrm((L, D_MODEL, N_GROUPS), D_MODEL ** -0.5),
        'b_rg': nrm((L, N_GROUPS), 0.01),
        'w_re': nrm((L, D_MODEL, N_EXPERTS), D_MODEL ** -0.5),
        'b_re': nrm((L, N_EXPERTS), 0.01),
        'w_gate': nrm((L, N_EXPERTS, D_MODEL, D_EXPERT), D_MODEL ** -0.5),
        'w_up': nrm((L, N_EXPERTS, D_MODEL, D_EXPERT), D_MODEL ** -0.5),
        'w_down': nrm((L, N_EXPERTS, D_EXPERT, D_MODEL), D_EXPERT ** -0.5),
        'g_final': gain((D_MODEL,)),
    }

def second_block(x, mem, g_mix, w_in, g_q, g_k, w_att_out, sgu_ln_g, sgu_ln_b, w_s, b_s,
              w_sgu_out, w_out, g_cross, g_mem, w_cq, w_ckv, w_co, g_moe, w_rg, b_rg,
              w_re, b_re, w_gate, w_up, w_down, g_final):
    B, S, _ = x.shape
    cos, sin = axial_rope_tables(S)
    splits = [ATT_WIDTH,
              ATT_WIDTH + KV_WIDTH,
              ATT_WIDTH + 2 * KV_WIDTH,
              ATT_WIDTH + 2 * KV_WIDTH + SGU_WIDTH,
              ATT_WIDTH + 2 * KV_WIDTH + 2 * SGU_WIDTH,
              ATT_WIDTH + 2 * KV_WIDTH + 2 * SGU_WIDTH + D_MODEL]
    for l in range(DEPTH_2):
        h = rms_norm_2(x, g_mix[l])
        z = h @ w_in[l]
        q, k, v, su, sv, ga, gb = jnp.split(z, splits, axis=-1)
        q = rms_norm_2(q.reshape(B, S, ATT_HEADS, ATT_HEAD_DIM), g_q[l])
        k = rms_norm_2(k.reshape(B, S, ATT_KV_HEADS, ATT_HEAD_DIM), g_k[l])
        q = apply_rope(q, cos, sin)
        k = apply_rope(k, cos, sin)
        v = v.reshape(B, S, ATT_KV_HEADS, ATT_HEAD_DIM)
        y_att = gqa_attention(q, k, v) @ w_att_out[l]
        y_sgu = spatial_gating(jax.nn.gelu(su), jax.nn.gelu(sv), w_s[l], b_s[l],
                               sgu_ln_g[l], sgu_ln_b[l]) @ w_sgu_out[l]
        merged = jax.nn.sigmoid(ga) * y_att + jax.nn.sigmoid(gb) * y_sgu
        x = x + merged @ w_out[l]
        x = x + memory_cross_attention(rms_norm_2(x, g_cross[l]), rms_norm_2(mem, g_mem[l]),
                                       w_cq[l], w_ckv[l], w_co[l])
        x = x + hierarchical_moe(rms_norm_2(x, g_moe[l]), w_rg[l], b_rg[l], w_re[l], b_re[l],
                                 w_gate[l], w_up[l], w_down[l])
    return rms_norm_2(x, g_final)


def setup_inputs(seed=0):
    out = dict(first_inputs(seed))
    for name, value in second_inputs(seed + 1).items():
        if name != "x":
            out[name + "_2"] = value
    return out


def reference(
    x, p, ev_w_in, ev_w_out, da_lambda, da_subln_g, hg_lb_logits, hg_norm_g, od_w_in, od_w_out,
    ln1_g, ln1_b, ffn_w1, ffn_w2, ln2_g, ln2_b, ple_w_proj, ple_w_gate, ple_norm_g, mem_2,
    g_mix_2, w_in_2, g_q_2, g_k_2, w_att_out_2, sgu_ln_g_2, sgu_ln_b_2, w_s_2, b_s_2,
    w_sgu_out_2, w_out_2, g_cross_2, g_mem_2, w_cq_2, w_ckv_2, w_co_2, g_moe_2, w_rg_2, b_rg_2,
    w_re_2, b_re_2, w_gate_2, w_up_2, w_down_2, g_final_2,
):
    x = first_block(
        x, p, ev_w_in, ev_w_out, da_lambda, da_subln_g, hg_lb_logits, hg_norm_g, od_w_in,
        od_w_out, ln1_g, ln1_b, ffn_w1, ffn_w2, ln2_g, ln2_b, ple_w_proj, ple_w_gate,
        ple_norm_g,
    )
    return second_block(
        x, mem_2, g_mix_2, w_in_2, g_q_2, g_k_2, w_att_out_2, sgu_ln_g_2, sgu_ln_b_2, w_s_2,
        b_s_2, w_sgu_out_2, w_out_2, g_cross_2, g_mem_2, w_cq_2, w_ckv_2, w_co_2, g_moe_2,
        w_rg_2, b_rg_2, w_re_2, b_re_2, w_gate_2, w_up_2, w_down_2, g_final_2,
    )


_drawn_inputs = setup_inputs


def setup_inputs(seed=0):
    import zlib

    import numpy as np

    out = dict(_drawn_inputs(seed))
    spreads = {}
    factors = {'da_lambda': 7.727,
     'da_subln_g': 7.756,
     'hg_lb_logits': 8.0,
     'hg_norm_g': 7.515,
     'ple_norm_g': 3.038,
     'g_q_2': 8.0,
     'g_k_2': 5.934,
     'sgu_ln_b_2': 5.336,
     'g_cross_2': 3.749,
     'g_mem_2': 2.675,
     'b_rg_2': 35.388,
     'b_re_2': 39.403}
    for name, (base, spread) in spreads.items():
        noise = np.random.default_rng([zlib.crc32(name.encode()), seed]).standard_normal(out[name].shape)
        drawn = base * np.exp(spread * noise) if base else spread * noise
        out[name] = __import__('jax').numpy.asarray(drawn.astype(out[name].dtype))
    for name, factor in factors.items():
        out[name] = (out[name] * factor).astype(out[name].dtype)
    return out
```

```python
import numpy as np
import concourse.bass as bass
from concourse import mybir
from contextlib import ExitStack


class Tok:
    __slots__ = ("sem", "val", "t")

    def __init__(self, sem, val, t):
        self.sem, self.val, self.t = sem, val, t


class Fut:
    __slots__ = ("v",)

    def __init__(self):
        self.v = None

    def set(self, v):
        self.v = v


class AllOf:

    def __init__(self, fs):
        self.fs = fs

    @property
    def v(self):
        if any(f.v is None for f in self.fs):
            return None
        return tuple(t for f in self.fs for t in f.v)


class Pool:

    def __init__(self, items):
        self.free = [(it, ()) for it in items]

    def put(self, item, *toks):
        self.free.append((item, toks))

    def pick(self):
        best = min(range(len(self.free)), key=lambda i: (max([t.t for t in self.free[i][1]], default=0.0), i))
        return self.free.pop(best)


class Op:
    __slots__ = ("eng", "cost", "fn", "waits", "inc", "sem", "nbytes")

    def __init__(self, eng, cost, fn, waits, inc=1, sem=None, nbytes=0):
        self.eng, self.cost, self.fn, self.waits, self.inc, self.sem, self.nbytes = eng, cost, fn, waits, inc, sem, nbytes


class Queue:
    def __init__(self, name):
        self.name, self.items, self.n, self.t, self.seen = name, [], 0, 0.0, {}


class Thread:
    __slots__ = ("gen", "prio", "req", "name")


class Board:

    LAT = 70.0

    def __init__(self, mark=""):
        self.q = {n: Queue(n + mark) for n in ("T", "A", "V", "G", "S")}
        self.threads = []
        self.dma_t = 0.0
        self.dsem = {}

    def spawn(self, gen, prio=5, name=""):
        th = Thread()
        th.gen, th.prio, th.req, th.name = gen, prio, None, name
        self.threads.append(th)
        self.step(th, None)

    def step(self, th, value):
        try:
            th.req = th.gen.send(value)
        except StopIteration:
            self.threads.remove(th)

    def start(self, op):
        q = self.q[op.eng]
        t = q.t
        for w in op.waits:
            if w.t > t:
                t = w.t
        return t

    def emit(self, op):
        q = self.q[op.eng]
        t = self.start(op)
        waits = []
        for w in op.waits:
            if q.seen.get(w.sem, 0) < w.val:
                q.seen[w.sem] = w.val
                waits.append((w.sem, w.val))
        if op.sem is not None:
            v = self.dsem.get(op.sem, 0) + 16
            self.dsem[op.sem] = v
            q.items.append((waits, op.fn, op.sem, 16))
            self.dma_t = max(self.dma_t, t) + op.nbytes / 380.0
            q.t = t + 60.0
            return Tok(op.sem, v, self.dma_t + 2000.0)
        q.t = t + op.cost
        if op.inc:
            q.n += 1
            q.items.append((waits, op.fn, q.name, 1))
            return Tok(q.name, q.n, q.t + self.LAT)
        q.items.append((waits, op.fn, None, 0))
        return Tok(q.name, q.n + 1, q.t + self.LAT)

    def run(self):
        while self.threads:
            moved = True
            while moved:
                moved = False
                for th in sorted(self.threads, key=lambda h: h.prio):
                    r = th.req
                    if isinstance(r, (Fut, AllOf)):
                        if r.v is not None:
                            self.step(th, r.v)
                            moved = True
                    elif isinstance(r, Pool):
                        if r.free:
                            self.step(th, r.pick())
                            moved = True
                    elif callable(r):
                        if r():
                            self.step(th, None)
                            moved = True
            best, key = None, None
            for th in self.threads:
                if isinstance(th.req, Op):
                    k = (self.start(th.req) + 20.0 * th.prio, th.prio)
                    if best is None or k < key:
                        best, key = th, k
            if best is None:
                if self.threads:
                    raise RuntimeError("stuck: " + ", ".join(t.name for t in self.threads))
                return
            self.step(best, self.emit(best.req))


F32, F32R, U32, I32 = mybir.dt.float32, mybir.dt.float32r, mybir.dt.uint32, mybir.dt.int32
ALU, AF, AX = mybir.AluOpType, mybir.ActivationFunctionType, mybir.AxisListType
BIG = 1.0e30


def constants():
    c = {}
    c["ident"] = np.eye(128, dtype=np.float32)
    d = np.arange(128)[:, None] - np.arange(128)[None, :]
    causal = np.where(d >= 0, 0.0, -BIG).astype(np.float32)
    m0 = np.zeros((128, 512), np.float32)
    m0[:, 384:] = causal
    c["mask0"] = m0

    def mult(dist):
        n = ((dist >= 0) & (dist <= 128)).astype(np.float64) + ((dist >= 0) & (dist % 4 == 0)) \
            + ((dist >= 0) & (dist % 16 == 0))
        return np.where(n > 0, 8.0 * np.log(np.maximum(n, 1.0)), -BIG).astype(np.float32)

    c["mask1"] = np.concatenate([mult(d + 384), mult(d + 256), mult(d + 128), mult(d)], axis=1)
    h = np.arange(128) // 64
    c["tri"] = ((d <= 0) & (h[:, None] == h[None, :])).astype(np.uint32)
    reset = np.ones((128, 512), np.float32)
    reset[:, ::64] = 0.0
    c["reset"] = reset
    inv = (np.float32(500000.0) ** (-np.arange(0, 16, 2, dtype=np.float32) / np.float32(16))).astype(np.float32)
    ang = (np.arange(512, dtype=np.float32)[:, None] * inv[None, :]).astype(np.float32)
    cs, sn = np.cos(ang).astype(np.float32), np.sin(ang).astype(np.float32)
    c["rope"] = np.concatenate([cs, cs, -sn, sn], axis=1).reshape(4, 128, 32).transpose(1, 0, 2).copy()
    inv = (np.float32(10000.0) ** (-np.arange(16, dtype=np.float32) / np.float32(16))).astype(np.float32)
    ang = np.concatenate([np.repeat(np.arange(8), 64)[:, None].astype(np.float32) * inv,
                          np.tile(np.arange(64), 8)[:, None].astype(np.float32) * inv], axis=1).astype(np.float32)
    cs, sn = np.cos(ang).astype(np.float32), np.sin(ang).astype(np.float32)
    ax = np.stack([np.repeat(cs, 2, axis=1), np.stack([-sn, sn], axis=2).reshape(512, 64)], axis=1)
    p = np.arange(128)
    route = np.zeros((128, 428), np.float32)
    route[:, 0:16] = np.arange(16)
    route[:, 16:20] = 128 * np.arange(4)[None, :] + p[:, None]
    route[:, 20:148] = (np.arange(128) % 8 != 0)
    route[:, 148:164] = 1.0
    route[:, 164:172] = np.arange(8)
    route[:, 172:300] = (p[:, None] < p[None, :])
    route[:, 300:428] = 1.0
    c["route"] = route
    c["axial"] = ax.reshape(4, 128, 128).transpose(1, 0, 2).copy()
    return c


def build(nc, A, out):
    ctx = ExitStack()
    KB = 1024
    BASE = 16512
    ALPHA = float(np.float32(4.0 ** 0.25))

    def at(name, off, shape, dt):
        return nc.alloc_sbuf_tensor_at(name, shape, dt, offset=BASE + int(off * KB))

    X = at("X", 0, [128, 4, 1024], F32)
    XH = at("XH", 16, [128, 8, 512], F32R)
    XL = at("XL", 32, [128, 8, 512], F32R)
    WH = at("WH", 48, [128, 8, 1024], F32R)
    WL = at("WL", 80, [128, 8, 1024], F32R)
    RAW = [at(f"RAW{i}", 112 + 4 * i, [128, 1024], F32) for i in range(3)]
    ST = [at(f"ST{i}", 124 + 4 * i, [128, 1024], F32) for i in range(2)]
    C0 = 132
    ident = at("ident", C0, [128, 128], F32)
    MASK = at("MASK", C0 + 0.5, [128, 512], F32)
    TRI = at("TRI", C0 + 2.5, [128, 128], U32)
    ROPE = at("ROPE", C0 + 3, [128, 4, 32], F32)
    GDA = at("GDA", C0 + 3.5, [128, 128], F32)
    GHG = at("GHG", C0 + 4, [128, 128], F32)
    SM = at("SM", C0 + 4.5, [128, 256], F32)
    ropes = [at(f"RT{i}", C0 + 5.5 + i, [128, 2, 8, 16], F32) for i in range(1)]
    D0 = 138.5

    CW = at("CW", D0 + 68, [128, 8], F32)
    SLOT = at("SLOT", D0 + 68.03125, [128, 8], U32)
    IDX = at("IDX", D0 + 68.0625, [128, 24], U32)
    OVF = at("OVF", D0 + 68.1875, [128, 8], I32)
    RAW += [at(f"RAW{i + 3}", D0 + 44 + 4 * i, [128, 1024], F32) for i in range(3)]

    def small(a, n):
        return SM[:, a:a + n]

    half = small(0, 4)
    half8 = small(40, 8)
    lam = small(4, 4)
    vecT = small(8, 16)
    lbs = small(24, 16)
    stats = [small(48 + 16 * i, 16) for i in range(13)]

    dram = lambda name, shape: nc.dram_tensor(name, shape, F32).ap()
    QKD = [dram(f"qkd{g}", [4, 128, 1024]) for g in range(6)]
    ED = [dram(f"ed{l}", [4, 128, 1024]) for l in range(2)]
    VD = dram("vd", [4, 128, 512])
    QQD = dram("qqd", [4, 128, 1024])
    KTD, MVD = dram("ktd", [4, 128, 256]), dram("mvd", [2, 128, 512])
    HD, YD, TAB = dram("hd", [512, 1024]), dram("yd", [23 * 128, 1024]), dram("tab", [23 * 128, 1])
    TGD = dram("tgd", [2, 8, 128, 512])

    ps = [ctx.enter_context(nc.psum_tensor(f"ps{i}", [128, 512], F32)) for i in range(8)]
    sems = {n: ctx.enter_context(nc.semaphore("s_" + n)) for n in ("T", "A", "V", "G", "T2", "A2", "V2", "G2")}
    RS = []
    for i in range(12):
        RS.append(f"raw{i}")
    DS = [f"d{i}" for i in range(16)]
    RS2, DS2 = [f"rawb{i}" for i in range(12)], [f"e{i}" for i in range(4)]
    IS, IS2 = [f"i{i}" for i in range(8)], [f"j{i}" for i in range(2)]
    for n in RS + DS + RS2 + DS2 + IS + IS2:
        sems[n] = ctx.enter_context(nc.semaphore("s_" + n))

    def mm(o, l, r, st, sp, cost, *w, inc=None):
        return Op("T", cost, lambda e: e.matmul(o, lhsT=l, rhs=r, start=st, stop=sp), w, sp if inc is None else inc)

    def tr(o, i, *w, inc=False):
        return Op("T", 110.0, lambda e: e.transpose(o, i, ident[:, :]), w, inc)

    def act(o, i, f, n, *w, bias=None, scale=1.0, acc=None):
        k = {}
        if bias is not None:
            k["bias"] = bias
        if acc is not None:
            k["accum_out"] = acc
        return Op("A", 0.83 * n + 90.0 + (90.0 if bias is not None else 0.0) + (220.0 if acc is not None else 0.0),
                  lambda e: e.activation(o, i, f, scale=scale, **k), w)

    def tt(o, a, b, op, n, *w):
        return Op("V", 1.04 * n + 68.0, lambda e: e.tensor_tensor(o, a, b, op), w)

    def cp(o, i, n, *w):
        return Op("V", 1.04 * n + 68.0, lambda e: e.tensor_copy(o, i), w)

    def ts(o, i, s1, s2, op0, op1, n, *w):
        if op1 is None:
            return Op("V", 0.52 * n + 130.0, lambda e: e.tensor_scalar(o, i, s1, None, op0), w)
        return Op("V", 0.52 * n + 130.0, lambda e: e.tensor_scalar(o, i, s1, s2, op0, op1), w)

    def stt(o, a, s, b, op0, op1, n, *w):
        return Op("V", 1.04 * n + 130.0,
                  lambda e: e.scalar_tensor_tensor(out=o, in0=a, scalar=s, in1=b, op0=op0, op1=op1), w)

    def vop(fn, n, *w):
        return Op("V", 1.04 * n + 68.0, fn, w)

    def gop(fn, n, *w):
        return Op("G", 3.0 * n + 100.0, fn, w)

    def dma(o, i, nbytes, sem, *w):
        return Op("S", 60.0, lambda e: e.dma_start(o, i() if callable(i) else i), w, 1, sem, nbytes)

    def play(bd):
        blk = ctx.enter_context(nc.Block())

        def steps(e, items):
            for waits, fn, sem, inc in items:
                for s, v in waits:
                    e.wait_ge(sems[s], v)
                if fn is not None:
                    i = fn(e)
                    if sem is not None:
                        i.then_inc(sems[sem], inc)

        def run(name):
            def body(e):
                first, extra, rest = bd.parts[name]
                steps(e, first)
                if extra:
                    n = e.value_load(OVF[0:1, 0:1], min_val=0, max_val=7)
                    for j, items in enumerate(extra):
                        with e.If(n > j):
                            steps(e, items)
                steps(e, rest)
            return body

        blk.sync(run("S"))
        blk.tensor(run("T"))
        blk.scalar(run("A"))
        blk.vector(run("V"))
        blk.gpsimd(run("G"))

    order = []

    def view(ap, kind):
        if kind == "A":
            return ap.rearrange("p (a c) -> p a c", a=4)
        if kind == "B":
            return ap.rearrange("p (a c) -> p a c", a=2)
        return ap.rearrange("p (a s c) -> p a s c", a=2, s=2)

    alloc = {}

    def at_(name, off, shape, dt=F32):
        key = (name, off)
        if key not in alloc:
            alloc[key] = at(name, D0 + off, shape, dt)
        return alloc[key]

    def emission(record):
        bd = Board()
        spawn = bd.spawn
        G, S, TP, OP = Pool(ps[0:3]), Pool(ps[3:5]), Pool(ps[5:7]), Pool(ps[7:8])
        STG = Pool(ST)
        DQ = Pool(DS)
        IQ = Pool(IS)
        SP = Pool(stats)
        SP2 = SP
        RP = Pool(ropes)
        g = {}

        def load(o, i, nbytes, *w):
            sem, toks = yield DQ
            tok = yield dma(o, i, nbytes, sem, *toks, *w)
            DQ.put(sem, tok)
            return tok

        class Stream:
            def __init__(self, board, order_, raw, names, rel0, record_):
                self.board, self.order, self.raw, self.names, self.rel0 = board, order_, raw, names, rel0
                self.record, self.cursor, self.over = record_, 0, False
                self.loaded, self.hi, self.lo, self.rel = {}, {}, {}, {}

            def fut(self, d, k):
                if k not in d:
                    d[k] = Fut()
                return d[k]

            def go(self, c0, c1):
                self.board.spawn(self.loader(c0, c1), 0, "loader")
                self.board.spawn(self.parts("hi", c0, c1), 3, "hi")
                self.board.spawn(self.parts("lo", c0, c1), 3, "lo")

            def loader(self, c, end):
                while c < end:
                    yield lambda: len(self.order) > c or self.over
                    if c >= len(self.order):
                        return
                    slot, toks = yield self.raw
                    src, kind = self.order[c]
                    dst = view(RAW[slot][:, :], kind)
                    if kind == "Q":
                        tok = []
                        for j in range(2):
                            tok.append((yield dma(dst[:, :, j, :], src[:, :, j, :], 262144, self.names[2 * slot + j],
                                                  *toks)))
                        tok = tuple(tok)
                    else:
                        tok = ((yield dma(dst, src, 524288, self.names[2 * slot], *toks)),)
                    self.fut(self.loaded, c).set((slot, tok))
                    c += 1

            def parts(self, which, c, end):
                while c < end:
                    yield lambda: c in self.loaded or (self.over and c >= len(self.order))
                    if c not in self.loaded:
                        return
                    slot, tok = yield self.loaded[c]
                    free = (yield self.fut(self.rel, c - 8)) if c >= 8 else self.rel0(c)
                    w = (*tok, *free)
                    x, h, l = RAW[slot][:, :], WH[:, c % 8, :], WL[:, c % 8, :]
                    if which == "hi":
                        t = yield act(h, x, AF.Copy, 1024, *w)
                        self.fut(self.hi, c).set(t)
                    else:
                        th = yield self.fut(self.hi, c)
                        t = yield tt(l, x, h.bitcast(F32), ALU.subtract, 1024, *w, th)
                        self.fut(self.lo, c).set(t)
                        self.raw.put(slot, th, t)
                    c += 1

            def use(self, src, kind):
                c = self.cursor
                self.cursor += 1
                if self.record:
                    self.order.append((src, kind))
                th = yield self.fut(self.hi, c)
                tl = yield self.fut(self.lo, c)
                k = "B" if kind == "Q" else kind
                return c, view(WH[:, c % 8, :], k), view(WL[:, c % 8, :], k), (th, tl)

        raw = Pool([0, 1, 2])
        strm = Stream(bd, order, raw, RS, lambda c: (), record)

        def xh(k):
            return XH[:, k, :]

        def xl(k):
            return XL[:, k, :]

        def rows(buf, k0=0):
            return lambda k: buf[:, k + k0, :]

        def wA(w, k, n):
            return w[k * 128:(k + 4) * 128, n:n + 256].rearrange("(a p) c -> p a c", p=128), "A"

        def wB(w, k, n):
            return w[k * 128:(k + 2) * 128, n:n + 512].rearrange("(a p) c -> p a c", p=128), "B"

        def wQ(w, k, q0, k0):
            a = w[k * 128:(k + 2) * 128, :].rearrange("(a p) c -> p a c", p=128)
            n = k0 - q0
            return a[:, :, q0:q0 + 2 * n].rearrange("p a (s c) -> p a s c", s=2)[:, :, :, 0:256], "Q"

        def gemmA(w, n0, n1, K, H, L, ready, evac, N=512):
            cost = 216 if N == 512 else 110
            for n in range(n0, n1, 256):
                got = []
                for nt in range(2):
                    bank, free = yield G
                    for k in range(K):
                        if k // 4 == len(got):
                            got.append((yield from strm.use(*wA(w, k, n))))
                        c, wh, wl, tw = got[k // 4]
                        x = yield ready(k, None)
                        h = wh[:, k % 4, nt * 128:nt * 128 + 128]
                        l = wl[:, k % 4, nt * 128:nt * 128 + 128]
                        last = k == K - 1
                        drop = nt == 1 and (k % 4 == 3 or last)
                        o = bank[:, 0:N]
                        yield mm(o, h, H(k), k == 0, False, cost, *tw, *x, *free)
                        yield mm(o, h, L(k), False, False, cost)
                        t = yield mm(o, l, H(k), False, last, cost, inc=last or drop)
                        if drop:
                            strm.fut(strm.rel, c).set((t,))
                        g["last"] = t
                    spawn(evac((n - n0) // 128 + nt, bank, t), 2, "evacA")

        def gemmB(src, halves, K, H, L, ready, evac, TN=4, N=512, strm=strm, spawn=spawn):
            kc = 1024 // N
            cost = 216 if N == 512 else 110
            for nh in range(halves):
                got = []
                for T in range(TN):
                    bank, free = yield G
                    for k in range(K):
                        if k // kc == len(got):
                            got.append((yield from strm.use(*src(nh, kc * (k // kc)))))
                        c, wh, wl, tw = got[k // kc]
                        x = yield ready(k, T)
                        h = H(k)[:, T * 128:T * 128 + 128]
                        l = L(k)[:, T * 128:T * 128 + 128]
                        last = k == K - 1
                        drop = T == TN - 1 and (k % kc == kc - 1 or last)
                        o, j = bank[:, 0:N], k % kc
                        yield mm(o, h, wh[:, j, :], k == 0, False, cost, *tw, *x, *free)
                        yield mm(o, h, wl[:, j, :], False, False, cost)
                        t = yield mm(o, l, wh[:, j, :], False, last, cost, inc=last or drop)
                        if drop:
                            strm.fut(strm.rel, c).set((t,))
                        g["last"] = t
                    spawn(evac(nh, T, bank, t), 2, "evacB")

        class Ready:

            def __init__(self, n=4):
                self.n = n
                self.f = {(k, T): Fut() for k in range(8) for T in range(n)}

            def __call__(self, k, T):
                return self.f[(k, T)] if T is not None else AllOf([self.f[(k, t)] for t in range(self.n)])

        def turn_T(nat, T, H, L, ready, k0, kn, *w):
            bank, free = yield TP
            for j in range(kn):
                t = yield tr(bank[:, j * 128:j * 128 + 128], nat[:, (k0 + j) * 128:(k0 + j + 1) * 128], *w, *free,
                             inc=j == kn - 1)
            b3 = bank[:, 0:kn * 128].rearrange("p (a c) -> p a c", a=kn)
            h = H[:, k0:k0 + kn, T * 128:T * 128 + 128]
            l = L[:, k0:k0 + kn, T * 128:T * 128 + 128]
            th = yield act(h, b3, AF.Copy, kn * 128, t)
            tl = yield tt(l, b3, h.bitcast(F32), ALU.subtract, kn * 128, t, th)
            TP.put(bank, tl)
            for j in range(kn):
                ready.f[(k0 + j, T)].set((th, tl))


        def start():
            g["ident"] = yield from load(ident[:, :], A["ident"], 65536)
            for T in range(4):
                g["x", T] = yield from load(X[:, T, :], A["x"][0, T * 128:(T + 1) * 128, :], 524288)
            t = yield gop(lambda e: e.memset(half, -0.5), 4)
            t = yield gop(lambda e: e.memset(half8, -0.5), 4)
            g["half"] = t

        def turns_x(ready, H, L, after):
            for T in range(4):
                for k0 in (0, 4):
                    spawn(turn_T(X[:, T, :], T, H, L, ready, k0, 4, g["ident"], *after(T)), 3, "turn_x")

        def ev_qk(g_, w=()):
            def ev(nh, T, bank, tok):
                slot, free = yield STG
                nd = slot[:, :].rearrange("p (h d c) -> p h d c", h=8, d=2)
                b3 = bank[:, :].rearrange("p (h c) -> p h c", h=8)
                t = yield act(nd, b3.unsqueeze(2).broadcast_to([128, 8, 2, 64]), AF.Copy, 1024, tok, *free)
                r, rf = yield RP
                m1, m2 = r[:, 0, :, :], r[:, 1, :, :]
                cc = ROPE[:, T, 0:16].unsqueeze(1).broadcast_to([128, 8, 16])
                ns = ROPE[:, T, 16:24].unsqueeze(1).broadcast_to([128, 8, 8])
                sn = ROPE[:, T, 24:32].unsqueeze(1).broadcast_to([128, 8, 8])
                t1 = yield tt(m1, b3[:, :, 0:16], cc, ALU.mult, 128, t, g["rope"], *rf)
                t2 = yield tt(m2[:, :, 0:8], b3[:, :, 8:16], ns, ALU.mult, 64, t, *rf)
                t3 = yield tt(m2[:, :, 8:16], b3[:, :, 0:8], sn, ALU.mult, 64, t)
                G.put(bank, t3)
                t4 = yield tt(nd[:, :, :, 0:16], m1.unsqueeze(2).broadcast_to([128, 8, 2, 16]),
                              m2.unsqueeze(2).broadcast_to([128, 8, 2, 16]), ALU.add, 256, t1, t3)
                RP.put(r, t4)
                t = yield from load(QKD[g_][T], slot[:, :], 524288, t4)
                STG.put(slot, t)
                qkd[(g_, T)].set((t,))
            return ev

        qkd = {}

        def stacks(base, P, stk, free, ndp, done, *w):
            for T in range(4):
                (d,) = yield qkd[(base + P // 2, T)]
                nd, nf = yield ndp
                o = 256 * (P % 2)
                src = QKD[base + P // 2][T].rearrange("p (s f) -> p s f", s=2)[:, :, o:o + 256]
                t = yield from load(nd[:, :].rearrange("p (s f) -> p s f", s=2), src, 262144, d, *nf, *w)
                spawn(stack_T(stk, free, ndp, nd, T, t, done[T]), 4, f"stk{P}.{T}")

        def stack_T(stk, free, ndp, nd, T, t, done):
            bank, bf = yield TP
            for j in range(4):
                u = yield tr(bank[:, j * 128:j * 128 + 128], nd[:, j * 128:j * 128 + 128], t, *bf, inc=j == 3)
            ndp.put(nd, u)
            c = slice(T * 128, T * 128 + 128)
            b3 = bank[:, :].rearrange("p (a c) -> p a c", a=4)
            th = yield act(stk[:, 0:4, c], b3, AF.Copy, 512, u, *free)
            t1 = yield tt(stk[:, 4:6, c], b3[:, 0:2, :], stk[:, 0:2, c].bitcast(F32), ALU.subtract, 256, th)
            k = stk[64:128, 2:4, c]
            t2 = yield tt(k, b3[64:128, 2:4, :], k.bitcast(F32), ALU.subtract, 256, th)
            TP.put(bank, t2)
            done.set((th, t1, t2))

        def soft_row(s, n, mask, scale, e, t, ef):
            v, vf = yield SP
            tm = yield vop(lambda x: x.tensor_tensor_reduce(e[:, 0:n], s[:, 0:n], mask[:, 512 - n:512], -scale, 3.0e38,
                                                            ALU.add, ALU.min, v[:, 0:1]), n, t, *ef, *vf)
            S.put(s, tm)
            te = yield act(e[:, 0:n], e[:, 0:n], AF.Exp, n, tm, bias=v[:, 0:1], scale=-1.0, acc=v[:, 1:2])
            tr_ = yield vop(lambda x: x.reciprocal(v[:, 2:3], v[:, 1:2]), 8, te)
            return v, te, tr_

        def scores(stk, hh, i, mask, e, ef, rdy):
            n = 128 * (i + 1)
            w = []
            for T in range(i + 1):
                w += list((yield rdy[T]))
            s, sf = yield S
            c = 110 if n < 512 else 216
            q = slice(128 * i, 128 * i + 128)
            yield mm(s[:, 0:n], stk[:, hh, q], stk[:, 2 + hh, 0:n], True, False, c, *w, *sf)
            t = yield mm(s[:, 0:n], stk[:, 4 + hh, q], stk[:, 2 + hh, 0:n], False, True, c)
            return (yield from soft_row(s, n, mask, 0.125, e, t, ef))

        def turn_P(e, n, pt, pf, *w):
            bank, bf = yield TP
            for j in range(n // 128):
                t = yield tr(bank[:, j * 128:j * 128 + 128], e[:, j * 128:j * 128 + 128], *w, *bf,
                             inc=j == n // 128 - 1)
            u = yield act(pt[:, 0:n], bank[:, 0:n], AF.Copy, n, t, *pf)
            TP.put(bank, u)
            return t, u

        def add_x(scale, xtok, then=None, mul=None):
            def ev(nh, T, bank, tok):
                x = X[:, T, nh * 512:nh * 512 + 512]
                w = yield xtok[(T, nh)]
                if mul is not None:
                    t = yield stt(x, bank[:, :], mul, x, ALU.mult, ALU.add, 512, tok, *w)
                elif scale == 1.0:
                    t = yield tt(x, x, bank[:, :], ALU.add, 512, tok, *w)
                else:
                    t = yield stt(x, x, scale, bank[:, :], ALU.mult, ALU.add, 512, tok, *w)
                G.put(bank, t)
                then[(T, nh)].set((t,))
            return ev

        def gather(fs):
            r = []
            for f in fs:
                r += list((yield f))
            return tuple(r)

        def xfuts():
            return {(T, nh): Fut() for T in range(4) for nh in range(2)}

        def gains(names, bufs, *w):
            out_ = []
            for a, b in zip(names, bufs):
                t = yield from load(b, a.broadcast_to([128, 1024]), 524288, *w)
                out_.append(t)
            return tuple(out_)

        def norm_ln(T, xt, gb, G1, B1, ready, out_x):
            a = yield xt[(T, 0)]
            v, vf = yield SP
            x0, x1 = X[:, T, 0:512], X[:, T, 512:1024]
            t0 = yield vop(lambda e: e.bn_stats(v[:, 0:6], x0), 512, *a, *vf)
            b = yield xt[(T, 1)]
            t1 = yield vop(lambda e: e.bn_stats(v[:, 6:12], x1), 512, *b, *vf)
            t = yield vop(lambda e: e.bn_aggr(v[:, 12:14], v[:, 0:12].rearrange("p (a b) -> p a b", a=2)), 12, t0, t1)
            t2 = yield gop(lambda e: e.tensor_scalar(v[:, 14:15], v[:, 13:14], 1e-5, None, ALU.add), 1, t)
            t2 = yield gop(lambda e: e.tensor_tensor(v[:, 15:16], v[:, 14:15], half[:, 0:1], ALU.pow), 1, t2, g["half"])
            gt = yield gb
            ok = []
            for h in range(2):
                x = (x0, x1)[h]
                c = slice(h * 512, h * 512 + 512)
                u = yield stt(x, x, v[:, 12:13], G1[:, c], ALU.subtract, ALU.mult, 512, t, *gt)
                u = yield stt(x, x, v[:, 15:16], B1[:, c], ALU.mult, ALU.add, 512, u, t2)
                ok.append(u)
                out_x[(T, h)].set((u,))
                spawn(turn_T(X[:, T, :], T, XH, XL, ready, 4 * h, 4, u), 2, "turn_ln")
            SP.put(v, *ok)

        def ple(l, base):
            pn = at_(f"pn{l}", base, [128, 4, 256])
            ph, pl = at_(f"ph{l}", base + 4, [128, 2, 512], F32R), at_(f"pl{l}", base + 8, [128, 2, 512], F32R)
            pg = at_(f"pg{l}", 40 + 4 * l, [128, 1024])
            rd = Ready()

            def prep():
                t = yield from load(pn[:, :, :], A["p"][l, 0].rearrange("(a p) c -> p a c", p=128), 524288)
                for T in range(4):
                    spawn(turn_T(pn[:, T, :], T, ph, pl, rd, 0, 2, t, g["ident"]), 3, "turn_p")
                g["pg", l] = yield from load(pg[:, :], A["ple_norm_g"][l:l + 1].broadcast_to([128, 1024]), 524288)

            spawn(prep(), 0, "ple_prep")
            tiles = {}

            def ev(nh, T, bank, tok):
                if nh == 0:
                    tiles[T] = yield ETP
                e, free = tiles[T]
                t = yield act(e[:, nh * 512:nh * 512 + 512], bank[:, :], AF.Copy, 512, tok, *free)
                G.put(bank, t)
                tiles[T] = (e, (t,))
                if nh == 0:
                    return
                v, vf = yield SP
                j, jf = yield STG
                t = yield vop(lambda x: x.tensor_tensor_reduce(j[:, :], e[:, :], e[:, :], 1.0, 0.0, ALU.mult, ALU.add,
                                                               v[:, 0:1]), 1024, t, *vf, *jf)
                STG.put(j, t)
                t = yield gop(lambda x: x.tensor_scalar(v[:, 1:2], v[:, 0:1], 1.0 / 1024, 1e-5, ALU.mult, ALU.add), 1, t)
                t = yield gop(lambda x: x.tensor_tensor(v[:, 2:3], v[:, 1:2], half[:, 0:1], ALU.pow), 1, t, g["half"])
                t = yield stt(e[:, :], e[:, :], v[:, 2:3], pg[:, :], ALU.mult, ALU.mult, 1024, t, g["pg", l])
                SP.put(v, t)
                t = yield from load(ED[l][T], e[:, :], 524288, t)
                ETP.put(e, t)
                ed[(l, T)].set((t,))

            yield from gemmB(lambda nh, k: wB(A["ple_w_proj"][l], k, nh * 512), 2, 2, rows(ph), rows(pl), rd, ev)

        ed = {(l, T): Fut() for l in range(2) for T in range(4)}
        ETP = Pool([at_(f"et{i}", 24 + 4 * i, [128, 1024]) for i in range(4)])

        def ffn(l, xr_, x0, x2, x1_ln, gb_w):
            W1, W2 = A["ffn_w1"][l], A["ffn_w2"][l]
            HH, HL = at_("HH", 0, [128, 10, 512], F32R), at_("HL", 20, [128, 10, 512], F32R)
            R = Pool([at_(f"FR{i}", 40 + 2 * i, [128, 512]) for i in range(2)])
            G1, B1 = at_("G2", 44, [128, 1024]), at_("B2", 48, [128, 1024])
            hr = {j: Fut() for j in range(32)}
            hrel = {}
            gb = Fut()

            def ld():
                r = yield from gains((A["ln2_g"][l:l + 1], A["ln2_b"][l:l + 1]), (G1[:, :], B1[:, :]), *gb_w)
                gb.set(r)

            spawn(ld(), 6, "ld2")

            def ev_h(j0):
                def ev(n, bank, tok):
                    j = j0 + n
                    r, rf = yield R
                    w = hrel.get(j - 10, ())
                    t = yield act(r[:, :], bank[:, :], AF.Relu, 512, tok, *rf, *gb_w)
                    G.put(bank, t)
                    t = yield tt(r[:, :], r[:, :], r[:, :], ALU.mult, 512, t)
                    th = yield act(HH[:, j % 10, :], r[:, :], AF.Copy, 512, t, *w)
                    tl = yield tt(HL[:, j % 10, :], r[:, :], HH[:, j % 10, :].bitcast(F32), ALU.subtract, 512, th, *w)
                    R.put(r, th, tl)
                    hr[j].set((th, tl))
                return ev

            rdy = Ready()
            for T in range(4):
                spawn(norm_ln(T, x2, gb, G1, B1, rdy, x1_ln), 2 + T, f"ln2.{T}")
            steps = [xfuts() for _ in range(3)] + [x2]
            cur = x0
            lo_ = 0
            for q in range(4):
                hi_ = min(8 * q + 10, 32)
                yield from gemmA(W1, lo_ * 128, hi_ * 128, 8, xh, xl, xr_, ev_h(lo_))
                lo_ = hi_
                yield from gemmB(lambda nh, k: wB(W2, 8 * q + k, nh * 512), 2, 8,
                                 lambda k: HH[:, (8 * q + k) % 10, :], lambda k: HL[:, (8 * q + k) % 10, :],
                                 lambda k, T: hr[8 * q + k], add_x(ALPHA if q == 0 else 1.0, cur, steps[q]))
                cur = steps[q]
                for k in range(8):
                    hrel[8 * q + k] = (g["last"],)
            return rdy

        def gate(l, rdy, x_in, x_out, zone):
            E_ = at_("EE", 52, [128, 4, 1024])
            R = Pool([at_(f"FR{i}", 40 + 2 * i, [128, 512]) for i in range(2)])
            er = {T: Fut() for T in range(4)}

            def ld():
                for T in range(4):
                    (d,) = yield ed[(l, T)]
                    t = yield from load(E_[:, T, :], ED[l][T], 524288, d, *zone)
                    er[T].set((t,))

            spawn(ld(), 6, "ld_e")

            def ev(nh, T, bank, tok):
                r, rf = yield R
                et = yield er[T]
                w = yield x_in[(T, nh)]
                x = X[:, T, nh * 512:nh * 512 + 512]
                t = yield act(r[:, :], bank[:, :], AF.Sigmoid, 512, tok, *rf, *zone)
                G.put(bank, t)
                t = yield tt(r[:, :], r[:, :], E_[:, T, nh * 512:nh * 512 + 512], ALU.mult, 512, t, *et)
                t = yield tt(x, x, r[:, :], ALU.add, 512, t, *w)
                R.put(r, t)
                x_out[(T, nh)].set((t,))

            yield from gemmB(lambda nh, k: wB(A["ple_w_gate"][l], k, nh * 512), 2, 8, xh, xl, rdy, ev)

        def after_first(l, xr1, x3, zone, pre):
            x4, x5, x6 = xfuts(), xfuts(), xfuts()
            rdy = yield from ffn(l, xr1, x3, x4, x5, zone)
            z = (yield from gather(x4.values())) + (g["last"],)
            zz = (yield from gather(x5.values()))
            nxt = pre(x6, z)
            yield from gate(l, rdy, x5, x6, z + zz)
            z2 = yield from gather(x6.values())
            return x6, z2 + z + zz, nxt

        def layer0(pre):
            W = A["ev_w_in"][0]
            xr = Ready()
            turns_x(xr, XH, XL, lambda T: (g["x", T],))
            yield from ple(0, 0)
            yield from ple(1, 12)
            pw = []
            for f in ed.values():
                pw += list((yield f))
            pw = tuple(pw) + (g["last"],)
            HI = at_("HI", 16, [128, 4, 512])
            GS = at_("GS", 24, [128, 4, 512])
            FS = at_("FS", 32, [128, 4, 512])
            QS = at_("QS", 40, [128, 4, 512])
            BUF = [at_(f"HB{i}", 48 + 2 * i, [128, 512]) for i in range(6)]
            AT = at_("AT", 60, [128, 512])
            KN = at_("KN", 62, [128, 512])
            STA = at_("STA", 64, [128, 7, 128])
            RESET = MASK
            ON = at_("ON", 0, [128, 4, 1024])
            quad, tmps = Pool([0]), Pool(BUF[4:6])
            small_pools = Pool([0])
            fs = [Fut() for _ in range(4)]
            qs = [Fut() for _ in range(4)]
            gs = [Fut() for _ in range(4)]
            his = [Fut() for _ in range(4)]
            onr = Ready()
            hg_done = []
            lb = Fut()

            def vectors():
                t1 = yield from load(BUF[5][0:8, 0:128], A["hg_lb_logits"].rearrange("a (h k) -> (a h) k", h=4), 4096,
                                     *pw)
                bank, free = yield TP
                t = yield mm(bank[:, 0:8], BUF[5][0:8, 0:128], ident[0:8, 0:8], True, True, 30, t1, g["ident"], *free)
                t = yield cp(vecT[:, 0:8], bank[:, 0:8], 8, t)
                TP.put(bank, t)
                tmps.put(BUF[5], t)
                m = lbs[:, 0:4]
                t = yield tt(m, vecT[:, 0:4], vecT[:, 4:8], ALU.max, 4, t)
                t = yield tt(vecT[:, 0:4], vecT[:, 0:4], m, ALU.subtract, 4, t)
                t = yield tt(vecT[:, 4:8], vecT[:, 4:8], m, ALU.subtract, 4, t)
                t = yield act(vecT[:, 0:8], vecT[:, 0:8], AF.Exp, 8, t)
                t = yield tt(m, vecT[:, 0:4], vecT[:, 4:8], ALU.add, 4, t)
                t = yield vop(lambda e: e.reciprocal(lbs[:, 0:4], lbs[:, 0:4]), 30, t)
                t = yield tt(lbs[:, 4:8], lbs[:, 0:4], vecT[:, 0:4], ALU.mult, 4, t)
                t = yield tt(lbs[:, 8:12], lbs[:, 0:4], vecT[:, 4:8], ALU.mult, 4, t)
                lb.set((t,))

            def lambdas():
                slot, free = yield STG
                L = slot[:, 0:256]
                src = A["da_lambda"].rearrange("o a b -> o (a b)")
                t = yield from load(L, src.broadcast_to([128, 256]), 131072, *free)
                tmp = slot[:, 256:320]
                t = yield vop(lambda e: e.tensor_tensor_reduce(tmp, L[:, 0:64], L[:, 64:128], 1.0, 0.0, ALU.mult,
                                                               ALU.add, lam[:, 0:1]), 64, t)
                t = yield vop(lambda e: e.tensor_tensor_reduce(tmp, L[:, 128:192], L[:, 192:256], 1.0, 0.0, ALU.mult,
                                                               ALU.add, lam[:, 1:2]), 64, t)
                STG.put(slot, t)
                t = yield act(lam[:, 0:2], lam[:, 0:2], AF.Exp, 2, t)
                t = yield tt(lam[:, 2:3], lam[:, 1:2], lam[:, 0:1], ALU.subtract, 1, t)
                t = yield ts(lam[:, 3:4], lam[:, 2:3], -0.2, None, ALU.add, None, 1, t)
                g["nlam"] = t

            def ev_hf(n, bank, tok):
                w = yield lb
                t = yield act(FS[:, n, :], bank[:, :], AF.Sigmoid, 512, tok, *pw)
                G.put(bank, t)
                t = yield ts(FS[:, n, :], FS[:, n, :], lbs[:, 8 + n:9 + n], lbs[:, 4 + n:5 + n], ALU.mult, ALU.add, 512,
                             t, *w)
                fs[n].set((t,))

            def ev_hq(n, bank, tok):
                tmp, free = yield tmps
                t = yield act(tmp[:, :], bank[:, :], AF.Sigmoid, 512, tok, *free, *pw)
                t = yield tt(QS[:, n, :], bank[:, :], tmp[:, :], ALU.mult, 512, t)
                G.put(bank, t)
                tmps.put(tmp, t)
                qs[n].set((t,))

            def ev_hg(nh, T, bank, tok):
                tmp, free = yield tmps
                t = yield act(tmp[:, :], bank[:, :], AF.Sigmoid, 512, tok, *free, *pw)
                g["hg", T] = t
                t = yield tt(GS[:, T, :], bank[:, :], tmp[:, :], ALU.mult, 512, t)
                G.put(bank, t)
                tmps.put(tmp, t)
                g3 = GS[:, T, :].rearrange("p (h v) -> p h v", h=4)
                t = yield tt(g3, g3, GHG[:, :].unsqueeze(1).broadcast_to([128, 4, 128]), ALU.mult, 512, t, g["ghg"])
                gs[T].set((t,))

            def ev_hi(nh, T, bank, tok):
                t = yield act(HI[:, T, :], bank[:, :], AF.Copy, 512, tok, *pw)
                G.put(bank, t)
                his[T].set((t,))

            def chunks(ap):
                return ap.rearrange("p (c t) -> p c t", c=8)

            def finish(bank, tok, gain, c0, done, tpool, *w):
                tmp, free = yield tpool
                sq = tmp[:, 0:512]
                t = yield act(sq, bank[:, :], AF.Square, 512, tok, *free)
                s, sf = yield SP
                t = yield vop(lambda e: e.tensor_reduce(s[:, 0:4], sq.rearrange("p (a v) -> p a v", a=4), AX.X,
                                                        ALU.add), 512, t, *sf)
                tpool.put(tmp, t)
                t = yield gop(lambda e: e.tensor_scalar(s[:, 4:8], s[:, 0:4], 1.0 / 128, 1e-5, ALU.mult, ALU.add), 4, t)
                t = yield gop(lambda e: e.tensor_tensor(s[:, 8:12], s[:, 4:8], half, ALU.pow), 4, t, g["half"])
                for T in range(4):
                    u = yield stt(ON[:, T, c0:c0 + 128], bank[:, T * 128:(T + 1) * 128], s[:, 8 + T:9 + T], gain(T),
                                  ALU.mult, ALU.mult, 128, t, *w)
                    onr.f[(c0 // 128, T)].set((u,))
                SP.put(s, u)
                OP.put(bank, u)
                done(u)

            def hgrn(h):
                w = yield fs[h]
                q = yield qs[h]
                gg = yield AllOf(gs)
                gg = gg + tuple(g["hg", T] for T in range(4))
                _, free = yield quad
                KK, T1, D1, D2 = BUF[0], BUF[1], BUF[2], BUF[3]
                F, Q = FS[:, h, :], QS[:, h, :]
                tk = yield ts(KK[:, :], F, -1.0, 1.0, ALU.mult, ALU.add, 512, *w, *free)
                t = yield act(F, F, AF.Ln, 512, tk, *gg)
                tb = yield vop(lambda e: e.tensor_tensor_scan(F, RESET[:, :], F, 0.0, ALU.mult, ALU.add),
                               512, t, g["reset"])
                b3 = chunks(F)
                t1 = yield tt(chunks(D1[:, :]), b3, b3[:, :, 31:32].broadcast_to([128, 8, 64]), ALU.subtract, 512, tb,
                              *free)
                t2 = yield tt(chunks(D2[:, :]), b3, b3[:, :, 63:64].broadcast_to([128, 8, 64]), ALU.subtract, 512, tb,
                              *free)
                te = yield act(T1[:, :], D1[:, :], AF.Exp, 512, t1, *free)
                tq = yield tt(T1[:, :], Q, T1[:, :], ALU.mult, 512, te, *q)
                te = yield act(D1[:, :], D1[:, :], AF.Exp, 512, te, scale=-1.0)
                ta = yield tt(D1[:, :], KK[:, :], D1[:, :], ALU.mult, 512, te, tk)
                te = yield act(D2[:, :], D2[:, :], AF.Exp, 512, t2, scale=-1.0)
                ts_ = yield tt(KK[:, :], KK[:, :], D2[:, :], ALU.mult, 512, te, ta)
                te = yield act(F, F, AF.Exp, 512, t2)
                to = yield tt(Q, Q, F, ALU.mult, 512, te, tq)
                _, pf = yield small_pools
                a, free = yield S
                for T in range(4):
                    c = slice(T * 128, T * 128 + 128)
                    t = yield mm(a[:, c], D1[:, c], T1[:, c], True, True, 219, tq, ta, *free, inc=T == 3)
                at3 = AT[:, :].rearrange("p (a c) -> p a c", a=4)
                tat = yield vop(lambda e: e.copy_predicated(at3, TRI[:, :].unsqueeze(1).broadcast_to([128, 4, 128]),
                                                            a[:, :].rearrange("p (a c) -> p a c", a=4)), 512, t,
                                g["tri"], g["at0"], *pf)
                S.put(a, tat)
                bank, free = yield TP
                for T in range(4):
                    c = slice(T * 128, T * 128 + 128)
                    t = yield tr(bank[:, c], KK[:, c], ts_, *free, inc=T == 3)
                tkn = yield act(KN[:, :], bank[:, :], AF.Copy, 512, t, *pf)
                TP.put(bank, tkn)
                quad.put(0, t)
                hv = yield AllOf(his)
                st = None
                ue, fe = yield S
                uo, fo = yield S
                for c in range(7):
                    p0, T = 64 * (c % 2), c // 2
                    u = (ue, uo)[c % 2][:, T * 128:T * 128 + 128]
                    t = yield mm(u, KN[p0:p0 + 64, T * 128:T * 128 + 128],
                                 HI[p0:p0 + 64, T, h * 128:h * 128 + 128], True, True, 219, tkn, *hv, *fe, *fo,
                                 inc=c >= 5)
                    both = (t,) if c == 5 else (*both, t) if c == 6 else ()
                for c in range(7):
                    u = (ue, uo)[c % 2][:, c // 2 * 128:c // 2 * 128 + 128]
                    if c == 0:
                        st = yield cp(STA[:, 0, :], u, 128, *both, *pf)
                    else:
                        st = yield stt(STA[:, c, :], STA[:, c - 1, :], F[:, c * 64 + 63:c * 64 + 64], u, ALU.mult,
                                       ALU.add, 128, st)
                S.put(ue, st)
                S.put(uo, st)
                o, free = yield OP
                for T in range(4):
                    for c in (2 * T, 2 * T + 1):
                        p0 = 64 * (c % 2)
                        r = o[p0:p0 + 64, T * 128:T * 128 + 128]
                        t = yield mm(r, AT[:, T * 128 + p0:T * 128 + p0 + 64], HI[:, T, h * 128:h * 128 + 128], True,
                                     c == 0, 135, tat, *free, inc=c == 0)
                        if c:
                            t = yield mm(r, Q[:, c * 64:c * 64 + 64], STA[:, c - 1, :], False, True, 135, to, st)
                small_pools.put(0, t)

                def done(u):
                    hg_done.append(u)
                    hg_done.append(t)
                    if len(hg_done) == 8:
                        hgf.set(tuple(hg_done))

                spawn(finish(o, t, lambda T: GS[:, T, h * 128:h * 128 + 128], 512 + h * 128, done, tmps, *gg), 4,
                      f"fin{h}")

            hgf = Fut()

            def loads():
                g["reset"] = yield from load(RESET[:, :], A["reset"], 262144)
                g["ghg"] = yield from load(GHG[:, :], A["hg_norm_g"].broadcast_to([128, 128]), 65536)
                g["tri"] = yield from load(TRI[:, :], A["tri"], 65536)
                g["at0"] = yield vop(lambda e: e.memset(AT[:, :], 0.0), 512, *pw)

            tmps.free.pop()
            spawn(loads(), 1, "loads")
            spawn(vectors(), 1, "vectors")
            for h in range(4):
                spawn(hgrn(h), 5 + h, f"hgrn{h}")
            yield from gemmA(W, 2048, 2560, 8, xh, xl, xr, ev_hf)
            yield from gemmA(W, 1536, 2048, 8, xh, xl, xr, ev_hq)
            yield from gemmB(lambda nh, k: wB(W, k, 3072), 1, 8, xh, xl, xr, ev_hg)
            yield from gemmB(lambda nh, k: wB(W, k, 2560), 1, 8, xh, xl, xr, ev_hi)

            V = at_("DV", 16, [128, 4, 512])
            STK = Pool([at_(f"STK{i}", 24 + 12 * i, [128, 6, 512], F32R) for i in range(2)])
            EP = Pool([at_(f"EP{i}", 48 + 4 * i, [128, 2, 512]) for i in range(2)])
            PT = Pool([at_(f"PT{i}", 56 + 2 * i, [128, 512]) for i in range(3)])
            NDP = Pool([at_(f"NDP{i}", 62 + 2 * i, [128, 512]) for i in range(3)])
            for g_ in range(2):
                for T in range(4):
                    qkd[(g_, T)] = Fut()
            vd = {T: Fut() for T in range(4)}
            vr = {T: Fut() for T in range(4)}

            def ev_va(nh, T, bank, tok):
                slot, free = yield STG
                t = yield act(slot[:, 0:512], bank[:, :], AF.Copy, 512, tok, *free)
                G.put(bank, t)
                t = yield from load(VD[T], slot[:, 0:512], 262144, t)
                STG.put(slot, t)
                vd[T].set((t,))

            def reload_v():
                w = yield hgf
                for T in range(4):
                    (d,) = yield vd[T]
                    t = yield from load(V[:, T, :], VD[T], 262144, d, *w)
                    vr[T].set((t,))

            soft = {}
            stk_done = {}

            def da_scores():
                w = yield hgf
                w += yield mk
                for P in range(4):
                    stk, free = yield STK
                    rdy = [Fut() for _ in range(4)]
                    spawn(stacks(0, P, stk, free + w, NDP, rdy, *w), 4, f"stacks{P}")
                    stk_done[P] = []
                    for i in range(4):
                        ep, ef = yield EP
                        soft[(P, i)] = Fut()
                        spawn(da_unit(P, i, stk, ep, ef + w, rdy), 5, f"unit{P}.{i}")

            def da_unit(P, i, stk, ep, ef, rdy):
                n = 128 * (i + 1)
                v0, t0, r0 = yield from scores(stk, 0, i, MASK, ep[:, 0, :], ef, rdy)
                v1, t1, r1 = yield from scores(stk, 1, i, MASK, ep[:, 1, :], ef, rdy)
                stk_done[P].append(t1)
                if len(stk_done[P]) == 4:
                    STK.put(stk, *stk_done[P])
                e0, e1 = ep[:, 0, 0:n], ep[:, 1, 0:n]
                t = yield ts(e0, e0, v0[:, 2:3], None, ALU.mult, None, n, t0, r0)
                u = yield tt(v1[:, 3:4], v1[:, 2:3], lam[:, 3:4], ALU.mult, 1, r1, g["nlam"])
                t = yield stt(e0, e1, v1[:, 3:4], e0, ALU.mult, ALU.add, n, t, u, t1)
                SP.put(v0, t)
                SP.put(v1, t)
                soft[(P, i)].set((ep, t))

            def da_out():
                yield hgf
                for P in range(4):
                    o, of = yield OP
                    for i in range(4):
                        yield lambda: (P, i) in soft
                        ep, t = yield soft[(P, i)]
                        pt, pf = yield PT
                        n = 128 * (i + 1)
                        t, u = yield from turn_P(ep[:, 0, :], n, pt, pf, t)
                        EP.put(ep, t)
                        for j in range(i + 1):
                            (vt,) = yield vr[j]
                            t = yield mm(o[:, i * 128:i * 128 + 128], pt[:, j * 128:j * 128 + 128],
                                         V[:, j, P * 128:P * 128 + 128], j == 0, j == i, 219, u, vt, *of)
                        PT.put(pt, t)
                    spawn(finish(o, t, lambda T: GDA[:, :], P * 128, lambda u: None, STG, g["gda"]), 4, f"finda{P}")

            def load_da():
                g["rope"] = yield from load(ROPE[:, :, :], A["rope"], 65536)
                t = yield from load(GDA[:, :], A["da_subln_g"].broadcast_to([128, 128]), 65536)
                g["gda"] = yield ts(GDA[:, :], GDA[:, :], 0.8, None, ALU.mult, None, 128, t)
                w = yield hgf
                g["mask0"] = yield from load(MASK[:, :], A["mask0"], 262144, *w)
                mk.set((g["mask0"],))

            mk = Fut()
            spawn(load_da(), 6, "load_da")
            spawn(lambdas(), 6, "lambdas")
            spawn(da_scores(), 5, "da_scores")
            spawn(da_out(), 4, "da_out")
            spawn(reload_v(), 6, "reload_v")
            yield from gemmB(lambda nh, k: wQ(W, k, 0, 512), 1, 8, xh, xl, xr, ev_qk(0))
            yield from gemmB(lambda nh, k: wQ(W, k, 256, 768), 1, 8, xh, xl, xr, ev_qk(1))
            yield from gemmB(lambda nh, k: wB(W, k, 1024), 1, 8, xh, xl, xr, ev_va)
            w_in_done = g["last"]

            orr = Ready()

            def turn_k(kt):
                w = yield AllOf([onr.f[(kt, T)] for T in range(4)])
                bank, free = yield TP
                for T in range(4):
                    t = yield tr(bank[:, T * 128:T * 128 + 128], ON[:, T, kt * 128:kt * 128 + 128], *w, *free, inc=T == 3)
                th = yield act(XH[:, kt, :], bank[:, :], AF.Copy, 512, t, w_in_done)
                tl = yield tt(XL[:, kt, :], bank[:, :], XH[:, kt, :].bitcast(F32), ALU.subtract, 512, t, th, w_in_done)
                TP.put(bank, tl)
                for T in range(4):
                    orr.f[(kt, T)].set((th, tl))

            for kt in (4, 5, 6, 7, 0, 1, 2, 3):
                spawn(turn_k(kt), 4, f"turn_k{kt}")
            WO = A["ev_w_out"][0]
            x0 = {(T, nh): Fut() for T in range(4) for nh in range(2)}
            for f in x0.values():
                f.set(tuple(g["x", T] for T in range(4)))
            x1, x2, x3 = xfuts(), xfuts(), xfuts()
            off = lambda k0: (lambda k, T: orr(k + k0, T))
            yield from gemmB(lambda nh, k: wB(WO, k + 4, nh * 512), 2, 4, rows(XH, 4), rows(XL, 4), off(4),
                             add_x(ALPHA, x0, x1))
            G1, B1 = at_("LG1", 60, [128, 1024]), at_("LB1", 64, [128, 1024])
            gb = Fut()

            def ld():
                w = yield from gather([onr.f[(3, T)] for T in range(4)])
                for p in (PT, NDP, EP):
                    for it, tk in p.free:
                        w += tuple(tk)
                r = yield from gains((A["ln1_g"][0:1], A["ln1_b"][0:1]), (G1[:, :], B1[:, :]), *w)
                gb.set(r)

            spawn(ld(), 1, "ld")
            xr1 = Ready()
            for T in range(4):
                spawn(norm_ln(T, x2, gb, G1, B1, xr1, x3), 2 + T, f"ln1.{T}")
            yield from gemmB(lambda nh, k: wB(WO, k, nh * 512), 2, 4, xh, xl, off(0), add_x(1.0, x1, x2))
            z = (yield from gather(x3.values())) + (g["last"],)
            return (yield from after_first(0, xr1, x3, z, pre))

        def pre1(x_in, _):
            xr = Ready()
            for T in range(4):
                for k0 in (0, 4):
                    def turn(T=T, k0=k0):
                        w = yield x_in[(T, 0)]
                        w += yield x_in[(T, 1)]
                        yield from turn_T(X[:, T, :], T, XH, XL, xr, k0, 4, *w)
                    spawn(turn(), 2, "turn_x1")
            return xr

        def layer1(x_in, zone, xr, pre):
            W, WO = A["od_w_in"][0], A["od_w_out"][0]
            V = at_("OV", 0, [128, 4, 1024])
            STK = Pool([at_(f"OSTK{i}", 16 + 12 * i, [128, 6, 512], F32R) for i in range(2)])
            OHL = Pool([at_(f"OHL{i}", 40 + 4 * i, [128, 2, 512], F32R) for i in range(2)])
            EP = Pool([at_(f"OE{i}", 48 + 2 * i, [128, 512]) for i in range(4)])
            PT = Pool([at_(f"OPT{i}", 56 + 2 * i, [128, 512]) for i in range(4)])
            NDP = Pool([at_(f"ONDP{i}", 64 + 2 * i, [128, 512]) for i in range(2)])
            for g_ in range(2, 6):
                for T in range(4):
                    qkd[(g_, T)] = Fut()
            vr = xfuts()
            soft = {}
            left = {}

            def ev_v(nh, T, bank, tok):
                t = yield act(V[:, T, nh * 512:nh * 512 + 512], bank[:, :], AF.Copy, 512, tok, *zone)
                G.put(bank, t)
                vr[(T, nh)].set((t,))

            def load_mask():
                t = yield from load(MASK[:, :], A["mask1"], 262144, *zone)
                mk.set((t,))

            mk = Fut()

            def sc():
                w = yield mk
                for P in range(8):
                    stk, free = yield STK
                    rdy = [Fut() for _ in range(4)]
                    spawn(stacks(2, P, stk, free + zone, NDP, rdy, *zone), 4, f"stacks{P}")
                    left[P] = []
                    for i in range(4):
                        for hh in range(2):
                            e, ef = yield EP
                            soft[(P, i, hh)] = Fut()
                            spawn(unit(P, i, hh, stk, e, ef + zone + w, rdy), 5, f"unit{P}.{i}")

            def unit(P, i, hh, stk, e, ef, rdy):
                n = 128 * (i + 1)
                v, t, r = yield from scores(stk, hh, i, MASK, e, ef, rdy)
                left[P].append(t)
                if len(left[P]) == 8:
                    STK.put(stk, *left[P])
                t = yield ts(e[:, 0:n], e[:, 0:n], v[:, 2:3], None, ALU.mult, None, n, t, r)
                SP.put(v, t)
                soft[(P, i, hh)].set((e, t))

            ok = {P: Fut() for P in range(8)}
            ohl = {}

            def outs():
                for P in range(8):
                    o, of = yield OP
                    for i in range(4):
                        pts = []
                        n = 128 * (i + 1)
                        for hh in range(2):
                            yield lambda: (P, i, hh) in soft
                            e, t = yield soft[(P, i, hh)]
                            pt, pf = yield PT
                            t, u = yield from turn_P(e, n, pt, pf + zone, t)
                            EP.put(e, t)
                            pts.append((pt, u))
                        for j in range(i + 1):
                            (vt,) = yield vr[(j, P // 4)]
                            for hh in range(2):
                                pt, u = pts[hh]
                                c = (2 * P + hh) * 64
                                t = yield mm(o[64 * hh:64 * hh + 64, i * 128:i * 128 + 128], V[:, j, c:c + 64],
                                             pt[:, j * 128:j * 128 + 128], j == 0, j == i, 135, u, vt, *of,
                                             inc=j == i)
                        for pt, _ in pts:
                            PT.put(pt, t)
                    spawn(out_ev(P, o, t), 3, f"oev{P}")

            def out_ev(P, o, t):
                hl, hf = yield OHL
                ohl[P] = hl
                th = yield act(hl[:, 0, :], o[:, :], AF.Copy, 512, t, *hf, *zone)
                tl = yield tt(hl[:, 1, :], o[:, :], hl[:, 0, :].bitcast(F32), ALU.subtract, 512, th)
                OP.put(o, tl)
                ok[P].set((th, tl))

            spawn(load_mask(), 6, "mask1")
            spawn(sc(), 5, "scores1")
            spawn(outs(), 4, "outs1")
            yield from gemmB(lambda nh, k: wB(W, k, 2048 + nh * 512), 2, 8, xh, xl, xr, ev_v)
            steps = [x_in] + [xfuts() for _ in range(4)]

            def proj(g_):
                for k in range(2):
                    yield ok[2 * g_ + k]
                yield from gemmB(lambda nh, k: wB(WO, 2 * g_ + k, nh * 512), 2, 2,
                                 lambda k: ohl[2 * g_ + k][:, 0, :], lambda k: ohl[2 * g_ + k][:, 1, :],
                                 lambda k, T: ok[2 * g_ + k], add_x(ALPHA if g_ == 0 else 1.0, steps[g_], steps[g_ + 1]))
                for k in range(2):
                    OHL.put(ohl[2 * g_ + k], g["last"])

            G1, B1 = at_("OLG1", 60, [128, 1024]), at_("OLB1", 64, [128, 1024])
            gb = Fut()

            def ld():
                w = yield ok[7]
                for p in (PT, NDP, EP):
                    for it, tk in p.free:
                        w += tuple(tk)
                r = yield from gains((A["ln1_g"][1:2], A["ln1_b"][1:2]), (G1[:, :], B1[:, :]), *w)
                gb.set(r)

            spawn(ld(), 1, "ld")
            xr1, x3 = Ready(), xfuts()
            for T in range(4):
                spawn(norm_ln(T, steps[4], gb, G1, B1, xr1, x3), 2 + T, f"ln1.{T}")
            for what in ("q0", "q1", "q2", "w0", "q3", "w1", "w2", "w3"):
                n = int(what[1])
                if what[0] == "q":
                    yield from gemmB(lambda nh, k: wQ(W, k, 256 * n, 1024 + 256 * n), 1, 8, xh, xl, xr, ev_qk(2 + n))
                else:
                    yield from proj(n)
            z = (yield from gather(x3.values())) + (g["last"],)
            return (yield from after_first(1, xr1, x3, z, pre))

        def rms_rows(T, x, xw, tmp, tf, gain, gt, ready, eps, H, L, w=(), also=None):
            v, vf = yield SP
            n0 = yield xw[0]
            t0 = yield act(tmp[:, 0:512], x[:, 0:512], AF.Square, 512, *n0, *tf, *vf, *w, acc=v[:, 0:1])
            n1 = yield xw[1]
            t1 = yield act(tmp[:, 512:1024], x[:, 512:1024], AF.Square, 512, *n1, acc=v[:, 1:2])
            t = yield gop(lambda e: e.tensor_tensor(v[:, 2:3], v[:, 0:1], v[:, 1:2], ALU.add), 1, t0, t1)
            t = yield gop(lambda e: e.tensor_scalar(v[:, 3:4], v[:, 2:3], 1.0 / 1024, eps, ALU.mult, ALU.add), 1, t)
            t = yield gop(lambda e: e.tensor_tensor(v[:, 4:5], v[:, 3:4], half[:, 0:1], ALU.pow), 1, t, g["half"])
            u, last = [], []
            for h in range(2):
                c = slice(h * 512, h * 512 + 512)
                u.append((yield stt(tmp[:, c], x[:, c], v[:, 4:5], gain[:, c], ALU.mult, ALU.mult, 512, t, *gt)))
                last.append(u[h])
                if H is not None:
                    f = Fut()

                    def turn(h=h, u=u[h], f=f):
                        yield from turn_T(tmp, T, H, L, ready, 4 * h, 4, u)
                        f.set(ready.f[(4 * h, T)].v)
                    spawn(turn(), 2, "turn_r")
                    u[h] = f
            SP.put(v, *last)
            if H is not None:
                a, b = u
                r = (yield a) + (yield b)
                if also is not None:
                    r += ((yield from also(T, tmp, last)),)
                return r
            return tuple(u)

        def rms_all(x_in, gname, goff, hoff, zone, also=None):
            gt_ = at_("RG", goff, [128, 1024])
            HT = Pool([at_(f"RT{i}", hoff + 4 * i, [128, 1024]) for i in range(2)])
            rdy = Ready()
            gf = Fut()
            done = [Fut() for _ in range(4)]

            def ld():
                t = yield from load(gt_[:, :], A[gname].broadcast_to([128, 1024]), 524288, *zone)
                gf.set((t,))

            def one(T):
                tmp, tf = yield HT
                gt = yield gf
                d = yield from rms_rows(T, X[:, T, :], (x_in[(T, 0)], x_in[(T, 1)]), tmp, tf + zone, gt_, gt, rdy, 1e-6,
                                        XH, XL, also=also)
                HT.put(tmp, *d)
                done[T].set(d)

            spawn(ld(), 1, "ld_g")
            for T in range(4):
                spawn(one(T), 2 + T, f"rms{T}")
            return rdy, done

        def mem_kv(zone, done):
            MN = at_("MN", 0, [128, 2, 1024])
            MH, ML = at_("MH", 8, [128, 8, 256], F32R), at_("ML", 16, [128, 8, 256], F32R)
            MG = at_("MG", 24, [128, 1024])
            JK = at_("JK", 44, [128, 2, 1024])
            rdy = Ready(2)
            gf = Fut()

            def prep(T):
                t = yield from load(MN[:, T, :], A["mem_2"][0, T * 128:T * 128 + 128, :], 524288, *zone)
                gt = yield gf
                f = Fut()
                f.set((t,))
                yield from rms_rows(T, MN[:, T, :], (f, f), JK[:, T, :], zone, MG, gt, rdy, 1e-6, MH, ML)

            def ld():
                t = yield from load(MG[:, :], A["g_mem_2"].broadcast_to([128, 1024]), 524288, *zone)
                gf.set((t,))

            spawn(ld(), 1, "ld_gm")
            for T in range(2):
                spawn(prep(T), 3, f"mem{T}")
            sent = []

            def ev_k(n, bank, tok):
                s_, f = yield STG
                t = yield act(s_[:, 0:256], bank[:, 0:256], AF.Copy, 256, tok, *f)
                G.put(bank, t)
                t = yield from load(KTD[n], s_[:, 0:256], 131072, t)
                STG.put(s_, t)
                sent.append(t)

            def ev_v(nh, T, bank, tok):
                s_, f = yield STG
                t = yield act(s_[:, 0:512], bank[:, :], AF.Copy, 512, tok, *f)
                G.put(bank, t)
                t = yield from load(MVD[T], s_[:, 0:512], 262144, t)
                STG.put(s_, t)
                sent.append(t)

            W = A["w_ckv_2"][0]
            yield from gemmA(W, 0, 512, 8, rows(MH), rows(ML), rdy, ev_k, N=256)
            yield from gemmB(lambda nh, k: wB(W, k, 512), 1, 8, rows(MH), rows(ML), rdy, ev_v, TN=2)
            last = g["last"]

            def fin():
                yield lambda: len(sent) == 6
                done.set(tuple(sent) + (last,))
            spawn(fin(), 3, "memfin")

        def pre2(x_in, zone):
            return rms_all(x_in, "g_mix_2", 28, 32, zone)

        def block2(x_in, zone, nxt):
            W = A["w_in_2"][0]
            memd = Fut()
            rdy, hdone = nxt
            yield from mem_kv(zone, memd)
            z = yield from gather(hdone + [memd])
            SGH, SGL = at_("SGH", 0, [128, 4, 512], F32R), at_("SGL", 8, [128, 4, 512], F32R)
            OAH, OAL = at_("OAH", 16, [128, 4, 512], F32R), at_("OAL", 24, [128, 4, 512], F32R)
            K2, V2 = at_("K2", 32, [128, 2, 512], F32R), at_("V2", 36, [128, 4, 128])
            UT, SV = at_("UT", 38, [128, 4, 512]), at_("SV", 46, [128, 4, 512])
            GS_, BS_ = at_("SGg", 54, [128, 512]), at_("SGb", 56, [128, 512])
            WS, WST = at_("WS", 58, [128, 4, 128]), at_("WST", 60, [128, 4, 128])
            BSG = at_("BSG", 62, [128, 512])
            R = Pool([at_(f"BR{i}", 64 + 2 * i, [128, 512]) for i in range(2)])
            wst = Fut()
            sgl = Fut()

            def ld_sgu():
                t = yield from load(WS[:, :, :], A["w_s_2"][0].rearrange("g p q -> p g q"), 262144, *z)
                bank, free = yield TP
                for j in range(4):
                    t = yield tr(bank[:, j * 128:j * 128 + 128], WS[:, j, :], t, *free, inc=j == 3) if j == 0 else \
                        tr(bank[:, j * 128:j * 128 + 128], WS[:, j, :], inc=j == 3)
                t = yield cp(WST[:, :, :], bank[:, :].rearrange("p (a c) -> p a c", a=4), 512, t, *z)
                TP.put(bank, t)
                wst.set((t,))
                a = yield from load(GS_[:, :], A["sgu_ln_g_2"].broadcast_to([128, 512]), 262144, *z)
                b = yield from load(BS_[:, :], A["sgu_ln_b_2"].broadcast_to([128, 512]), 262144, *z)
                c = yield from load(BSG[:, :], A["b_s_2"].rearrange("o g p -> o (g p)").broadcast_to([128, 512]), 262144,
                                    *z)
                sgl.set((a, b, c))

            ut = [Fut() for _ in range(4)]
            sv = [Fut() for _ in range(4)]
            sg = Ready()

            def ev_su(n, bank, tok):
                t = yield act(UT[:, n, :], bank[:, :], AF.Gelu_apprx_tanh, 512, tok, *z)
                G.put(bank, t)
                ut[n].set((t,))

            def ev_sv(nh, T, bank, tok):
                x = SV[:, T, :]
                t = yield act(x, bank[:, :], AF.Gelu_apprx_tanh, 512, tok, *z)
                G.put(bank, t)
                g["gelu", T] = t
                v, vf = yield SP
                t = yield vop(lambda e: e.bn_stats(v[:, 0:6], x), 512, t, *vf)
                t = yield vop(lambda e: e.bn_aggr(v[:, 12:14], v[:, 0:6]), 12, t)
                t = yield gop(lambda e: e.tensor_scalar(v[:, 14:15], v[:, 13:14], 1e-6, None, ALU.add), 1, t)
                t = yield gop(lambda e: e.tensor_tensor(v[:, 15:16], v[:, 14:15], half[:, 0:1], ALU.pow), 1, t, g["half"])
                w = yield sgl
                u = yield stt(x, x, v[:, 12:13], GS_[:, :], ALU.subtract, ALU.mult, 512, t, *w)
                u = yield stt(x, x, v[:, 15:16], BS_[:, :], ALU.mult, ALU.add, 512, u)
                SP.put(v, u)
                sv[T].set((u,))

            def sgu():
                tv = yield AllOf(sv)
                tw = yield wst
                for n in range(4):
                    bank, free = yield S
                    for T in range(4):
                        t = yield mm(bank[:, T * 128:T * 128 + 128], SV[:, T, n * 128:n * 128 + 128], WST[:, n, :], True,
                                     True, 219, *tv, *tw, *free, inc=T == 3)
                    spawn(sgu_ev(n, bank, t), 4, "sgu_ev")

            sgd = []
            sgf = Fut()

            def sgu_ev(n, bank, t):
                r, rf = yield R
                (tu,) = yield ut[n]
                r3 = r[:, :].rearrange("p (a c) -> p a c", a=4)
                t = yield tt(r3, bank[:, :].rearrange("p (a c) -> p a c", a=4),
                             BSG[:, n * 128:n * 128 + 128].unsqueeze(1).broadcast_to([128, 4, 128]), ALU.add, 512, t, *rf,
                             *z)
                S.put(bank, t)
                t = yield tt(r[:, :], r[:, :], UT[:, n, :], ALU.mult, 512, t, tu)
                th = yield act(SGH[:, n, :], r[:, :], AF.Copy, 512, t, *z)
                tl = yield tt(SGL[:, n, :], r[:, :], SGH[:, n, :].bitcast(F32), ALU.subtract, 512, th, *z)
                R.put(r, th, tl)
                for T in range(4):
                    sg.f[(n, T)].set((th, tl))
                sgd.append(tl)
                if len(sgd) == 4:
                    sgf.set(tuple(sgd) + (t,))

            spawn(ld_sgu(), 5, "ld_sgu")
            spawn(sgu(), 6, "sgu")
            yield from gemmA(W, 768, 1280, 8, xh, xl, rdy, ev_su)
            yield from gemmB(lambda nh, k: wB(W, k, 1280), 1, 8, xh, xl, rdy, ev_sv)

            AXT = ax_tables(z, g)
            z2 = z
            NDK = at_("NDK", 68, [128, 256])
            NDKP = Pool([NDK])
            NDQ = Pool([at_("NDQ0", 20, [128, 1024]), at_("NDQ1", 28, [128, 1024])])
            JP = Pool([at_("JP", 24, [128, 1024])])
            qd = {T: Fut() for T in range(4)}
            kd = [Fut() for _ in range(4)]
            vd2 = [Fut() for _ in range(4)]

            def head_rot(bank, b0, nh_, T, which, outap, ofree, tok):
                n = nh_ * 64
                x3 = bank[:, b0:b0 + n].rearrange("p (h c) -> p h c", h=nh_)
                r, rf = yield R
                q3 = r[:, 0:n].rearrange("p (h c) -> p h c", h=nh_)
                t = yield act(r[:, 0:n], bank[:, b0:b0 + n], AF.Square, n, tok, *rf, *z)
                v, vf = yield SP
                t = yield vop(lambda e: e.tensor_reduce(v[:, 0:nh_], q3, AX.X, ALU.add), n, t, *vf)
                t = yield gop(lambda e: e.tensor_scalar(v[:, 0:nh_], v[:, 0:nh_], 1.0 / 64, 1e-6, ALU.mult, ALU.add), 8,
                              t)
                t = yield gop(lambda e: e.tensor_tensor(v[:, 8:8 + nh_], v[:, 0:nh_], half8[:, 0:nh_], ALU.pow), 8, t,
                              g["half"])
                t = yield tt(q3, x3, v[:, 8:8 + nh_].unsqueeze(2).broadcast_to([128, nh_, 64]), ALU.mult, n, t)
                tb = t
                SP.put(v, t)
                j, jf = yield JP
                jf += z
                P_ = AXT[:, which, T, 0:64].unsqueeze(1).broadcast_to([128, nh_, 64])
                Q_ = AXT[:, which, T, 64:128].rearrange("p (c s) -> p c s", s=2).unsqueeze(1).broadcast_to(
                    [128, nh_, 32, 2])
                m1 = j[:, 0:n].rearrange("p (h c) -> p h c", h=nh_)
                m2 = j[:, 512:512 + n].rearrange("p (h c s) -> p h c s", h=nh_, s=2)
                q4 = r[:, 0:n].rearrange("p (h c s) -> p h c s", h=nh_, s=2)
                t1 = yield tt(m1, q3, P_, ALU.mult, n, t, *jf, *g["axt"])
                t2 = yield tt(m2[:, :, :, 0], q4[:, :, :, 1], Q_[:, :, :, 0], ALU.mult, n // 2, t, *jf)
                t3 = yield tt(m2[:, :, :, 1], q4[:, :, :, 0], Q_[:, :, :, 1], ALU.mult, n // 2, t)
                R.put(r, t3)
                t = yield tt(outap, m1.unsqueeze(2).broadcast_to([128, nh_, 2, 64]),
                             j[:, 512:512 + n].rearrange("p (h c) -> p h c", h=nh_).unsqueeze(2).broadcast_to(
                                 [128, nh_, 2, 64]), ALU.add, 2 * n, t1, t2, t3, *ofree)
                JP.put(j, t)
                return tb, t

            def ev_q(nh, T, bank, tok):
                nd, nf = yield NDQ
                tb, t = yield from head_rot(bank, 0, 8, T, 0, nd[:, :].rearrange("p (h d c) -> p h d c", h=8, d=2), nf + z,
                                            tok)
                G.put(bank, tb)
                t = yield from load(QQD[T], nd[:, :], 524288, t)
                NDQ.put(nd, t)
                qd[T].set((t,))


            def ev_kv(nh, T, bank, tok):
                nd, nf = yield NDKP
                t = yield act(V2[:, T, :], bank[:, 128:256], AF.Copy, 128, tok, *z)
                vd2[T].set((t,))
                tb, t = yield from head_rot(bank, 0, 2, T, 1, nd[:, :].rearrange("p (h d c) -> p h d c", h=2, d=2),
                                            nf + z, t)
                G.put(bank, tb)
                bk, bf = yield TP
                for j in range(2):
                    u = yield tr(bk[:, j * 128:j * 128 + 128], nd[:, j * 128:j * 128 + 128], t, *bf, inc=j == 1)
                NDKP.put(nd, u)
                c = slice(T * 128, T * 128 + 128)
                b3 = bk[:, 0:256].rearrange("p (a c) -> p a c", a=2)
                th = yield act(K2[:, 0:2, c], b3, AF.Copy, 256, u, *z)
                k = K2[64:128, 0:2, c]
                tl = yield tt(k, b3[64:128, :, :], k.bitcast(F32), ALU.subtract, 256, th)
                TP.put(bk, tl)
                kd[T].set((th, tl))

            yield from gemmB(lambda nh, k: (wA(W, k, 512)), 1, 8, xh, xl, rdy, ev_kv, N=256)
            yield from gemmB(lambda nh, k: wB(W, k, 0), 1, 8, xh, xl, rdy, ev_q)

            QST = Pool([at_(f"QST{i}", 38 + 8 * i, [128, 4, 512], F32R) for i in range(2)])
            EP = Pool([at_(f"QE{i}", 54 + 2 * i, [128, 512]) for i in range(4)])
            PT = Pool([at_(f"QP{i}", 62 + 2 * i, [128, 512]) for i in range(2)])
            NQ = Pool([at_(f"NQ{i}", 66 + i, [128, 256]) for i in range(2)])
            soft, left = {}, {}

            def q_stacks(P, st, free, done):
                for T in range(4):
                    (d,) = yield qd[T]
                    nd, nf = yield NQ
                    t = yield from load(nd[:, :], QQD[T][:, P * 256:P * 256 + 256], 131072, d, *nf, *free)
                    bank, bf = yield TP
                    for j in range(2):
                        u = yield tr(bank[:, j * 128:j * 128 + 128], nd[:, j * 128:j * 128 + 128], t, *bf, inc=j == 1)
                    NQ.put(nd, u)
                    c = slice(T * 128, T * 128 + 128)
                    b3 = bank[:, 0:256].rearrange("p (a c) -> p a c", a=2)
                    th = yield act(st[:, 0:2, c], b3, AF.Copy, 256, u, *free)
                    tl = yield tt(st[:, 2:4, c], b3, st[:, 0:2, c].bitcast(F32), ALU.subtract, 256, th, *free)
                    TP.put(bank, tl)
                    done[T].set((th, tl))

            def sc():
                w = yield sgf
                w += yield AllOf(list(qd.values()))
                m = yield vop(lambda e: e.memset(MASK[:, :], 0.0), 512, *zone)
                spawn(zero_fill(m), 6, "zero")
                kk = yield AllOf(kd)
                for P in range(4):
                    st, free = yield QST
                    rdy_ = [Fut() for _ in range(4)]
                    spawn(q_stacks(P, st, free + w, rdy_), 4, f"qst{P}")
                    left[P] = []
                    for i in range(4):
                        for hh in range(2):
                            e, ef = yield EP
                            soft[(P, i, hh)] = Fut()
                            spawn(unit(P, i, hh, st, e, ef + w + (m,), rdy_, kk), 5, "unit")

            def unit(P, i, hh, st, e, ef, rdy_, kk):
                w = yield rdy_[i]
                s, sf = yield S
                q = slice(i * 128, i * 128 + 128)
                yield mm(s[:, :], st[:, hh, q], K2[:, P // 2, :], True, False, 216, *w, *sf, *kk)
                t = yield mm(s[:, :], st[:, 2 + hh, q], K2[:, P // 2, :], False, True, 216)
                left[P].append(t)
                if len(left[P]) == 8:
                    QST.put(st, *left[P])
                v, t, r = yield from soft_row(s, 512, MASK, 0.125, e, t, ef)
                t = yield ts(e[:, :], e[:, :], v[:, 2:3], None, ALU.mult, None, 512, t, r)
                SP.put(v, t)
                soft[(P, i, hh)].set((e, t))

            oa = Ready()

            def outs():
                w = yield sgf
                w += yield AllOf(list(qd.values()))
                vv = yield AllOf(vd2)
                for P in range(4):
                    o, of = yield OP
                    for i in range(4):
                        pts = []
                        for hh in range(2):
                            yield lambda: (P, i, hh) in soft
                            e, t = yield soft[(P, i, hh)]
                            pt, pf = yield PT
                            t, u = yield from turn_P(e, 512, pt, pf + w, t)
                            EP.put(e, t)
                            pts.append((pt, u))
                        for j in range(4):
                            for hh in range(2):
                                pt, u = pts[hh]
                                c = (P // 2) * 64
                                t = yield mm(o[64 * hh:64 * hh + 64, i * 128:i * 128 + 128], V2[:, j, c:c + 64],
                                             pt[:, j * 128:j * 128 + 128], j == 0, j == 3, 135, u, *vv, *of, inc=j == 3)
                        for pt, _ in pts:
                            PT.put(pt, t)
                    spawn(split_out(P, o, t, OAH[:, P, :], OAL[:, P, :], oa, w), 3, "oa")

            spawn(sc(), 5, "scores2")
            spawn(outs(), 4, "outs2")

            tg = {(a, n): Fut() for a in range(2) for n in range(8)}

            def ev_g(a):
                def ev(n, bank, tok):
                    s_, f = yield STG
                    t = yield act(s_[:, 0:512], bank[:, :], AF.Tanh, 512, tok, *f, scale=0.5)
                    G.put(bank, t)
                    t = yield from load(TGD[a, n], s_[:, 0:512], 262144, t)
                    STG.put(s_, t)
                    tg[(a, n)].set((t,))
                return ev

            yield from gemmA(W, 1792, 2816, 8, xh, xl, rdy, ev_g(0))
            yield from gemmA(W, 2816, 3840, 8, xh, xl, rdy, ev_g(1))
            in_done = g["last"]

            TG = Pool([at_(f"TG{i}", 54 + 2 * i, [128, 512]) for i in range(4)])
            MP = Pool([at_(f"MP{i}", 38 + 2 * i, [128, 512]) for i in range(4)])
            z3 = yield from gather([oa.f[(k, 0)] for k in range(4)])
            z3 += (g["oa_last"],)
            part = {}
            mr = Ready()
            tgr = {}

            def ld_tg():
                for q in range(4):
                    for a in range(2):
                        for n in (2 * q, 2 * q + 1):
                            (d,) = yield tg[(a, n)]
                            b, f = yield TG
                            t = yield from load(b[:, :], TGD[a, n], 262144, d, *f, *z3)
                            tgr[(a, n)] = (b, t)

            def ev_y(a, n0):
                def ev(n_, bank, tok):
                    n = n0 + n_
                    yield lambda: (a, n) in tgr
                    b, tb = tgr[(a, n)]
                    if a == 0:
                        m, mf = yield MP
                        t = yield stt(m[:, :], b[:, :], 1.0, bank[:, :], ALU.add, ALU.mult, 512, tok, tb, *mf, *z3)
                        G.put(bank, t)
                        TG.put(b, t)
                        part[n] = (m, t)
                        return
                    yield lambda: n in part
                    m, tm = part[n]
                    t = yield stt(b[:, :], b[:, :], 1.0, bank[:, :], ALU.add, ALU.mult, 512, tok, tb)
                    G.put(bank, t)
                    t = yield tt(m[:, :], m[:, :], b[:, :], ALU.add, 512, t, tm)
                    TG.put(b, t)
                    th = yield act(XH[:, n, :], m[:, :], AF.Copy, 512, t, in_done)
                    tl = yield tt(XL[:, n, :], m[:, :], XH[:, n, :].bitcast(F32), ALU.subtract, 512, th, in_done)
                    MP.put(m, th, tl)
                    for T in range(4):
                        mr.f[(n, T)].set((th, tl))
                return ev

            spawn(ld_tg(), 1, "ld_tg")
            for q in range(4):
                yield from gemmA(A["w_att_out_2"][0], 256 * q, 256 * q + 256, 4, rows(OAH), rows(OAL), oa, ev_y(0, 2 * q))
                yield from gemmA(A["w_sgu_out_2"][0], 256 * q, 256 * q + 256, 4, rows(SGH), rows(SGL), sg, ev_y(1, 2 * q))
            ylast = g["last"]
            x1, x2, x3 = xfuts(), xfuts(), xfuts()
            z4 = z3 + (ylast,)
            rdyc, cdone = rms_all(x1, "g_cross_2", 56, 60, z4 + ((yield from gather([mr.f[(7, 0)]]))))
            yield from gemmB(lambda nh, k: wB(A["w_out_2"][0], k, nh * 512), 2, 8, xh, xl, mr,
                             add_x(None, x_in, x1, mul=0.5))

            CQH, CQL = at_("CQH", 0, [128, 4, 512], F32R), at_("CQL", 8, [128, 4, 512], F32R)
            COH, COL = at_("COH", 16, [128, 4, 512], F32R), at_("COL", 24, [128, 4, 512], F32R)
            KTr = at_("KTr", 32, [128, 4, 256])
            KTH, KTL = at_("KTH", 36, [128, 4, 256], F32R), at_("KTL", 40, [128, 4, 256], F32R)
            MV = at_("MV", 44, [128, 2, 512])
            CE = Pool([at_(f"CE{i}", 48 + i, [128, 256]) for i in range(4)])
            CP = Pool([at_(f"CP{i}", 52 + i, [128, 256]) for i in range(4)])
            kv = Fut()

            def ld_kv():
                t = yield from load(KTr[:, :, :], KTD.rearrange("h p m -> p h m"), 524288, *z4, *memd.v)
                u = yield from load(MV[:, :, :], MVD.rearrange("a p c -> p a c"), 524288, *z4, *memd.v)
                th = yield act(KTH[:, :, :], KTr[:, :, :], AF.Copy, 1024, t, *z4)
                tl = yield tt(KTL[:, :, :], KTr[:, :, :], KTH[:, :, :].bitcast(F32), ALU.subtract, 1024, t, th, *z4)
                kv.set((th, tl, u))

            spawn(ld_kv(), 3, "ld_kv")
            qr = [Fut() for _ in range(4)]

            def ev_cq(n, bank, tok):
                th = yield act(CQH[:, n, :], bank[:, :], AF.Copy, 512, tok, *z4)
                tl = yield tt(CQL[:, n, :], bank[:, :], CQH[:, n, :].bitcast(F32), ALU.subtract, 512, th, *z4)
                G.put(bank, tl)
                qr[n].set((th, tl))

            csoft = {}

            def csc():
                for h in range(4):
                    for i in range(4):
                        e, ef = yield CE
                        csoft[(h, i)] = Fut()
                        spawn(cunit(h, i, e, ef + z4), 5, "cunit")

            def cunit(h, i, e, ef):
                w = yield qr[h]
                w += yield kv
                s, sf = yield S
                q = slice(i * 128, i * 128 + 128)
                yield mm(s[:, 0:256], CQH[:, h, q], KTH[:, h, :], True, False, 110, *w, *sf)
                yield mm(s[:, 0:256], CQH[:, h, q], KTL[:, h, :], False, False, 110)
                t = yield mm(s[:, 0:256], CQL[:, h, q], KTH[:, h, :], False, True, 110)
                v, t, r = yield from soft_row(s, 256, MASK, float(np.float32(128.0 ** -0.5)), e, t, ef)
                t = yield ts(e[:, :], e[:, :], v[:, 2:3], None, ALU.mult, None, 256, t, r)
                SP.put(v, t)
                csoft[(h, i)].set((e, t))

            co = Ready()

            def couts():
                w = yield kv
                for h in range(4):
                    o, of = yield OP
                    for i in range(4):
                        yield lambda: (h, i) in csoft
                        e, t = yield csoft[(h, i)]
                        pt, pf = yield CP
                        t, u = yield from turn_P(e, 256, pt, pf + z4, t)
                        CE.put(e, t)
                        for j in range(2):
                            t = yield mm(o[:, i * 128:i * 128 + 128], MV[:, j, h * 128:h * 128 + 128],
                                         pt[:, j * 128:j * 128 + 128], j == 0, j == 1, 219, u, *w, *of)
                        CP.put(pt, t)
                    spawn(split_out(h, o, t, COH[:, h, :], COL[:, h, :], co, z4), 3, "co")

            spawn(csc(), 5, "csc")
            spawn(couts(), 4, "couts")
            yield from gemmA(A["w_cq_2"][0], 0, 512, 8, xh, xl, rdyc, ev_cq)
            WC = A["w_co_2"][0]
            yield from gemmB(lambda nh, k: wB(WC, k, nh * 512), 2, 2, rows(COH), rows(COL), co, add_x(1.0, x1, x2))
            yield from gemmB(lambda nh, k: wB(WC, 2 + k, nh * 512), 2, 2, rows(COH, 2), rows(COL, 2),
                             lambda k, T: co(k + 2, T), add_x(1.0, x2, x3))
            z5 = yield from gather(x3.values())
            return x3, z5 + (g["last"],)

        def route(x_in, zone, idx):
            RT_ = at_("ROUTE", 44, [128, 428])
            WR, WRS = at_("WRr", 46, [128, 8, 20]), at_("WRS", 46.75, [128, 8, 40], F32R)
            WK = at_("WK", 48, [128, 1800])
            pos = [0]

            def wk(n, dt=None):
                a = WK[:, pos[0]:pos[0] + n]
                pos[0] += n
                return a if dt is None else a.bitcast(dt)

            hd = []

            def also(T, tmp, w):
                t = yield from load(HD[T * 128:T * 128 + 128, :], tmp[:, :], 524288, *w)
                hd.append(t)
                return t

            rdy, done = rms_all(x_in, "g_moe_2", 56, 60, zone, also)
            g["moe_rms"] = done
            t0 = yield from load(RT_[:, :], A["route"], 219136, *zone)
            t1 = yield from load(WR[:, :, 0:4], A["w_rg_2"][0].rearrange("(k p) c -> p k c", p=128), 16384, *zone)
            t2 = yield from load(WR[:, :, 4:20], A["w_re_2"][0].rearrange("(k p) c -> p k c", p=128), 65536, *zone)
            BI = wk(20)
            t3 = yield from load(BI[:, 0:4], A["b_rg_2"].broadcast_to([128, 4]), 2048, *zone)
            t4 = yield from load(BI[:, 4:20], A["b_re_2"].broadcast_to([128, 16]), 8192, *zone)
            th = yield act(WRS[:, :, 0:20], WR[:, :, :], AF.Copy, 160, t1, t2, *zone)
            tl = yield tt(WRS[:, :, 20:40], WR[:, :, :], WRS[:, :, 0:20].bitcast(F32), ALU.subtract, 160, th)
            iota16, tokid, reset8, ones16, iota8 = RT_[:, 0:16], RT_[:, 16:20], RT_[:, 20:148], RT_[:, 148:164], \
                RT_[:, 164:172]
            tri, ones = RT_[:, 172:300], RT_[:, 300:428]
            GE = wk(32)
            tg0 = yield vop(lambda e: e.memset(GE, -1.0), 32, *zone)
            ge3 = GE.rearrange("p (t c) -> p t c", t=4)
            o, of = yield OP
            for T in range(4):
                for k in range(8):
                    w = yield rdy(k, T)
                    a = (o[:, T * 40:T * 40 + 40], XH[:, k, T * 128:T * 128 + 128], WRS[:, k, :])
                    b = (o[:, T * 40:T * 40 + 20], XL[:, k, T * 128:T * 128 + 128], WRS[:, k, 0:20])
                    p, q = (a, b) if k == 0 else (b, a)
                    yield mm(*p, k == 0, False, 107, *w, *of, th, tl)
                    t = yield mm(*q, False, k == 7, 107, inc=k == 7)
            LG = wk(80).rearrange("p (t c) -> p t c", t=4)
            o3 = o[:, 0:160].rearrange("p (t c) -> p t c", t=4)
            t = yield tt(LG, o3[:, :, 0:20], BI.unsqueeze(1).broadcast_to([128, 4, 20]), ALU.add, 80, t, t3, t4, *zone)
            t = yield tt(LG, LG, o3[:, :, 20:40], ALU.add, 80, t)
            OP.put(o, t)
            gm, gs, gv = wk(4), wk(4), wk(4)
            t = yield vop(lambda e: e.tensor_reduce(gm, LG[:, :, 0:4], AX.X, ALU.max), 16, t)
            t = yield tt(ge3[:, :, 0:4], LG[:, :, 0:4], gm.unsqueeze(2).broadcast_to([128, 4, 4]), ALU.subtract, 16, t, tg0)
            t = yield act(ge3[:, :, 0:4], ge3[:, :, 0:4], AF.Exp, 16, t)
            tge = t
            v8, i8 = wk(32), wk(32, U32)
            for T in range(4):
                c = slice(8 * T, 8 * T + 8)
                ta = yield vop(lambda e, c=c: e.max(v8[:, c], GE[:, c]), 8, tge)
                tb = yield vop(lambda e, c=c: e.max_index(i8[:, c], v8[:, c], GE[:, c]), 8, ta)
            gi = wk(4)
            t = yield cp(gi, i8.rearrange("p (t c) -> p t c", t=4)[:, :, 0], 4, tb)
            oh = wk(16).rearrange("p (t c) -> p t c", t=4)
            t = yield tt(oh, iota16[:, 0:4].unsqueeze(1).broadcast_to([128, 4, 4]),
                         gi.unsqueeze(2).broadcast_to([128, 4, 4]), ALU.is_equal, 16, t, t0)
            t = yield ts(oh, oh, -1.0, BIG, ALU.add, ALU.mult, 16, t)
            EM = wk(64)
            em4 = EM.rearrange("p (t a c) -> p t a c", t=4, a=4)
            for T in range(4):
                t = yield tt(em4[:, T], LG[:, T, 4:20].rearrange("p (a c) -> p a c", a=4),
                             oh[:, T, :].unsqueeze(2).broadcast_to([128, 4, 4]), ALU.add, 16, t)
            tem = t
            w8, j8 = wk(32), wk(32, U32)
            for T in range(4):
                c, d = slice(8 * T, 8 * T + 8), slice(16 * T, 16 * T + 16)
                ta = yield vop(lambda e, c=c, d=d: e.max(w8[:, c], EM[:, d]), 16, tem)
                tb = yield vop(lambda e, c=c, d=d: e.max_index(j8[:, c], w8[:, c], EM[:, d]), 16, ta)
            ID = wk(8)
            tid_ = yield cp(ID.rearrange("p (t k) -> p t k", t=4), j8.rearrange("p (t c) -> p t c", t=4)[:, :, 0:2], 8, tb)
            O = wk(128)
            o_eb = O.rearrange("p (e b) -> p e b", e=16)
            to = yield tt(o_eb, iota16.unsqueeze(2).broadcast_to([128, 16, 8]), ID.unsqueeze(1).broadcast_to([128, 16, 8]),
                          ALU.is_equal, 128, tid_)
            bank, bf = yield OP
            yield mm(bank[:, 0:128], tri, O, True, True, 219, to, *bf, inc=False)
            t = yield mm(bank[:, 128:256], ones, O, True, True, 219)
            w83 = w8.rearrange("p (t c) -> p t c", t=4)
            e2, r2 = wk(4), wk(4)
            u = yield tt(e2, w83[:, :, 1], w83[:, :, 0], ALU.subtract, 4, tb)
            u = yield act(e2, e2, AF.Exp, 4, u)
            INC, RK = wk(128), wk(128)
            tot = wk(128)
            tc = yield cp(tot, bank[:, 128:256], 128, t)
            ti = yield vop(lambda e: e.tensor_tensor_scan(INC, reset8, tot, 0.0, ALU.mult, ALU.add), 128, tc)
            t = yield tt(RK, INC, tot, ALU.subtract, 128, ti)
            t = yield tt(RK, RK, bank[:, 0:128], ALU.add, 128, t)
            OP.put(bank, t)
            t = yield tt(RK, RK, O, ALU.mult, 128, t)
            r = wk(8)
            tr_ = yield vop(lambda e: e.tensor_reduce(r, RK.rearrange("p (e b) -> p b e", e=16), AX.X, ALU.add), 128, t)
            n_e = INC.rearrange("p (e b) -> p e b", e=16)[:, :, 7]
            nov = wk(16)
            t = yield ts(nov, n_e, 128.0, None, ALU.is_gt, None, 16, ti)
            t = yield stt(nov, n_e, 256.0, nov, ALU.is_gt, ALU.add, 16, t)
            t = yield stt(nov, n_e, 384.0, nov, ALU.is_gt, ALU.add, 16, t)
            incl, ob = wk(16), wk(16)
            til = yield vop(lambda e: e.tensor_tensor_scan(incl, ones16, nov, 0.0, ALU.mult, ALU.add), 16, t)
            t = yield tt(ob, incl, nov, ALU.subtract, 16, til)
            OB = wk(128)
            t = yield tt(OB.rearrange("p (e b) -> p e b", e=16), o_eb, ob.unsqueeze(2).broadcast_to([128, 16, 8]), ALU.mult,
                         128, t)
            obb = wk(8)
            t = yield vop(lambda e: e.tensor_reduce(obb, OB.rearrange("p (e b) -> p b e", e=16), AX.X, ALU.add), 128, t)
            c1, q = wk(8), wk(8)
            a = yield ts(c1, r, 128.0, None, ALU.is_ge, None, 8, tr_)
            a = yield stt(q, r, 256.0, c1, ALU.is_ge, ALU.add, 8, a)
            a = yield stt(q, r, 384.0, q, ALU.is_ge, ALU.add, 8, a)
            t = yield tt(obb, obb, q, ALU.add, 8, t, a)
            t = yield stt(obb, obb, 15.0, ID, ALU.add, ALU.subtract, 8, t)
            t = yield tt(obb, obb, c1, ALU.mult, 8, t)
            t = yield tt(obb, obb, ID, ALU.add, 8, t)
            t = yield stt(obb, obb, 128.0, r, ALU.mult, ALU.add, 8, t)
            t = yield stt(obb, q, -128.0, obb, ALU.mult, ALU.add, 8, t)
            ts_ = yield cp(SLOT[:, :], obb, 8, t, *zone)
            sc = []
            z0 = g["zeros"]
            for b in range(8):
                sem, toks = yield IQ
                tk = yield Op("G", 1000.0, lambda e, b=b: e.indirect_dma_start(
                    TAB[:, :], bass.IndirectOffsetOnAxis(SLOT[:, b:b + 1], axis=0), tokid[:, b // 2:b // 2 + 1], None),
                    (*toks, ts_, z0), 1, sem, 512)
                IQ.put(sem, tk)
                sc.append(tk)
            TT_ = wk(128)
            t = yield from load(TT_[0:23, :], TAB.rearrange("(t s) o -> t (s o)", t=23), 11776, *sc, *zone)
            bank, bf = yield OP
            t = yield mm(bank[:, 0:23], TT_[0:23, :], ident[0:23, 0:23], True, True, 50, t, *bf)
            t = yield cp(IDX[:, 0:23], bank[:, 0:23], 23, t, *zone)
            OP.put(bank, t)
            idx.set((t, *hd))
            cw3 = CW[:, :].rearrange("p (t k) -> p t k", t=4)
            u = yield ts(r2, e2, 1.0, None, ALU.add, None, 4, u)
            u = yield vop(lambda e: e.reciprocal(r2, r2), 24, u)
            a = yield vop(lambda e: e.tensor_reduce(gs, ge3[:, :, 0:4], AX.X, ALU.add), 16, tge)
            a = yield vop(lambda e: e.reciprocal(gv, gs), 24, a)
            u = yield tt(cw3[:, :, 0], r2, gv, ALU.mult, 4, a, u, *zone)
            u = yield tt(cw3[:, :, 1], cw3[:, :, 0], e2, ALU.mult, 4, u)
            g["cw"] = u
            ce = wk(128)
            t = yield tt(ce.rearrange("p (j e) -> p j e", j=8), incl.unsqueeze(1).broadcast_to([128, 8, 16]),
                         iota8.unsqueeze(2).broadcast_to([128, 8, 16]), ALU.is_le, 128, til)
            of_ = wk(8)
            t = yield vop(lambda e: e.tensor_reduce(of_, ce.rearrange("p (j e) -> p j e", j=8), AX.X, ALU.add), 128, t)
            t = yield cp(OVF[:, 1:8], of_[:, 0:7], 7, t, *zone)
            t1 = yield cp(OVF[:, 0:1], incl[:, 15:16], 1, t)
            g["ovf"] = (t1,)
            g["route_end"] = (t1, t, u)

        class Tiles:

            def __init__(self):
                self.XG = Pool([at_(f"XG{i}", 4 * i, [128, 1024]) for i in range(2)])
                self.EX = Pool([at_(f"EX{i}", 8 + 8 * i, [128, 16, 128], F32R) for i in range(2)])
                self.SG = Pool([at_(f"ES{i}", 24 + 2 * i, [128, 512]) for i in range(2)])
                self.EH = Pool([at_(f"EH{i}", 28 + 4 * i, [128, 8, 128], F32R) for i in range(2)])
                self.Y = Pool([at_(f"EY{i}", 36 + 4 * i, [128, 1024]) for i in range(2)])

        def experts(board, strm, tiles, src, R, idx, zone, DQ, IQ, TP, sent):
            sp = board.spawn
            ex = {i: Fut() for i in tiles}
            eh = {i: Fut() for i in tiles}
            ss = {}

            def turn8(get, K, h, l, free, w):
                r = []
                for k0 in range(0, K, 4):
                    bank, bf = yield TP
                    for j in range(4):
                        t = yield tr(bank[:, j * 128:j * 128 + 128], get(k0 + j), *w, *bf, inc=j == 3)
                    b3 = bank[:, :].rearrange("p (a c) -> p a c", a=4)
                    th = yield act(h[:, k0:k0 + 4, :], b3, AF.Copy, 512, t, *free)
                    tl = yield tt(l[:, k0:k0 + 4, :], b3, h[:, k0:k0 + 4, :].bitcast(F32), ALU.subtract, 512, th, *free)
                    TP.put(bank, tl)
                    r += [th, tl]
                return t, tuple(r)

            def prep(i):
                x, xf = yield R.XG
                w = yield idx
                sem, toks = yield IQ
                t = yield Op("G", 1000.0, lambda e: e.indirect_dma_start(
                    x[:, :], None, HD[:, :], bass.IndirectOffsetOnAxis(IDX[:, i:i + 1], axis=0)),
                    (*toks, *w, *xf, *zone), 1, sem, 524288)
                IQ.put(sem, t)
                e, ef = yield R.EX
                t, r = yield from turn8(lambda k: x[:, k * 128:k * 128 + 128], 8, e[:, 0:8, :], e[:, 8:16, :], ef + zone,
                                        (t,))
                R.XG.put(x, t)
                ex[i].set((e, r))

            def preps():
                for i in tiles:
                    yield from prep(i)

            def ev_gate(i):
                def ev(nh, T, bank, tok):
                    s_, sf = yield R.SG
                    t = yield act(s_[:, :], bank[:, :], AF.Silu, 512, tok, *sf, *zone)
                    G.put(bank, t)
                    ss[i] = (s_, t)
                return ev

            def ev_up(i):
                def ev(nh, T, bank, tok):
                    yield lambda: i in ss
                    s_, t = ss[i]
                    t = yield tt(s_[:, :], s_[:, :], bank[:, :], ALU.mult, 512, tok, t)
                    G.put(bank, t)
                    h, hf = yield R.EH
                    t, r = yield from turn8(lambda k: s_[:, k * 128:k * 128 + 128], 4, h[:, 0:4, :], h[:, 4:8, :],
                                            hf + zone, (t,))
                    R.SG.put(s_, t)
                    eh[i].set((h, r))
                return ev

            ys = {}

            def ev_down(i):
                def ev(nh, T, bank, tok):
                    if nh == 0:
                        ys[i] = yield R.Y
                        y, yf = ys[i]
                    else:
                        yield lambda: i in ys
                        y, yf = ys[i]
                    t = yield act(y[:, nh * 512:nh * 512 + 512], bank[:, :], AF.Copy, 512, tok, *yf, *zone)
                    G.put(bank, t)
                    if nh == 1:
                        sem, toks = yield DQ
                        t = yield dma(YD[i * 128:i * 128 + 128, :], y[:, :], 524288, sem, *toks, t)
                        DQ.put(sem, t)
                        R.Y.put(y, t)
                        sent.append(t)
                return ev

            def up_or_gate(i, name, ev):
                e, r = yield ex[i]
                f = Fut()
                f.set(r)
                yield from gemmB(lambda nh, k: src(i, name, k, 0), 1, 8, lambda k: e[:, k, :], lambda k: e[:, 8 + k, :],
                                 lambda k, T: f, ev, TN=1, strm=strm, spawn=sp)
                if name == "w_up_2":
                    R.EX.put(e, g["last"])

            def down(i):
                h, r = yield eh[i]
                f = Fut()
                f.set(r)
                yield from gemmB(lambda nh, k: src(i, "w_down_2", k, nh * 512), 2, 4, lambda k: h[:, k, :],
                                 lambda k: h[:, 4 + k, :], lambda k, T: f, ev_down(i), TN=1, strm=strm, spawn=sp)
                R.EH.put(h, g["last"])

            sp(preps(), 4, "preps")
            for n, i in enumerate(tiles):
                yield from up_or_gate(i, "w_gate_2", ev_gate(i))
                if n:
                    yield from down(tiles[n - 1])
                yield from up_or_gate(i, "w_up_2", ev_up(i))
            yield from down(tiles[-1])

        def moe(x_in, zone):
            idx = Fut()
            spawn(route(x_in, zone, idx), 2, "route")
            R = Tiles()
            sent = []

            def src(i, name, k, n):
                return wB(A[name][0, i], k, n)

            def more_raw():
                yield idx
                yield lambda: "route_end" in g
                for i in range(3, 6):
                    raw.put(i, *g["route_end"])

            spawn(more_raw(), 2, "more_raw")
            yield from experts(bd, strm, list(range(16)), src, R, idx, zone, DQ, IQ, TP, sent)
            yield lambda: len(sent) == 16
            g["moe"] = (R, idx, sent)

        def further(zone):
            R, idx, sent = g["moe"]
            b2 = Board("2")
            for n, q in b2.q.items():
                q.t = bd.q[n].t
            regs = {}
            order2 = []
            for j in range(7):
                for name, K, H in (("w_gate_2", 8, 1), ("w_up_2", 8, 1), ("w_down_2", 4, 2)):
                    for nh in range(H):
                        for k in range(0, K, 2):
                            def src(name=name, k=k, nh=nh):
                                w = A[name][0, bass.ds(regs["e"], 1), k * 128:(k + 2) * 128, nh * 512:nh * 512 + 512]
                                return w.rearrange("o (a p) c -> p (o a) c", p=128)
                            order2.append((src, "B"))
            last = strm.cursor

            def rel0(c):
                d = [strm.rel[m].v for m in strm.rel if m % 8 == c % 8]
                return tuple(t for v in d[-1:] for t in v)

            s2 = Stream(b2, order2, raw, RS2, rel0, False)
            DQ2, IQ2 = Pool(DS2), Pool(IS2)
            parts = {n: [] for n in b2.q}
            sent2 = []
            for j in range(7):
                mark = {n: len(q.items) for n, q in b2.q.items()}

                def reg(e, j=j):
                    regs["e"] = e.value_load(OVF[0:1, j + 1:j + 2], min_val=0, max_val=15)
                b2.q["S"].items.append(([], reg, None, 0))
                s2.go(12 * j, 12 * j + 12)

                def src(i, name, k, n):
                    return None, "B"

                b2.spawn(experts(b2, s2, [16 + j], src, R, idx, zone, DQ2, IQ2, TP, sent2), 10, "extra")
                b2.run()
                for n, q in b2.q.items():
                    if n == "S":
                        for s_ in RS2 + DS2:
                            if s_ in b2.dsem:
                                q.items.append(([(s_, b2.dsem[s_])], None, None, 0))
                    elif n == "G":
                        for s_ in IS2:
                            if s_ in b2.dsem:
                                q.items.append(([(s_, b2.dsem[s_])], None, None, 0))
                    if q.n:
                        q.items.append(([(q.name, q.n)], None, None, 0))
                    parts[n].append(q.items[mark[n]:])
            return parts

        def final(x_in, zone):
            GX = [nc_at(f"GX{i}", 16 + 4 * i, [128, 1024]) for i in range(8)]
            FG = at_("FG", 56, [128, 1024])
            FT = [at_(f"FT{i}", 4 * i, [128, 1024]) for i in range(4)]
            j = yield from load(TAB[0:1, :], SLOT[0:1, 0:1].bitcast(F32), 4, *g["moe"][2])
            gt = yield from load(FG[:, :], A["g_final_2"].rearrange("(o c) -> o c", o=1).broadcast_to([128, 1024]), 524288,
                                 j)
            gx = {}
            for b in range(8):
                sem, toks = yield IQ
                gx[b] = yield Op("G", 1000.0, lambda e, b=b: e.indirect_dma_start(
                    GX[b][:, :], None, YD[:, :], bass.IndirectOffsetOnAxis(SLOT[:, b:b + 1], axis=0)),
                    (*toks, j, *g["zeros2"]), 1, sem, 524288)
                IQ.put(sem, gx[b])

            def one(T):
                for k in range(2):
                    for h in range(2):
                        x = X[:, T, h * 512:h * 512 + 512]
                        w = (yield x_in[(T, h)]) if k == 0 else (us[h],)
                        u = yield stt(x, GX[2 * T + k][:, h * 512:h * 512 + 512], CW[:, 2 * T + k:2 * T + k + 1], x,
                                      ALU.mult, ALU.add, 512, gx[2 * T + k], g["cw"], *w)
                        us = (u, None) if h == 0 and k == 0 else us
                        us = (u, us[1]) if h == 0 else (us[0], u)
                fa, fb = Fut(), Fut()
                fa.set((us[0],))
                fb.set((us[1],))
                r = yield from rms_rows(T, X[:, T, :], (fa, fb), FT[T], (j,), FG, (gt,), None, 1e-6, None, None)
                yield from load(out[0, T * 128:T * 128 + 128, :], FT[T][:, :], 524288, *r)

            for T in range(4):
                spawn(one(T), 2 + T, f"final{T}")

        def zero_fill(m):
            g["zeros"] = yield from load(TAB.rearrange("(t s) o -> t (s o)", t=23), MASK[0:23, 0:128], 11776, m)
            dst = YD[16 * 128:23 * 128, :].rearrange("(t p) c -> p t c", p=128)
            z_ = MASK[:, :].unsqueeze(1).broadcast_to([128, 7, 512])
            a = yield from load(dst[:, :, 0:512], z_, 1835008, m)
            b = yield from load(dst[:, :, 512:1024], z_, 1835008, m)
            g["zeros2"] = (a, b)

        def split_out(k, o, t, h, l, rdy, w):
            th = yield act(h, o[:, :], AF.Copy, 512, t, *w)
            tl = yield tt(l, o[:, :], h.bitcast(F32), ALU.subtract, 512, th, *w)
            OP.put(o, tl)
            g["oa_last"] = tl
            for T in range(4):
                rdy.f[(k, T)].set((th, tl))

        def ax_tables(z, g):
            AXT = at_("AXT", 16, [128, 2, 4, 128])

            def th():
                stage, sf = yield STG
                gv = stage[:, 0:128]
                t0 = yield from load(gv[:, 0:64], A["g_q_2"].broadcast_to([128, 64]), 32768, *sf)
                t1 = yield from load(gv[:, 64:128], A["g_k_2"].broadcast_to([128, 64]), 32768, *sf)
                ax = stage[:, 128:640].rearrange("p (t c) -> p t c", t=4)
                t2 = yield from load(ax, A["axial"], 262144, *sf)
                gsw = stage[:, 640:768]
                g4 = gv.rearrange("p (c s) -> p c s", s=2)
                s4 = gsw.rearrange("p (c s) -> p c s", s=2)
                u0 = yield cp(s4[:, :, 0], g4[:, :, 1], 64, t0, t1)
                u1 = yield cp(s4[:, :, 1], g4[:, :, 0], 64)
                r = []
                for w_ in range(2):
                    r.append((yield tt(AXT[:, w_, :, 0:64], ax[:, :, 0:64],
                                       gv[:, w_ * 64:w_ * 64 + 64].unsqueeze(1).broadcast_to([128, 4, 64]), ALU.mult, 256,
                                       t2, t0, t1, *z)))
                    r.append((yield tt(AXT[:, w_, :, 64:128], ax[:, :, 64:128],
                                       gsw[:, w_ * 64:w_ * 64 + 64].unsqueeze(1).broadcast_to([128, 4, 64]), ALU.mult, 256,
                                       u0, u1)))
                STG.put(stage, *r)
                g["axt"] = tuple(r)
            spawn(th(), 2, "axt")
            return AXT

        def nc_at(name, off, shape):
            if name not in alloc:
                alloc[name] = at(name, off, shape, F32)
            return alloc[name]

        def root():
            yield from start()
            x6, zone, nxt = yield from layer0(pre1)
            x6, zone, nxt = yield from layer1(x6, zone, nxt, pre2)
            x6, zone = yield from block2(x6, zone, nxt)
            yield from moe(x6, zone)
            g["fin"] = (x6, zone)
            mm_ = yield from gather(g["moe_rms"])
            g["moe_rms_t"] = mm_
            strm.over = True
        def wait_all():
            for s in DS:
                if s in bd.dsem:
                    bd.q["S"].items.append(([(s, bd.dsem[s])], None, None, 0))

        strm.go(0, 1 << 30)
        spawn(root(), 10, "spine")
        bd.run()
        bd.parts = {n: [q.items, [], []] for n, q in bd.q.items()}
        if "fin" in g:
            x6, zone = g["fin"]
            for n, q in bd.q.items():
                q.items.append(([(t.sem, t.val) for t in g["ovf"]], None, None, 0))
            extra = further(zone)
            for n, q in bd.q.items():
                q.items = []
                bd.parts[n][1:] = [extra[n], q.items]
            spawn(final(x6, zone), 1, "final")
            bd.run()
        wait_all()
        return bd

    emission(True)
    bd = emission(False)
    play(bd)
    ctx.close()
    return bd


_INS = ["x", "p", "ev_w_in", "ev_w_out", "da_lambda", "da_subln_g", "hg_lb_logits", "hg_norm_g", "od_w_in", "od_w_out",
        "ln1_g", "ln1_b", "ffn_w1", "ffn_w2", "ln2_g", "ln2_b", "ple_w_proj", "ple_w_gate", "ple_norm_g", "mem_2",
        "g_mix_2", "w_in_2", "g_q_2", "g_k_2", "w_att_out_2", "sgu_ln_g_2", "sgu_ln_b_2", "w_s_2", "b_s_2",
        "w_sgu_out_2", "w_out_2", "g_cross_2", "g_mem_2", "w_cq_2", "w_ckv_2", "w_co_2", "g_moe_2", "w_rg_2", "b_rg_2",
        "w_re_2", "b_re_2", "w_gate_2", "w_up_2", "w_down_2", "g_final_2"]


def kernel(**inputs):
    import numpy as _np
    import concourse.bacc as _bacc
    from concourse import mybir as _mybir
    from concourse.bass_utils import run_bass_kernel_spmd as _run

    nc = _bacc.Bacc("TRN2", target_bir_lowering=False, num_devices=1)
    arrays, A = {}, {}
    given = [(name, inputs[name]) for name in _INS] + list(constants().items())
    for name, value in given:
        a = _np.ascontiguousarray(value)
        arrays[f"in_{name}_dram"] = a
        A[name] = nc.dram_tensor(f"in_{name}_dram", a.shape, _mybir.dt.from_np(a.dtype), kind="ExternalInput").ap()
    out = nc.dram_tensor("out_0_dram", (1, 512, 1024), _mybir.dt.from_np(_np.dtype("float32")),
                         kind="ExternalOutput").ap()
    build(nc, A, out)
    r = _run(nc, [arrays], core_ids=[0])
    return r.results[0]["out_0_dram"]
```

```python
import numpy as np
import concourse.bass as bass
from concourse import mybir
from contextlib import ExitStack


class Tok:
    __slots__ = ("sem", "val", "t")

    def __init__(self, sem, val, t):
        self.sem, self.val, self.t = sem, val, t


class Fut:
    __slots__ = ("v",)

    def __init__(self):
        self.v = None

    def set(self, v):
        self.v = v


class AllOf:

    def __init__(self, fs):
        self.fs = fs

    @property
    def v(self):
        if any(f.v is None for f in self.fs):
            return None
        return tuple(t for f in self.fs for t in f.v)


class Pool:

    def __init__(self, items):
        self.free = [(it, ()) for it in items]

    def put(self, item, *toks):
        self.free.append((item, toks))

    def pick(self):
        best = min(range(len(self.free)), key=lambda i: (max([t.t for t in self.free[i][1]], default=0.0), i))
        return self.free.pop(best)


class Op:
    __slots__ = ("eng", "cost", "fn", "waits", "inc", "sem", "nbytes")

    def __init__(self, eng, cost, fn, waits, inc=1, sem=None, nbytes=0):
        self.eng, self.cost, self.fn, self.waits, self.inc, self.sem, self.nbytes = eng, cost, fn, waits, inc, sem, nbytes


class Queue:
    def __init__(self, name):
        self.name, self.items, self.n, self.t, self.seen = name, [], 0, 0.0, {}


class Thread:
    __slots__ = ("gen", "prio", "req", "name")


PR = (-5, 3, 40)


class Board:

    LAG = {"TT": 200.0, "TA": 197.0, "TV": 196.0, "TG": 222.0, "AT": 280.0, "AA": 200.0, "AV": 235.0, "AG": 109.0,
           "VT": 230.0, "VA": 128.0, "VV": 127.0, "VG": 155.0, "GT": 200.0, "GA": 128.0, "GV": 60.0, "GG": 96.0}

    def __init__(self, mark=""):
        self.q = {n: Queue(n + mark) for n in ("T", "A", "V", "G", "S")}
        self.threads = []
        self.dma_t = 0.0
        self.dsem = {}

    def spawn(self, gen, prio=5, name=""):
        th = Thread()
        th.gen, th.prio, th.req, th.name = gen, prio, None, name
        self.threads.append(th)
        self.step(th, None)

    def step(self, th, value):
        try:
            th.req = th.gen.send(value)
        except StopIteration:
            self.threads.remove(th)

    def start(self, op):
        q = self.q[op.eng]
        t = q.t
        for w in op.waits:
            k = self.LAG.get(w.sem[0] + op.eng, 150.0) if w.sem[0].isupper() else 950.0
            if w.t + k > t:
                t = w.t + k
        return t

    def emit(self, op):
        q = self.q[op.eng]
        t = self.start(op)
        waits = []
        for w in op.waits:
            if q.seen.get(w.sem, 0) < w.val:
                q.seen[w.sem] = w.val
                waits.append((w.sem, w.val))
        if op.sem is not None:
            v = self.dsem.get(op.sem, 0) + 16
            self.dsem[op.sem] = v
            q.items.append((waits, op.fn, op.sem, 16))
            self.dma_t = max(self.dma_t, t + 1400.0) + op.nbytes / 360.0
            q.t = t + op.cost
            return Tok(op.sem, v, self.dma_t)
        q.t = t + op.cost
        if op.inc:
            q.n += 1
            q.items.append((waits, op.fn, q.name, 1))
            return Tok(q.name, q.n, q.t)
        q.items.append((waits, op.fn, None, 0))
        return Tok(q.name, q.n + 1, q.t)

    def run(self):
        while self.threads:
            moved = True
            while moved:
                moved = False
                for th in list(self.threads):
                    r = th.req
                    if isinstance(r, (Fut, AllOf)):
                        if r.v is not None:
                            self.step(th, r.v)
                            moved = True
                    elif isinstance(r, Pool):
                        if r.free:
                            self.step(th, r.pick())
                            moved = True
                    elif callable(r):
                        if r():
                            self.step(th, None)
                            moved = True
            best, key = None, None
            for th in self.threads:
                if isinstance(th.req, Op):
                    p = th.prio() if callable(th.prio) else th.prio
                    k = (self.start(th.req) + 20.0 * p, p)
                    if best is None or k < key:
                        best, key = th, k
            if best is None:
                if self.threads:
                    raise RuntimeError("stuck: " + ", ".join(t.name for t in self.threads))
                return
            self.step(best, self.emit(best.req))


F32, F32R, U32, I32 = mybir.dt.float32, mybir.dt.float32r, mybir.dt.uint32, mybir.dt.int32
ALU, AF, AX = mybir.AluOpType, mybir.ActivationFunctionType, mybir.AxisListType
BIG = 1.0e30


def constants():
    c = {}
    c["ident"] = np.eye(128, dtype=np.float32)
    d = np.arange(128)[:, None] - np.arange(128)[None, :]
    causal = np.where(d >= 0, 0.0, -BIG).astype(np.float32)
    m0 = np.zeros((128, 512), np.float32)
    m0[:, 384:] = causal
    c["mask0"] = m0

    def mult(dist):
        n = ((dist >= 0) & (dist <= 128)).astype(np.float64) + ((dist >= 0) & (dist % 4 == 0)) \
            + ((dist >= 0) & (dist % 16 == 0))
        return np.where(n > 0, 8.0 * np.log(np.maximum(n, 1.0)), -BIG).astype(np.float32)

    c["mask1"] = np.concatenate([mult(d + 384), mult(d + 256), mult(d + 128), mult(d)], axis=1)
    h = np.arange(128) // 64
    c["tri"] = ((d <= 0) & (h[:, None] == h[None, :])).astype(np.uint32)
    reset = np.ones((128, 512), np.float32)
    reset[:, ::64] = 0.0
    c["reset"] = reset
    inv = (np.float32(500000.0) ** (-np.arange(0, 16, 2, dtype=np.float32) / np.float32(16))).astype(np.float32)
    ang = (np.arange(512, dtype=np.float32)[:, None] * inv[None, :]).astype(np.float32)
    cs, sn = np.cos(ang).astype(np.float32), np.sin(ang).astype(np.float32)
    c["rope"] = np.concatenate([cs, cs, -sn, sn], axis=1).reshape(4, 128, 32).transpose(1, 0, 2).copy()
    inv = (np.float32(10000.0) ** (-np.arange(16, dtype=np.float32) / np.float32(16))).astype(np.float32)
    ang = np.concatenate([np.repeat(np.arange(8), 64)[:, None].astype(np.float32) * inv,
                          np.tile(np.arange(64), 8)[:, None].astype(np.float32) * inv], axis=1).astype(np.float32)
    cs, sn = np.cos(ang).astype(np.float32), np.sin(ang).astype(np.float32)
    ax = np.stack([np.repeat(cs, 2, axis=1), np.stack([-sn, sn], axis=2).reshape(512, 64)], axis=1)
    p = np.arange(128)
    route = np.zeros((128, 544), np.float32)
    route[:, 0:128] = np.arange(128)
    route[:, 128:136] = 128 * (np.arange(8) // 2)[None, :] + p[:, None] - 1000
    route[:, 136:264] = (np.arange(128) % 8 != 0)
    route[:, 264:280] = 1.0
    route[:, 280:408] = (p[:, None] < p[None, :])
    route[:, 408:536] = 1.0
    route[:, 536:540] = (8, 4, 2, 1)
    route[:, 540:543] = (128, 256, 384)
    route[:, 543] = np.arange(128) + 512 - 1000
    c["route"] = route
    c["axial"] = ax.reshape(4, 128, 128).transpose(1, 0, 2).copy()
    return c


def build(nc, A, out):
    ctx = ExitStack()
    KB = 1024
    BASE = 16512
    MORE = 2
    ALPHA = float(np.float32(4.0 ** 0.25))

    def at(name, off, shape, dt):
        return nc.alloc_sbuf_tensor_at(name, shape, dt, offset=BASE + int(off * KB))

    X = at("X", 0, [128, 4, 1024], F32)
    XH = at("XH", 16, [128, 8, 512], F32R)
    XL = at("XL", 32, [128, 8, 512], F32R)
    WH = at("WH", 48, [128, 8, 1024], F32R)
    WL = at("WL", 80, [128, 8, 1024], F32R)
    RAW = [at(f"RAW{i}", 112 + 4 * i, [128, 1024], F32) for i in range(3)]
    ST = [at(f"ST{i}", 124 + 4 * i, [128, 1024], F32) for i in range(2)]
    C0 = 132
    ident = at("ident", C0, [128, 128], F32)
    MASK = at("MASK", C0 + 0.5, [128, 512], F32)
    TRI = at("TRI", C0 + 2.5, [128, 128], U32)
    ROPE = at("ROPE", C0 + 3, [128, 4, 32], F32)
    GDA = at("GDA", C0 + 3.5, [128, 128], F32)
    GHG = at("GHG", C0 + 4, [128, 128], F32)
    SM = at("SM", C0 + 4.5, [128, 256], F32)
    ropes = [at(f"RT{i}", C0 + 5.5 + i, [128, 2, 8, 16], F32) for i in range(1)]
    D0 = 138.5

    IDX = at("IDX", D0 + 68.0625, [128, 24], U32)
    OVF = at("OVF", D0 + 68.1875, [128, 8], I32)
    IOTA = at("IOTA", D0 + 68.25, [128, 128], F32)
    ROWT = at("ROWT", D0 + 68.75, [128, 7, 4], F32)
    ROWW = at("ROWW", D0 + 68.875, [128, 24], F32)
    PUT = at("PUT", D0 + 69, [128, 24], U32)
    SEL = at("SEL", C0 + 0.5, [128, 512], F32R)
    RAW += [at(f"RAW{i + 3}", D0 + 44 + 4 * i, [128, 1024], F32) for i in range(6)]
    RAW += [at(f"RAW{i + 9}", D0 + 4 * i, [128, 1024], F32) for i in range(7)]
    RAW += [ST[1]] + [X[:, T, :] for T in range(4)]

    def small(a, n):
        return SM[:, a:a + n]

    half = small(0, 4)
    half8 = small(40, 8)
    lam = small(4, 4)
    vecT = small(8, 16)
    lbs = small(24, 16)
    stats = [small(48 + 16 * i, 16) for i in range(13)]

    dram = lambda name, shape: nc.dram_tensor(name, shape, F32).ap()
    QKD = [dram(f"qkd{g}", [4, 128, 1024]) for g in range(6)]
    ED = [dram(f"ed{l}", [4, 128, 1024]) for l in range(2)]
    VD = dram("vd", [4, 128, 512])
    QQD = dram("qqd", [4, 128, 1024])
    KTD, MVD = dram("ktd", [4, 128, 256]), dram("mvd", [2, 128, 512])
    HD, SUM = dram("hd", [512, 1024]), dram("sum", [640, 1024])
    TGD = dram("tgd", [2, 8, 128, 512])

    ps = [ctx.enter_context(nc.psum_tensor(f"ps{i}", [128, 512], F32)) for i in range(8)]
    sems = {n: ctx.enter_context(nc.semaphore("s_" + n)) for n in ("T", "A", "V", "G", "T2", "A2", "V2", "G2")}
    RS = [[f"raw{i}"] for i in range(21)]
    RS2 = [[f"rawb{i}"] for i in range(17)]
    for i in range(3):
        RS[i].append(f"rawq{i}")
    DS = [f"d{i}" for i in range(16)]
    DS2 = [f"e{i}" for i in range(4)]
    IS, IS2 = [f"i{i}" for i in range(8)], [f"j{i}" for i in range(2)]
    for n in sum(RS + RS2, []) + DS + DS2 + IS + IS2:
        sems[n] = ctx.enter_context(nc.semaphore("s_" + n))

    def mm(o, l, r, st, sp, cost, *w, inc=None):
        return Op("T", cost, lambda e: e.matmul(o, lhsT=l, rhs=r, start=st, stop=sp), w, sp if inc is None else inc)

    def tr(o, i, *w, inc=False):
        return Op("T", 110.0, lambda e: e.transpose(o, i, ident[:, :]), w, inc)

    def act(o, i, f, n, *w, bias=None, scale=1.0, acc=None):
        k = {}
        if bias is not None:
            k["bias"] = bias
        if acc is not None:
            k["accum_out"] = acc
        return Op("A", 0.83 * n + 55.0 + (130.0 if bias is not None else 0.0) + (100.0 if acc is not None else 0.0),
                  lambda e: e.activation(o, i, f, scale=scale, **k), w)

    def tt(o, a, b, op, n, *w):
        return Op("V", 1.04 * n + 68.0, lambda e: e.tensor_tensor(o, a, b, op), w)

    def cp(o, i, n, *w):
        return Op("V", 1.04 * n + 68.0, lambda e: e.tensor_copy(o, i), w)

    def ts(o, i, s1, s2, op0, op1, n, *w):
        if op1 is None:
            return Op("V", 0.52 * n + 130.0, lambda e: e.tensor_scalar(o, i, s1, None, op0), w)
        return Op("V", 0.52 * n + 130.0, lambda e: e.tensor_scalar(o, i, s1, s2, op0, op1), w)

    def stt(o, a, s, b, op0, op1, n, *w):
        return Op("V", 1.04 * n + 130.0,
                  lambda e: e.scalar_tensor_tensor(out=o, in0=a, scalar=s, in1=b, op0=op0, op1=op1), w)

    def vop(fn, n, *w):
        return Op("V", 1.04 * n + 68.0, fn, w)

    def gop(fn, n, *w):
        return Op("G", 3.0 * n + 280.0, fn, w)

    def dma(o, i, nbytes, sem, *w, eng="S"):
        return Op(eng, 60.0, lambda e: e.dma_start(o, i() if callable(i) else i), w, 1, sem, nbytes)

    def play(bd):
        blk = ctx.enter_context(nc.Block())

        def steps(e, items):
            for waits, fn, sem, inc in items:
                for s, v in waits:
                    e.wait_ge(sems[s], v)
                if fn is not None:
                    i = fn(e)
                    if sem is not None:
                        i.then_inc(sems[sem], inc)

        def run(name):
            def body(e):
                first, extra, rest = bd.parts[name]
                steps(e, first)
                deeper(e, name, MORE, extra)
                steps(e, rest)
            return body

        def deeper(e, name, j, extra):
            if extra:
                with e.If(regs[name] > j):
                    steps(e, extra[0])
                    deeper(e, name, j + 1, extra[1:])

        blk.sync(run("S"))
        blk.tensor(run("T"))
        blk.scalar(run("A"))
        blk.vector(run("V"))
        blk.gpsimd(run("G"))

    order = []
    regs = {}

    def view(ap, kind):
        if kind == "A":
            return ap.rearrange("p (a c) -> p a c", a=4)
        if kind == "B":
            return ap.rearrange("p (a c) -> p a c", a=2)
        return ap.rearrange("p (a s c) -> p a s c", a=2, s=2)

    alloc = {}

    def at_(name, off, shape, dt=F32):
        key = (name, off)
        if key not in alloc:
            alloc[key] = at(name, D0 + off, shape, dt)
        return alloc[key]

    def emission(record):
        bd = Board()
        spawn = bd.spawn
        G, S, TP, OP = Pool(ps[0:3]), Pool(ps[3:5]), Pool(ps[5:7]), Pool(ps[7:8])
        STG = Pool(ST)
        DQ = Pool(DS)
        IQ = Pool(IS)
        SP = Pool(stats)
        SP2 = SP
        RP = Pool(ropes)
        g = {}

        def load(o, i, nbytes, *w):
            sem, toks = yield DQ
            tok = yield dma(o, i, nbytes, sem, *toks, *w)
            DQ.put(sem, tok)
            return tok

        class Stream:
            def __init__(self, board, order_, raw, names, rel0, record_):
                self.board, self.order, self.raw, self.names, self.rel0 = board, order_, raw, names, rel0
                self.record, self.cursor, self.over = record_, 0, False
                self.expert = None
                self.loaded, self.hi, self.lo, self.rel = {}, {}, {}, {}

            def fut(self, d, k):
                if k not in d:
                    d[k] = Fut()
                return d[k]

            def go(self, c0, c1):
                self.board.spawn(self.loader(c0, c1), 0, "loader")
                self.at = {}
                for w in ("hi", "lo"):
                    self.at[w] = c0
                    self.board.spawn(self.parts(w, c0, c1), lambda w=w: self.urgency(self.at[w]), w)

            def loader(self, c, end):
                while c < end:
                    yield lambda: len(self.order) > c or self.over
                    if c >= len(self.order):
                        return
                    slot, toks = yield self.raw
                    src, kind = self.order[c]
                    if callable(src) and src.j != self.expert:
                        w = yield g["ovf"]
                        yield Op("S", 60.0, read_expert(src.j), w, 0)
                        self.expert = src.j
                    dst = view(RAW[slot][:, :], kind)
                    if kind == "Q":
                        tok = []
                        for j in range(2):
                            tok.append((yield dma(dst[:, :, j, :], src[:, :, j, :], 262144, self.names[slot][j],
                                                  *toks)))
                        tok = tuple(tok)
                    else:
                        tok = ((yield dma(dst, src, 524288, self.names[slot][0], *toks)),)
                    self.fut(self.loaded, c).set((slot, tok))
                    c += 1

            def parts(self, which, c, end):
                while c < end:
                    yield lambda: c in self.loaded or (self.over and c >= len(self.order))
                    if c not in self.loaded:
                        return
                    slot, tok = yield self.loaded[c]
                    free = (yield self.fut(self.rel, c - 8)) if c >= 8 else self.rel0(c)
                    w = (*tok, *free)
                    x, h, l = RAW[slot][:, :], WH[:, c % 8, :], WL[:, c % 8, :]
                    if which == "hi":
                        t = yield act(h, x, AF.Copy, 1024, *w)
                        self.fut(self.hi, c).set(t)
                    else:
                        th = yield self.fut(self.hi, c)
                        t = yield tt(l, x, h.bitcast(F32), ALU.subtract, 1024, *w, th)
                        self.fut(self.lo, c).set(t)
                        if slot < 17:
                            self.raw.put(slot, th, t)
                        else:
                            g["x_read"][slot - 17].set((th, t))
                    c += 1
                    self.at[which] = c

            def urgency(self, c):
                d = c - self.cursor
                return PR[0] if d <= 1 else PR[1] if d <= 3 else PR[2]

            def use(self, src, kind):
                c = self.cursor
                self.cursor += 1
                if self.record:
                    self.order.append((src, kind))
                th = yield self.fut(self.hi, c)
                tl = yield self.fut(self.lo, c)
                k = "B" if kind == "Q" else kind
                return c, view(WH[:, c % 8, :], k), view(WL[:, c % 8, :], k), (th, tl)

        raw = Pool([0, 1, 2])
        strm = Stream(bd, order, raw, RS, lambda c: (), record)

        def xh(k):
            return XH[:, k, :]

        def xl(k):
            return XL[:, k, :]

        def rows(buf, k0=0):
            return lambda k: buf[:, k + k0, :]

        def wA(w, k, n):
            return w[k * 128:(k + 4) * 128, n:n + 256].rearrange("(a p) c -> p a c", p=128), "A"

        def wB(w, k, n):
            return w[k * 128:(k + 2) * 128, n:n + 512].rearrange("(a p) c -> p a c", p=128), "B"

        def wQ(w, k, q0, k0):
            a = w[k * 128:(k + 2) * 128, :].rearrange("(a p) c -> p a c", p=128)
            n = k0 - q0
            return a[:, :, q0:q0 + 2 * n].rearrange("p a (s c) -> p a s c", s=2)[:, :, :, 0:256], "Q"

        def gemmA(w, n0, n1, K, H, L, ready, evac, N=512):
            cost = 216 if N == 512 else 110
            for n in range(n0, n1, 256):
                got = []
                for nt in range(2):
                    bank, free = yield G
                    for k in range(K):
                        if k // 4 == len(got):
                            got.append((yield from strm.use(*wA(w, k, n))))
                        c, wh, wl, tw = got[k // 4]
                        x = yield ready(k, None)
                        h = wh[:, k % 4, nt * 128:nt * 128 + 128]
                        l = wl[:, k % 4, nt * 128:nt * 128 + 128]
                        last = k == K - 1
                        drop = nt == 1 and (k % 4 == 3 or last)
                        o = bank[:, 0:N]
                        yield mm(o, h, H(k), k == 0, False, cost, *tw, *x, *free)
                        yield mm(o, h, L(k), False, False, cost)
                        t = yield mm(o, l, H(k), False, last, cost, inc=last or drop)
                        if drop:
                            strm.fut(strm.rel, c).set((t,))
                        g["last"] = t
                    spawn(evac((n - n0) // 128 + nt, bank, t), 2, "evacA")

        def gemmB(src, halves, K, H, L, ready, evac, TN=4, N=512, strm=strm, spawn=spawn, rows_first=False):
            kc = 1024 // N
            cost = 216 if N == 512 else 110
            got = [[] for _ in range(halves)]
            for u in range(halves * TN):
                nh, T = (u % halves, u // halves) if rows_first else (u // TN, u % TN)
                bank, free = yield G
                for k in range(K):
                    if k // kc == len(got[nh]):
                        got[nh].append((yield from strm.use(*src(nh, kc * (k // kc)))))
                    c, wh, wl, tw = got[nh][k // kc]
                    x = yield ready(k, T)
                    h = H(k)[:, T * 128:T * 128 + 128]
                    l = L(k)[:, T * 128:T * 128 + 128]
                    last = k == K - 1
                    drop = T == TN - 1 and (k % kc == kc - 1 or last)
                    o, j = bank[:, 0:N], k % kc
                    yield mm(o, h, wh[:, j, :], k == 0, False, cost, *tw, *x, *free)
                    yield mm(o, h, wl[:, j, :], False, False, cost)
                    t = yield mm(o, l, wh[:, j, :], False, last, cost, inc=last or drop)
                    if drop:
                        strm.fut(strm.rel, c).set((t,))
                    g["last"] = t
                spawn(evac(nh, T, bank, t), 2, "evacB")

        class Ready:

            def __init__(self, n=4):
                self.n = n
                self.f = {(k, T): Fut() for k in range(8) for T in range(n)}

            def __call__(self, k, T):
                return self.f[(k, T)] if T is not None else AllOf([self.f[(k, t)] for t in range(self.n)])

        def turn_T(nat, T, H, L, ready, k0, kn, *w):
            bank, free = yield TP
            for j in range(kn):
                t = yield tr(bank[:, j * 128:j * 128 + 128], nat[:, (k0 + j) * 128:(k0 + j + 1) * 128], *w, *free,
                             inc=j == kn - 1)
            b3 = bank[:, 0:kn * 128].rearrange("p (a c) -> p a c", a=kn)
            h = H[:, k0:k0 + kn, T * 128:T * 128 + 128]
            l = L[:, k0:k0 + kn, T * 128:T * 128 + 128]
            th = yield act(h, b3, AF.Copy, kn * 128, t)
            tl = yield tt(l, b3, h.bitcast(F32), ALU.subtract, kn * 128, t, th)
            TP.put(bank, tl)
            for j in range(kn):
                ready.f[(k0 + j, T)].set((th, tl))


        def start():
            g["ident"] = yield from load(ident[:, :], A["ident"], 65536)
            for T in range(4):
                g["x", T] = yield from load(X[:, T, :], A["x"][0, T * 128:(T + 1) * 128, :], 524288)
            t = yield gop(lambda e: e.memset(half, -0.5), 4)
            t = yield gop(lambda e: e.memset(half8, -0.5), 4)
            g["half"] = t

        def turns_x(ready, H, L, after):
            for T in range(4):
                for k0 in (0, 4):
                    spawn(turn_T(X[:, T, :], T, H, L, ready, k0, 4, g["ident"], *after(T)), 3, "turn_x")

        def ev_qk(g_, w=()):
            def ev(nh, T, bank, tok):
                slot, free = yield STG
                nd = slot[:, :].rearrange("p (h d c) -> p h d c", h=8, d=2)
                b3 = bank[:, :].rearrange("p (h c) -> p h c", h=8)
                t = yield act(nd, b3.unsqueeze(2).broadcast_to([128, 8, 2, 64]), AF.Copy, 1024, tok, *free)
                r, rf = yield RP
                m1, m2 = r[:, 0, :, :], r[:, 1, :, :]
                cc = ROPE[:, T, 0:16].unsqueeze(1).broadcast_to([128, 8, 16])
                ns = ROPE[:, T, 16:24].unsqueeze(1).broadcast_to([128, 8, 8])
                sn = ROPE[:, T, 24:32].unsqueeze(1).broadcast_to([128, 8, 8])
                t1 = yield tt(m1, b3[:, :, 0:16], cc, ALU.mult, 128, t, g["rope"], *rf)
                t2 = yield tt(m2[:, :, 0:8], b3[:, :, 8:16], ns, ALU.mult, 64, t, *rf)
                t3 = yield tt(m2[:, :, 8:16], b3[:, :, 0:8], sn, ALU.mult, 64, t)
                G.put(bank, t3)
                t4 = yield tt(nd[:, :, :, 0:16], m1.unsqueeze(2).broadcast_to([128, 8, 2, 16]),
                              m2.unsqueeze(2).broadcast_to([128, 8, 2, 16]), ALU.add, 256, t1, t3)
                RP.put(r, t4)
                t = yield from load(QKD[g_][T], slot[:, :], 524288, t4)
                STG.put(slot, t)
                qkd[(g_, T)].set((t,))
            return ev

        qkd = {}

        def stacks(base, P, stk, free, ndp, done, *w):
            for T in range(4):
                (d,) = yield qkd[(base + P // 2, T)]
                nd, nf = yield ndp
                o = 256 * (P % 2)
                src = QKD[base + P // 2][T].rearrange("p (s f) -> p s f", s=2)[:, :, o:o + 256]
                t = yield from load(nd[:, :].rearrange("p (s f) -> p s f", s=2), src, 262144, d, *nf, *w)
                spawn(stack_T(stk, free, ndp, nd, T, t, done[T]), 4, f"stk{P}.{T}")

        def stack_T(stk, free, ndp, nd, T, t, done):
            bank, bf = yield TP
            for j in range(4):
                u = yield tr(bank[:, j * 128:j * 128 + 128], nd[:, j * 128:j * 128 + 128], t, *bf, inc=j == 3)
            ndp.put(nd, u)
            c = slice(T * 128, T * 128 + 128)
            b3 = bank[:, :].rearrange("p (a c) -> p a c", a=4)
            th = yield act(stk[:, 0:4, c], b3, AF.Copy, 512, u, *free)
            t1 = yield tt(stk[:, 4:6, c], b3[:, 0:2, :], stk[:, 0:2, c].bitcast(F32), ALU.subtract, 256, th)
            k = stk[64:128, 2:4, c]
            t2 = yield tt(k, b3[64:128, 2:4, :], k.bitcast(F32), ALU.subtract, 256, th)
            TP.put(bank, t2)
            done.set((th, t1, t2))

        def soft_row(s, n, mask, scale, e, t, ef):
            v, vf = yield SP
            tm = yield vop(lambda x: x.tensor_tensor_reduce(e[:, 0:n], s[:, 0:n], mask[:, 512 - n:512], -scale, 3.0e38,
                                                            ALU.add, ALU.min, v[:, 0:1]), n, t, *ef, *vf)
            S.put(s, tm)
            te = yield act(e[:, 0:n], e[:, 0:n], AF.Exp, n, tm, bias=v[:, 0:1], scale=-1.0, acc=v[:, 1:2])
            tr_ = yield vop(lambda x: x.reciprocal(v[:, 2:3], v[:, 1:2]), 8, te)
            return v, te, tr_

        def scores(stk, hh, i, mask, e, ef, rdy):
            n = 128 * (i + 1)
            w = []
            for T in range(i + 1):
                w += list((yield rdy[T]))
            s, sf = yield S
            c = 110 if n < 512 else 216
            q = slice(128 * i, 128 * i + 128)
            yield mm(s[:, 0:n], stk[:, hh, q], stk[:, 2 + hh, 0:n], True, False, c, *w, *sf)
            t = yield mm(s[:, 0:n], stk[:, 4 + hh, q], stk[:, 2 + hh, 0:n], False, True, c)
            return (yield from soft_row(s, n, mask, 0.125, e, t, ef))

        def turn_P(e, n, pt, pf, *w):
            bank, bf = yield TP
            for j in range(n // 128):
                t = yield tr(bank[:, j * 128:j * 128 + 128], e[:, j * 128:j * 128 + 128], *w, *bf,
                             inc=j == n // 128 - 1)
            u = yield act(pt[:, 0:n], bank[:, 0:n], AF.Copy, n, t, *pf)
            TP.put(bank, u)
            return t, u

        def add_x(scale, xtok, then=None, mul=None):
            def ev(nh, T, bank, tok):
                x = X[:, T, nh * 512:nh * 512 + 512]
                w = yield xtok[(T, nh)]
                if mul is not None:
                    t = yield stt(x, bank[:, :], mul, x, ALU.mult, ALU.add, 512, tok, *w)
                elif scale == 1.0:
                    t = yield tt(x, x, bank[:, :], ALU.add, 512, tok, *w)
                else:
                    t = yield stt(x, x, scale, bank[:, :], ALU.mult, ALU.add, 512, tok, *w)
                G.put(bank, t)
                then[(T, nh)].set((t,))
            return ev

        def gather(fs):
            r = []
            for f in fs:
                r += list((yield f))
            return tuple(r)

        def pairs(d):
            r = []
            for k in sorted(d):
                r.append((yield d[k]))
            return r

        def xfuts():
            return {(T, nh): Fut() for T in range(4) for nh in range(2)}

        def gains(names, bufs, *w):
            out_ = []
            for a, b in zip(names, bufs):
                t = yield from load(b, a.broadcast_to([128, 1024]), 524288, *w)
                out_.append(t)
            return tuple(out_)

        def norm_ln(T, xt, gb, G1, B1, ready, out_x):
            a = yield xt[(T, 0)]
            v, vf = yield SP
            x0, x1 = X[:, T, 0:512], X[:, T, 512:1024]
            t0 = yield vop(lambda e: e.bn_stats(v[:, 0:6], x0), 512, *a, *vf)
            b = yield xt[(T, 1)]
            t1 = yield vop(lambda e: e.bn_stats(v[:, 6:12], x1), 512, *b, *vf)
            t = yield vop(lambda e: e.bn_aggr(v[:, 12:14], v[:, 0:12].rearrange("p (a b) -> p a b", a=2)), 12, t0, t1)
            t2 = yield gop(lambda e: e.tensor_scalar(v[:, 14:15], v[:, 13:14], 1e-5, None, ALU.add), 1, t)
            t2 = yield gop(lambda e: e.tensor_tensor(v[:, 15:16], v[:, 14:15], half[:, 0:1], ALU.pow), 1, t2, g["half"])
            gt = yield gb
            ok = []
            for h in range(2):
                x = (x0, x1)[h]
                c = slice(h * 512, h * 512 + 512)
                u = yield stt(x, x, v[:, 12:13], G1[:, c], ALU.subtract, ALU.mult, 512, t, *gt)
                u = yield stt(x, x, v[:, 15:16], B1[:, c], ALU.mult, ALU.add, 512, u, t2)
                ok.append(u)
                out_x[(T, h)].set((u,))
                spawn(turn_T(X[:, T, :], T, XH, XL, ready, 4 * h, 4, u), 2, "turn_ln")
            SP.put(v, *ok)

        def ple(l, base):
            pn = at_(f"pn{l}", base, [128, 4, 256])
            ph, pl = at_(f"ph{l}", base + 4, [128, 2, 512], F32R), at_(f"pl{l}", base + 8, [128, 2, 512], F32R)
            pg = at_(f"pg{l}", 40 + 4 * l, [128, 1024])
            rd = Ready()

            def prep():
                t = yield from load(pn[:, :, :], A["p"][l, 0].rearrange("(a p) c -> p a c", p=128), 524288)
                for T in range(4):
                    spawn(turn_T(pn[:, T, :], T, ph, pl, rd, 0, 2, t, g["ident"]), 3, "turn_p")
                g["pg", l] = yield from load(pg[:, :], A["ple_norm_g"][l:l + 1].broadcast_to([128, 1024]), 524288)

            spawn(prep(), 0, "ple_prep")
            tiles = {}

            def ev(nh, T, bank, tok):
                if nh == 0:
                    tiles[T] = yield ETP
                e, free = tiles[T]
                t = yield act(e[:, nh * 512:nh * 512 + 512], bank[:, :], AF.Copy, 512, tok, *free)
                G.put(bank, t)
                tiles[T] = (e, (t,))
                if nh == 0:
                    return
                v, vf = yield SP
                j, jf = yield STG
                t = yield vop(lambda x: x.tensor_tensor_reduce(j[:, :], e[:, :], e[:, :], 1.0, 0.0, ALU.mult, ALU.add,
                                                               v[:, 0:1]), 1024, t, *vf, *jf)
                STG.put(j, t)
                t = yield gop(lambda x: x.tensor_scalar(v[:, 1:2], v[:, 0:1], 1.0 / 1024, 1e-5, ALU.mult, ALU.add), 1, t)
                t = yield gop(lambda x: x.tensor_tensor(v[:, 2:3], v[:, 1:2], half[:, 0:1], ALU.pow), 1, t, g["half"])
                t = yield stt(e[:, :], e[:, :], v[:, 2:3], pg[:, :], ALU.mult, ALU.mult, 1024, t, g["pg", l])
                SP.put(v, t)
                t = yield from load(ED[l][T], e[:, :], 524288, t)
                ETP.put(e, t)
                ed[(l, T)].set((t,))

            yield from gemmB(lambda nh, k: wB(A["ple_w_proj"][l], k, nh * 512), 2, 2, rows(ph), rows(pl), rd, ev)

        ed = {(l, T): Fut() for l in range(2) for T in range(4)}
        ETP = Pool([at_(f"et{i}", 24 + 4 * i, [128, 1024]) for i in range(4)])

        def ffn(l, xr_, x0, x2, x1_ln, gb_w):
            W1, W2 = A["ffn_w1"][l], A["ffn_w2"][l]
            HH, HL = at_("HH", 0, [128, 10, 512], F32R), at_("HL", 20, [128, 10, 512], F32R)
            R = Pool([at_(f"FR{i}", 40 + 2 * i, [128, 512]) for i in range(2)])
            G1, B1 = at_("G2", 44, [128, 1024]), at_("B2", 48, [128, 1024])
            hr = {j: Fut() for j in range(32)}
            hrel = {}
            gb = Fut()

            def ld():
                r = yield from gains((A["ln2_g"][l:l + 1], A["ln2_b"][l:l + 1]), (G1[:, :], B1[:, :]), *gb_w)
                gb.set(r)

            spawn(ld(), 6, "ld2")
            if l == 0:
                spawn(spare(), 30, "spare")

            def ev_h(j0):
                def ev(n, bank, tok):
                    j = j0 + n
                    r, rf = yield R
                    w = hrel.get(j - 10, ())
                    t = yield act(r[:, :], bank[:, :], AF.Relu, 512, tok, *rf, *gb_w)
                    G.put(bank, t)
                    t = yield tt(r[:, :], r[:, :], r[:, :], ALU.mult, 512, t)
                    th = yield act(HH[:, j % 10, :], r[:, :], AF.Copy, 512, t, *w)
                    tl = yield tt(HL[:, j % 10, :], r[:, :], HH[:, j % 10, :].bitcast(F32), ALU.subtract, 512, th, *w)
                    R.put(r, th, tl)
                    hr[j].set((th, tl))
                return ev

            rdy = Ready()
            for T in range(4):
                spawn(norm_ln(T, x2, gb, G1, B1, rdy, x1_ln), 2 + T, f"ln2.{T}")
            steps = [xfuts() for _ in range(3)] + [x2]
            cur = x0
            lo_ = 0
            for q in range(4):
                hi_ = min(8 * q + 10, 32)
                yield from gemmA(W1, lo_ * 128, hi_ * 128, 8, xh, xl, xr_, ev_h(lo_))
                lo_ = hi_
                yield from gemmB(lambda nh, k: wB(W2, 8 * q + k, nh * 512), 2, 8,
                                 lambda k: HH[:, (8 * q + k) % 10, :], lambda k: HL[:, (8 * q + k) % 10, :],
                                 lambda k, T: hr[8 * q + k], add_x(ALPHA if q == 0 else 1.0, cur, steps[q]))
                cur = steps[q]
                for k in range(8):
                    hrel[8 * q + k] = (g["last"],)
            return rdy

        def gate(l, rdy, x_in, x_out, zone):
            E_ = at_("EE", 52, [128, 4, 1024])
            R = Pool([at_(f"FR{i}", 40 + 2 * i, [128, 512]) for i in range(2)])
            er = {T: Fut() for T in range(4)}

            def ld():
                for T in range(4):
                    (d,) = yield ed[(l, T)]
                    t = yield from load(E_[:, T, :], ED[l][T], 524288, d, *zone)
                    er[T].set((t,))

            spawn(ld(), 6, "ld_e")

            def ev(nh, T, bank, tok):
                r, rf = yield R
                et = yield er[T]
                w = yield x_in[(T, nh)]
                x = X[:, T, nh * 512:nh * 512 + 512]
                t = yield act(r[:, :], bank[:, :], AF.Sigmoid, 512, tok, *rf, *zone)
                G.put(bank, t)
                t = yield tt(r[:, :], r[:, :], E_[:, T, nh * 512:nh * 512 + 512], ALU.mult, 512, t, *et)
                t = yield tt(x, x, r[:, :], ALU.add, 512, t, *w)
                R.put(r, t)
                x_out[(T, nh)].set((t,))

            yield from gemmB(lambda nh, k: wB(A["ple_w_gate"][l], k, nh * 512), 2, 8, xh, xl, rdy, ev)

        def after_first(l, xr1, x3, zone, pre):
            x4, x5, x6 = xfuts(), xfuts(), xfuts()
            rdy = yield from ffn(l, xr1, x3, x4, x5, zone)
            z = (yield from gather(x4.values())) + (g["last"],)
            zz = (yield from gather(x5.values()))
            nxt = pre(x6, z)
            yield from gate(l, rdy, x5, x6, z + zz)
            z2 = yield from gather(x6.values())
            return x6, z2 + z + zz, nxt

        def layer0(pre):
            W = A["ev_w_in"][0]
            xr = Ready()
            turns_x(xr, XH, XL, lambda T: (g["x", T],))
            yield from ple(0, 0)
            yield from ple(1, 12)
            pw = []
            for f in ed.values():
                pw += list((yield f))
            pw = tuple(pw) + (g["last"],)
            HI = at_("HI", 16, [128, 4, 512])
            GS = at_("GS", 24, [128, 4, 512])
            FS = at_("FS", 32, [128, 4, 512])
            QS = at_("QS", 40, [128, 4, 512])
            BUF = [at_(f"HB{i}", 48 + 2 * i, [128, 512]) for i in range(6)]
            AT = at_("AT", 60, [128, 512])
            KN = at_("KN", 62, [128, 512])
            STA = at_("STA", 64, [128, 7, 128])
            RESET = MASK
            ON = at_("ON", 0, [128, 4, 1024])
            quad, tmps = Pool([0]), Pool(BUF[4:6])
            small_pools = Pool([0])
            fs = [Fut() for _ in range(4)]
            qs = [Fut() for _ in range(4)]
            gs = [Fut() for _ in range(4)]
            his = [Fut() for _ in range(4)]
            onr = Ready()
            hg_done = []
            lb = Fut()

            def vectors():
                t1 = yield from load(BUF[5][0:8, 0:128], A["hg_lb_logits"].rearrange("a (h k) -> (a h) k", h=4), 4096,
                                     *pw)
                bank, free = yield TP
                t = yield mm(bank[:, 0:8], BUF[5][0:8, 0:128], ident[0:8, 0:8], True, True, 30, t1, g["ident"], *free)
                t = yield cp(vecT[:, 0:8], bank[:, 0:8], 8, t)
                TP.put(bank, t)
                tmps.put(BUF[5], t)
                m = lbs[:, 0:4]
                t = yield tt(m, vecT[:, 0:4], vecT[:, 4:8], ALU.max, 4, t)
                t = yield tt(vecT[:, 0:4], vecT[:, 0:4], m, ALU.subtract, 4, t)
                t = yield tt(vecT[:, 4:8], vecT[:, 4:8], m, ALU.subtract, 4, t)
                t = yield act(vecT[:, 0:8], vecT[:, 0:8], AF.Exp, 8, t)
                t = yield tt(m, vecT[:, 0:4], vecT[:, 4:8], ALU.add, 4, t)
                t = yield vop(lambda e: e.reciprocal(lbs[:, 0:4], lbs[:, 0:4]), 30, t)
                t = yield tt(lbs[:, 4:8], lbs[:, 0:4], vecT[:, 0:4], ALU.mult, 4, t)
                t = yield tt(lbs[:, 8:12], lbs[:, 0:4], vecT[:, 4:8], ALU.mult, 4, t)
                lb.set((t,))

            def lambdas():
                slot, free = yield STG
                L = slot[:, 0:256]
                src = A["da_lambda"].rearrange("o a b -> o (a b)")
                t = yield from load(L, src.broadcast_to([128, 256]), 131072, *free)
                tmp = slot[:, 256:320]
                t = yield vop(lambda e: e.tensor_tensor_reduce(tmp, L[:, 0:64], L[:, 64:128], 1.0, 0.0, ALU.mult,
                                                               ALU.add, lam[:, 0:1]), 64, t)
                t = yield vop(lambda e: e.tensor_tensor_reduce(tmp, L[:, 128:192], L[:, 192:256], 1.0, 0.0, ALU.mult,
                                                               ALU.add, lam[:, 1:2]), 64, t)
                STG.put(slot, t)
                t = yield act(lam[:, 0:2], lam[:, 0:2], AF.Exp, 2, t)
                t = yield tt(lam[:, 2:3], lam[:, 1:2], lam[:, 0:1], ALU.subtract, 1, t)
                t = yield ts(lam[:, 3:4], lam[:, 2:3], -0.2, None, ALU.add, None, 1, t)
                g["nlam"] = t

            def ev_hf(n, bank, tok):
                w = yield lb
                t = yield act(FS[:, n, :], bank[:, :], AF.Sigmoid, 512, tok, *pw)
                G.put(bank, t)
                t = yield ts(FS[:, n, :], FS[:, n, :], lbs[:, 8 + n:9 + n], lbs[:, 4 + n:5 + n], ALU.mult, ALU.add, 512,
                             t, *w)
                fs[n].set((t,))

            def ev_hq(n, bank, tok):
                tmp, free = yield tmps
                t = yield act(tmp[:, :], bank[:, :], AF.Sigmoid, 512, tok, *free, *pw)
                t = yield tt(QS[:, n, :], bank[:, :], tmp[:, :], ALU.mult, 512, t)
                G.put(bank, t)
                tmps.put(tmp, t)
                qs[n].set((t,))

            def ev_hg(nh, T, bank, tok):
                tmp, free = yield tmps
                t = yield act(tmp[:, :], bank[:, :], AF.Sigmoid, 512, tok, *free, *pw)
                g["hg", T] = t
                t = yield tt(GS[:, T, :], bank[:, :], tmp[:, :], ALU.mult, 512, t)
                G.put(bank, t)
                tmps.put(tmp, t)
                g3 = GS[:, T, :].rearrange("p (h v) -> p h v", h=4)
                t = yield tt(g3, g3, GHG[:, :].unsqueeze(1).broadcast_to([128, 4, 128]), ALU.mult, 512, t, g["ghg"])
                gs[T].set((t,))

            def ev_hi(nh, T, bank, tok):
                t = yield act(HI[:, T, :], bank[:, :], AF.Copy, 512, tok, *pw)
                G.put(bank, t)
                his[T].set((t,))

            def chunks(ap):
                return ap.rearrange("p (c t) -> p c t", c=8)

            def finish(bank, tok, gain, c0, done, tpool, *w):
                tmp, free = yield tpool
                sq = tmp[:, 0:512]
                t = yield act(sq, bank[:, :], AF.Square, 512, tok, *free)
                s, sf = yield SP
                t = yield vop(lambda e: e.tensor_reduce(s[:, 0:4], sq.rearrange("p (a v) -> p a v", a=4), AX.X,
                                                        ALU.add), 512, t, *sf)
                tpool.put(tmp, t)
                t = yield gop(lambda e: e.tensor_scalar(s[:, 4:8], s[:, 0:4], 1.0 / 128, 1e-5, ALU.mult, ALU.add), 4, t)
                t = yield gop(lambda e: e.tensor_tensor(s[:, 8:12], s[:, 4:8], half, ALU.pow), 4, t, g["half"])
                for T in range(4):
                    u = yield stt(ON[:, T, c0:c0 + 128], bank[:, T * 128:(T + 1) * 128], s[:, 8 + T:9 + T], gain(T),
                                  ALU.mult, ALU.mult, 128, t, *w)
                    onr.f[(c0 // 128, T)].set((u,))
                SP.put(s, u)
                OP.put(bank, u)
                done(u)

            def hgrn(h):
                w = yield fs[h]
                q = yield qs[h]
                gg = yield AllOf(gs)
                gg = gg + tuple(g["hg", T] for T in range(4))
                _, free = yield quad
                KK, T1, D1, D2 = BUF[0], BUF[1], BUF[2], BUF[3]
                F, Q = FS[:, h, :], QS[:, h, :]
                tk = yield ts(KK[:, :], F, -1.0, 1.0, ALU.mult, ALU.add, 512, *w, *free)
                t = yield act(F, F, AF.Ln, 512, tk, *gg)
                tb = yield vop(lambda e: e.tensor_tensor_scan(F, RESET[:, :], F, 0.0, ALU.mult, ALU.add),
                               512, t, g["reset"])
                b3 = chunks(F)
                t1 = yield tt(chunks(D1[:, :]), b3, b3[:, :, 31:32].broadcast_to([128, 8, 64]), ALU.subtract, 512, tb,
                              *free)
                t2 = yield tt(chunks(D2[:, :]), b3, b3[:, :, 63:64].broadcast_to([128, 8, 64]), ALU.subtract, 512, tb,
                              *free)
                te = yield act(T1[:, :], D1[:, :], AF.Exp, 512, t1, *free)
                tq = yield tt(T1[:, :], Q, T1[:, :], ALU.mult, 512, te, *q)
                te = yield act(D1[:, :], D1[:, :], AF.Exp, 512, te, scale=-1.0)
                ta = yield tt(D1[:, :], KK[:, :], D1[:, :], ALU.mult, 512, te, tk)
                te = yield act(D2[:, :], D2[:, :], AF.Exp, 512, t2, scale=-1.0)
                ts_ = yield tt(KK[:, :], KK[:, :], D2[:, :], ALU.mult, 512, te, ta)
                te = yield act(F, F, AF.Exp, 512, t2)
                to = yield tt(Q, Q, F, ALU.mult, 512, te, tq)
                _, pf = yield small_pools
                a, free = yield S
                for T in range(4):
                    c = slice(T * 128, T * 128 + 128)
                    t = yield mm(a[:, c], D1[:, c], T1[:, c], True, True, 219, tq, ta, *free, inc=T == 3)
                at3 = AT[:, :].rearrange("p (a c) -> p a c", a=4)
                tat = yield vop(lambda e: e.copy_predicated(at3, TRI[:, :].unsqueeze(1).broadcast_to([128, 4, 128]),
                                                            a[:, :].rearrange("p (a c) -> p a c", a=4)), 512, t,
                                g["tri"], g["at0"], *pf)
                S.put(a, tat)
                bank, free = yield TP
                for T in range(4):
                    c = slice(T * 128, T * 128 + 128)
                    t = yield tr(bank[:, c], KK[:, c], ts_, *free, inc=T == 3)
                tkn = yield act(KN[:, :], bank[:, :], AF.Copy, 512, t, *pf)
                TP.put(bank, tkn)
                quad.put(0, t)
                hv = yield AllOf(his)
                st = None
                ue, fe = yield S
                uo, fo = yield S
                for c in range(7):
                    p0, T = 64 * (c % 2), c // 2
                    u = (ue, uo)[c % 2][:, T * 128:T * 128 + 128]
                    t = yield mm(u, KN[p0:p0 + 64, T * 128:T * 128 + 128],
                                 HI[p0:p0 + 64, T, h * 128:h * 128 + 128], True, True, 219, tkn, *hv, *fe, *fo,
                                 inc=c >= 5)
                    both = (t,) if c == 5 else (*both, t) if c == 6 else ()
                for c in range(7):
                    u = (ue, uo)[c % 2][:, c // 2 * 128:c // 2 * 128 + 128]
                    if c == 0:
                        st = yield cp(STA[:, 0, :], u, 128, *both, *pf)
                    else:
                        st = yield stt(STA[:, c, :], STA[:, c - 1, :], F[:, c * 64 + 63:c * 64 + 64], u, ALU.mult,
                                       ALU.add, 128, st)
                S.put(ue, st)
                S.put(uo, st)
                o, free = yield OP
                for T in range(4):
                    for c in (2 * T, 2 * T + 1):
                        p0 = 64 * (c % 2)
                        r = o[p0:p0 + 64, T * 128:T * 128 + 128]
                        t = yield mm(r, AT[:, T * 128 + p0:T * 128 + p0 + 64], HI[:, T, h * 128:h * 128 + 128], True,
                                     c == 0, 135, tat, *free, inc=c == 0)
                        if c:
                            t = yield mm(r, Q[:, c * 64:c * 64 + 64], STA[:, c - 1, :], False, True, 135, to, st)
                small_pools.put(0, t)

                def done(u):
                    hg_done.append(u)
                    hg_done.append(t)
                    if len(hg_done) == 8:
                        hgf.set(tuple(hg_done))

                spawn(finish(o, t, lambda T: GS[:, T, h * 128:h * 128 + 128], 512 + h * 128, done, tmps, *gg), 4,
                      f"fin{h}")

            hgf = Fut()

            def loads():
                g["reset"] = yield from load(RESET[:, :], A["reset"], 262144)
                g["ghg"] = yield from load(GHG[:, :], A["hg_norm_g"].broadcast_to([128, 128]), 65536)
                g["tri"] = yield from load(TRI[:, :], A["tri"], 65536)
                g["at0"] = yield vop(lambda e: e.memset(AT[:, :], 0.0), 512, *pw)

            tmps.free.pop()
            spawn(loads(), 1, "loads")
            spawn(vectors(), 1, "vectors")
            for h in range(4):
                spawn(hgrn(h), 5 + h, f"hgrn{h}")
            yield from gemmA(W, 2048, 2560, 8, xh, xl, xr, ev_hf)
            yield from gemmA(W, 1536, 2048, 8, xh, xl, xr, ev_hq)
            yield from gemmB(lambda nh, k: wB(W, k, 3072), 1, 8, xh, xl, xr, ev_hg)
            yield from gemmB(lambda nh, k: wB(W, k, 2560), 1, 8, xh, xl, xr, ev_hi)

            V = at_("DV", 16, [128, 4, 512])
            STK = Pool([at_(f"STK{i}", 24 + 12 * i, [128, 6, 512], F32R) for i in range(2)])
            EP = Pool([at_(f"EP{i}", 48 + 4 * i, [128, 2, 512]) for i in range(2)])
            PT = Pool([at_(f"PT{i}", 56 + 2 * i, [128, 512]) for i in range(3)])
            NDP = Pool([at_(f"NDP{i}", 62 + 2 * i, [128, 512]) for i in range(3)])
            for g_ in range(2):
                for T in range(4):
                    qkd[(g_, T)] = Fut()
            vd = {T: Fut() for T in range(4)}
            vr = {T: Fut() for T in range(4)}

            def ev_va(nh, T, bank, tok):
                slot, free = yield STG
                t = yield act(slot[:, 0:512], bank[:, :], AF.Copy, 512, tok, *free)
                G.put(bank, t)
                t = yield from load(VD[T], slot[:, 0:512], 262144, t)
                STG.put(slot, t)
                vd[T].set((t,))

            def reload_v():
                w = yield hgf
                for T in range(4):
                    (d,) = yield vd[T]
                    t = yield from load(V[:, T, :], VD[T], 262144, d, *w)
                    vr[T].set((t,))

            soft = {}
            stk_done = {}

            def da_scores():
                w = yield hgf
                w += yield mk
                for P in range(4):
                    stk, free = yield STK
                    rdy = [Fut() for _ in range(4)]
                    spawn(stacks(0, P, stk, free + w, NDP, rdy, *w), 4, f"stacks{P}")
                    stk_done[P] = []
                    for i in range(4):
                        ep, ef = yield EP
                        soft[(P, i)] = Fut()
                        spawn(da_unit(P, i, stk, ep, ef + w, rdy), 5, f"unit{P}.{i}")

            def da_unit(P, i, stk, ep, ef, rdy):
                n = 128 * (i + 1)
                v0, t0, r0 = yield from scores(stk, 0, i, MASK, ep[:, 0, :], ef, rdy)
                v1, t1, r1 = yield from scores(stk, 1, i, MASK, ep[:, 1, :], ef, rdy)
                stk_done[P].append(t1)
                if len(stk_done[P]) == 4:
                    STK.put(stk, *stk_done[P])
                e0, e1 = ep[:, 0, 0:n], ep[:, 1, 0:n]
                t = yield ts(e0, e0, v0[:, 2:3], None, ALU.mult, None, n, t0, r0)
                u = yield tt(v1[:, 3:4], v1[:, 2:3], lam[:, 3:4], ALU.mult, 1, r1, g["nlam"])
                t = yield stt(e0, e1, v1[:, 3:4], e0, ALU.mult, ALU.add, n, t, u, t1)
                SP.put(v0, t)
                SP.put(v1, t)
                soft[(P, i)].set((ep, t))

            def da_out():
                yield hgf
                for P in range(4):
                    o, of = yield OP
                    for i in range(4):
                        yield lambda: (P, i) in soft
                        ep, t = yield soft[(P, i)]
                        pt, pf = yield PT
                        n = 128 * (i + 1)
                        t, u = yield from turn_P(ep[:, 0, :], n, pt, pf, t)
                        EP.put(ep, t)
                        for j in range(i + 1):
                            (vt,) = yield vr[j]
                            t = yield mm(o[:, i * 128:i * 128 + 128], pt[:, j * 128:j * 128 + 128],
                                         V[:, j, P * 128:P * 128 + 128], j == 0, j == i, 219, u, vt, *of)
                        PT.put(pt, t)
                    spawn(finish(o, t, lambda T: GDA[:, :], P * 128, lambda u: None, STG, g["gda"]), 4, f"finda{P}")

            def load_da():
                g["rope"] = yield from load(ROPE[:, :, :], A["rope"], 65536)
                t = yield from load(GDA[:, :], A["da_subln_g"].broadcast_to([128, 128]), 65536)
                g["gda"] = yield ts(GDA[:, :], GDA[:, :], 0.8, None, ALU.mult, None, 128, t)
                w = yield hgf
                g["mask0"] = yield from load(MASK[:, :], A["mask0"], 262144, *w)
                mk.set((g["mask0"],))

            mk = Fut()
            spawn(load_da(), 6, "load_da")
            spawn(lambdas(), 6, "lambdas")
            spawn(da_scores(), 5, "da_scores")
            spawn(da_out(), 4, "da_out")
            spawn(reload_v(), 6, "reload_v")
            yield from gemmB(lambda nh, k: wQ(W, k, 0, 512), 1, 8, xh, xl, xr, ev_qk(0))
            yield from gemmB(lambda nh, k: wQ(W, k, 256, 768), 1, 8, xh, xl, xr, ev_qk(1))
            yield from gemmB(lambda nh, k: wB(W, k, 1024), 1, 8, xh, xl, xr, ev_va)
            w_in_done = g["last"]

            orr = Ready()

            def turn_k(kt):
                w = yield AllOf([onr.f[(kt, T)] for T in range(4)])
                bank, free = yield TP
                for T in range(4):
                    t = yield tr(bank[:, T * 128:T * 128 + 128], ON[:, T, kt * 128:kt * 128 + 128], *w, *free, inc=T == 3)
                th = yield act(XH[:, kt, :], bank[:, :], AF.Copy, 512, t, w_in_done)
                tl = yield tt(XL[:, kt, :], bank[:, :], XH[:, kt, :].bitcast(F32), ALU.subtract, 512, t, th, w_in_done)
                TP.put(bank, tl)
                for T in range(4):
                    orr.f[(kt, T)].set((th, tl))

            for kt in (4, 5, 6, 7, 0, 1, 2, 3):
                spawn(turn_k(kt), 4, f"turn_k{kt}")
            WO = A["ev_w_out"][0]
            x0 = {(T, nh): Fut() for T in range(4) for nh in range(2)}
            for f in x0.values():
                f.set(tuple(g["x", T] for T in range(4)))
            x1, x2, x3 = xfuts(), xfuts(), xfuts()
            off = lambda k0: (lambda k, T: orr(k + k0, T))
            yield from gemmB(lambda nh, k: wB(WO, k + 4, nh * 512), 2, 4, rows(XH, 4), rows(XL, 4), off(4),
                             add_x(ALPHA, x0, x1))
            G1, B1 = at_("LG1", 60, [128, 1024]), at_("LB1", 64, [128, 1024])
            gb = Fut()

            def ld():
                w = yield from gather([onr.f[(3, T)] for T in range(4)])
                for p in (PT, NDP, EP):
                    for it, tk in p.free:
                        w += tuple(tk)
                r = yield from gains((A["ln1_g"][0:1], A["ln1_b"][0:1]), (G1[:, :], B1[:, :]), *w)
                gb.set(r)

            spawn(ld(), 1, "ld")
            xr1 = Ready()
            for T in range(4):
                spawn(norm_ln(T, x2, gb, G1, B1, xr1, x3), 2 + T, f"ln1.{T}")
            yield from gemmB(lambda nh, k: wB(WO, k, nh * 512), 2, 4, xh, xl, off(0), add_x(1.0, x1, x2))
            z = (yield from gather(x3.values())) + (g["last"],)
            return (yield from after_first(0, xr1, x3, z, pre))

        def pre1(x_in, _):
            xr = Ready()
            for T in range(4):
                for k0 in (0, 4):
                    def turn(T=T, k0=k0):
                        w = yield x_in[(T, 0)]
                        w += yield x_in[(T, 1)]
                        yield from turn_T(X[:, T, :], T, XH, XL, xr, k0, 4, *w)
                    spawn(turn(), 2, "turn_x1")
            return xr

        def layer1(x_in, zone, xr, pre):
            W, WO = A["od_w_in"][0], A["od_w_out"][0]
            V = at_("OV", 0, [128, 4, 1024])
            STK = Pool([at_(f"OSTK{i}", 16 + 12 * i, [128, 6, 512], F32R) for i in range(2)])
            OHL = Pool([at_(f"OHL{i}", 40 + 4 * i, [128, 2, 512], F32R) for i in range(2)])
            EP = Pool([at_(f"OE{i}", 48 + 2 * i, [128, 512]) for i in range(4)])
            PT = Pool([at_(f"OPT{i}", 56 + 2 * i, [128, 512]) for i in range(4)])
            NDP = Pool([at_(f"ONDP{i}", 64 + 2 * i, [128, 512]) for i in range(2)])
            for g_ in range(2, 6):
                for T in range(4):
                    qkd[(g_, T)] = Fut()
            vr = xfuts()
            soft = {}
            left = {}

            def ev_v(nh, T, bank, tok):
                t = yield act(V[:, T, nh * 512:nh * 512 + 512], bank[:, :], AF.Copy, 512, tok, *zone)
                G.put(bank, t)
                vr[(T, nh)].set((t,))

            def load_mask():
                t = yield from load(MASK[:, :], A["mask1"], 262144, *zone)
                mk.set((t,))

            mk = Fut()

            def sc():
                w = yield mk
                for P in range(8):
                    stk, free = yield STK
                    rdy = [Fut() for _ in range(4)]
                    spawn(stacks(2, P, stk, free + zone, NDP, rdy, *zone), 4, f"stacks{P}")
                    left[P] = []
                    for i in range(4):
                        for hh in range(2):
                            e, ef = yield EP
                            soft[(P, i, hh)] = Fut()
                            spawn(unit(P, i, hh, stk, e, ef + zone + w, rdy), 5, f"unit{P}.{i}")

            def unit(P, i, hh, stk, e, ef, rdy):
                n = 128 * (i + 1)
                v, t, r = yield from scores(stk, hh, i, MASK, e, ef, rdy)
                left[P].append(t)
                if len(left[P]) == 8:
                    STK.put(stk, *left[P])
                t = yield ts(e[:, 0:n], e[:, 0:n], v[:, 2:3], None, ALU.mult, None, n, t, r)
                SP.put(v, t)
                soft[(P, i, hh)].set((e, t))

            ok = {P: Fut() for P in range(8)}
            ohl = {}

            def outs():
                for P in range(8):
                    o, of = yield OP
                    for i in range(4):
                        pts = []
                        n = 128 * (i + 1)
                        for hh in range(2):
                            yield lambda: (P, i, hh) in soft
                            e, t = yield soft[(P, i, hh)]
                            pt, pf = yield PT
                            t, u = yield from turn_P(e, n, pt, pf + zone, t)
                            EP.put(e, t)
                            pts.append((pt, u))
                        for j in range(i + 1):
                            (vt,) = yield vr[(j, P // 4)]
                            for hh in range(2):
                                pt, u = pts[hh]
                                c = (2 * P + hh) * 64
                                t = yield mm(o[64 * hh:64 * hh + 64, i * 128:i * 128 + 128], V[:, j, c:c + 64],
                                             pt[:, j * 128:j * 128 + 128], j == 0, j == i, 135, u, vt, *of,
                                             inc=j == i)
                        for pt, _ in pts:
                            PT.put(pt, t)
                    spawn(out_ev(P, o, t), 3, f"oev{P}")

            def out_ev(P, o, t):
                hl, hf = yield OHL
                ohl[P] = hl
                th = yield act(hl[:, 0, :], o[:, :], AF.Copy, 512, t, *hf, *zone)
                tl = yield tt(hl[:, 1, :], o[:, :], hl[:, 0, :].bitcast(F32), ALU.subtract, 512, th)
                OP.put(o, tl)
                ok[P].set((th, tl))

            spawn(load_mask(), 6, "mask1")
            spawn(sc(), 5, "scores1")
            spawn(outs(), 4, "outs1")
            yield from gemmB(lambda nh, k: wB(W, k, 2048 + nh * 512), 2, 8, xh, xl, xr, ev_v)
            steps = [x_in] + [xfuts() for _ in range(4)]

            def proj(g_):
                for k in range(2):
                    yield ok[2 * g_ + k]
                yield from gemmB(lambda nh, k: wB(WO, 2 * g_ + k, nh * 512), 2, 2,
                                 lambda k: ohl[2 * g_ + k][:, 0, :], lambda k: ohl[2 * g_ + k][:, 1, :],
                                 lambda k, T: ok[2 * g_ + k], add_x(ALPHA if g_ == 0 else 1.0, steps[g_], steps[g_ + 1]))
                for k in range(2):
                    OHL.put(ohl[2 * g_ + k], g["last"])

            G1, B1 = at_("OLG1", 60, [128, 1024]), at_("OLB1", 64, [128, 1024])
            gb = Fut()

            def ld():
                w = yield ok[7]
                for p in (PT, NDP, EP):
                    for it, tk in p.free:
                        w += tuple(tk)
                r = yield from gains((A["ln1_g"][1:2], A["ln1_b"][1:2]), (G1[:, :], B1[:, :]), *w)
                gb.set(r)

            spawn(ld(), 1, "ld")
            xr1, x3 = Ready(), xfuts()
            for T in range(4):
                spawn(norm_ln(T, steps[4], gb, G1, B1, xr1, x3), 2 + T, f"ln1.{T}")
            for what in ("q0", "q1", "q2", "w0", "q3", "w1", "w2", "w3"):
                n = int(what[1])
                if what[0] == "q":
                    yield from gemmB(lambda nh, k: wQ(W, k, 256 * n, 1024 + 256 * n), 1, 8, xh, xl, xr, ev_qk(2 + n))
                else:
                    yield from proj(n)
            z = (yield from gather(x3.values())) + (g["last"],)
            return (yield from after_first(1, xr1, x3, z, pre))

        def rms_rows(T, x, xw, tmp, tf, gain, gt, ready, eps, H, L, w=(), each=None):
            v, vf = yield SP
            n0 = yield xw[0]
            t0 = yield act(tmp[:, 0:512], x[:, 0:512], AF.Square, 512, *n0, *tf, *vf, *w, acc=v[:, 0:1])
            n1 = yield xw[1]
            t1 = yield act(tmp[:, 512:1024], x[:, 512:1024], AF.Square, 512, *n1, acc=v[:, 1:2])
            t = yield gop(lambda e: e.tensor_tensor(v[:, 2:3], v[:, 0:1], v[:, 1:2], ALU.add), 1, t0, t1)
            t = yield gop(lambda e: e.tensor_scalar(v[:, 3:4], v[:, 2:3], 1.0 / 1024, eps, ALU.mult, ALU.add), 1, t)
            t = yield gop(lambda e: e.tensor_tensor(v[:, 4:5], v[:, 3:4], half[:, 0:1], ALU.pow), 1, t, g["half"])
            u, last = [], []
            for h in range(2):
                c = slice(h * 512, h * 512 + 512)
                u.append((yield stt(tmp[:, c], x[:, c], v[:, 4:5], gain[:, c], ALU.mult, ALU.mult, 512, t, *gt)))
                last.append(u[h])
                if each is not None:
                    each(h, u[h])
                if H is not None:
                    f = Fut()

                    def turn(h=h, u=u[h], f=f):
                        yield from turn_T(tmp, T, H, L, ready, 4 * h, 4, u)
                        f.set(ready.f[(4 * h, T)].v)
                    spawn(turn(), 2, "turn_r")
                    u[h] = f
            SP.put(v, *last)
            if H is not None:
                a, b = u
                r = (yield a) + (yield b)
                return r
            return tuple(u)

        def rms_all(x_in, gname, goff, hoff, zone):
            gt_ = at_("RG", goff, [128, 1024])
            HT = Pool([at_(f"RT{i}", hoff + 4 * i, [128, 1024]) for i in range(2)])
            rdy = Ready()
            gf = Fut()
            done = [Fut() for _ in range(4)]

            def ld():
                t = yield from load(gt_[:, :], A[gname].broadcast_to([128, 1024]), 524288, *zone)
                gf.set((t,))

            def one(T):
                tmp, tf = yield HT
                gt = yield gf
                d = yield from rms_rows(T, X[:, T, :], (x_in[(T, 0)], x_in[(T, 1)]), tmp, tf + zone, gt_, gt, rdy, 1e-6,
                                        XH, XL)
                HT.put(tmp, *d)
                done[T].set(d)

            spawn(ld(), 1, "ld_g")
            for T in range(4):
                spawn(one(T), 2 + T, f"rms{T}")
            return rdy, done

        def mem_kv(zone, done):
            MN = at_("MN", 0, [128, 2, 1024])
            MH, ML = at_("MH", 8, [128, 8, 256], F32R), at_("ML", 16, [128, 8, 256], F32R)
            MG = at_("MG", 24, [128, 1024])
            JK = at_("JK", 44, [128, 2, 1024])
            rdy = Ready(2)
            gf = Fut()

            def prep(T):
                t = yield from load(MN[:, T, :], A["mem_2"][0, T * 128:T * 128 + 128, :], 524288, *zone)
                gt = yield gf
                f = Fut()
                f.set((t,))
                yield from rms_rows(T, MN[:, T, :], (f, f), JK[:, T, :], zone, MG, gt, rdy, 1e-6, MH, ML)

            def ld():
                t = yield from load(MG[:, :], A["g_mem_2"].broadcast_to([128, 1024]), 524288, *zone)
                gf.set((t,))

            spawn(ld(), 1, "ld_gm")
            for T in range(2):
                spawn(prep(T), 3, f"mem{T}")
            sent = []

            def ev_k(n, bank, tok):
                s_, f = yield STG
                t = yield act(s_[:, 0:256], bank[:, 0:256], AF.Copy, 256, tok, *f)
                G.put(bank, t)
                t = yield from load(KTD[n], s_[:, 0:256], 131072, t)
                STG.put(s_, t)
                sent.append(t)

            def ev_v(nh, T, bank, tok):
                s_, f = yield STG
                t = yield act(s_[:, 0:512], bank[:, :], AF.Copy, 512, tok, *f)
                G.put(bank, t)
                t = yield from load(MVD[T], s_[:, 0:512], 262144, t)
                STG.put(s_, t)
                sent.append(t)

            W = A["w_ckv_2"][0]
            yield from gemmA(W, 0, 512, 8, rows(MH), rows(ML), rdy, ev_k, N=256)
            yield from gemmB(lambda nh, k: wB(W, k, 512), 1, 8, rows(MH), rows(ML), rdy, ev_v, TN=2)
            last = g["last"]

            def fin():
                yield lambda: len(sent) == 6
                done.set(tuple(sent) + (last,))
            spawn(fin(), 3, "memfin")

        def pre2(x_in, zone):
            return rms_all(x_in, "g_mix_2", 28, 32, zone)

        def block2(x_in, zone, nxt):
            W = A["w_in_2"][0]
            memd = Fut()
            rdy, hdone = nxt
            yield from mem_kv(zone, memd)
            z = yield from gather(hdone + [memd])
            SGH, SGL = at_("SGH", 0, [128, 4, 512], F32R), at_("SGL", 8, [128, 4, 512], F32R)
            OAH, OAL = at_("OAH", 16, [128, 4, 512], F32R), at_("OAL", 24, [128, 4, 512], F32R)
            K2, V2 = at_("K2", 32, [128, 2, 512], F32R), at_("V2", 36, [128, 4, 128])
            UT, SV = at_("UT", 38, [128, 4, 512]), at_("SV", 46, [128, 4, 512])
            GS_, BS_ = at_("SGg", 54, [128, 512]), at_("SGb", 56, [128, 512])
            WS, WST = at_("WS", 58, [128, 4, 128]), at_("WST", 60, [128, 4, 128])
            BSG = at_("BSG", 62, [128, 512])
            R = Pool([at_(f"BR{i}", 64 + 2 * i, [128, 512]) for i in range(2)])
            wst = Fut()
            sgl = Fut()

            def ld_sgu():
                t = yield from load(WS[:, :, :], A["w_s_2"][0].rearrange("g p q -> p g q"), 262144, *z)
                bank, free = yield TP
                for j in range(4):
                    t = yield tr(bank[:, j * 128:j * 128 + 128], WS[:, j, :], t, *free, inc=j == 3) if j == 0 else \
                        tr(bank[:, j * 128:j * 128 + 128], WS[:, j, :], inc=j == 3)
                t = yield cp(WST[:, :, :], bank[:, :].rearrange("p (a c) -> p a c", a=4), 512, t, *z)
                TP.put(bank, t)
                wst.set((t,))
                a = yield from load(GS_[:, :], A["sgu_ln_g_2"].broadcast_to([128, 512]), 262144, *z)
                b = yield from load(BS_[:, :], A["sgu_ln_b_2"].broadcast_to([128, 512]), 262144, *z)
                c = yield from load(BSG[:, :], A["b_s_2"].rearrange("o g p -> o (g p)").broadcast_to([128, 512]), 262144,
                                    *z)
                sgl.set((a, b, c))

            ut = [Fut() for _ in range(4)]
            sv = [Fut() for _ in range(4)]
            sg = Ready()

            def ev_su(n, bank, tok):
                t = yield act(UT[:, n, :], bank[:, :], AF.Gelu_apprx_tanh, 512, tok, *z)
                G.put(bank, t)
                ut[n].set((t,))

            def ev_sv(nh, T, bank, tok):
                x = SV[:, T, :]
                t = yield act(x, bank[:, :], AF.Gelu_apprx_tanh, 512, tok, *z)
                G.put(bank, t)
                g["gelu", T] = t
                v, vf = yield SP
                t = yield vop(lambda e: e.bn_stats(v[:, 0:6], x), 512, t, *vf)
                t = yield vop(lambda e: e.bn_aggr(v[:, 12:14], v[:, 0:6]), 12, t)
                t = yield gop(lambda e: e.tensor_scalar(v[:, 14:15], v[:, 13:14], 1e-6, None, ALU.add), 1, t)
                t = yield gop(lambda e: e.tensor_tensor(v[:, 15:16], v[:, 14:15], half[:, 0:1], ALU.pow), 1, t, g["half"])
                w = yield sgl
                u = yield stt(x, x, v[:, 12:13], GS_[:, :], ALU.subtract, ALU.mult, 512, t, *w)
                u = yield stt(x, x, v[:, 15:16], BS_[:, :], ALU.mult, ALU.add, 512, u)
                SP.put(v, u)
                sv[T].set((u,))

            def sgu():
                tv = yield AllOf(sv)
                tw = yield wst
                for n in range(4):
                    bank, free = yield S
                    for T in range(4):
                        t = yield mm(bank[:, T * 128:T * 128 + 128], SV[:, T, n * 128:n * 128 + 128], WST[:, n, :], True,
                                     True, 219, *tv, *tw, *free, inc=T == 3)
                    spawn(sgu_ev(n, bank, t), 4, "sgu_ev")

            sgd = []
            sgf = Fut()

            def sgu_ev(n, bank, t):
                r, rf = yield R
                (tu,) = yield ut[n]
                r3 = r[:, :].rearrange("p (a c) -> p a c", a=4)
                t = yield tt(r3, bank[:, :].rearrange("p (a c) -> p a c", a=4),
                             BSG[:, n * 128:n * 128 + 128].unsqueeze(1).broadcast_to([128, 4, 128]), ALU.add, 512, t, *rf,
                             *z)
                S.put(bank, t)
                t = yield tt(r[:, :], r[:, :], UT[:, n, :], ALU.mult, 512, t, tu)
                th = yield act(SGH[:, n, :], r[:, :], AF.Copy, 512, t, *z)
                tl = yield tt(SGL[:, n, :], r[:, :], SGH[:, n, :].bitcast(F32), ALU.subtract, 512, th, *z)
                R.put(r, th, tl)
                for T in range(4):
                    sg.f[(n, T)].set((th, tl))
                sgd.append(tl)
                if len(sgd) == 4:
                    sgf.set(tuple(sgd) + (t,))

            spawn(ld_sgu(), 5, "ld_sgu")
            spawn(sgu(), 6, "sgu")
            yield from gemmA(W, 768, 1280, 8, xh, xl, rdy, ev_su)
            yield from gemmB(lambda nh, k: wB(W, k, 1280), 1, 8, xh, xl, rdy, ev_sv)

            AXT = ax_tables(z, g)
            z2 = z
            NDK = at_("NDK", 68, [128, 256])
            NDKP = Pool([NDK])
            NDQ = Pool([at_("NDQ0", 20, [128, 1024]), at_("NDQ1", 28, [128, 1024])])
            JP = Pool([at_("JP", 24, [128, 1024])])
            qd = {T: Fut() for T in range(4)}
            kd = [Fut() for _ in range(4)]
            vd2 = [Fut() for _ in range(4)]

            def head_rot(bank, b0, nh_, T, which, outap, ofree, tok):
                n = nh_ * 64
                x3 = bank[:, b0:b0 + n].rearrange("p (h c) -> p h c", h=nh_)
                r, rf = yield R
                q3 = r[:, 0:n].rearrange("p (h c) -> p h c", h=nh_)
                t = yield act(r[:, 0:n], bank[:, b0:b0 + n], AF.Square, n, tok, *rf, *z)
                v, vf = yield SP
                t = yield vop(lambda e: e.tensor_reduce(v[:, 0:nh_], q3, AX.X, ALU.add), n, t, *vf)
                t = yield gop(lambda e: e.tensor_scalar(v[:, 0:nh_], v[:, 0:nh_], 1.0 / 64, 1e-6, ALU.mult, ALU.add), 8,
                              t)
                t = yield gop(lambda e: e.tensor_tensor(v[:, 8:8 + nh_], v[:, 0:nh_], half8[:, 0:nh_], ALU.pow), 8, t,
                              g["half"])
                t = yield tt(q3, x3, v[:, 8:8 + nh_].unsqueeze(2).broadcast_to([128, nh_, 64]), ALU.mult, n, t)
                tb = t
                SP.put(v, t)
                j, jf = yield JP
                jf += z
                P_ = AXT[:, which, T, 0:64].unsqueeze(1).broadcast_to([128, nh_, 64])
                Q_ = AXT[:, which, T, 64:128].rearrange("p (c s) -> p c s", s=2).unsqueeze(1).broadcast_to(
                    [128, nh_, 32, 2])
                m1 = j[:, 0:n].rearrange("p (h c) -> p h c", h=nh_)
                m2 = j[:, 512:512 + n].rearrange("p (h c s) -> p h c s", h=nh_, s=2)
                q4 = r[:, 0:n].rearrange("p (h c s) -> p h c s", h=nh_, s=2)
                t1 = yield tt(m1, q3, P_, ALU.mult, n, t, *jf, *g["axt"])
                t2 = yield tt(m2[:, :, :, 0], q4[:, :, :, 1], Q_[:, :, :, 0], ALU.mult, n // 2, t, *jf)
                t3 = yield tt(m2[:, :, :, 1], q4[:, :, :, 0], Q_[:, :, :, 1], ALU.mult, n // 2, t)
                R.put(r, t3)
                t = yield tt(outap, m1.unsqueeze(2).broadcast_to([128, nh_, 2, 64]),
                             j[:, 512:512 + n].rearrange("p (h c) -> p h c", h=nh_).unsqueeze(2).broadcast_to(
                                 [128, nh_, 2, 64]), ALU.add, 2 * n, t1, t2, t3, *ofree)
                JP.put(j, t)
                return tb, t

            def ev_q(nh, T, bank, tok):
                nd, nf = yield NDQ
                tb, t = yield from head_rot(bank, 0, 8, T, 0, nd[:, :].rearrange("p (h d c) -> p h d c", h=8, d=2), nf + z,
                                            tok)
                G.put(bank, tb)
                t = yield from load(QQD[T], nd[:, :], 524288, t)
                NDQ.put(nd, t)
                qd[T].set((t,))


            def ev_kv(nh, T, bank, tok):
                nd, nf = yield NDKP
                t = yield act(V2[:, T, :], bank[:, 128:256], AF.Copy, 128, tok, *z)
                vd2[T].set((t,))
                tb, t = yield from head_rot(bank, 0, 2, T, 1, nd[:, :].rearrange("p (h d c) -> p h d c", h=2, d=2),
                                            nf + z, t)
                G.put(bank, tb)
                bk, bf = yield TP
                for j in range(2):
                    u = yield tr(bk[:, j * 128:j * 128 + 128], nd[:, j * 128:j * 128 + 128], t, *bf, inc=j == 1)
                NDKP.put(nd, u)
                c = slice(T * 128, T * 128 + 128)
                b3 = bk[:, 0:256].rearrange("p (a c) -> p a c", a=2)
                th = yield act(K2[:, 0:2, c], b3, AF.Copy, 256, u, *z)
                k = K2[64:128, 0:2, c]
                tl = yield tt(k, b3[64:128, :, :], k.bitcast(F32), ALU.subtract, 256, th)
                TP.put(bk, tl)
                kd[T].set((th, tl))

            yield from gemmB(lambda nh, k: (wA(W, k, 512)), 1, 8, xh, xl, rdy, ev_kv, N=256)
            yield from gemmB(lambda nh, k: wB(W, k, 0), 1, 8, xh, xl, rdy, ev_q)

            QST = Pool([at_(f"QST{i}", 38 + 8 * i, [128, 4, 512], F32R) for i in range(2)])
            EP = Pool([at_(f"QE{i}", 54 + 2 * i, [128, 512]) for i in range(4)])
            PT = Pool([at_(f"QP{i}", 62 + 2 * i, [128, 512]) for i in range(2)])
            NQ = Pool([at_(f"NQ{i}", 66 + i, [128, 256]) for i in range(2)])
            soft, left = {}, {}

            def q_stacks(P, st, free, done):
                for T in range(4):
                    (d,) = yield qd[T]
                    nd, nf = yield NQ
                    t = yield from load(nd[:, :], QQD[T][:, P * 256:P * 256 + 256], 131072, d, *nf, *free)
                    bank, bf = yield TP
                    for j in range(2):
                        u = yield tr(bank[:, j * 128:j * 128 + 128], nd[:, j * 128:j * 128 + 128], t, *bf, inc=j == 1)
                    NQ.put(nd, u)
                    c = slice(T * 128, T * 128 + 128)
                    b3 = bank[:, 0:256].rearrange("p (a c) -> p a c", a=2)
                    th = yield act(st[:, 0:2, c], b3, AF.Copy, 256, u, *free)
                    tl = yield tt(st[:, 2:4, c], b3, st[:, 0:2, c].bitcast(F32), ALU.subtract, 256, th, *free)
                    TP.put(bank, tl)
                    done[T].set((th, tl))

            def sc():
                w = yield sgf
                w += yield AllOf(list(qd.values()))
                m = yield vop(lambda e: e.memset(MASK[:, :], 0.0), 512, *zone)
                kk = yield AllOf(kd)
                for P in range(4):
                    st, free = yield QST
                    rdy_ = [Fut() for _ in range(4)]
                    spawn(q_stacks(P, st, free + w, rdy_), 4, f"qst{P}")
                    left[P] = []
                    for i in range(4):
                        for hh in range(2):
                            e, ef = yield EP
                            soft[(P, i, hh)] = Fut()
                            spawn(unit(P, i, hh, st, e, ef + w + (m,), rdy_, kk), 5, "unit")

            def unit(P, i, hh, st, e, ef, rdy_, kk):
                w = yield rdy_[i]
                s, sf = yield S
                q = slice(i * 128, i * 128 + 128)
                yield mm(s[:, :], st[:, hh, q], K2[:, P // 2, :], True, False, 216, *w, *sf, *kk)
                t = yield mm(s[:, :], st[:, 2 + hh, q], K2[:, P // 2, :], False, True, 216)
                left[P].append(t)
                if len(left[P]) == 8:
                    QST.put(st, *left[P])
                v, t, r = yield from soft_row(s, 512, MASK, 0.125, e, t, ef)
                t = yield ts(e[:, :], e[:, :], v[:, 2:3], None, ALU.mult, None, 512, t, r)
                SP.put(v, t)
                soft[(P, i, hh)].set((e, t))

            oa = Ready()

            def outs():
                w = yield sgf
                w += yield AllOf(list(qd.values()))
                vv = yield AllOf(vd2)
                for P in range(4):
                    o, of = yield OP
                    for i in range(4):
                        pts = []
                        for hh in range(2):
                            yield lambda: (P, i, hh) in soft
                            e, t = yield soft[(P, i, hh)]
                            pt, pf = yield PT
                            t, u = yield from turn_P(e, 512, pt, pf + w, t)
                            EP.put(e, t)
                            pts.append((pt, u))
                        for j in range(4):
                            for hh in range(2):
                                pt, u = pts[hh]
                                c = (P // 2) * 64
                                t = yield mm(o[64 * hh:64 * hh + 64, i * 128:i * 128 + 128], V2[:, j, c:c + 64],
                                             pt[:, j * 128:j * 128 + 128], j == 0, j == 3, 135, u, *vv, *of, inc=j == 3)
                        for pt, _ in pts:
                            PT.put(pt, t)
                    spawn(split_out(P, o, t, OAH[:, P, :], OAL[:, P, :], oa, w), 3, "oa")

            spawn(sc(), 5, "scores2")
            spawn(outs(), 4, "outs2")

            tg = {(a, n): Fut() for a in range(2) for n in range(8)}

            def ev_g(a):
                def ev(n, bank, tok):
                    s_, f = yield STG
                    t = yield act(s_[:, 0:512], bank[:, :], AF.Tanh, 512, tok, *f, scale=0.5)
                    G.put(bank, t)
                    t = yield from load(TGD[a, n], s_[:, 0:512], 262144, t)
                    STG.put(s_, t)
                    tg[(a, n)].set((t,))
                return ev

            yield from gemmA(W, 1792, 2816, 8, xh, xl, rdy, ev_g(0))
            yield from gemmA(W, 2816, 3840, 8, xh, xl, rdy, ev_g(1))
            in_done = g["last"]

            TG = Pool([at_(f"TG{i}", 54 + 2 * i, [128, 512]) for i in range(4)])
            MP = Pool([at_(f"MP{i}", 38 + 2 * i, [128, 512]) for i in range(4)])
            z3 = yield from gather([oa.f[(k, 0)] for k in range(4)])
            z3 += (g["oa_last"],)
            part = {}
            mr = Ready()
            tgr = {}

            def ld_tg():
                for q in range(4):
                    for a in range(2):
                        for n in (2 * q, 2 * q + 1):
                            (d,) = yield tg[(a, n)]
                            b, f = yield TG
                            t = yield from load(b[:, :], TGD[a, n], 262144, d, *f, *z3)
                            tgr[(a, n)] = (b, t)

            def ev_y(a, n0):
                def ev(n_, bank, tok):
                    n = n0 + n_
                    yield lambda: (a, n) in tgr
                    b, tb = tgr[(a, n)]
                    if a == 0:
                        m, mf = yield MP
                        t = yield stt(m[:, :], b[:, :], 1.0, bank[:, :], ALU.add, ALU.mult, 512, tok, tb, *mf, *z3)
                        G.put(bank, t)
                        TG.put(b, t)
                        part[n] = (m, t)
                        return
                    yield lambda: n in part
                    m, tm = part[n]
                    t = yield stt(b[:, :], b[:, :], 1.0, bank[:, :], ALU.add, ALU.mult, 512, tok, tb)
                    G.put(bank, t)
                    t = yield tt(m[:, :], m[:, :], b[:, :], ALU.add, 512, t, tm)
                    TG.put(b, t)
                    th = yield act(XH[:, n, :], m[:, :], AF.Copy, 512, t, in_done)
                    tl = yield tt(XL[:, n, :], m[:, :], XH[:, n, :].bitcast(F32), ALU.subtract, 512, th, in_done)
                    MP.put(m, th, tl)
                    for T in range(4):
                        mr.f[(n, T)].set((th, tl))
                return ev

            spawn(ld_tg(), 1, "ld_tg")
            for q in range(4):
                yield from gemmA(A["w_att_out_2"][0], 256 * q, 256 * q + 256, 4, rows(OAH), rows(OAL), oa, ev_y(0, 2 * q))
                yield from gemmA(A["w_sgu_out_2"][0], 256 * q, 256 * q + 256, 4, rows(SGH), rows(SGL), sg, ev_y(1, 2 * q))
            ylast = g["last"]
            x1, x2, x3 = xfuts(), xfuts(), xfuts()
            z4 = z3 + (ylast,)
            rdyc, cdone = rms_all(x1, "g_cross_2", 56, 60, z4 + ((yield from gather([mr.f[(7, 0)]]))))
            yield from gemmB(lambda nh, k: wB(A["w_out_2"][0], k, nh * 512), 2, 8, xh, xl, mr,
                             add_x(None, x_in, x1, mul=0.5))

            CQH, CQL = at_("CQH", 0, [128, 4, 512], F32R), at_("CQL", 8, [128, 4, 512], F32R)
            COH, COL = at_("COH", 16, [128, 4, 512], F32R), at_("COL", 24, [128, 4, 512], F32R)
            KTr = at_("KTr", 32, [128, 4, 256])
            KTH, KTL = at_("KTH", 36, [128, 4, 256], F32R), at_("KTL", 40, [128, 4, 256], F32R)
            MV = at_("MV", 44, [128, 2, 512])
            CE = Pool([at_(f"CE{i}", 48 + i, [128, 256]) for i in range(4)])
            CP = Pool([at_(f"CP{i}", 52 + i, [128, 256]) for i in range(4)])
            kv = Fut()

            def ld_kv():
                t = yield from load(KTr[:, :, :], KTD.rearrange("h p m -> p h m"), 524288, *z4, *memd.v)
                u = yield from load(MV[:, :, :], MVD.rearrange("a p c -> p a c"), 524288, *z4, *memd.v)
                th = yield act(KTH[:, :, :], KTr[:, :, :], AF.Copy, 1024, t, *z4)
                tl = yield tt(KTL[:, :, :], KTr[:, :, :], KTH[:, :, :].bitcast(F32), ALU.subtract, 1024, t, th, *z4)
                kv.set((th, tl, u))

            spawn(ld_kv(), 3, "ld_kv")
            qr = [Fut() for _ in range(4)]

            def ev_cq(n, bank, tok):
                th = yield act(CQH[:, n, :], bank[:, :], AF.Copy, 512, tok, *z4)
                tl = yield tt(CQL[:, n, :], bank[:, :], CQH[:, n, :].bitcast(F32), ALU.subtract, 512, th, *z4)
                G.put(bank, tl)
                qr[n].set((th, tl))

            csoft = {}

            def csc():
                for h in range(4):
                    for i in range(4):
                        e, ef = yield CE
                        csoft[(h, i)] = Fut()
                        spawn(cunit(h, i, e, ef + z4), 5, "cunit")

            def cunit(h, i, e, ef):
                w = yield qr[h]
                w += yield kv
                s, sf = yield S
                q = slice(i * 128, i * 128 + 128)
                yield mm(s[:, 0:256], CQH[:, h, q], KTH[:, h, :], True, False, 110, *w, *sf)
                yield mm(s[:, 0:256], CQH[:, h, q], KTL[:, h, :], False, False, 110)
                t = yield mm(s[:, 0:256], CQL[:, h, q], KTH[:, h, :], False, True, 110)
                v, t, r = yield from soft_row(s, 256, MASK, float(np.float32(128.0 ** -0.5)), e, t, ef)
                t = yield ts(e[:, :], e[:, :], v[:, 2:3], None, ALU.mult, None, 256, t, r)
                SP.put(v, t)
                csoft[(h, i)].set((e, t))

            co = Ready()

            def couts():
                w = yield kv
                for h in range(4):
                    o, of = yield OP
                    for i in range(4):
                        yield lambda: (h, i) in csoft
                        e, t = yield csoft[(h, i)]
                        pt, pf = yield CP
                        t, u = yield from turn_P(e, 256, pt, pf + z4, t)
                        CE.put(e, t)
                        for j in range(2):
                            t = yield mm(o[:, i * 128:i * 128 + 128], MV[:, j, h * 128:h * 128 + 128],
                                         pt[:, j * 128:j * 128 + 128], j == 0, j == 1, 219, u, *w, *of)
                        CP.put(pt, t)
                    spawn(split_out(h, o, t, COH[:, h, :], COL[:, h, :], co, z4), 3, "co")

            spawn(csc(), 5, "csc")
            spawn(couts(), 4, "couts")
            g["rp"] = Fut()

            def rp():
                th, tl, u = yield kv
                yield from route_prep((th, tl, *z4))

            spawn(rp(), 6, "route_prep")
            yield from gemmA(A["w_cq_2"][0], 0, 512, 8, xh, xl, rdyc, ev_cq)
            WC = A["w_co_2"][0]
            yield lambda: len(csoft) == 16
            z_r = z4 + (yield from gather(cdone)) + tuple(t for _, t in (yield from pairs(csoft)))
            z5f = Fut()
            for n in ("idx", "logits", "ovf", "roww", "sum0"):
                g[n] = Fut()
            g["x_read"] = [Fut() for _ in range(4)]
            spawn(route(x3, z_r, z5f, g["idx"], g["logits"]), 2, "route")

            def early_raw():
                for i in range(9, 13):
                    raw.put(i, *z_r)
                w = yield AllOf([co.f[(k, 0)] for k in range(4)])
                for i in range(3, 6):
                    raw.put(i, *w)

            spawn(early_raw(), 2, "early_raw")
            yield from gemmB(lambda nh, k: wB(WC, k, nh * 512), 2, 2, rows(COH), rows(COL), co, add_x(1.0, x1, x2))
            yield from gemmB(lambda nh, k: wB(WC, 2 + k, nh * 512), 2, 2, rows(COH, 2), rows(COL, 2),
                             lambda k, T: co(k + 2, T), add_x(1.0, x2, x3), rows_first=True)
            z5 = (yield from gather(x3.values())) + (g["last"],)
            z5f.set(z5)
            return x3, z5

        def route_prep(w):
            RT_, WRS, BI = at_("ROUTE", 32, [128, 544]), at_("WRS", 34.125, [128, 8, 40], F32R), at_("BI", 35.375, [128, 28])
            t0 = yield from load(RT_[:, :], A["route"], 278528, *w)
            stage, sf = yield STG
            WR = stage[:, 0:160].rearrange("p (k c) -> p k c", k=8)
            GR = stage[0:8, 160:288]
            t1 = yield from load(WR[:, :, 0:4], A["w_rg_2"][0].rearrange("(k p) c -> p k c", p=128), 16384, *sf)
            t2 = yield from load(WR[:, :, 4:20], A["w_re_2"][0].rearrange("(k p) c -> p k c", p=128), 65536, *sf)
            t5 = yield from load(GR, A["g_moe_2"].rearrange("o (k p) -> (o k) p", p=128), 4096, *sf)
            t3 = yield from load(BI[:, 0:4], A["b_rg_2"].broadcast_to([128, 4]), 2048, *w)
            t4 = yield from load(BI[:, 4:20], A["b_re_2"].broadcast_to([128, 16]), 8192, *w)
            bank, free = yield TP
            t = yield mm(bank[:, 0:8], GR, ident[0:8, 0:8], True, True, 30, t5, *free)
            t = yield cp(BI[:, 20:28], bank[:, 0:8], 8, t, *w)
            TP.put(bank, t)
            t = yield tt(WR, WR, BI[:, 20:28].unsqueeze(2).broadcast_to([128, 8, 20]), ALU.mult, 160, t, t1, t2)
            th = yield act(WRS[:, :, 0:20], WR, AF.Copy, 160, t, *w)
            tl = yield tt(WRS[:, :, 20:40], WR, WRS[:, :, 0:20].bitcast(F32), ALU.subtract, 160, th)
            STG.put(stage, th, tl)
            g["rp"].set((t0, (t3, t4), th, tl))

        def route(x_in, zone, later, idx, logits):
            RT_, WRS, BI = at_("ROUTE", 32, [128, 544]), at_("WRS", 34.125, [128, 8, 40], F32R), at_("BI", 35.375, [128, 28])
            R8 = at_("R8", 28, [128, 8, 128])
            WK = at_("WK", 36, [128, 2048])
            pos = [0]

            def wk(n, dt=None):
                a = WK[:, pos[0]:pos[0] + n]
                pos[0] += n
                return a if dt is None else a.bitcast(dt)

            hd = []
            rdy = Ready()
            HT = Pool([at_(f"RT{i}", 60 + 4 * i, [128, 1024]) for i in range(2)])
            GM = at_("RG", 56, [128, 1024])
            gf = Fut()
            done = [Fut() for _ in range(4)]
            g["moe_rms"] = done
            RS_, rsf = wk(4), [Fut() for _ in range(4)]

            def ld():
                t = yield from load(GM[:, :], A["g_moe_2"].broadcast_to([128, 1024]), 524288, *zone)
                gf.set((t,))

            def turn(T, h):
                w = yield x_in[(T, h)]
                yield from turn_T(X[:, T, :], T, XH, XL, rdy, 4 * h, 4, *w)

            JK = WK[:, 1536:2048]

            js = [Fut() for _ in range(5)]
            js[0].set(zone)

            def norm(T):
                j = yield js[T]
                v, vf = yield SP
                w = []
                for h in range(2):
                    n_ = yield x_in[(T, h)]
                    t = yield act(JK, X[:, T, h * 512:h * 512 + 512], AF.Square, 512, *n_, *vf, *j, acc=v[:, h:h + 1])
                    j = (t,)
                    w.append(t)
                js[T + 1].set(j)
                t = yield gop(lambda e: e.tensor_tensor(v[:, 2:3], v[:, 0:1], v[:, 1:2], ALU.add), 1, *w)
                t = yield gop(lambda e: e.tensor_scalar(v[:, 3:4], v[:, 2:3], 1.0 / 1024, 1e-6, ALU.mult, ALU.add), 1, t)
                t = yield gop(lambda e: e.tensor_tensor(RS_[:, T:T + 1], v[:, 3:4], half[:, 0:1], ALU.pow), 1, t,
                              g["half"])
                SP.put(v, t)
                rsf[T].set((t,))

            def rows_out():
                gt = yield gf
                for T in range(4):
                    tmp, tf = yield HT
                    w = yield rsf[T]
                    for h in range(2):
                        c = slice(h * 512, h * 512 + 512)
                        n_ = yield x_in[(T, h)]
                        t = yield stt(tmp[:, c], X[:, T, c], RS_[:, T:T + 1], GM[:, c], ALU.mult, ALU.mult, 512, *w, *tf,
                                      *gt, *n_, *zone)
                    t = yield from load(HD[T * 128:T * 128 + 128, :], tmp[:, :], 524288, t)
                    HT.put(tmp, t)
                    hd.append(t)
                    done[T].set((t,))

            def keep():
                ts_ = list(g["spare"])
                for T in range(4):
                    w = (yield x_in[(T, 0)]) + (yield x_in[(T, 1)])
                    ts_.append((yield from load(SUM[T * 128:T * 128 + 128, :], X[:, T, :], 524288, *w)))
                g["sum0"].set(tuple(ts_))

            spawn(ld(), 1, "ld_g")
            spawn(keep(), 14, "keep")
            for T in range(4):
                for h in range(2):
                    spawn(turn(T, h), -10, "turn_m")
            for T in range(4):
                spawn(norm(T), 3, "norm")
            spawn(rows_out(), 12, "rows_out")
            t0, t3, th, tl = yield g["rp"]
            iota, tokid, reset8, ones16 = RT_[:, 0:128], RT_[:, 128:136], RT_[:, 136:264], RT_[:, 264:280]
            tri, ones, first4, lim = RT_[:, 280:408], RT_[:, 408:536], RT_[:, 536:540], RT_[:, 540:543]
            iota16, iota8 = iota[:, 0:16], iota[:, 0:8]
            o, of = yield OP
            for T in range(4):
                for k in range(8):
                    w = yield rdy(k, T)
                    a = (o[:, T * 40:T * 40 + 40], XH[:, k, T * 128:T * 128 + 128], WRS[:, k, :])
                    b = (o[:, T * 40:T * 40 + 20], XL[:, k, T * 128:T * 128 + 128], WRS[:, k, 0:20])
                    p, q = (a, b) if k == 0 else (b, a)
                    yield mm(*p, k == 0, False, 107, *w, *of, th, tl)
                    t = yield mm(*q, False, k == 7, 107, inc=k == 7)
            logits.set((t,))
            LG = wk(80).rearrange("p (t c) -> p t c", t=4)
            o3 = o[:, 0:160].rearrange("p (t c) -> p t c", t=4)
            t = yield cp(LG, o3[:, :, 0:20], 80, t, *zone)
            t = yield tt(LG, LG, o3[:, :, 20:40], ALU.add, 80, t)
            OP.put(o, t)
            tr_ = yield AllOf(rsf)
            t = yield tt(LG, LG, RS_.unsqueeze(2).broadcast_to([128, 4, 20]), ALU.mult, 80, t, *tr_)
            t = yield tt(LG, LG, BI[:, 0:20].unsqueeze(1).broadcast_to([128, 4, 20]), ALU.add, 80, t, *t3)
            gm, gs, gv, g2 = wk(4), wk(4), wk(4), wk(4)
            oh = wk(16).rearrange("p (t c) -> p t c", t=4)
            lg = LG[:, :, 0:4]
            t = yield vop(lambda e: e.tensor_reduce(gm, lg, AX.X, ALU.max), 16, t)
            tgm = t
            t = yield tt(oh, lg, gm.unsqueeze(2).broadcast_to([128, 4, 4]), ALU.is_ge, 16, t)
            t = yield tt(oh, oh, first4.unsqueeze(1).broadcast_to([128, 4, 4]), ALU.mult, 16, t, t0)
            t = yield vop(lambda e: e.tensor_reduce(g2, oh, AX.X, ALU.max), 16, t)
            t = yield tt(oh, oh, g2.unsqueeze(2).broadcast_to([128, 4, 4]), ALU.is_lt, 16, t)
            t = yield ts(oh, oh, -BIG, None, ALU.mult, None, 16, t)
            EM = wk(64)
            em4 = EM.rearrange("p (t a c) -> p t a c", t=4, a=4)
            t = yield tt(em4, LG[:, :, 4:20].rearrange("p t (a c) -> p t a c", a=4),
                         oh.unsqueeze(3).broadcast_to([128, 4, 4, 4]), ALU.add, 64, t)
            tem = t
            w8, j8 = wk(32), wk(32, U32)
            for T in range(4):
                c, d = slice(8 * T, 8 * T + 8), slice(16 * T, 16 * T + 16)
                ta = yield vop(lambda e, c=c, d=d: e.max(w8[:, c], EM[:, d]), 16, tem)
                tb = yield vop(lambda e, c=c, d=d: e.max_index(j8[:, c], w8[:, c], EM[:, d]), 16, ta)
            ID = wk(8)
            tid_ = yield cp(ID.rearrange("p (t k) -> p t k", t=4), j8.rearrange("p (t c) -> p t c", t=4)[:, :, 0:2], 8, tb)
            O = wk(128)
            o_eb = O.rearrange("p (e b) -> p e b", e=16)
            to = yield tt(o_eb, iota16.unsqueeze(2).broadcast_to([128, 16, 8]), ID.unsqueeze(1).broadcast_to([128, 16, 8]),
                          ALU.is_equal, 128, tid_)
            INC, EXC = wk(128), wk(128)
            ti = yield vop(lambda e: e.tensor_tensor_scan(INC, reset8, O, 0.0, ALU.mult, ALU.add), 128, to)
            te = yield tt(EXC, INC, O, ALU.subtract, 128, ti)
            bank, bf = yield OP
            yield mm(bank[:, 0:128], tri, O, True, False, 219, to, *bf, inc=False)
            yield mm(bank[:, 0:128], ones, EXC, False, True, 219, te, inc=False)
            t = yield mm(bank[:, 128:144], ones, INC.rearrange("p (e b) -> p e b", e=16)[:, :, 7], True, True, 60)
            LT = wk(128)
            lt3 = LT.rearrange("p (b e) -> p b e", b=8)
            tl_ = yield tt(lt3, ID.unsqueeze(2).broadcast_to([128, 8, 16]), iota16.unsqueeze(1).broadcast_to([128, 8, 16]),
                           ALU.is_gt, 128, tid_)
            m15 = wk(8)
            tm_ = yield ts(m15, ID, -1.0, 15.0, ALU.mult, ALU.add, 8, tid_)
            w83 = w8.rearrange("p (t c) -> p t c", t=4)
            e2, r2, ge = wk(4), wk(4), wk(16)
            ge3 = ge.rearrange("p (t c) -> p t c", t=4)
            u = yield tt(e2, w83[:, :, 1], w83[:, :, 0], ALU.subtract, 4, tb)
            ue = yield act(e2, e2, AF.Exp, 4, u)
            u = yield tt(ge3, lg, gm.unsqueeze(2).broadcast_to([128, 4, 4]), ALU.subtract, 16, tgm)
            tge = yield act(ge3, ge3, AF.Exp, 16, u)
            RK = wk(128)
            n_e = bank[:, 128:144]
            no3, nov, r = wk(48).rearrange("p (e j) -> p e j", e=16), wk(16), wk(8)
            tr_ = yield tt(RK, bank[:, 0:128], O, ALU.mult, 128, t)
            tn = yield tt(no3, n_e.unsqueeze(2).broadcast_to([128, 16, 3]), lim.unsqueeze(1).broadcast_to([128, 16, 3]),
                          ALU.is_gt, 48, t)
            OP.put(bank, tn)
            tr_ = yield vop(lambda e: e.tensor_reduce(r, RK.rearrange("p (e b) -> p b e", e=16), AX.X, ALU.add), 128, tr_)
            tn = yield vop(lambda e: e.tensor_reduce(nov, no3, AX.X, ALU.add), 48, tn)
            obb, q, c1 = wk(8), wk(8), wk(8)
            q3 = wk(24).rearrange("p (b j) -> p b j", b=8)
            a = yield tt(q3, r.unsqueeze(2).broadcast_to([128, 8, 3]), lim.unsqueeze(1).broadcast_to([128, 8, 3]),
                         ALU.is_ge, 24, tr_)
            t = yield tt(lt3, lt3, nov.unsqueeze(1).broadcast_to([128, 8, 16]), ALU.mult, 128, tn, tl_)
            a = yield vop(lambda e: e.tensor_reduce(q, q3, AX.X, ALU.add), 24, a)
            t = yield vop(lambda e: e.tensor_reduce(obb, lt3, AX.X, ALU.add), 128, t)
            rm = wk(8)
            tq = yield stt(rm, q, -128.0, r, ALU.mult, ALU.add, 8, a)
            t = yield tt(obb, obb, m15, ALU.add, 8, t, tm_)
            c = yield ts(c1, q, 1.0, None, ALU.min, None, 8, a)
            t = yield tt(obb, obb, q, ALU.add, 8, t, a)
            t = yield tt(obb, obb, c1, ALU.mult, 8, t, c)
            t = yield tt(obb, obb, ID, ALU.add, 8, t)
            OT = wk(192)
            ot3 = OT.rearrange("p (b t) -> p b t", b=8)
            u = yield tt(ot3, iota[:, 0:24].unsqueeze(1).broadcast_to([128, 8, 24]),
                         obb.unsqueeze(2).broadcast_to([128, 8, 24]), ALU.is_equal, 192, t)
            u = yield tt(ot3, ot3, tokid.unsqueeze(2).broadcast_to([128, 8, 24]), ALU.mult, 192, u)
            z = yield later
            bank, bf = yield OP
            for h in range(2):
                c = slice(4 * h, 4 * h + 4)
                t8 = yield tt(R8[:, c, :], iota.unsqueeze(1).broadcast_to([128, 4, 128]),
                              rm[:, c].unsqueeze(2).broadcast_to([128, 4, 128]), ALU.is_equal, 512, tq, *z)
                for b in range(4 * h, 4 * h + 4):
                    ti_ = yield mm(bank[:, 0:24], R8[:, b, :], ot3[:, b, :], b == 0, b == 7, 60, u, t8, *bf)
            ti_ = yield ts(IDX[:, :], bank[:, 0:24], 1000.0, None, ALU.add, None, 24, ti_, *zone)
            idx.set((ti_, *hd))
            pf_ = wk(24)
            tp_ = yield ts(pf_, bank[:, 0:24], 1000.0, None, ALU.add, None, 24, ti_)
            tf_ = []
            for T in range(4):
                tf_.append((yield ts(ROWT[:, :, T], pf_[:, 16:23], -128.0 * T, None, ALU.add, None, 8, tp_, *zone)))
            OP.put(bank, tp_)
            ti2 = yield cp(IOTA[:, :], iota, 128)
            j = MORE - 1
            tse = yield tt(SEL[:, :].rearrange("p (a c) -> p a c", a=4), iota.unsqueeze(1).broadcast_to([128, 4, 128]),
                           ROWT[:, j, :].unsqueeze(2).broadcast_to([128, 4, 128]), ALU.is_equal, 512, *tf_, *zone)
            g["iota"], g["sel"] = (ti2, *tf_), (tse,)
            em, pt = wk(24), wk(24)
            a = yield stt(em, pf_, 1000.0, RT_[:, 543:544].broadcast_to([128, 24]), ALU.is_ge, ALU.mult, 24, tp_)
            tput = yield tt(PUT[:, :], em, pf_, ALU.add, 24, a, *zone)
            CW = wk(8)
            cw3 = CW.rearrange("p (t k) -> p t k", t=4)
            u = yield ts(r2, e2, 1.0, None, ALU.add, None, 4, ue)
            u = yield vop(lambda e: e.reciprocal(r2, r2), 24, u)
            a = yield vop(lambda e: e.tensor_reduce(gs, ge3, AX.X, ALU.add), 16, tge)
            a = yield vop(lambda e: e.reciprocal(gv, gs), 24, a)
            u = yield tt(cw3[:, :, 0], r2, gv, ALU.mult, 4, a, u, *zone)
            u = yield tt(cw3[:, :, 1], cw3[:, :, 0], e2, ALU.mult, 4, u)
            a = yield tt(ot3, iota[:, 0:24].unsqueeze(1).broadcast_to([128, 8, 24]),
                         obb.unsqueeze(2).broadcast_to([128, 8, 24]), ALU.is_equal, 192, ti_)
            a = yield tt(ot3, ot3, CW.unsqueeze(2).broadcast_to([128, 8, 24]), ALU.mult, 192, a, u)
            bank, bf = yield OP
            for b in range(8):
                t = yield mm(bank[:, 0:24], R8[:, b, :], ot3[:, b, :], b == 0, b == 7, 60, a, *bf)
            t = yield cp(ROWW[:, :], bank[:, 0:24], 24, t, *zone)
            OP.put(bank, t)
            g["roww"].set((t, tput))
            ce = wk(128)
            incl = wk(16)
            til = yield vop(lambda e: e.tensor_tensor_scan(incl, ones16, nov, 0.0, ALU.mult, ALU.add), 16, tn)
            t = yield tt(ce.rearrange("p (j e) -> p j e", j=8), incl.unsqueeze(1).broadcast_to([128, 8, 16]),
                         iota8.unsqueeze(2).broadcast_to([128, 8, 16]), ALU.is_le, 128, til)
            of_ = wk(8)
            t = yield vop(lambda e: e.tensor_reduce(of_, ce.rearrange("p (j e) -> p j e", j=8), AX.X, ALU.add), 128, t)
            t = yield ts(OVF[:, 1:8], of_[:, 0:7], 15.0, None, ALU.min, None, 7, t, *zone)
            t1 = yield cp(OVF[:, 0:1], incl[:, 15:16], 1, t)
            g["ovf"].set((t, t1))
            assert pos[0] <= 1536

        class Tiles:

            def __init__(self):
                at = lambda name, off, shape, dt=F32: at_(name, off - D0, shape, dt)
                self.XG = Pool([at(f"XG{i}", 16 + 4 * i, [128, 1024]) for i in range(2)])
                self.EX = Pool([at(f"EX{i}", 24 + 8 * i, [128, 16, 128], F32R) for i in range(2)])
                self.SG = Pool([at(f"ES{i}", 40 + 2 * i, [128, 512]) for i in range(2)])
                self.EH = Pool([at("EH0", 44, [128, 8, 128], F32R), at_("EH1", 28, [128, 8, 128], F32R)])
                self.Y = Pool([(at_(f"EY{i}", 36 + 4 * i, [128, 1024]), at_(f"EZ{i}", 36 + 4 * i, [128, 1024], F32R))
                               for i in range(2)])
                self.got = {}

        def experts(board, strm, tiles, ahead, src, R, idx, zone, IQ, TP, sums, acc):
            sp = board.spawn
            ex = {i: Fut() for i in tiles}
            eh = {i: Fut() for i in tiles}
            ss = {}

            def turn8(get, K, h, l, free, w):
                r = []
                for k0 in range(0, K, 4):
                    bank, bf = yield TP
                    for j in range(4):
                        t = yield tr(bank[:, j * 128:j * 128 + 128], get(k0 + j), *w, *bf, inc=j == 3)
                    b3 = bank[:, :].rearrange("p (a c) -> p a c", a=4)
                    th = yield act(h[:, k0:k0 + 4, :], b3, AF.Copy, 512, t, *free)
                    tl = yield tt(l[:, k0:k0 + 4, :], b3, h[:, k0:k0 + 4, :].bitcast(F32), ALU.subtract, 512, th, *free)
                    TP.put(bank, tl)
                    r += [th, tl]
                return t, tuple(r)

            def fetch(i):
                x, xf = yield R.XG
                w = yield idx
                sem, toks = yield IQ
                t = yield Op("G", 1000.0, lambda e: e.indirect_dma_start(
                    x[:, :], None, HD[:, :], bass.IndirectOffsetOnAxis(IDX[:, i:i + 1], axis=0), bounds_check=511,
                    oob_is_err=False), (*toks, *w, *xf, *zone), 1, sem, 262144)
                IQ.put(sem, t)
                R.got[i] = (x, t)

            def preps():
                for i in tiles:
                    yield lambda: i in R.got
                    x, t = R.got[i]
                    e, ef = yield R.EX
                    t, r = yield from turn8(lambda k: x[:, k * 128:k * 128 + 128], 8, e[:, 0:8, :], e[:, 8:16, :],
                                            ef + zone, (t,))
                    R.XG.put(x, t)
                    ex[i].set((e, r))

            def fetches():
                for i in ahead:
                    yield from fetch(i)

            def ev_gate(i):
                def ev(nh, T, bank, tok):
                    s_, sf = yield R.SG
                    t = yield act(s_[:, :], bank[:, :], AF.Silu, 512, tok, *sf, *zone)
                    G.put(bank, t)
                    ss[i] = (s_, t)
                return ev

            def ev_up(i):
                def ev(nh, T, bank, tok):
                    yield lambda: i in ss
                    s_, t = ss[i]
                    t = yield tt(s_[:, :], s_[:, :], bank[:, :], ALU.mult, 512, tok, t)
                    G.put(bank, t)
                    h, hf = yield R.EH
                    t, r = yield from turn8(lambda k: s_[:, k * 128:k * 128 + 128], 4, h[:, 0:4, :], h[:, 4:8, :],
                                            hf + zone, (t,))
                    R.SG.put(s_, t)
                    eh[i].set((h, r))
                return ev

            ys = {}

            def ev_split(i):
                def ev(nh, T, bank, tok):
                    w = yield g["roww"]
                    if nh == 0:
                        ys[i] = ((yield R.Y), (yield R.Y), [])
                    else:
                        yield lambda: i in ys
                    (yh, fh), (yl, fl), ts_ = ys[i]
                    c = slice(nh * 512, nh * 512 + 512)
                    h, l = yh[1][:, c], yl[1][:, c]
                    th = yield act(h, bank[:, :], AF.Copy, 512, tok, *fh, *fl, *w, *zone, scale=ROWW[:, i:i + 1])
                    tl = yield stt(l, bank[:, :], ROWW[:, i:i + 1], h.bitcast(F32), ALU.mult, ALU.subtract, 512, th, *fh, *fl,
                                   *zone)
                    G.put(bank, tl)
                    ts_ += [th, tl]
                    if nh == 1:
                        sp(spread(i, yh, yl, tuple(ts_)), 1, "spread")
                return ev

            def spread(i, yh, yl, w):
                j = i - 16
                if j >= MORE:
                    t = yield tt(SEL[:, :].rearrange("p (a c) -> p a c", a=4), IOTA[:, :].unsqueeze(1).broadcast_to(
                        [128, 4, 128]), ROWT[:, j, :].unsqueeze(2).broadcast_to([128, 4, 128]), ALU.is_equal, 512,
                        *g["iota"], *g["sel"])
                    sel = (t,)
                else:
                    sel = g["sel"]
                for T in range(4):
                    for h in range(2):
                        bank, free = yield S
                        c, d = slice(T * 128, T * 128 + 128), slice(h * 512, h * 512 + 512)
                        yield mm(bank[:, :], SEL[:, c], yh[1][:, d], True, False, 216, *w, *sel, *free)
                        t = yield mm(bank[:, :], SEL[:, c], yl[1][:, d], False, True, 216)
                        sp(spread_ev(j, T, h, bank, t), 1, "spread_ev")
                g["sel"] = (t,)
                R.Y.put(yh, t)
                R.Y.put(yl, t)

            def spread_ev(j, T, h, bank, t):
                w = yield acc[j + 1 - MORE][(T, h)]
                x = X[:, T, h * 512:h * 512 + 512]
                t = yield tt(x, bank[:, :], x, ALU.add, 512, t, *w)
                S.put(bank, t)
                acc[j + 2 - MORE][(T, h)].set((t,))

            def ev_down(i):
                if i >= 15 + MORE:
                    return ev_split(i)

                def ev(nh, T, bank, tok):
                    rw = yield g["roww"]
                    if nh == 0:
                        ys[i] = yield R.Y
                        y, yf = ys[i]
                    else:
                        yield lambda: i in ys
                        y, yf = ys[i]
                    t = yield act(y[0][:, nh * 512:nh * 512 + 512], bank[:, :], AF.Copy, 512, tok, *yf, *rw, *zone,
                                  scale=ROWW[:, i:i + 1])
                    G.put(bank, t)
                    if nh == 1:
                        before = yield sums[i]
                        sem, toks = yield IQ
                        t = yield Op("G", 1000.0, lambda e: e.indirect_dma_start(
                            SUM[:, :], bass.IndirectOffsetOnAxis(PUT[:, i:i + 1], axis=0), y[0][:, :], None,
                            bounds_check=639, oob_is_err=True, compute_op=ALU.add), (*toks, t, *rw, *before), 1, sem,
                            524288)
                        IQ.put(sem, t)
                        R.Y.put(y, t)
                        sums[i + 1].set((t,))
                return ev

            def take(eng):
                w = yield g["ovf"]

                def fn(e):
                    regs[eng] = e.value_load(OVF[0:1, 0:1], min_val=0, max_val=7)
                yield Op(eng, 60.0, fn, w, 0)

            def up_or_gate(i, name, ev):
                e, r = yield ex[i]
                f = Fut()
                f.set(r)
                yield from gemmB(lambda nh, k: src(i, name, k, 0), 1, 8, lambda k: e[:, k, :], lambda k: e[:, 8 + k, :],
                                 lambda k, T: f, ev, TN=1, strm=strm, spawn=sp)
                if name == "w_up_2":
                    R.EX.put(e, g["last"])

            def down(i):
                h, r = yield eh[i]
                f = Fut()
                f.set(r)
                yield from gemmB(lambda nh, k: src(i, "w_down_2", k, nh * 512), 2, 4, lambda k: h[:, k, :],
                                 lambda k: h[:, 4 + k, :], lambda k, T: f, ev_down(i), TN=1, strm=strm, spawn=sp)
                R.EH.put(h, g["last"])

            sp(fetches(), 4, "fetches")
            sp(preps(), 4, "preps")
            for n, i in enumerate(tiles):
                if n == 4:
                    for e in "TAVGS":
                        sp(take(e), 8, "take")
                yield from up_or_gate(i, "w_gate_2", ev_gate(i))
                if n:
                    yield from down(tiles[n - 1])
                yield from up_or_gate(i, "w_up_2", ev_up(i))
            yield from down(tiles[-1])

        def chosen(name, k, n, j):
            def src():
                w = A[name][0, bass.ds(regs["e"], 1), k * 128:(k + 2) * 128, n:n + 512]
                return w.rearrange("o (a p) c -> p (o a) c", p=128)
            src.j = j
            return src

        def read_expert(j):
            def fn(e):
                regs["e"] = e.value_load(OVF[0:1, j + 1:j + 2], min_val=0, max_val=15)
            return fn

        def reload(w, x_out):
            w = yield w
            for T in range(4):
                r = yield g["x_read"][T]
                t = yield from load(X[:, T, :], SUM[T * 128:T * 128 + 128, :], 524288, *w, *r)
                for h in range(2):
                    x_out[(T, h)].set((t,))

        def moe(x_in, zone):
            idx, logits = g["idx"], g["logits"]
            R = Tiles()

            def src(i, name, k, n):
                if i < 16:
                    return wB(A[name][0, i], k, n)
                return chosen(name, k, n, i - 16), "B"

            def more_raw():
                for i in range(13, 16):
                    raw.put(i, *zone)
                w = yield from gather(g["moe_rms"])
                for i in range(6, 9):
                    raw.put(i, *w)
                st = []
                for _ in range(2):
                    st += list((yield STG)[1])
                raw.put(16, *st)
                w += (yield g["sum0"])
                for i in range(17, 21):
                    raw.put(i, *w, *zone)

            def xg():
                w = []
                for x, _ in R.XG.free:
                    w.append((yield Op("G", 1200.0, lambda e, x=x: e.memset(x[:, :], 0.0), zone)))
                R.XG.free = [(x, (t,)) for (x, _), t in zip(R.XG.free, w)]
                FG = ST[0]
                f = yield from load(FG[:, :], A["g_final_2"].rearrange("(o c) -> o c", o=1).broadcast_to([128, 1024]),
                                    524288, *zone)
                g["fg"] = f

            zone = zone + (yield logits)
            yield from xg()
            spawn(more_raw(), 2, "more_raw")
            acc = [xfuts() for _ in range(8)]
            sums = [g["sum0"]] + [Fut() for _ in range(15 + MORE)]
            spawn(reload(sums[15 + MORE], acc[0]), 1, "reload")
            yield from experts(bd, strm, list(range(16 + MORE)), list(range(16 + MORE)), src, R, idx, zone, IQ, TP, sums,
                               acc)
            yield from gather(acc[1].values())
            g["moe"] = (R, idx, acc, dict(raw.free))

        def further(zone):
            R, idx, acc, _ = g["moe"]
            b2 = Board("2")
            for n, q in b2.q.items():
                q.t = bd.q[n].t
            order2 = []
            for j in range(MORE, 7):
                for name, K, H in (("w_gate_2", 8, 1), ("w_up_2", 8, 1), ("w_down_2", 4, 2)):
                    for nh in range(H):
                        for k in range(0, K, 2):
                            order2.append((chosen(name, k, nh * 512, j), "B"))

            def rel0(c):
                d = [strm.rel[m].v for m in strm.rel if m % 8 == c % 8]
                return tuple(t for v in d[-1:] for t in v)

            s2 = Stream(b2, order2, raw, RS2, rel0, False)
            IQ2 = Pool(IS2)
            parts = {n: [] for n in b2.q}
            for j in range(MORE, 7):
                mark = {n: len(q.items) for n, q in b2.q.items()}
                s2.go(12 * (j - MORE), 12 * (j - MORE) + 12)

                def src(i, name, k, n):
                    return None, "B"

                b2.spawn(experts(b2, s2, [16 + j], [16 + j], src, R, idx, zone, IQ2, TP, None, acc), 10, "extra")
                b2.run()
                ends = [(q.name, q.n) for q in b2.q.values() if q.n]
                for n, q in b2.q.items():
                    q.items.append((ends, None, None, 0))
                    parts[n].append(q.items[mark[n]:])
            return parts

        def final(zone):
            _, _, acc, free = g["moe"]

            def one(T):
                tmp = RAW[T]
                x = acc[1]
                yield from rms_rows(T, X[:, T, :], (x[(T, 0)], x[(T, 1)]), tmp, free[T], ST[0], (g["fg"],), None, 1e-6, None,
                                    None, each=lambda h, u: spawn(store(T, h, tmp, u), 1, "store"))

            def store(T, h, tmp, u):
                c = slice(h * 512, h * 512 + 512)
                yield from load(out[0, T * 128:T * 128 + 128, c], tmp[:, c], 262144, u)

            for T in range(4):
                spawn(one(T), 2 + T, f"final{T}")

        def spare():
            t = yield from load(SUM[512:640, :].rearrange("p (a c) -> p a c", a=8),
                                ident[:, :].unsqueeze(1).broadcast_to([128, 8, 128]), 524288, g["ident"])
            g["spare"] = (t,)

        def split_out(k, o, t, h, l, rdy, w):
            th = yield act(h, o[:, :], AF.Copy, 512, t, *w)
            tl = yield tt(l, o[:, :], h.bitcast(F32), ALU.subtract, 512, th, *w)
            OP.put(o, tl)
            g["oa_last"] = tl
            for T in range(4):
                rdy.f[(k, T)].set((th, tl))

        def ax_tables(z, g):
            AXT = at_("AXT", 16, [128, 2, 4, 128])

            def th():
                stage, sf = yield STG
                gv = stage[:, 0:128]
                t0 = yield from load(gv[:, 0:64], A["g_q_2"].broadcast_to([128, 64]), 32768, *sf)
                t1 = yield from load(gv[:, 64:128], A["g_k_2"].broadcast_to([128, 64]), 32768, *sf)
                ax = stage[:, 128:640].rearrange("p (t c) -> p t c", t=4)
                t2 = yield from load(ax, A["axial"], 262144, *sf)
                gsw = stage[:, 640:768]
                g4 = gv.rearrange("p (c s) -> p c s", s=2)
                s4 = gsw.rearrange("p (c s) -> p c s", s=2)
                u0 = yield cp(s4[:, :, 0], g4[:, :, 1], 64, t0, t1)
                u1 = yield cp(s4[:, :, 1], g4[:, :, 0], 64)
                r = []
                for w_ in range(2):
                    r.append((yield tt(AXT[:, w_, :, 0:64], ax[:, :, 0:64],
                                       gv[:, w_ * 64:w_ * 64 + 64].unsqueeze(1).broadcast_to([128, 4, 64]), ALU.mult, 256,
                                       t2, t0, t1, *z)))
                    r.append((yield tt(AXT[:, w_, :, 64:128], ax[:, :, 64:128],
                                       gsw[:, w_ * 64:w_ * 64 + 64].unsqueeze(1).broadcast_to([128, 4, 64]), ALU.mult, 256,
                                       u0, u1)))
                STG.put(stage, *r)
                g["axt"] = tuple(r)
            spawn(th(), 2, "axt")
            return AXT

        def root():
            yield from start()
            x6, zone, nxt = yield from layer0(pre1)
            x6, zone, nxt = yield from layer1(x6, zone, nxt, pre2)
            x6, zone = yield from block2(x6, zone, nxt)
            yield from moe(x6, zone)
            g["fin"] = (x6, zone)
            strm.over = True
        def wait_all():
            for s in DS:
                if s in bd.dsem:
                    bd.q["S"].items.append(([(s, bd.dsem[s])], None, None, 0))

        strm.go(0, 1 << 30)
        spawn(root(), 10, "spine")
        bd.run()
        bd.parts = {n: [q.items, [], []] for n, q in bd.q.items()}
        if "fin" in g:
            x6, zone = g["fin"]
            extra = further(zone)
            for n, q in bd.q.items():
                q.items = []
                bd.parts[n][1:] = [extra[n], q.items]
            final(zone)
            bd.run()
        wait_all()
        return bd

    emission(True)
    bd = emission(False)
    play(bd)
    ctx.close()
    return bd


_INS = ["x", "p", "ev_w_in", "ev_w_out", "da_lambda", "da_subln_g", "hg_lb_logits", "hg_norm_g", "od_w_in", "od_w_out",
        "ln1_g", "ln1_b", "ffn_w1", "ffn_w2", "ln2_g", "ln2_b", "ple_w_proj", "ple_w_gate", "ple_norm_g", "mem_2",
        "g_mix_2", "w_in_2", "g_q_2", "g_k_2", "w_att_out_2", "sgu_ln_g_2", "sgu_ln_b_2", "w_s_2", "b_s_2",
        "w_sgu_out_2", "w_out_2", "g_cross_2", "g_mem_2", "w_cq_2", "w_ckv_2", "w_co_2", "g_moe_2", "w_rg_2", "b_rg_2",
        "w_re_2", "b_re_2", "w_gate_2", "w_up_2", "w_down_2", "g_final_2"]


def kernel(**inputs):
    import numpy as _np
    import concourse.bacc as _bacc
    from concourse import mybir as _mybir
    from concourse.bass_utils import run_bass_kernel_spmd as _run

    nc = _bacc.Bacc("TRN2", target_bir_lowering=False, num_devices=1)
    arrays, A = {}, {}
    given = [(name, inputs[name]) for name in _INS] + list(constants().items())
    for name, value in given:
        a = _np.ascontiguousarray(value)
        arrays[f"in_{name}_dram"] = a
        A[name] = nc.dram_tensor(f"in_{name}_dram", a.shape, _mybir.dt.from_np(a.dtype), kind="ExternalInput").ap()
    out = nc.dram_tensor("out_0_dram", (1, 512, 1024), _mybir.dt.from_np(_np.dtype("float32")),
                         kind="ExternalOutput").ap()
    build(nc, A, out)
    r = _run(nc, [arrays], core_ids=[0])
    return r.results[0]["out_0_dram"]
```

```python
import numpy as np
import concourse.bass as bass
from concourse import mybir
from contextlib import ExitStack


class Tok:
    __slots__ = ("sem", "val", "t")

    def __init__(self, sem, val, t):
        self.sem, self.val, self.t = sem, val, t


class Fut:
    __slots__ = ("v",)

    def __init__(self):
        self.v = None

    def set(self, v):
        self.v = v


class AllOf:

    def __init__(self, fs):
        self.fs = fs

    @property
    def v(self):
        if any(f.v is None for f in self.fs):
            return None
        return tuple(t for f in self.fs for t in f.v)


class Pool:

    def __init__(self, items):
        self.free = [(it, ()) for it in items]

    def put(self, item, *toks):
        self.free.append((item, toks))

    def pick(self):
        best = min(range(len(self.free)), key=lambda i: (max([t.t for t in self.free[i][1]], default=0.0), i))
        return self.free.pop(best)


class Banks(Pool):

    def __init__(self, items):
        super().__init__(items)
        self.lent = []

    def borrow(self, pool):
        item, toks = yield pool
        self.lent.append((item, pool))
        return item, toks

    def put(self, item, *toks):
        for n, (it, pool) in enumerate(self.lent):
            if it is item:
                del self.lent[n]
                pool.put(item, *toks)
                return
        super().put(item, *toks)


class Op:
    __slots__ = ("eng", "cost", "fn", "waits", "inc", "sem", "nbytes")

    def __init__(self, eng, cost, fn, waits, inc=1, sem=None, nbytes=0):
        self.eng, self.cost, self.fn, self.waits, self.inc, self.sem, self.nbytes = eng, cost, fn, waits, inc, sem, nbytes


class Queue:
    def __init__(self, name):
        self.name, self.items, self.n, self.t, self.seen = name, [], 0, 0.0, {}


class Thread:
    __slots__ = ("gen", "prio", "req", "name")


PR = (-12, 30)
LP = (2, 1, 2)
ACT_ROWS = 4


class Board:

    LAG = {"TT": 200.0, "TA": 197.0, "TV": 196.0, "TG": 222.0, "AT": 280.0, "AA": 200.0, "AV": 235.0, "AG": 109.0,
           "VT": 230.0, "VA": 128.0, "VV": 127.0, "VG": 155.0, "GT": 200.0, "GA": 128.0, "GV": 60.0, "GG": 96.0}

    def __init__(self, mark=""):
        self.q = {n: Queue(n + mark) for n in ("T", "A", "V", "G", "S")}
        self.threads = []
        self.dma_t = 0.0
        self.dsem = {}

    def spawn(self, gen, prio=5, name=""):
        th = Thread()
        th.gen, th.prio, th.req, th.name = gen, prio, None, name
        self.threads.append(th)
        self.step(th, None)

    def step(self, th, value):
        try:
            th.req = th.gen.send(value)
        except StopIteration:
            self.threads.remove(th)

    def start(self, op):
        q = self.q[op.eng]
        t = q.t
        for w in op.waits:
            k = self.LAG.get(w.sem[0] + op.eng, 150.0) if w.sem[0].isupper() else 950.0
            if w.t + k > t:
                t = w.t + k
        return t

    def emit(self, op):
        q = self.q[op.eng]
        t = self.start(op)
        waits = []
        for w in op.waits:
            if q.seen.get(w.sem, 0) < w.val:
                q.seen[w.sem] = w.val
                waits.append((w.sem, w.val))
        if op.sem is not None:
            v = self.dsem.get(op.sem, 0) + 16
            self.dsem[op.sem] = v
            q.items.append((waits, op.fn, op.sem, 16))
            self.dma_t = max(self.dma_t, t + 1400.0) + op.nbytes / 360.0
            q.t = t + op.cost
            return Tok(op.sem, v, self.dma_t)
        q.t = t + op.cost
        if op.inc:
            q.n += 1
            q.items.append((waits, op.fn, q.name, 1))
            return Tok(q.name, q.n, q.t)
        q.items.append((waits, op.fn, None, 0))
        return Tok(q.name, q.n + 1, q.t)

    def run(self):
        while self.threads:
            moved = True
            while moved:
                moved = False
                for th in list(self.threads):
                    r = th.req
                    if isinstance(r, (Fut, AllOf)):
                        if r.v is not None:
                            self.step(th, r.v)
                            moved = True
                    elif isinstance(r, Pool):
                        if r.free:
                            self.step(th, r.pick())
                            moved = True
                    elif callable(r):
                        if r():
                            self.step(th, None)
                            moved = True
            best, key = None, None
            for th in self.threads:
                if isinstance(th.req, Op):
                    p = th.prio() if callable(th.prio) else th.prio
                    k = (self.start(th.req) + 20.0 * p, p)
                    if best is None or k < key:
                        best, key = th, k
            if best is None:
                if self.threads:
                    raise RuntimeError("stuck: " + ", ".join(t.name for t in self.threads))
                return
            self.step(best, self.emit(best.req))


F32, F32R, U32, I32 = mybir.dt.float32, mybir.dt.float32r, mybir.dt.uint32, mybir.dt.int32
ALU, AF, AX = mybir.AluOpType, mybir.ActivationFunctionType, mybir.AxisListType
BIG = 1.0e30


def constants():
    c = {}
    c["ident"] = np.eye(128, dtype=np.float32)
    d = np.arange(128)[:, None] - np.arange(128)[None, :]
    causal = np.where(d >= 0, 0.0, -BIG).astype(np.float32)
    m0 = np.zeros((128, 512), np.float32)
    m0[:, 384:] = causal
    c["mask0"] = m0

    def mult(dist):
        n = ((dist >= 0) & (dist <= 128)).astype(np.float64) + ((dist >= 0) & (dist % 4 == 0)) \
            + ((dist >= 0) & (dist % 16 == 0))
        return np.where(n > 0, 8.0 * np.log(np.maximum(n, 1.0)), -BIG).astype(np.float32)

    c["mask1"] = np.concatenate([mult(d + 384), mult(d + 256), mult(d + 128), mult(d)], axis=1)
    h = np.arange(128) // 64
    c["tri"] = ((d <= 0) & (h[:, None] == h[None, :])).astype(np.uint32)
    reset = np.ones((128, 512), np.float32)
    reset[:, ::64] = 0.0
    c["reset"] = reset
    inv = (np.float32(500000.0) ** (-np.arange(0, 16, 2, dtype=np.float32) / np.float32(16))).astype(np.float32)
    ang = (np.arange(512, dtype=np.float32)[:, None] * inv[None, :]).astype(np.float32)
    cs, sn = np.cos(ang).astype(np.float32), np.sin(ang).astype(np.float32)
    c["rope"] = np.concatenate([cs, cs, -sn, sn], axis=1).reshape(4, 128, 32).transpose(1, 0, 2).copy()
    inv = (np.float32(10000.0) ** (-np.arange(16, dtype=np.float32) / np.float32(16))).astype(np.float32)
    ang = np.concatenate([np.repeat(np.arange(8), 64)[:, None].astype(np.float32) * inv,
                          np.tile(np.arange(64), 8)[:, None].astype(np.float32) * inv], axis=1).astype(np.float32)
    cs, sn = np.cos(ang).astype(np.float32), np.sin(ang).astype(np.float32)
    ax = np.stack([np.repeat(cs, 2, axis=1), np.stack([-sn, sn], axis=2).reshape(512, 64)], axis=1)
    p = np.arange(128)
    route = np.zeros((128, 608), np.float32)
    route[:, 0:128] = np.arange(128)
    route[:, 128:136] = 128 * (np.arange(8) // 2)[None, :] + p[:, None] - 1000
    route[:, 136:264] = (np.arange(128) % 8 != 0)
    route[:, 264:280] = 1.0
    route[:, 280:408] = (p[:, None] < p[None, :])
    route[:, 408:536] = 1.0
    route[:, 536:540] = (8, 4, 2, 1)
    route[:, 540:543] = (128, 256, 384)
    route[:, 543] = np.arange(128) + 512 - 1000
    e = np.arange(16)
    route[:, 544:560] = 15 - e
    route[:, 560:576] = 16 - e
    route[:, 576:592] = e >= 2
    route[:, 592:608] = 2.0
    c["route"] = route
    c["axial"] = ax.reshape(4, 128, 128).transpose(1, 0, 2).copy()
    return c


def build(nc, A, out):
    ctx = ExitStack()
    KB = 1024
    BASE = 16512
    ALPHA = float(np.float32(4.0 ** 0.25))

    def at(name, off, shape, dt):
        return nc.alloc_sbuf_tensor_at(name, shape, dt, offset=BASE + int(off * KB))

    X = at("X", 0, [128, 4, 1024], F32)
    XH = at("XH", 16, [128, 8, 512], F32R)
    XL = at("XL", 32, [128, 8, 512], F32R)
    WH = at("WH", 48, [128, 8, 1024], F32R)
    WL = at("WL", 80, [128, 8, 1024], F32R)
    RAW = [at(f"RAW{i}", 112 + 4 * i, [128, 1024], F32) for i in range(3)]
    ST = [at(f"ST{i}", 124 + 4 * i, [128, 1024], F32) for i in range(2)]
    C0 = 132
    ident = at("ident", C0, [128, 128], F32)
    MASK = at("MASK", C0 + 0.5, [128, 512], F32)
    TRI = at("TRI", C0 + 2.5, [128, 128], U32)
    ROPE = at("ROPE", C0 + 3, [128, 4, 32], F32)
    GDA = at("GDA", C0 + 3.5, [128, 128], F32)
    GHG = at("GHG", C0 + 4, [128, 128], F32)
    SM = at("SM", C0 + 4.5, [128, 256], F32)
    ropes = [at(f"RT{i}", C0 + 5.5 + i, [128, 2, 8, 16], F32) for i in range(1)]
    D0 = 138.5

    IDX = at("IDX", D0 + 68.0625, [128, 24], U32)
    OVF = at("OVF", D0 + 68.75, [128, 24], I32)
    IOTA = at("IOTA", D0 + 68.25, [128, 128], F32)
    ROWT = at("ROWT", D0 + 69.09375, [128, 11, 4], F32)
    ROWW = at("ROWW", D0 + 68.875, [128, 24], F32)
    PUT = at("PUT", D0 + 69, [128, 24], U32)
    SEL = at("SEL", C0 + 0.5, [128, 512], F32R)
    TRO = at("TRO", C0 + 2.5, [128, 256], F32R)
    RAW += [at(f"RAW{i + 3}", D0 + 44 + 4 * i, [128, 1024], F32) for i in range(6)]
    RAW += [at(f"RAW{i + 9}", D0 + 4 * i, [128, 1024], F32) for i in range(7)]
    RAW += [ST[1]] + [X[:, T, :] for T in range(4)]

    def small(a, n):
        return SM[:, a:a + n]

    half = small(0, 4)
    half8 = small(40, 8)
    lam = small(4, 4)
    vecT = small(8, 16)
    lbs = small(24, 16)
    stats = [small(48 + 16 * i, 16) for i in range(13)]

    dram = lambda name, shape: nc.dram_tensor(name, shape, F32).ap()
    QKD = [dram(f"qkd{g}", [4, 128, 1024]) for g in range(6)]
    ED = [dram(f"ed{l}", [4, 128, 1024]) for l in range(2)]
    VD = dram("vd", [4, 128, 512])
    QQD = dram("qqd", [4, 128, 1024])
    KTD, MVD = dram("ktd", [4, 128, 256]), dram("mvd", [2, 128, 512])
    HD, SUM = dram("hd", [512, 1024]), dram("sum", [640, 1024])
    TGD = dram("tgd", [2, 8, 128, 512])

    ps = [ctx.enter_context(nc.psum_tensor(f"ps{i}", [128, 512], F32)) for i in range(8)]
    sems = {n: ctx.enter_context(nc.semaphore("s_" + n)) for n in ("T", "A", "V", "G", "T2", "A2", "V2", "G2")}
    RS = [[f"raw{i}"] for i in range(21)]
    RS2 = [[f"rawb{i}"] for i in range(17)]
    for i in range(3):
        RS[i].append(f"rawq{i}")
    DS = [f"d{i}" for i in range(16)]
    IS, IS2 = [f"i{i}" for i in range(8)], [f"j{i}" for i in range(2)]
    for n in sum(RS + RS2, []) + DS + IS + IS2:
        sems[n] = ctx.enter_context(nc.semaphore("s_" + n))

    def mm(o, l, r, st, sp, cost, *w, inc=None):
        return Op("T", cost, lambda e: e.matmul(o, lhsT=l, rhs=r, start=st, stop=sp), w, sp if inc is None else inc)

    def tr(o, i, *w, inc=False):
        return Op("T", 110.0, lambda e: e.transpose(o, i, ident[:, :]), w, inc)

    def act(o, i, f, n, *w, bias=None, scale=1.0, acc=None):
        k = {}
        if bias is not None:
            k["bias"] = bias
        if acc is not None:
            k["accum_out"] = acc
        return Op("A", 0.83 * n + 55.0 + (130.0 if bias is not None else 0.0) + (100.0 if acc is not None else 0.0),
                  lambda e: e.activation(o, i, f, scale=scale, **k), w)

    def tt(o, a, b, op, n, *w):
        return Op("V", 1.04 * n + 68.0, lambda e: e.tensor_tensor(o, a, b, op), w)

    def cp(o, i, n, *w):
        return Op("V", 1.04 * n + 68.0, lambda e: e.tensor_copy(o, i), w)

    def ts(o, i, s1, s2, op0, op1, n, *w):
        if op1 is None:
            return Op("V", 0.52 * n + 130.0, lambda e: e.tensor_scalar(o, i, s1, None, op0), w)
        return Op("V", 0.52 * n + 130.0, lambda e: e.tensor_scalar(o, i, s1, s2, op0, op1), w)

    def stt(o, a, s, b, op0, op1, n, *w):
        return Op("V", 1.04 * n + 130.0,
                  lambda e: e.scalar_tensor_tensor(out=o, in0=a, scalar=s, in1=b, op0=op0, op1=op1), w)

    def vop(fn, n, *w):
        return Op("V", 1.04 * n + 68.0, fn, w)

    def gop(fn, n, *w):
        return Op("G", 3.0 * n + 280.0, fn, w)

    def dma(o, i, nbytes, sem, *w, eng="S"):
        return Op(eng, 60.0, lambda e: e.dma_start(o, i() if callable(i) else i), w, 1, sem, nbytes)

    def play(bd):
        blk = ctx.enter_context(nc.Block())

        def steps(e, items):
            for waits, fn, sem, inc in items:
                for s, v in waits:
                    e.wait_ge(sems[s], v)
                if fn is not None:
                    i = fn(e)
                    if sem is not None:
                        i.then_inc(sems[sem], inc)

        def run(name):
            def body(e):
                first, extra, rest = bd.parts[name]
                steps(e, first)
                deeper(e, name, 0, extra)
                steps(e, rest)
            return body

        def deeper(e, name, j, extra):
            if extra:
                with e.If(regs[name] > j):
                    steps(e, extra[0])
                    deeper(e, name, j + 1, extra[1:])

        blk.sync(run("S"))
        blk.tensor(run("T"))
        blk.scalar(run("A"))
        blk.vector(run("V"))
        blk.gpsimd(run("G"))

    order = []
    regs = {}

    def view(ap, kind):
        if kind == "A":
            return ap.rearrange("p (a c) -> p a c", a=4)
        if kind == "B":
            return ap.rearrange("p (a c) -> p a c", a=2)
        return ap.rearrange("p (a s c) -> p a s c", a=2, s=2)

    alloc = {}

    def at_(name, off, shape, dt=F32):
        key = (name, off)
        if key not in alloc:
            alloc[key] = at(name, D0 + off, shape, dt)
        return alloc[key]

    def emission(record):
        bd = Board()
        spawn = bd.spawn
        G, S, TP, OP = Banks(ps[0:3]), Pool(ps[3:5]), Pool(ps[5:7]), Pool(ps[7:8])
        STG = Pool(ST)
        DQ = Pool(DS)
        IQ = Pool(IS)
        SP = Pool(stats)
        SP2 = SP
        RP = Pool(ropes)
        g = {}

        def load(o, i, nbytes, *w):
            sem, toks = yield DQ
            tok = yield dma(o, i, nbytes, sem, *toks, *w)
            DQ.put(sem, tok)
            return tok

        class Stream:
            def __init__(self, board, order_, raw, names, rel0, record_):
                self.board, self.order, self.raw, self.names, self.rel0 = board, order_, raw, names, rel0
                self.record, self.cursor, self.over = record_, 0, False
                self.expert = None
                self.loaded, self.hi, self.lo, self.rel = {}, {}, {}, {}

            def fut(self, d, k):
                if k not in d:
                    d[k] = Fut()
                return d[k]

            def go(self, c0, c1):
                self.board.spawn(self.loader(c0, c1), 0, "loader")
                self.at = {}
                for w in ("hi", "lo"):
                    self.at[w] = c0
                    self.board.spawn(self.parts(w, c0, c1), lambda w=w: self.urgency(self.at[w]), w)

            def loader(self, c, end):
                while c < end:
                    yield lambda: len(self.order) > c or self.over
                    if c >= len(self.order):
                        return
                    slot, toks = yield self.raw
                    src, kind = self.order[c]
                    if callable(src) and src.j != self.expert:
                        w = yield g["ovf"]
                        yield Op("S", 60.0, read_expert(src.j), w, 0)
                        self.expert = src.j
                    dst = view(RAW[slot][:, :], kind)
                    if kind == "Q":
                        tok = []
                        for j in range(2):
                            tok.append((yield dma(dst[:, :, j, :], src[:, :, j, :], 262144, self.names[slot][j],
                                                  *toks)))
                        tok = tuple(tok)
                    else:
                        tok = ((yield dma(dst, src, 524288, self.names[slot][0], *toks)),)
                    self.fut(self.loaded, c).set((slot, tok))
                    c += 1

            def parts(self, which, c, end):
                while c < end:
                    yield lambda: c in self.loaded or (self.over and c >= len(self.order))
                    if c not in self.loaded:
                        return
                    slot, tok = yield self.loaded[c]
                    free = (yield self.fut(self.rel, c - 8)) if c >= 8 else self.rel0(c)
                    w = (*tok, *free)
                    x, h, l = RAW[slot][:, :], WH[:, c % 8, :], WL[:, c % 8, :]
                    if which == "hi":
                        t = yield act(h, x, AF.Copy, 1024, *w)
                        self.fut(self.hi, c).set(t)
                    else:
                        th = yield self.fut(self.hi, c)
                        t = yield tt(l, x, h.bitcast(F32), ALU.subtract, 1024, *w, th)
                        self.fut(self.lo, c).set(t)
                        if slot < 17:
                            self.raw.put(slot, th, t)
                        else:
                            g["x_read"][slot - 17].set((th, t))
                    c += 1
                    self.at[which] = c

            def urgency(self, c):
                d = c - self.cursor
                return PR[0] if d <= 2 else PR[1]

            def use(self, src, kind):
                c = self.cursor
                self.cursor += 1
                if self.record:
                    self.order.append((src, kind))
                th = yield self.fut(self.hi, c)
                tl = yield self.fut(self.lo, c)
                k = "B" if kind == "Q" else kind
                return c, view(WH[:, c % 8, :], k), view(WL[:, c % 8, :], k), (th, tl)

        raw = Pool([0, 1, 2])
        strm = Stream(bd, order, raw, RS, lambda c: (), record)

        def xh(k):
            return XH[:, k, :]

        def xl(k):
            return XL[:, k, :]

        def rows(buf, k0=0):
            return lambda k: buf[:, k + k0, :]

        def wA(w, k, n):
            return w[k * 128:(k + 4) * 128, n:n + 256].rearrange("(a p) c -> p a c", p=128), "A"

        def wB(w, k, n):
            return w[k * 128:(k + 2) * 128, n:n + 512].rearrange("(a p) c -> p a c", p=128), "B"

        def wQ(w, k, q0, k0):
            a = w[k * 128:(k + 2) * 128, :].rearrange("(a p) c -> p a c", p=128)
            n = k0 - q0
            return a[:, :, q0:q0 + 2 * n].rearrange("p a (s c) -> p a s c", s=2)[:, :, :, 0:256], "Q"

        def gemmA(w, n0, n1, K, H, L, ready, evac, N=512, early=0):
            cost = 216 if N == 512 else 110
            if early:
                got, banks = [], []
                for half in range(2):
                    for u in range(2 * early):
                        b, nt = u // 2, u % 2
                        if half == 0:
                            banks.append((yield G) if u < 3 else (yield from G.borrow(S)))
                        bank, free = banks[u]
                        for k in range(K):
                            if 2 * b + k // 4 == len(got):
                                got.append((yield from strm.use(*wA(w, k, n0 + 256 * b))))
                            c, wh, wl, tw = got[2 * b + k // 4]
                            xa = yield ready(k, 2 * half)
                            xb = yield ready(k, 2 * half + 1)
                            h = wh[:, k % 4, nt * 128:nt * 128 + 128]
                            l = wl[:, k % 4, nt * 128:nt * 128 + 128]
                            last = k == K - 1
                            drop = half == 1 and nt == 1 and (k % 4 == 3 or last)
                            cols = slice(256 * half, 256 * half + 256)
                            o = bank[:, cols]
                            yield mm(o, h, H(k)[:, cols], k == 0, False, 110, *tw, *xa, *xb, *free)
                            yield mm(o, h, L(k)[:, cols], False, False, 110)
                            t = yield mm(o, l, H(k)[:, cols], False, last, 110, inc=last or drop)
                            if drop:
                                strm.fut(strm.rel, c).set((t,))
                            g["last"] = t
                        if half == 1:
                            spawn(evac(u, bank, t), 2, "evacA")
            for n in range(n0 + 256 * early, n1, 256):
                got = []
                for nt in range(2):
                    bank, free = yield G
                    for k in range(K):
                        if k // 4 == len(got):
                            got.append((yield from strm.use(*wA(w, k, n))))
                        c, wh, wl, tw = got[k // 4]
                        x = yield ready(k, None)
                        h = wh[:, k % 4, nt * 128:nt * 128 + 128]
                        l = wl[:, k % 4, nt * 128:nt * 128 + 128]
                        last = k == K - 1
                        drop = nt == 1 and (k % 4 == 3 or last)
                        o = bank[:, 0:N]
                        yield mm(o, h, H(k), k == 0, False, cost, *tw, *x, *free)
                        yield mm(o, h, L(k), False, False, cost)
                        t = yield mm(o, l, H(k), False, last, cost, inc=last or drop)
                        if drop:
                            strm.fut(strm.rel, c).set((t,))
                        g["last"] = t
                    spawn(evac((n - n0) // 128 + nt, bank, t), 2, "evacA")

        def gemmB(src, halves, K, H, L, ready, evac, TN=4, N=512, strm=strm, spawn=spawn, rows_first=False,
                  tile=lambda H, k, T: H(k)[:, T * 128:T * 128 + 128]):
            kc = 1024 // N
            cost = 216 if N == 512 else 110
            got = [[] for _ in range(halves)]
            for u in range(halves * TN):
                nh, T = (u % halves, u // halves) if rows_first else (u // TN, u % TN)
                bank, free = yield G
                for k in range(K):
                    if k // kc == len(got[nh]):
                        got[nh].append((yield from strm.use(*src(nh, kc * (k // kc)))))
                    c, wh, wl, tw = got[nh][k // kc]
                    x = yield ready(k, T)
                    h, l = tile(H, k, T), tile(L, k, T)
                    last = k == K - 1
                    drop = T == TN - 1 and (k % kc == kc - 1 or last)
                    o, j = bank[:, 0:N], k % kc
                    yield mm(o, h, wh[:, j, :], k == 0, False, cost, *tw, *x, *free)
                    yield mm(o, h, wl[:, j, :], False, False, cost)
                    t = yield mm(o, l, wh[:, j, :], False, last, cost, inc=last or drop)
                    if drop:
                        strm.fut(strm.rel, c).set((t,))
                    g["last"] = t
                spawn(evac(nh, T, bank, t), 2, "evacB")

        class Ready:

            def __init__(self, n=4):
                self.n = n
                self.f = {(k, T): Fut() for k in range(8) for T in range(n)}

            def __call__(self, k, T):
                return self.f[(k, T)] if T is not None else AllOf([self.f[(k, t)] for t in range(self.n)])

        def turn_T(nat, T, H, L, ready, k0, kn, *w, banks=None):
            banks = banks or TP
            bank, free = yield banks
            for j in range(kn):
                t = yield tr(bank[:, j * 128:j * 128 + 128], nat[:, (k0 + j) * 128:(k0 + j + 1) * 128], *w, *free,
                             inc=j == kn - 1)
            b3 = bank[:, 0:kn * 128].rearrange("p (a c) -> p a c", a=kn)
            h = H[:, k0:k0 + kn, T * 128:T * 128 + 128]
            l = L[:, k0:k0 + kn, T * 128:T * 128 + 128]
            th = yield act(h, b3, AF.Copy, kn * 128, t)
            tl = yield tt(l, b3, h.bitcast(F32), ALU.subtract, kn * 128, t, th)
            banks.put(bank, tl)
            for j in range(kn):
                ready.f[(k0 + j, T)].set((th, tl))


        def start():
            t = yield gop(lambda e: e.memset(half, -0.5), 4)
            g["half"] = yield gop(lambda e: e.memset(half8, -0.5), 4, t)
            g["ident"] = yield from load(ident[:, :], A["ident"], 65536)
            for T in range(4):
                if T == 2:
                    strm.go(0, 1 << 30)
                g["x", T].set(((yield from load(X[:, T, :], A["x"][0, T * 128:(T + 1) * 128, :], 524288)),))

        def turns_x(ready, H, L):
            def turn(T, k0):
                w = yield g["x", T]
                yield from turn_T(X[:, T, :], T, H, L, ready, k0, 4, g["ident"], *w, banks=S if k0 else TP)

            for T in range(4):
                for k0 in (0, 4):
                    spawn(turn(T, k0), 3, "turn_x")

        def ev_qk(g_, w=()):
            def ev(nh, T, bank, tok):
                slot, free = yield STG
                nd = slot[:, :].rearrange("p (h d c) -> p h d c", h=8, d=2)
                b3 = bank[:, :].rearrange("p (h c) -> p h c", h=8)
                t = yield act(nd, b3.unsqueeze(2).broadcast_to([128, 8, 2, 64]), AF.Copy, 1024, tok, *free)
                r, rf = yield RP
                m1, m2 = r[:, 0, :, :], r[:, 1, :, :]
                cc = ROPE[:, T, 0:16].unsqueeze(1).broadcast_to([128, 8, 16])
                ns = ROPE[:, T, 16:24].unsqueeze(1).broadcast_to([128, 8, 8])
                sn = ROPE[:, T, 24:32].unsqueeze(1).broadcast_to([128, 8, 8])
                t1 = yield tt(m1, b3[:, :, 0:16], cc, ALU.mult, 128, t, g["rope"], *rf)
                t2 = yield tt(m2[:, :, 0:8], b3[:, :, 8:16], ns, ALU.mult, 64, t, *rf)
                t3 = yield tt(m2[:, :, 8:16], b3[:, :, 0:8], sn, ALU.mult, 64, t)
                G.put(bank, t3)
                t4 = yield tt(nd[:, :, :, 0:16], m1.unsqueeze(2).broadcast_to([128, 8, 2, 16]),
                              m2.unsqueeze(2).broadcast_to([128, 8, 2, 16]), ALU.add, 256, t1, t3)
                RP.put(r, t4)
                t = yield from load(QKD[g_][T], slot[:, :], 524288, t4)
                STG.put(slot, t)
                qkd[(g_, T)].set((t,))
            return ev

        qkd = {}

        def stacks(base, P, stk, free, ndp, done, *w):
            for T in range(4):
                (d,) = yield qkd[(base + P // 2, T)]
                nd, nf = yield ndp
                o = 256 * (P % 2)
                src = QKD[base + P // 2][T].rearrange("p (s f) -> p s f", s=2)[:, :, o:o + 256]
                t = yield from load(nd[:, :].rearrange("p (s f) -> p s f", s=2), src, 262144, d, *nf, *w)
                spawn(stack_T(stk, free, ndp, nd, T, t, done[T]), 4, f"stk{P}.{T}")

        def stack_T(stk, free, ndp, nd, T, t, done):
            bank, bf = yield TP
            for j in range(4):
                u = yield tr(bank[:, j * 128:j * 128 + 128], nd[:, j * 128:j * 128 + 128], t, *bf, inc=j == 3)
            ndp.put(nd, u)
            c = slice(T * 128, T * 128 + 128)
            b3 = bank[:, :].rearrange("p (a c) -> p a c", a=4)
            th = yield act(stk[:, 0:4, c], b3, AF.Copy, 512, u, *free)
            t1 = yield tt(stk[:, 4:6, c], b3[:, 0:2, :], stk[:, 0:2, c].bitcast(F32), ALU.subtract, 256, th)
            k = stk[64:128, 2:4, c]
            t2 = yield tt(k, b3[64:128, 2:4, :], k.bitcast(F32), ALU.subtract, 256, th)
            TP.put(bank, t2)
            done.set((th, t1, t2))

        def soft_row(s, n, mask, scale, e, t, ef):
            v, vf = yield SP
            tm = yield vop(lambda x: x.tensor_tensor_reduce(e[:, 0:n], s[:, 0:n], mask[:, 512 - n:512], -scale, 3.0e38,
                                                            ALU.add, ALU.min, v[:, 0:1]), n, t, *ef, *vf)
            S.put(s, tm)
            te = yield act(e[:, 0:n], e[:, 0:n], AF.Exp, n, tm, bias=v[:, 0:1], scale=-1.0, acc=v[:, 1:2])
            tr_ = yield vop(lambda x: x.reciprocal(v[:, 2:3], v[:, 1:2]), 8, te)
            return v, te, tr_

        def scores(stk, hh, i, mask, e, ef, rdy):
            n = 128 * (i + 1)
            w = []
            for T in range(i + 1):
                w += list((yield rdy[T]))
            s, sf = yield S
            c = 110 if n < 512 else 216
            q = slice(128 * i, 128 * i + 128)
            yield mm(s[:, 0:n], stk[:, hh, q], stk[:, 2 + hh, 0:n], True, False, c, *w, *sf)
            t = yield mm(s[:, 0:n], stk[:, 4 + hh, q], stk[:, 2 + hh, 0:n], False, True, c)
            return (yield from soft_row(s, n, mask, 0.125, e, t, ef))

        def turn_P(e, n, pt, pf, *w):
            bank, bf = yield TP
            for j in range(n // 128):
                t = yield tr(bank[:, j * 128:j * 128 + 128], e[:, j * 128:j * 128 + 128], *w, *bf,
                             inc=j == n // 128 - 1)
            u = yield act(pt[:, 0:n], bank[:, 0:n], AF.Copy, n, t, *pf)
            TP.put(bank, u)
            return t, u

        def add_x(scale, xtok, then=None, mul=None, sums=None):
            def ev(nh, T, bank, tok):
                x = X[:, T, nh * 512:nh * 512 + 512]
                w = yield xtok[(T, nh)]
                if sums is not None and T < ACT_ROWS:
                    if nh == 0:
                        sums[T] = yield SP
                    else:
                        yield lambda: T in sums
                    v, vf = sums[T]
                    t = yield vop(lambda e: e.tensor_tensor_reduce(x, x, bank[:, :], 1.0, 0.0, ALU.add, ALU.add,
                                                                   v[:, nh:nh + 1]), 512, tok, *w, *vf)
                elif mul is not None:
                    t = yield stt(x, bank[:, :], mul, x, ALU.mult, ALU.add, 512, tok, *w)
                elif scale == 1.0:
                    t = yield tt(x, x, bank[:, :], ALU.add, 512, tok, *w)
                else:
                    t = yield stt(x, x, scale, bank[:, :], ALU.mult, ALU.add, 512, tok, *w)
                G.put(bank, t)
                then[(T, nh)].set((t,))
            return ev

        def gather(fs):
            r = []
            for f in fs:
                r += list((yield f))
            return tuple(r)

        def later(gen):
            f = Fut()

            def run():
                f.set((yield from gen))
            spawn(run(), 0, "later")
            return f

        def freed(last, *dicts):
            r = tuple(last)
            for d in dicts:
                r += yield from gather(d.values())
            return r

        def pairs(d):
            r = []
            for k in sorted(d):
                r.append((yield d[k]))
            return r

        def xfuts():
            return {(T, nh): Fut() for T in range(4) for nh in range(2)}

        def gains(names, bufs, *w):
            out_ = []
            for a, b in zip(names, bufs):
                t = yield from load(b, a.broadcast_to([128, 1024]), 524288, *w)
                out_.append(t)
            return tuple(out_)

        def norm_ln(T, xt, gb, G1, B1, ready, out_x, sums):
            x0, x1 = X[:, T, 0:512], X[:, T, 512:1024]
            a = yield xt[(T, 0)]
            if T < ACT_ROWS:
                b = yield xt[(T, 1)]
                v, _ = sums[T]
                j, jf = yield STG
                t = yield gop(lambda e: e.tensor_tensor(v[:, 2:3], v[:, 0:1], v[:, 1:2], ALU.add), 1, *a, *b)
                t = yield gop(lambda e: e.tensor_scalar(v[:, 12:13], v[:, 2:3], 1.0 / 1024, None, ALU.mult), 1, t)
                t = yield gop(lambda e: e.tensor_scalar(v[:, 3:4], v[:, 2:3], -1.0 / 1024, None, ALU.mult), 1, t)
                t0 = yield act(j[:, 0:512], x0, AF.Square, 512, t, *jf, bias=v[:, 3:4], acc=v[:, 4:5])
                t1 = yield act(j[:, 512:1024], x1, AF.Square, 512, t, bias=v[:, 3:4], acc=v[:, 5:6])
                STG.put(j, t1)
                t2 = yield gop(lambda e: e.tensor_tensor(v[:, 6:7], v[:, 4:5], v[:, 5:6], ALU.add), 1, t0, t1)
                t2 = yield gop(lambda e: e.tensor_scalar(v[:, 14:15], v[:, 6:7], 1.0 / 1024, 1e-5, ALU.mult, ALU.add), 1,
                               t2)
                t = t1
            else:
                v, vf = yield SP
                t0 = yield vop(lambda e: e.bn_stats(v[:, 0:6], x0), 512, *a, *vf)
                b = yield xt[(T, 1)]
                t1 = yield vop(lambda e: e.bn_stats(v[:, 6:12], x1), 512, *b, *vf)
                t = yield vop(lambda e: e.bn_aggr(v[:, 12:14], v[:, 0:12].rearrange("p (a b) -> p a b", a=2)), 12, t0, t1)
                t2 = yield gop(lambda e: e.tensor_scalar(v[:, 14:15], v[:, 13:14], 1e-5, None, ALU.add), 1, t)
            t2 = yield gop(lambda e: e.tensor_tensor(v[:, 15:16], v[:, 14:15], half[:, 0:1], ALU.pow), 1, t2, g["half"])
            gt = yield gb
            ok = []
            for h in range(2):
                x = (x0, x1)[h]
                c = slice(h * 512, h * 512 + 512)
                u = yield stt(x, x, v[:, 12:13], G1[:, c], ALU.subtract, ALU.mult, 512, t, *gt)
                u = yield stt(x, x, v[:, 15:16], B1[:, c], ALU.mult, ALU.add, 512, u, t2)
                ok.append(u)
                out_x[(T, h)].set((u,))
                spawn(turn_T(X[:, T, :], T, XH, XL, ready, 4 * h, 4, u), LP[2] + LP[1] * T, "turn_ln")
            SP.put(v, *ok)

        def ple(l, after):
            r0 = 4 + 2 * l
            ph, pl = XH[:, r0:r0 + 2, :], XL[:, r0:r0 + 2, :]
            rd = Ready()

            def prep():
                slot, free = yield STG
                pn = slot[:, :].rearrange("p (a c) -> p a c", a=4)
                t = yield from load(pn, A["p"][l, 0].rearrange("(a p) c -> p a c", p=128), 524288, *free)
                w = yield after
                fs = []
                for T in range(4):
                    f = Fut()
                    fs.append(f)

                    def turn(T=T, f=f):
                        yield from turn_T(pn[:, T, :], T, ph, pl, rd, 0, 2, t, *w)
                        f.set(rd.f[(0, T)].v)
                    spawn(turn(), 3, "turn_p")
                for f in fs:
                    d = yield f
                STG.put(slot, *d)

            spawn(prep(), 3, "ple_prep")
            tiles = {}

            def ev(nh, T, bank, tok):
                if nh == 0:
                    tiles[T] = yield STG
                else:
                    yield lambda: T in tiles
                e, free = tiles[T]
                t = yield act(e[:, nh * 512:nh * 512 + 512], bank[:, :], AF.Copy, 512, tok, *free)
                G.put(bank, t)
                if nh == 0:
                    return
                t = yield from load(ED[l][T], e[:, :], 524288, t)
                STG.put(e, t)
                ed[(l, T)].set((t,))

            yield from gemmB(lambda nh, k: wB(A["ple_w_proj"][l], k, nh * 512), 2, 2, rows(ph), rows(pl), rd, ev,
                             rows_first=True)

        ed = {(l, T): Fut() for l in range(2) for T in range(4)}

        def normed_e(l, zone):
            E_ = at_("EE", 52, [128, 4, 1024])
            er = {T: Fut() for T in range(4)}
            pgf = Fut()

            def one(T):
                z = yield zone
                (d,) = yield ed[(l, T)]
                e = E_[:, T, :]
                t = yield from load(e, ED[l][T], 524288, d, *z)
                v, vf = yield SP
                j, jf = yield STG
                t = yield act(j[:, :], e, AF.Square, 1024, t, *vf, *jf, acc=v[:, 0:1])
                STG.put(j, t)
                t = yield gop(lambda x: x.tensor_scalar(v[:, 1:2], v[:, 0:1], 1.0 / 1024, 1e-5, ALU.mult, ALU.add), 1, t)
                t = yield gop(lambda x: x.tensor_tensor(v[:, 2:3], v[:, 1:2], half[:, 0:1], ALU.pow), 1, t, g["half"])
                pg, tg_ = yield pgf
                t = yield stt(e, e, v[:, 2:3], pg[:, :], ALU.mult, ALU.mult, 1024, t, tg_)
                SP.put(v, t)
                er[T].set((t,))

            def gain():
                yield zone
                pg, pf = yield STG
                t = yield from load(pg[:, :], A["ple_norm_g"][l:l + 1].broadcast_to([128, 1024]), 524288, *pf)
                pgf.set((pg, t))
                r = yield from gather(er.values())
                STG.put(pg, *r)

            spawn(gain(), 6, "pgain")
            for T in range(4):
                spawn(one(T), 8 + T, "ple_e")
            return E_, er

        def ffn(l, xr_, x0, x2, x1_ln, gb_w):
            W1, W2 = A["ffn_w1"][l], A["ffn_w2"][l]
            HH, HL = at_("HH", 0, [128, 10, 512], F32R), at_("HL", 20, [128, 10, 512], F32R)
            R = Pool([at_(f"FR{i}", 40 + 2 * i, [128, 512]) for i in range(2)])
            G1, B1 = at_("G2", 44, [128, 1024]), at_("B2", 48, [128, 1024])
            hr = {j: Fut() for j in range(32)}
            hrel = {}
            gb = Fut()

            def ld():
                r = yield from gains((A["ln2_g"][l:l + 1], A["ln2_b"][l:l + 1]), (G1[:, :], B1[:, :]), *gb_w)
                gb.set(r)

            spawn(ld(), 6, "ld2")
            if l == 0:
                spawn(spare(), 30, "spare")

            def ev_h(j0):
                def ev(n, bank, tok):
                    j = j0 + n
                    r, rf = yield R
                    w = hrel.get(j - 10, ())
                    t = yield act(r[:, :], bank[:, :], AF.Relu, 512, tok, *rf, *gb_w)
                    G.put(bank, t)
                    t = yield tt(r[:, :], r[:, :], r[:, :], ALU.mult, 512, t)
                    th = yield act(HH[:, j % 10, :], r[:, :], AF.Copy, 512, t, *w)
                    tl = yield tt(HL[:, j % 10, :], r[:, :], HH[:, j % 10, :].bitcast(F32), ALU.subtract, 512, th, *w)
                    R.put(r, th, tl)
                    hr[j].set((th, tl))
                return ev

            rdy = Ready()
            sums = {}
            for T in range(4):
                spawn(norm_ln(T, x2, gb, G1, B1, rdy, x1_ln, sums), LP[0] + LP[1] * T, f"ln2.{T}")
            steps = [xfuts() for _ in range(3)] + [x2]
            cur = x0
            lo_ = 0
            for q in range(4):
                hi_ = min(8 * q + 10, 32)
                yield from gemmA(W1, lo_ * 128, hi_ * 128, 8, xh, xl, xr_, ev_h(lo_), early=2 if q == 0 else 0)
                lo_ = hi_
                yield from gemmB(lambda nh, k: wB(W2, 8 * q + k, nh * 512), 2, 8,
                                 lambda k: HH[:, (8 * q + k) % 10, :], lambda k: HL[:, (8 * q + k) % 10, :],
                                 lambda k, T: hr[8 * q + k], add_x(ALPHA if q == 0 else 1.0, cur, steps[q], sums=sums if q == 3 else None))
                cur = steps[q]
                for k in range(8):
                    hrel[8 * q + k] = (g["last"],)
            return rdy

        def gate(l, rdy, x_in, x_out, zone, es):
            E_, er = es
            R = Pool([at_(f"FR{i}", 40 + 2 * i, [128, 512]) for i in range(2)])

            def ev(nh, T, bank, tok):
                z = yield zone
                r, rf = yield R
                et = yield er[T]
                w = yield x_in[(T, nh)]
                x = X[:, T, nh * 512:nh * 512 + 512]
                t = yield act(r[:, :], bank[:, :], AF.Sigmoid, 512, tok, *rf, *z)
                G.put(bank, t)
                t = yield tt(r[:, :], r[:, :], E_[:, T, nh * 512:nh * 512 + 512], ALU.mult, 512, t, *et)
                t = yield tt(x, x, r[:, :], ALU.add, 512, t, *w)
                R.put(r, t)
                x_out[(T, nh)].set((t,))

            yield from gemmB(lambda nh, k: wB(A["ple_w_gate"][l], k, nh * 512), 2, 8, xh, xl, rdy, ev)

        def after_first(l, xr1, x3, zone, pre):
            x4, x5, x6 = xfuts(), xfuts(), xfuts()
            es = normed_e(l, later(freed(zone, x3)))
            rdy = yield from ffn(l, xr1, x3, x4, x5, zone)
            last = (g["last"],)
            zf = later(freed(last, x4))
            nxt = pre(x6, later(freed(last, x4, x5)))
            yield from gate(l, rdy, x5, x6, zf, es)
            return x6, later(freed(last + (g["last"],), x4, x5, x6)), nxt

        def layer0(pre):
            W = A["ev_w_in"][0]
            xr = Ready()
            turns_x(xr, XH, XL)
            HI = at_("HI", 16, [128, 4, 512])
            GS = at_("GS", 24, [128, 4, 512])
            FS = at_("FS", 32, [128, 4, 512])
            QS = at_("QS", 40, [128, 4, 512])
            BUF = [at_(f"HB{i}", 48 + 2 * i, [128, 512]) for i in range(6)]
            AT = at_("AT", 60, [128, 512])
            KN = at_("KN", 62, [128, 512])
            STA = at_("STA", 64, [128, 7, 128])
            RESET = MASK
            ON = at_("ON", 0, [128, 4, 1024])
            quad, tmps = Pool([0]), Pool(BUF[4:6])
            small_pools = Pool([0])
            fs = [Fut() for _ in range(4)]
            qs = [Fut() for _ in range(4)]
            gs = [Fut() for _ in range(4)]
            his = [Fut() for _ in range(4)]
            onr = Ready()
            hg_done = []
            lb = Fut()

            def vectors():
                t1 = yield from load(BUF[5][0:8, 0:128], A["hg_lb_logits"].rearrange("a (h k) -> (a h) k", h=4), 4096)
                yield lambda: "ident" in g
                bank, free = yield TP
                t = yield mm(bank[:, 0:8], BUF[5][0:8, 0:128], ident[0:8, 0:8], True, True, 30, t1, g["ident"], *free)
                t = yield cp(vecT[:, 0:8], bank[:, 0:8], 8, t)
                TP.put(bank, t)
                tmps.put(BUF[5], t)
                m = lbs[:, 0:4]
                t = yield tt(m, vecT[:, 0:4], vecT[:, 4:8], ALU.max, 4, t)
                t = yield tt(vecT[:, 0:4], vecT[:, 0:4], m, ALU.subtract, 4, t)
                t = yield tt(vecT[:, 4:8], vecT[:, 4:8], m, ALU.subtract, 4, t)
                t = yield act(vecT[:, 0:8], vecT[:, 0:8], AF.Exp, 8, t)
                t = yield tt(m, vecT[:, 0:4], vecT[:, 4:8], ALU.add, 4, t)
                t = yield vop(lambda e: e.reciprocal(lbs[:, 0:4], lbs[:, 0:4]), 30, t)
                t = yield tt(lbs[:, 4:8], lbs[:, 0:4], vecT[:, 0:4], ALU.mult, 4, t)
                t = yield tt(lbs[:, 8:12], lbs[:, 0:4], vecT[:, 4:8], ALU.mult, 4, t)
                lb.set((t,))

            def lambdas():
                slot, free = yield STG
                L = slot[:, 0:256]
                src = A["da_lambda"].rearrange("o a b -> o (a b)")
                t = yield from load(L, src.broadcast_to([128, 256]), 131072, *free)
                tmp = slot[:, 256:320]
                t = yield vop(lambda e: e.tensor_tensor_reduce(tmp, L[:, 0:64], L[:, 64:128], 1.0, 0.0, ALU.mult,
                                                               ALU.add, lam[:, 0:1]), 64, t)
                t = yield vop(lambda e: e.tensor_tensor_reduce(tmp, L[:, 128:192], L[:, 192:256], 1.0, 0.0, ALU.mult,
                                                               ALU.add, lam[:, 1:2]), 64, t)
                STG.put(slot, t)
                t = yield act(lam[:, 0:2], lam[:, 0:2], AF.Exp, 2, t)
                t = yield tt(lam[:, 2:3], lam[:, 1:2], lam[:, 0:1], ALU.subtract, 1, t)
                t = yield ts(lam[:, 3:4], lam[:, 2:3], -0.2, None, ALU.add, None, 1, t)
                g["nlam"] = t

            def ev_hf(n, bank, tok):
                w = yield lb
                t = yield act(FS[:, n, :], bank[:, :], AF.Sigmoid, 512, tok)
                G.put(bank, t)
                t = yield ts(FS[:, n, :], FS[:, n, :], lbs[:, 8 + n:9 + n], lbs[:, 4 + n:5 + n], ALU.mult, ALU.add, 512,
                             t, *w)
                fs[n].set((t,))

            def ev_hq(n, bank, tok):
                tmp, free = yield tmps
                t = yield act(tmp[:, :], bank[:, :], AF.Sigmoid, 512, tok, *free)
                t = yield tt(QS[:, n, :], bank[:, :], tmp[:, :], ALU.mult, 512, t)
                G.put(bank, t)
                tmps.put(tmp, t)
                qs[n].set((t,))

            def ev_hg(nh, T, bank, tok):
                tmp, free = yield tmps
                t = yield act(tmp[:, :], bank[:, :], AF.Sigmoid, 512, tok, *free)
                g["hg", T] = t
                t = yield tt(GS[:, T, :], bank[:, :], tmp[:, :], ALU.mult, 512, t)
                G.put(bank, t)
                tmps.put(tmp, t)
                g3 = GS[:, T, :].rearrange("p (h v) -> p h v", h=4)
                t = yield tt(g3, g3, GHG[:, :].unsqueeze(1).broadcast_to([128, 4, 128]), ALU.mult, 512, t, g["ghg"])
                gs[T].set((t,))

            def ev_hi(nh, T, bank, tok):
                t = yield act(HI[:, T, :], bank[:, :], AF.Copy, 512, tok)
                G.put(bank, t)
                his[T].set((t,))

            def chunks(ap):
                return ap.rearrange("p (c t) -> p c t", c=8)

            def finish(bank, tok, gain, c0, done, tpool, *w):
                tmp, free = yield tpool
                sq = tmp[:, 0:512]
                t = yield act(sq, bank[:, :], AF.Square, 512, tok, *free)
                s, sf = yield SP
                t = yield vop(lambda e: e.tensor_reduce(s[:, 0:4], sq.rearrange("p (a v) -> p a v", a=4), AX.X,
                                                        ALU.add), 512, t, *sf)
                tpool.put(tmp, t)
                t = yield gop(lambda e: e.tensor_scalar(s[:, 4:8], s[:, 0:4], 1.0 / 128, 1e-5, ALU.mult, ALU.add), 4, t)
                t = yield gop(lambda e: e.tensor_tensor(s[:, 8:12], s[:, 4:8], half, ALU.pow), 4, t, g["half"])
                for T in range(4):
                    u = yield stt(ON[:, T, c0:c0 + 128], bank[:, T * 128:(T + 1) * 128], s[:, 8 + T:9 + T], gain(T),
                                  ALU.mult, ALU.mult, 128, t, *w)
                    onr.f[(c0 // 128, T)].set((u,))
                SP.put(s, u)
                OP.put(bank, u)
                done(u)

            def hgrn(h):
                w = yield fs[h]
                q = yield qs[h]
                gg = yield AllOf(gs)
                gg = gg + tuple(g["hg", T] for T in range(4))
                _, free = yield quad
                KK, T1, D1, D2 = BUF[0], BUF[1], BUF[2], BUF[3]
                F, Q = FS[:, h, :], QS[:, h, :]
                tk = yield ts(KK[:, :], F, -1.0, 1.0, ALU.mult, ALU.add, 512, *w, *free)
                t = yield act(F, F, AF.Ln, 512, tk, *gg)
                tb = yield vop(lambda e: e.tensor_tensor_scan(F, RESET[:, :], F, 0.0, ALU.mult, ALU.add),
                               512, t, g["reset"])
                b3 = chunks(F)
                t1 = yield tt(chunks(D1[:, :]), b3, b3[:, :, 31:32].broadcast_to([128, 8, 64]), ALU.subtract, 512, tb,
                              *free)
                t2 = yield tt(chunks(D2[:, :]), b3, b3[:, :, 63:64].broadcast_to([128, 8, 64]), ALU.subtract, 512, tb,
                              *free)
                te = yield act(T1[:, :], D1[:, :], AF.Exp, 512, t1, *free)
                tq = yield tt(T1[:, :], Q, T1[:, :], ALU.mult, 512, te, *q)
                te = yield act(D1[:, :], D1[:, :], AF.Exp, 512, te, scale=-1.0)
                ta = yield tt(D1[:, :], KK[:, :], D1[:, :], ALU.mult, 512, te, tk)
                te = yield act(D2[:, :], D2[:, :], AF.Exp, 512, t2, scale=-1.0)
                ts_ = yield tt(KK[:, :], KK[:, :], D2[:, :], ALU.mult, 512, te, ta)
                te = yield act(F, F, AF.Exp, 512, t2)
                to = yield tt(Q, Q, F, ALU.mult, 512, te, tq)
                _, pf = yield small_pools
                a, free = yield S
                for T in range(4):
                    c = slice(T * 128, T * 128 + 128)
                    t = yield mm(a[:, c], D1[:, c], T1[:, c], True, True, 219, tq, ta, *free, inc=T == 3)
                at3 = AT[:, :].rearrange("p (a c) -> p a c", a=4)
                tat = yield vop(lambda e: e.copy_predicated(at3, TRI[:, :].unsqueeze(1).broadcast_to([128, 4, 128]),
                                                            a[:, :].rearrange("p (a c) -> p a c", a=4)), 512, t,
                                g["tri"], g["at0"], *pf)
                S.put(a, tat)
                bank, free = yield TP
                for T in range(4):
                    c = slice(T * 128, T * 128 + 128)
                    t = yield tr(bank[:, c], KK[:, c], ts_, *free, inc=T == 3)
                tkn = yield act(KN[:, :], bank[:, :], AF.Copy, 512, t, *pf)
                TP.put(bank, tkn)
                quad.put(0, t)
                hv = yield AllOf(his)
                st = None
                ue, fe = yield S
                uo, fo = yield S
                for c in range(7):
                    p0, T = 64 * (c % 2), c // 2
                    u = (ue, uo)[c % 2][:, T * 128:T * 128 + 128]
                    t = yield mm(u, KN[p0:p0 + 64, T * 128:T * 128 + 128],
                                 HI[p0:p0 + 64, T, h * 128:h * 128 + 128], True, True, 219, tkn, *hv, *fe, *fo,
                                 inc=c >= 5)
                    both = (t,) if c == 5 else (*both, t) if c == 6 else ()
                for c in range(7):
                    u = (ue, uo)[c % 2][:, c // 2 * 128:c // 2 * 128 + 128]
                    if c == 0:
                        st = yield cp(STA[:, 0, :], u, 128, *both, *pf)
                    else:
                        st = yield stt(STA[:, c, :], STA[:, c - 1, :], F[:, c * 64 + 63:c * 64 + 64], u, ALU.mult,
                                       ALU.add, 128, st)
                S.put(ue, st)
                S.put(uo, st)
                o, free = yield OP
                for T in range(4):
                    for c in (2 * T, 2 * T + 1):
                        p0 = 64 * (c % 2)
                        r = o[p0:p0 + 64, T * 128:T * 128 + 128]
                        t = yield mm(r, AT[:, T * 128 + p0:T * 128 + p0 + 64], HI[:, T, h * 128:h * 128 + 128], True,
                                     c == 0, 135, tat, *free, inc=c == 0)
                        if c:
                            t = yield mm(r, Q[:, c * 64:c * 64 + 64], STA[:, c - 1, :], False, True, 135, to, st)
                small_pools.put(0, t)

                def done(u):
                    hg_done.append(u)
                    hg_done.append(t)
                    if len(hg_done) == 8:
                        hgf.set(tuple(hg_done))

                spawn(finish(o, t, lambda T: GS[:, T, h * 128:h * 128 + 128], 512 + h * 128, done, tmps, *gg), 4,
                      f"fin{h}")

            hgf = Fut()

            def loads():

                g["reset"] = yield from load(RESET[:, :], A["reset"], 262144)
                g["ghg"] = yield from load(GHG[:, :], A["hg_norm_g"].broadcast_to([128, 128]), 65536)
                g["tri"] = yield from load(TRI[:, :], A["tri"], 65536)
                g["at0"] = yield vop(lambda e: e.memset(AT[:, :], 0.0), 512)

            tmps.free.pop()
            spawn(loads(), 1, "loads")
            spawn(vectors(), 1, "vectors")
            for h in range(4):
                spawn(hgrn(h), 5 + h, f"hgrn{h}")
            yield from gemmA(W, 2048, 2560, 8, xh, xl, xr, ev_hf, early=1)
            yield from gemmA(W, 1536, 2048, 8, xh, xl, xr, ev_hq)
            yield from gemmB(lambda nh, k: wB(W, k, 3072), 1, 8, xh, xl, xr, ev_hg)
            yield from gemmB(lambda nh, k: wB(W, k, 2560), 1, 8, xh, xl, xr, ev_hi)

            V = at_("DV", 16, [128, 4, 512])
            STK = Pool([at_(f"STK{i}", 24 + 12 * i, [128, 6, 512], F32R) for i in range(2)])
            EP = Pool([at_(f"EP{i}", 48 + 4 * i, [128, 2, 512]) for i in range(2)])
            PT = Pool([at_(f"PT{i}", 56 + 2 * i, [128, 512]) for i in range(3)])
            NDP = Pool([at_(f"NDP{i}", 62 + 2 * i, [128, 512]) for i in range(3)])
            for g_ in range(2):
                for T in range(4):
                    qkd[(g_, T)] = Fut()
            vd = {T: Fut() for T in range(4)}
            vr = {T: Fut() for T in range(4)}

            def ev_va(nh, T, bank, tok):
                slot, free = yield STG
                t = yield act(slot[:, 0:512], bank[:, :], AF.Copy, 512, tok, *free)
                G.put(bank, t)
                t = yield from load(VD[T], slot[:, 0:512], 262144, t)
                STG.put(slot, t)
                vd[T].set((t,))

            def reload_v():
                w = yield hgf
                for T in range(4):
                    (d,) = yield vd[T]
                    t = yield from load(V[:, T, :], VD[T], 262144, d, *w)
                    vr[T].set((t,))

            soft = {}
            stk_done = {}

            def da_scores():
                w = yield hgf
                w += yield mk
                for P in range(4):
                    stk, free = yield STK
                    rdy = [Fut() for _ in range(4)]
                    spawn(stacks(0, P, stk, free + w, NDP, rdy, *w), 4, f"stacks{P}")
                    stk_done[P] = []
                    for i in range(4):
                        ep, ef = yield EP
                        soft[(P, i)] = Fut()
                        spawn(da_unit(P, i, stk, ep, ef + w, rdy), 5, f"unit{P}.{i}")

            def da_unit(P, i, stk, ep, ef, rdy):
                n = 128 * (i + 1)
                v0, t0, r0 = yield from scores(stk, 0, i, MASK, ep[:, 0, :], ef, rdy)
                v1, t1, r1 = yield from scores(stk, 1, i, MASK, ep[:, 1, :], ef, rdy)
                stk_done[P].append(t1)
                if len(stk_done[P]) == 4:
                    STK.put(stk, *stk_done[P])
                e0, e1 = ep[:, 0, 0:n], ep[:, 1, 0:n]
                t = yield ts(e0, e0, v0[:, 2:3], None, ALU.mult, None, n, t0, r0)
                u = yield tt(v1[:, 3:4], v1[:, 2:3], lam[:, 3:4], ALU.mult, 1, r1, g["nlam"])
                t = yield stt(e0, e1, v1[:, 3:4], e0, ALU.mult, ALU.add, n, t, u, t1)
                SP.put(v0, t)
                SP.put(v1, t)
                soft[(P, i)].set((ep, t))

            def da_out():
                yield hgf
                for P in range(4):
                    o, of = yield OP
                    for i in range(4):
                        yield lambda: (P, i) in soft
                        ep, t = yield soft[(P, i)]
                        pt, pf = yield PT
                        n = 128 * (i + 1)
                        t, u = yield from turn_P(ep[:, 0, :], n, pt, pf, t)
                        EP.put(ep, t)
                        for j in range(i + 1):
                            (vt,) = yield vr[j]
                            t = yield mm(o[:, i * 128:i * 128 + 128], pt[:, j * 128:j * 128 + 128],
                                         V[:, j, P * 128:P * 128 + 128], j == 0, j == i, 219, u, vt, *of)
                        PT.put(pt, t)
                    spawn(finish(o, t, lambda T: GDA[:, :], P * 128, lambda u: None, STG, g["gda"]), 4, f"finda{P}")

            def load_da():
                g["rope"] = yield from load(ROPE[:, :, :], A["rope"], 65536)
                t = yield from load(GDA[:, :], A["da_subln_g"].broadcast_to([128, 128]), 65536)
                g["gda"] = yield ts(GDA[:, :], GDA[:, :], 0.8, None, ALU.mult, None, 128, t)
                w = yield hgf
                g["mask0"] = yield from load(MASK[:, :], A["mask0"], 262144, *w)
                mk.set((g["mask0"],))

            mk = Fut()
            spawn(load_da(), 6, "load_da")
            spawn(lambdas(), 6, "lambdas")
            spawn(da_scores(), 5, "da_scores")
            spawn(da_out(), 4, "da_out")
            spawn(reload_v(), 6, "reload_v")
            yield from gemmB(lambda nh, k: wQ(W, k, 0, 512), 1, 8, xh, xl, xr, ev_qk(0))
            yield from gemmB(lambda nh, k: wQ(W, k, 256, 768), 1, 8, xh, xl, xr, ev_qk(1))
            yield from gemmB(lambda nh, k: wB(W, k, 1024), 1, 8, xh, xl, xr, ev_va)
            w_in_done = g["last"]

            orr = Ready()

            def turn_k(kt):
                w = yield AllOf([onr.f[(kt, T)] for T in range(4)])
                bank, free = yield TP
                for T in range(4):
                    t = yield tr(bank[:, T * 128:T * 128 + 128], ON[:, T, kt * 128:kt * 128 + 128], *w, *free, inc=T == 3)
                th = yield act(XH[:, kt, :], bank[:, :], AF.Copy, 512, t, w_in_done)
                tl = yield tt(XL[:, kt, :], bank[:, :], XH[:, kt, :].bitcast(F32), ALU.subtract, 512, t, th, w_in_done)
                TP.put(bank, tl)
                for T in range(4):
                    orr.f[(kt, T)].set((th, tl))

            for kt in (4, 5, 6, 7, 0, 1, 2, 3):
                spawn(turn_k(kt), 4, f"turn_k{kt}")
            WO = A["ev_w_out"][0]
            x0 = {(T, nh): Fut() for T in range(4) for nh in range(2)}
            for f in x0.values():
                f.set(sum((g["x", T].v for T in range(4)), ()))
            x1, x2, x3 = xfuts(), xfuts(), xfuts()
            off = lambda k0: (lambda k, T: orr(k + k0, T))
            yield from gemmB(lambda nh, k: wB(WO, k + 4, nh * 512), 2, 4, rows(XH, 4), rows(XL, 4), off(4),
                             add_x(ALPHA, x0, x1))
            four = Fut()
            four.set((g["last"],))
            yield from ple(0, four)
            yield from ple(1, four)
            G1, B1 = at_("LG1", 60, [128, 1024]), at_("LB1", 64, [128, 1024])
            gb = Fut()

            def ld():
                w = yield from gather([onr.f[(3, T)] for T in range(4)])
                for p in (PT, NDP, EP):
                    for it, tk in p.free:
                        w += tuple(tk)
                r = yield from gains((A["ln1_g"][0:1], A["ln1_b"][0:1]), (G1[:, :], B1[:, :]), *w)
                gb.set(r)

            spawn(ld(), 1, "ld")
            xr1 = Ready()
            sums = {}
            for T in range(4):
                spawn(norm_ln(T, x2, gb, G1, B1, xr1, x3, sums), LP[0] + LP[1] * T, f"ln1.{T}")
            yield from gemmB(lambda nh, k: wB(WO, k, nh * 512), 2, 4, xh, xl, off(0), add_x(1.0, x1, x2, sums=sums),
                             rows_first=True)
            return (yield from after_first(0, xr1, x3, (g["last"],), pre))

        def pre1(x_in, _):
            xr = Ready()
            for T in range(4):
                for k0 in (0, 4):
                    def turn(T=T, k0=k0):
                        w = yield x_in[(T, 0)]
                        w += yield x_in[(T, 1)]
                        yield from turn_T(X[:, T, :], T, XH, XL, xr, k0, 4, *w)
                    spawn(turn(), 2, "turn_x1")
            return xr

        def layer1(x_in, zone, xr, pre):
            W, WO = A["od_w_in"][0], A["od_w_out"][0]
            V = at_("OV", 0, [128, 4, 1024])
            STK = Pool([at_(f"OSTK{i}", 16 + 12 * i, [128, 6, 512], F32R) for i in range(2)])
            OHL = Pool([at_(f"OHL{i}", 40 + 4 * i, [128, 2, 512], F32R) for i in range(2)])
            EP = Pool([at_(f"OE{i}", 48 + 2 * i, [128, 512]) for i in range(4)])
            PT = Pool([at_(f"OPT{i}", 56 + 2 * i, [128, 512]) for i in range(4)])
            NDP = Pool([at_(f"ONDP{i}", 64 + 2 * i, [128, 512]) for i in range(2)])
            for g_ in range(2, 6):
                for T in range(4):
                    qkd[(g_, T)] = Fut()
            vr = xfuts()
            soft = {}
            left = {}

            def ev_v(nh, T, bank, tok):
                z = yield zone
                t = yield act(V[:, T, nh * 512:nh * 512 + 512], bank[:, :], AF.Copy, 512, tok, *z)
                G.put(bank, t)
                vr[(T, nh)].set((t,))

            def load_mask():
                z = yield zone
                t = yield from load(MASK[:, :], A["mask1"], 262144, *z)
                mk.set((t,))

            mk = Fut()

            def sc():
                w = yield mk
                z = yield zone
                for P in range(8):
                    stk, free = yield STK
                    rdy = [Fut() for _ in range(4)]
                    spawn(stacks(2, P, stk, free + z, NDP, rdy, *z), 4, f"stacks{P}")
                    left[P] = []
                    for i in range(4):
                        for hh in range(2):
                            e, ef = yield EP
                            soft[(P, i, hh)] = Fut()
                            spawn(unit(P, i, hh, stk, e, ef + z + w, rdy), 5, f"unit{P}.{i}")

            def unit(P, i, hh, stk, e, ef, rdy):
                n = 128 * (i + 1)
                v, t, r = yield from scores(stk, hh, i, MASK, e, ef, rdy)
                left[P].append(t)
                if len(left[P]) == 8:
                    STK.put(stk, *left[P])
                t = yield ts(e[:, 0:n], e[:, 0:n], v[:, 2:3], None, ALU.mult, None, n, t, r)
                SP.put(v, t)
                soft[(P, i, hh)].set((e, t))

            ok = {P: Fut() for P in range(8)}
            ohl = {}

            def outs():
                z = yield zone
                for P in range(8):
                    o, of = yield OP
                    for i in range(4):
                        pts = []
                        n = 128 * (i + 1)
                        for hh in range(2):
                            yield lambda: (P, i, hh) in soft
                            e, t = yield soft[(P, i, hh)]
                            pt, pf = yield PT
                            t, u = yield from turn_P(e, n, pt, pf + z, t)
                            EP.put(e, t)
                            pts.append((pt, u))
                        for j in range(i + 1):
                            (vt,) = yield vr[(j, P // 4)]
                            for hh in range(2):
                                pt, u = pts[hh]
                                c = (2 * P + hh) * 64
                                t = yield mm(o[64 * hh:64 * hh + 64, i * 128:i * 128 + 128], V[:, j, c:c + 64],
                                             pt[:, j * 128:j * 128 + 128], j == 0, j == i, 135, u, vt, *of,
                                             inc=j == i)
                        for pt, _ in pts:
                            PT.put(pt, t)
                    spawn(out_ev(P, o, t), 3, f"oev{P}")

            def out_ev(P, o, t):
                z = yield zone
                hl, hf = yield OHL
                ohl[P] = hl
                th = yield act(hl[:, 0, :], o[:, :], AF.Copy, 512, t, *hf, *z)
                tl = yield tt(hl[:, 1, :], o[:, :], hl[:, 0, :].bitcast(F32), ALU.subtract, 512, th)
                OP.put(o, tl)
                ok[P].set((th, tl))

            spawn(load_mask(), 6, "mask1")
            spawn(sc(), 5, "scores1")
            spawn(outs(), 4, "outs1")
            yield from gemmB(lambda nh, k: wB(W, k, 2048 + nh * 512), 2, 8, xh, xl, xr, ev_v)
            steps = [x_in] + [xfuts() for _ in range(4)]

            def proj(g_):
                for k in range(2):
                    yield ok[2 * g_ + k]
                yield from gemmB(lambda nh, k: wB(WO, 2 * g_ + k, nh * 512), 2, 2,
                                 lambda k: ohl[2 * g_ + k][:, 0, :], lambda k: ohl[2 * g_ + k][:, 1, :],
                                 lambda k, T: ok[2 * g_ + k], add_x(ALPHA if g_ == 0 else 1.0, steps[g_], steps[g_ + 1],
                                                               sums=sums if g_ == 3 else None),
                                 rows_first=g_ == 3)
                for k in range(2):
                    OHL.put(ohl[2 * g_ + k], g["last"])

            G1, B1 = at_("OLG1", 60, [128, 1024]), at_("OLB1", 64, [128, 1024])
            gb = Fut()

            def ld():
                w = yield ok[7]
                for p in (PT, NDP, EP):
                    for it, tk in p.free:
                        w += tuple(tk)
                r = yield from gains((A["ln1_g"][1:2], A["ln1_b"][1:2]), (G1[:, :], B1[:, :]), *w)
                gb.set(r)

            spawn(ld(), 1, "ld")
            xr1, x3 = Ready(), xfuts()
            sums = {}
            for T in range(4):
                spawn(norm_ln(T, steps[4], gb, G1, B1, xr1, x3, sums), LP[0] + LP[1] * T, f"ln1.{T}")
            for what in ("q0", "q1", "q2", "w0", "q3", "w1", "w2", "w3"):
                n = int(what[1])
                if what[0] == "q":
                    yield from gemmB(lambda nh, k: wQ(W, k, 256 * n, 1024 + 256 * n), 1, 8, xh, xl, xr, ev_qk(2 + n))
                else:
                    yield from proj(n)
            return (yield from after_first(1, xr1, x3, (g["last"],), pre))

        def rms_rows(T, x, xw, tmp, tf, gain, gt, ready, eps, H, L, w=(), each=None):
            v, vf = yield SP
            n0 = yield xw[0]
            t0 = yield act(tmp[:, 0:512], x[:, 0:512], AF.Square, 512, *n0, *tf, *vf, *w, acc=v[:, 0:1])
            n1 = yield xw[1]
            t1 = yield act(tmp[:, 512:1024], x[:, 512:1024], AF.Square, 512, *n1, acc=v[:, 1:2])
            t = yield gop(lambda e: e.tensor_tensor(v[:, 2:3], v[:, 0:1], v[:, 1:2], ALU.add), 1, t0, t1)
            t = yield gop(lambda e: e.tensor_scalar(v[:, 3:4], v[:, 2:3], 1.0 / 1024, eps, ALU.mult, ALU.add), 1, t)
            t = yield gop(lambda e: e.tensor_tensor(v[:, 4:5], v[:, 3:4], half[:, 0:1], ALU.pow), 1, t, g["half"])
            u, last = [], []
            for h in range(2):
                c = slice(h * 512, h * 512 + 512)
                u.append((yield stt(tmp[:, c], x[:, c], v[:, 4:5], gain[:, c], ALU.mult, ALU.mult, 512, t, *gt)))
                last.append(u[h])
                if each is not None:
                    each(h, u[h])
                if H is not None:
                    f = Fut()

                    def turn(h=h, u=u[h], f=f):
                        yield from turn_T(tmp, T, H, L, ready, 4 * h, 4, u)
                        f.set(ready.f[(4 * h, T)].v)
                    spawn(turn(), 2, "turn_r")
                    u[h] = f
            SP.put(v, *last)
            if H is not None:
                a, b = u
                r = (yield a) + (yield b)
                return r
            return tuple(u)

        def rms_all(x_in, gname, goff, hoff, zone):
            gt_ = at_("RG", goff, [128, 1024])
            HT = Pool([at_(f"RT{i}", hoff + 4 * i, [128, 1024]) for i in range(2)])
            rdy = Ready()
            gf = Fut()
            done = [Fut() for _ in range(4)]

            if isinstance(zone, tuple):
                zone = later(freed(zone))

            def ld():
                z = yield zone
                t = yield from load(gt_[:, :], A[gname].broadcast_to([128, 1024]), 524288, *z)
                gf.set((t,))

            def one(T):
                z = yield zone
                tmp, tf = yield HT
                gt = yield gf
                d = yield from rms_rows(T, X[:, T, :], (x_in[(T, 0)], x_in[(T, 1)]), tmp, tf + z, gt_, gt, rdy, 1e-6,
                                        XH, XL)
                HT.put(tmp, *d)
                done[T].set(d)

            spawn(ld(), 1, "ld_g")
            for T in range(4):
                spawn(one(T), 2 + T, f"rms{T}")
            return rdy, done

        def mem_norm(zone):
            MN = at_("MN", 0, [128, 2, 1024])
            MH, ML = at_("MH", 8, [128, 8, 256], F32R), at_("ML", 16, [128, 8, 256], F32R)
            MG = at_("MG", 24, [128, 1024])
            JK = at_("JK", 44, [128, 2, 1024])
            rdy = Ready(2)
            gf = Fut()

            def prep(T):
                z = yield zone
                t = yield from load(MN[:, T, :], A["mem_2"][0, T * 128:T * 128 + 128, :], 524288, *z)
                gt = yield gf
                f = Fut()
                f.set((t,))
                yield from rms_rows(T, MN[:, T, :], (f, f), JK[:, T, :], z, MG, gt, rdy, 1e-6, MH, ML)

            def ld():
                z = yield zone
                t = yield from load(MG[:, :], A["g_mem_2"].broadcast_to([128, 1024]), 524288, *z)
                gf.set((t,))

            spawn(ld(), 2, "ld_gm")
            for T in range(2):
                spawn(prep(T), 8, f"mem{T}")
            return rdy, MH, ML

        def mem_kv(normed, done):
            rdy, MH, ML = normed
            sent = []

            def ev_k(n, bank, tok):
                s_, f = yield STG
                t = yield act(s_[:, 0:256], bank[:, 0:256], AF.Copy, 256, tok, *f)
                G.put(bank, t)
                t = yield from load(KTD[n], s_[:, 0:256], 131072, t)
                STG.put(s_, t)
                sent.append(t)

            def ev_v(nh, T, bank, tok):
                s_, f = yield STG
                t = yield act(s_[:, 0:512], bank[:, :], AF.Copy, 512, tok, *f)
                G.put(bank, t)
                t = yield from load(MVD[T], s_[:, 0:512], 262144, t)
                STG.put(s_, t)
                sent.append(t)

            W = A["w_ckv_2"][0]
            yield from gemmA(W, 0, 512, 8, rows(MH), rows(ML), rdy, ev_k, N=256)
            yield from gemmB(lambda nh, k: wB(W, k, 512), 1, 8, rows(MH), rows(ML), rdy, ev_v, TN=2)
            last = g["last"]

            def fin():
                yield lambda: len(sent) == 6
                done.set(tuple(sent) + (last,))
            spawn(fin(), 3, "memfin")

        def pre2(x_in, zone):
            return rms_all(x_in, "g_mix_2", 28, 32, zone) + (mem_norm(zone),)

        def block2(x_in, zone, nxt):
            W = A["w_in_2"][0]
            memd = Fut()
            rdy, hdone, normed = nxt
            yield from mem_kv(normed, memd)
            zone = yield zone
            z = yield from gather(hdone + [memd])
            SGH, SGL = at_("SGH", 0, [128, 4, 512], F32R), at_("SGL", 8, [128, 4, 512], F32R)
            OAH, OAL = at_("OAH", 16, [128, 4, 512], F32R), at_("OAL", 24, [128, 4, 512], F32R)
            K2, V2 = at_("K2", 32, [128, 2, 512], F32R), at_("V2", 36, [128, 4, 128])
            UT, SV = at_("UT", 38, [128, 4, 512]), at_("SV", 46, [128, 4, 512])
            GS_, BS_ = at_("SGg", 54, [128, 512]), at_("SGb", 56, [128, 512])
            WS, WST = at_("WS", 58, [128, 4, 128]), at_("WST", 60, [128, 4, 128])
            BSG = at_("BSG", 62, [128, 512])
            R = Pool([at_(f"BR{i}", 64 + 2 * i, [128, 512]) for i in range(2)])
            wst = Fut()
            sgl = Fut()

            def ld_sgu():
                t = yield from load(WS[:, :, :], A["w_s_2"][0].rearrange("g p q -> p g q"), 262144, *z)
                bank, free = yield TP
                for j in range(4):
                    t = yield tr(bank[:, j * 128:j * 128 + 128], WS[:, j, :], t, *free, inc=j == 3) if j == 0 else \
                        tr(bank[:, j * 128:j * 128 + 128], WS[:, j, :], inc=j == 3)
                t = yield cp(WST[:, :, :], bank[:, :].rearrange("p (a c) -> p a c", a=4), 512, t, *z)
                TP.put(bank, t)
                wst.set((t,))
                a = yield from load(GS_[:, :], A["sgu_ln_g_2"].broadcast_to([128, 512]), 262144, *z)
                b = yield from load(BS_[:, :], A["sgu_ln_b_2"].broadcast_to([128, 512]), 262144, *z)
                c = yield from load(BSG[:, :], A["b_s_2"].rearrange("o g p -> o (g p)").broadcast_to([128, 512]), 262144,
                                    *z)
                sgl.set((a, b, c))

            ut = [Fut() for _ in range(4)]
            sv = [Fut() for _ in range(4)]
            sg = Ready()

            def ev_su(n, bank, tok):
                t = yield act(UT[:, n, :], bank[:, :], AF.Gelu_apprx_tanh, 512, tok, *z)
                G.put(bank, t)
                ut[n].set((t,))

            def ev_sv(nh, T, bank, tok):
                x = SV[:, T, :]
                t = yield act(x, bank[:, :], AF.Gelu_apprx_tanh, 512, tok, *z)
                G.put(bank, t)
                g["gelu", T] = t
                v, vf = yield SP
                t = yield vop(lambda e: e.bn_stats(v[:, 0:6], x), 512, t, *vf)
                t = yield vop(lambda e: e.bn_aggr(v[:, 12:14], v[:, 0:6]), 12, t)
                t = yield gop(lambda e: e.tensor_scalar(v[:, 14:15], v[:, 13:14], 1e-6, None, ALU.add), 1, t)
                t = yield gop(lambda e: e.tensor_tensor(v[:, 15:16], v[:, 14:15], half[:, 0:1], ALU.pow), 1, t, g["half"])
                w = yield sgl
                u = yield stt(x, x, v[:, 12:13], GS_[:, :], ALU.subtract, ALU.mult, 512, t, *w)
                u = yield stt(x, x, v[:, 15:16], BS_[:, :], ALU.mult, ALU.add, 512, u)
                SP.put(v, u)
                sv[T].set((u,))

            def sgu():
                tv = yield AllOf(sv)
                tw = yield wst
                for n in range(4):
                    bank, free = yield S
                    for T in range(4):
                        t = yield mm(bank[:, T * 128:T * 128 + 128], SV[:, T, n * 128:n * 128 + 128], WST[:, n, :], True,
                                     True, 219, *tv, *tw, *free, inc=T == 3)
                    spawn(sgu_ev(n, bank, t), 4, "sgu_ev")

            sgd = []
            sgf = Fut()

            def sgu_ev(n, bank, t):
                r, rf = yield R
                (tu,) = yield ut[n]
                r3 = r[:, :].rearrange("p (a c) -> p a c", a=4)
                t = yield tt(r3, bank[:, :].rearrange("p (a c) -> p a c", a=4),
                             BSG[:, n * 128:n * 128 + 128].unsqueeze(1).broadcast_to([128, 4, 128]), ALU.add, 512, t, *rf,
                             *z)
                S.put(bank, t)
                t = yield tt(r[:, :], r[:, :], UT[:, n, :], ALU.mult, 512, t, tu)
                th = yield act(SGH[:, n, :], r[:, :], AF.Copy, 512, t, *z)
                tl = yield tt(SGL[:, n, :], r[:, :], SGH[:, n, :].bitcast(F32), ALU.subtract, 512, th, *z)
                R.put(r, th, tl)
                for T in range(4):
                    sg.f[(n, T)].set((th, tl))
                sgd.append(tl)
                if len(sgd) == 4:
                    sgf.set(tuple(sgd) + (t,))

            spawn(ld_sgu(), 5, "ld_sgu")
            spawn(sgu(), 6, "sgu")
            yield from gemmA(W, 768, 1280, 8, xh, xl, rdy, ev_su)
            yield from gemmB(lambda nh, k: wB(W, k, 1280), 1, 8, xh, xl, rdy, ev_sv)

            AXT = ax_tables(z, g)
            z2 = z
            NDK = at_("NDK", 68, [128, 256])
            NDKP = Pool([NDK])
            NDQ = Pool([at_("NDQ0", 20, [128, 1024]), at_("NDQ1", 28, [128, 1024])])
            JP = Pool([at_("JP", 24, [128, 1024])])
            qd = {T: Fut() for T in range(4)}
            kd = [Fut() for _ in range(4)]
            vd2 = [Fut() for _ in range(4)]

            def head_rot(bank, b0, nh_, T, which, outap, ofree, tok):
                n = nh_ * 64
                x3 = bank[:, b0:b0 + n].rearrange("p (h c) -> p h c", h=nh_)
                r, rf = yield R
                q3 = r[:, 0:n].rearrange("p (h c) -> p h c", h=nh_)
                t = yield act(r[:, 0:n], bank[:, b0:b0 + n], AF.Square, n, tok, *rf, *z)
                v, vf = yield SP
                t = yield vop(lambda e: e.tensor_reduce(v[:, 0:nh_], q3, AX.X, ALU.add), n, t, *vf)
                t = yield gop(lambda e: e.tensor_scalar(v[:, 0:nh_], v[:, 0:nh_], 1.0 / 64, 1e-6, ALU.mult, ALU.add), 8,
                              t)
                t = yield gop(lambda e: e.tensor_tensor(v[:, 8:8 + nh_], v[:, 0:nh_], half8[:, 0:nh_], ALU.pow), 8, t,
                              g["half"])
                t = yield tt(q3, x3, v[:, 8:8 + nh_].unsqueeze(2).broadcast_to([128, nh_, 64]), ALU.mult, n, t)
                tb = t
                SP.put(v, t)
                j, jf = yield JP
                jf += z
                P_ = AXT[:, which, T, 0:64].unsqueeze(1).broadcast_to([128, nh_, 64])
                Q_ = AXT[:, which, T, 64:128].rearrange("p (c s) -> p c s", s=2).unsqueeze(1).broadcast_to(
                    [128, nh_, 32, 2])
                m1 = j[:, 0:n].rearrange("p (h c) -> p h c", h=nh_)
                m2 = j[:, 512:512 + n].rearrange("p (h c s) -> p h c s", h=nh_, s=2)
                q4 = r[:, 0:n].rearrange("p (h c s) -> p h c s", h=nh_, s=2)
                t1 = yield tt(m1, q3, P_, ALU.mult, n, t, *jf, *g["axt"])
                t2 = yield tt(m2[:, :, :, 0], q4[:, :, :, 1], Q_[:, :, :, 0], ALU.mult, n // 2, t, *jf)
                t3 = yield tt(m2[:, :, :, 1], q4[:, :, :, 0], Q_[:, :, :, 1], ALU.mult, n // 2, t)
                R.put(r, t3)
                t = yield tt(outap, m1.unsqueeze(2).broadcast_to([128, nh_, 2, 64]),
                             j[:, 512:512 + n].rearrange("p (h c) -> p h c", h=nh_).unsqueeze(2).broadcast_to(
                                 [128, nh_, 2, 64]), ALU.add, 2 * n, t1, t2, t3, *ofree)
                JP.put(j, t)
                return tb, t

            def ev_q(nh, T, bank, tok):
                nd, nf = yield NDQ
                tb, t = yield from head_rot(bank, 0, 8, T, 0, nd[:, :].rearrange("p (h d c) -> p h d c", h=8, d=2), nf + z,
                                            tok)
                G.put(bank, tb)
                t = yield from load(QQD[T], nd[:, :], 524288, t)
                NDQ.put(nd, t)
                qd[T].set((t,))


            def ev_kv(nh, T, bank, tok):
                nd, nf = yield NDKP
                t = yield act(V2[:, T, :], bank[:, 128:256], AF.Copy, 128, tok, *z)
                vd2[T].set((t,))
                tb, t = yield from head_rot(bank, 0, 2, T, 1, nd[:, :].rearrange("p (h d c) -> p h d c", h=2, d=2),
                                            nf + z, t)
                G.put(bank, tb)
                bk, bf = yield TP
                for j in range(2):
                    u = yield tr(bk[:, j * 128:j * 128 + 128], nd[:, j * 128:j * 128 + 128], t, *bf, inc=j == 1)
                NDKP.put(nd, u)
                c = slice(T * 128, T * 128 + 128)
                b3 = bk[:, 0:256].rearrange("p (a c) -> p a c", a=2)
                th = yield act(K2[:, 0:2, c], b3, AF.Copy, 256, u, *z)
                k = K2[64:128, 0:2, c]
                tl = yield tt(k, b3[64:128, :, :], k.bitcast(F32), ALU.subtract, 256, th)
                TP.put(bk, tl)
                kd[T].set((th, tl))

            yield from gemmB(lambda nh, k: (wA(W, k, 512)), 1, 8, xh, xl, rdy, ev_kv, N=256)
            yield from gemmB(lambda nh, k: wB(W, k, 0), 1, 8, xh, xl, rdy, ev_q)

            QST = Pool([at_(f"QST{i}", 38 + 8 * i, [128, 4, 512], F32R) for i in range(2)])
            EP = Pool([at_(f"QE{i}", 54 + 2 * i, [128, 512]) for i in range(4)])
            PT = Pool([at_(f"QP{i}", 62 + 2 * i, [128, 512]) for i in range(2)])
            NQ = Pool([at_(f"NQ{i}", 66 + i, [128, 256]) for i in range(2)])
            soft, left = {}, {}

            def q_stacks(P, st, free, done):
                for T in range(4):
                    (d,) = yield qd[T]
                    nd, nf = yield NQ
                    t = yield from load(nd[:, :], QQD[T][:, P * 256:P * 256 + 256], 131072, d, *nf, *free)
                    bank, bf = yield TP
                    for j in range(2):
                        u = yield tr(bank[:, j * 128:j * 128 + 128], nd[:, j * 128:j * 128 + 128], t, *bf, inc=j == 1)
                    NQ.put(nd, u)
                    c = slice(T * 128, T * 128 + 128)
                    b3 = bank[:, 0:256].rearrange("p (a c) -> p a c", a=2)
                    th = yield act(st[:, 0:2, c], b3, AF.Copy, 256, u, *free)
                    tl = yield tt(st[:, 2:4, c], b3, st[:, 0:2, c].bitcast(F32), ALU.subtract, 256, th, *free)
                    TP.put(bank, tl)
                    done[T].set((th, tl))

            def sc():
                w = yield sgf
                w += yield AllOf(list(qd.values()))
                m = yield vop(lambda e: e.memset(MASK[:, :], 0.0), 512, *zone)
                kk = yield AllOf(kd)
                for P in range(4):
                    st, free = yield QST
                    rdy_ = [Fut() for _ in range(4)]
                    spawn(q_stacks(P, st, free + w, rdy_), 4, f"qst{P}")
                    left[P] = []
                    for i in range(4):
                        for hh in range(2):
                            e, ef = yield EP
                            soft[(P, i, hh)] = Fut()
                            spawn(unit(P, i, hh, st, e, ef + w + (m,), rdy_, kk), 5, "unit")

            def unit(P, i, hh, st, e, ef, rdy_, kk):
                w = yield rdy_[i]
                s, sf = yield S
                q = slice(i * 128, i * 128 + 128)
                yield mm(s[:, :], st[:, hh, q], K2[:, P // 2, :], True, False, 216, *w, *sf, *kk)
                t = yield mm(s[:, :], st[:, 2 + hh, q], K2[:, P // 2, :], False, True, 216)
                left[P].append(t)
                if len(left[P]) == 8:
                    QST.put(st, *left[P])
                v, t, r = yield from soft_row(s, 512, MASK, 0.125, e, t, ef)
                t = yield ts(e[:, :], e[:, :], v[:, 2:3], None, ALU.mult, None, 512, t, r)
                SP.put(v, t)
                soft[(P, i, hh)].set((e, t))

            oa = Ready()

            def outs():
                w = yield sgf
                w += yield AllOf(list(qd.values()))
                vv = yield AllOf(vd2)
                for P in range(4):
                    o, of = yield OP
                    for i in range(4):
                        pts = []
                        for hh in range(2):
                            yield lambda: (P, i, hh) in soft
                            e, t = yield soft[(P, i, hh)]
                            pt, pf = yield PT
                            t, u = yield from turn_P(e, 512, pt, pf + w, t)
                            EP.put(e, t)
                            pts.append((pt, u))
                        for j in range(4):
                            for hh in range(2):
                                pt, u = pts[hh]
                                c = (P // 2) * 64
                                t = yield mm(o[64 * hh:64 * hh + 64, i * 128:i * 128 + 128], V2[:, j, c:c + 64],
                                             pt[:, j * 128:j * 128 + 128], j == 0, j == 3, 135, u, *vv, *of, inc=j == 3)
                        for pt, _ in pts:
                            PT.put(pt, t)
                    spawn(split_out(P, o, t, OAH[:, P, :], OAL[:, P, :], oa, w), 3, "oa")

            spawn(sc(), 5, "scores2")
            spawn(outs(), 4, "outs2")

            tg = {(a, n): Fut() for a in range(2) for n in range(8)}

            def ev_g(a):
                def ev(n, bank, tok):
                    s_, f = yield STG
                    t = yield act(s_[:, 0:512], bank[:, :], AF.Tanh, 512, tok, *f, scale=0.5)
                    G.put(bank, t)
                    t = yield from load(TGD[a, n], s_[:, 0:512], 262144, t)
                    STG.put(s_, t)
                    tg[(a, n)].set((t,))
                return ev

            yield from gemmA(W, 1792, 2816, 8, xh, xl, rdy, ev_g(0))
            yield from gemmA(W, 2816, 3840, 8, xh, xl, rdy, ev_g(1))
            in_done = g["last"]

            TG = Pool([at_(f"TG{i}", 54 + 2 * i, [128, 512]) for i in range(4)])
            MP = Pool([at_(f"MP{i}", 38 + 2 * i, [128, 512]) for i in range(4)])
            z3 = yield from gather([oa.f[(k, 0)] for k in range(4)])
            z3 += (g["oa_last"],)
            part = {}
            mr = Ready()
            tgr = {}

            def ld_tg():
                for q in range(4):
                    for a in range(2):
                        for n in (2 * q, 2 * q + 1):
                            (d,) = yield tg[(a, n)]
                            b, f = yield TG
                            t = yield from load(b[:, :], TGD[a, n], 262144, d, *f, *z3)
                            tgr[(a, n)] = (b, t)

            def ev_y(a, n0):
                def ev(n_, bank, tok):
                    n = n0 + n_
                    yield lambda: (a, n) in tgr
                    b, tb = tgr[(a, n)]
                    if a == 0:
                        m, mf = yield MP
                        t = yield stt(m[:, :], b[:, :], 1.0, bank[:, :], ALU.add, ALU.mult, 512, tok, tb, *mf, *z3)
                        G.put(bank, t)
                        TG.put(b, t)
                        part[n] = (m, t)
                        return
                    yield lambda: n in part
                    m, tm = part[n]
                    t = yield stt(b[:, :], b[:, :], 1.0, bank[:, :], ALU.add, ALU.mult, 512, tok, tb)
                    G.put(bank, t)
                    t = yield tt(m[:, :], m[:, :], b[:, :], ALU.add, 512, t, tm)
                    TG.put(b, t)
                    th = yield act(XH[:, n, :], m[:, :], AF.Copy, 512, t, in_done)
                    tl = yield tt(XL[:, n, :], m[:, :], XH[:, n, :].bitcast(F32), ALU.subtract, 512, th, in_done)
                    MP.put(m, th, tl)
                    for T in range(4):
                        mr.f[(n, T)].set((th, tl))
                return ev

            spawn(ld_tg(), 1, "ld_tg")
            for q in range(4):
                yield from gemmA(A["w_att_out_2"][0], 256 * q, 256 * q + 256, 4, rows(OAH), rows(OAL), oa, ev_y(0, 2 * q))
                yield from gemmA(A["w_sgu_out_2"][0], 256 * q, 256 * q + 256, 4, rows(SGH), rows(SGL), sg, ev_y(1, 2 * q))
            ylast = g["last"]
            x1, x2, x3 = xfuts(), xfuts(), xfuts()
            z4 = z3 + (ylast,)
            rdyc, cdone = rms_all(x1, "g_cross_2", 56, 60, z4 + ((yield from gather([mr.f[(7, 0)]]))))
            yield from gemmB(lambda nh, k: wB(A["w_out_2"][0], k, nh * 512), 2, 8, xh, xl, mr,
                             add_x(None, x_in, x1, mul=0.5))

            CQH, CQL = at_("CQH", 0, [128, 4, 512], F32R), at_("CQL", 8, [128, 4, 512], F32R)
            COH, COL = at_("COH", 16, [128, 4, 512], F32R), at_("COL", 24, [128, 4, 512], F32R)
            KTr = at_("KTr", 32, [128, 4, 256])
            KTH, KTL = at_("KTH", 36, [128, 4, 256], F32R), at_("KTL", 40, [128, 4, 256], F32R)
            MV = at_("MV", 44, [128, 2, 512])
            CE = Pool([at_(f"CE{i}", 48 + i, [128, 256]) for i in range(4)])
            CP = Pool([at_(f"CP{i}", 52 + i, [128, 256]) for i in range(4)])
            kv = Fut()

            def ld_kv():
                t = yield from load(KTr[:, :, :], KTD.rearrange("h p m -> p h m"), 524288, *z4, *memd.v)
                u = yield from load(MV[:, :, :], MVD.rearrange("a p c -> p a c"), 524288, *z4, *memd.v)
                th = yield act(KTH[:, :, :], KTr[:, :, :], AF.Copy, 1024, t, *z4)
                tl = yield tt(KTL[:, :, :], KTr[:, :, :], KTH[:, :, :].bitcast(F32), ALU.subtract, 1024, t, th, *z4)
                kv.set((th, tl, u))

            spawn(ld_kv(), 3, "ld_kv")
            qr = [Fut() for _ in range(4)]

            def ev_cq(n, bank, tok):
                th = yield act(CQH[:, n, :], bank[:, :], AF.Copy, 512, tok, *z4)
                tl = yield tt(CQL[:, n, :], bank[:, :], CQH[:, n, :].bitcast(F32), ALU.subtract, 512, th, *z4)
                G.put(bank, tl)
                qr[n].set((th, tl))

            csoft = {}

            def csc():
                for h in range(4):
                    for i in range(4):
                        e, ef = yield CE
                        csoft[(h, i)] = Fut()
                        spawn(cunit(h, i, e, ef + z4), 5, "cunit")

            def cunit(h, i, e, ef):
                w = yield qr[h]
                w += yield kv
                s, sf = yield S
                q = slice(i * 128, i * 128 + 128)
                yield mm(s[:, 0:256], CQH[:, h, q], KTH[:, h, :], True, False, 110, *w, *sf)
                yield mm(s[:, 0:256], CQH[:, h, q], KTL[:, h, :], False, False, 110)
                t = yield mm(s[:, 0:256], CQL[:, h, q], KTH[:, h, :], False, True, 110)
                v, t, r = yield from soft_row(s, 256, MASK, float(np.float32(128.0 ** -0.5)), e, t, ef)
                t = yield ts(e[:, :], e[:, :], v[:, 2:3], None, ALU.mult, None, 256, t, r)
                SP.put(v, t)
                csoft[(h, i)].set((e, t))

            co = Ready()

            def couts():
                w = yield kv
                for h in range(4):
                    o, of = yield OP
                    for i in range(4):
                        yield lambda: (h, i) in csoft
                        e, t = yield csoft[(h, i)]
                        pt, pf = yield CP
                        t, u = yield from turn_P(e, 256, pt, pf + z4, t)
                        CE.put(e, t)
                        for j in range(2):
                            t = yield mm(o[:, i * 128:i * 128 + 128], MV[:, j, h * 128:h * 128 + 128],
                                         pt[:, j * 128:j * 128 + 128], j == 0, j == 1, 219, u, *w, *of)
                        CP.put(pt, t)
                    spawn(split_out(h, o, t, COH[:, h, :], COL[:, h, :], co, z4), 3, "co")

            spawn(csc(), 5, "csc")
            spawn(couts(), 4, "couts")
            g["rp"] = Fut()

            def rp():
                th, tl, u = yield kv
                yield from route_prep((th, tl, *z4))

            spawn(rp(), 6, "route_prep")
            yield from gemmA(A["w_cq_2"][0], 0, 512, 8, xh, xl, rdyc, ev_cq, early=2)
            WC = A["w_co_2"][0]
            yield lambda: len(csoft) == 16
            z_r = z4 + (yield from gather(cdone)) + tuple(t for _, t in (yield from pairs(csoft)))
            z5f = Fut()
            for n in ("idx", "logits", "ovf", "roww", "sum0"):
                g[n] = Fut()
            g["x_read"] = [Fut() for _ in range(4)]
            spawn(route(x3, z_r, z5f, g["idx"], g["logits"]), 2, "route")

            def early_raw():
                for i in range(9, 13):
                    raw.put(i, *z_r)
                w = yield AllOf([co.f[(k, 0)] for k in range(4)])
                for i in range(3, 6):
                    raw.put(i, *w)

            spawn(early_raw(), 2, "early_raw")
            yield from gemmB(lambda nh, k: wB(WC, k, nh * 512), 2, 2, rows(COH), rows(COL), co, add_x(1.0, x1, x2))
            yield from gemmB(lambda nh, k: wB(WC, 2 + k, nh * 512), 2, 2, rows(COH, 2), rows(COL, 2),
                             lambda k, T: co(k + 2, T), add_x(1.0, x2, x3), rows_first=True)
            z5 = (yield from gather(x3.values())) + (g["last"],)
            z5f.set(z5)
            return x3, z5

        def route_prep(w):
            RT_, WRS, BI = at_("ROUTE", 32, [128, 608]), at_("WRS", 34.375, [128, 8, 40], F32R), at_("BI", 35.625, [128, 28])
            t0 = yield from load(RT_[:, :], A["route"], 311296, *w)
            stage, sf = yield STG
            WR = stage[:, 0:160].rearrange("p (k c) -> p k c", k=8)
            GR = stage[0:8, 160:288]
            t1 = yield from load(WR[:, :, 0:4], A["w_rg_2"][0].rearrange("(k p) c -> p k c", p=128), 16384, *sf)
            t2 = yield from load(WR[:, :, 4:20], A["w_re_2"][0].rearrange("(k p) c -> p k c", p=128), 65536, *sf)
            t5 = yield from load(GR, A["g_moe_2"].rearrange("o (k p) -> (o k) p", p=128), 4096, *sf)
            t3 = yield from load(BI[:, 0:4], A["b_rg_2"].broadcast_to([128, 4]), 2048, *w)
            t4 = yield from load(BI[:, 4:20], A["b_re_2"].broadcast_to([128, 16]), 8192, *w)
            bank, free = yield TP
            t = yield mm(bank[:, 0:8], GR, ident[0:8, 0:8], True, True, 30, t5, *free)
            t = yield cp(BI[:, 20:28], bank[:, 0:8], 8, t, *w)
            TP.put(bank, t)
            t = yield tt(WR, WR, BI[:, 20:28].unsqueeze(2).broadcast_to([128, 8, 20]), ALU.mult, 160, t, t1, t2)
            th = yield act(WRS[:, :, 0:20], WR, AF.Copy, 160, t, *w)
            tl = yield tt(WRS[:, :, 20:40], WR, WRS[:, :, 0:20].bitcast(F32), ALU.subtract, 160, th)
            STG.put(stage, th, tl)
            tr_ = yield cp(TRO[:, :], RT_[:, 280:536], 256, t0, *w)
            g["rp"].set((t0, (t3, t4), th, tl, tr_))

        def route(x_in, zone, later, idx, logits):
            RT_, WRS, BI = at_("ROUTE", 32, [128, 608]), at_("WRS", 34.375, [128, 8, 40], F32R), at_("BI", 35.625, [128, 28])
            R8 = at_("R8", 28, [128, 8, 128], F32R)
            RF = at_("RF", 36, [128, 576], F32R)
            WK = at_("WK", 38.25, [128, 1472])
            pos = [0]

            def wk(n, dt=None):
                a = WK[:, pos[0]:pos[0] + n]
                pos[0] += n
                return a if dt is None else a.bitcast(dt)

            hd = []
            rdy = Ready()
            HT = Pool([at_(f"RT{i}", 60 + 4 * i, [128, 1024]) for i in range(2)])
            GM = at_("RG", 56, [128, 1024])
            gf = Fut()
            done = [Fut() for _ in range(4)]
            g["moe_rms"] = done
            RS_, rsf = wk(4), [Fut() for _ in range(4)]

            def ld():
                t = yield from load(GM[:, :], A["g_moe_2"].broadcast_to([128, 1024]), 524288, *zone)
                gf.set((t,))

            def turn(T, h):
                w = yield x_in[(T, h)]
                yield from turn_T(X[:, T, :], T, XH, XL, rdy, 4 * h, 4, *w)

            JK = WK[:, 960:1472]

            js = [Fut() for _ in range(5)]
            js[0].set(zone)

            def norm(T):
                j = yield js[T]
                v, vf = yield SP
                w = []
                for h in range(2):
                    n_ = yield x_in[(T, h)]
                    t = yield act(JK, X[:, T, h * 512:h * 512 + 512], AF.Square, 512, *n_, *vf, *j, acc=v[:, h:h + 1])
                    j = (t,)
                    w.append(t)
                js[T + 1].set(j)
                t = yield gop(lambda e: e.tensor_tensor(v[:, 2:3], v[:, 0:1], v[:, 1:2], ALU.add), 1, *w)
                t = yield gop(lambda e: e.tensor_scalar(v[:, 3:4], v[:, 2:3], 1.0 / 1024, 1e-6, ALU.mult, ALU.add), 1, t)
                t = yield gop(lambda e: e.tensor_tensor(RS_[:, T:T + 1], v[:, 3:4], half[:, 0:1], ALU.pow), 1, t,
                              g["half"])
                SP.put(v, t)
                rsf[T].set((t,))

            def rows_out():
                gt = yield gf
                for T in range(4):
                    tmp, tf = yield HT
                    w = yield rsf[T]
                    for h in range(2):
                        c = slice(h * 512, h * 512 + 512)
                        n_ = yield x_in[(T, h)]
                        t = yield stt(tmp[:, c], X[:, T, c], RS_[:, T:T + 1], GM[:, c], ALU.mult, ALU.mult, 512, *w, *tf,
                                      *gt, *n_, *zone)
                    t = yield from load(HD[T * 128:T * 128 + 128, :], tmp[:, :], 524288, t)
                    HT.put(tmp, t)
                    hd.append(t)
                    done[T].set((t,))

            def keep():
                ts_ = list(g["spare"])
                for T in range(4):
                    w = (yield x_in[(T, 0)]) + (yield x_in[(T, 1)])
                    ts_.append((yield from load(SUM[T * 128:T * 128 + 128, :], X[:, T, :], 524288, *w)))
                g["sum0"].set(tuple(ts_))

            spawn(ld(), 1, "ld_g")
            spawn(keep(), 14, "keep")
            for T in range(4):
                for h in range(2):
                    spawn(turn(T, h), -10, "turn_m")
            for T in range(4):
                spawn(norm(T), 3, "norm")
            spawn(rows_out(), 12, "rows_out")
            t0, t3, th, tl, tro = yield g["rp"]
            iota, tokid, reset8, ones16 = RT_[:, 0:128], RT_[:, 128:136], RT_[:, 136:264], RT_[:, 264:280]
            tri, ones, first4, lim = TRO[:, 0:128], TRO[:, 128:256], RT_[:, 536:540], RT_[:, 540:543]
            iota16, iota8 = iota[:, 0:16], iota[:, 0:8]
            rev, down, after2, two = (RT_[:, 544 + 16 * i:560 + 16 * i] for i in range(4))
            GE, OE = wk(17), wk(17)
            tz = yield vop(lambda e: e.memset(GE[:, 0:1], 0.0), 1, *zone)
            tz = yield vop(lambda e: e.memset(OE[:, 0:1], 0.0), 1)
            o, of = yield OP
            for T in range(4):
                for k in range(8):
                    w = yield rdy(k, T)
                    a = (o[:, T * 40:T * 40 + 40], XH[:, k, T * 128:T * 128 + 128], WRS[:, k, :])
                    b = (o[:, T * 40:T * 40 + 20], XL[:, k, T * 128:T * 128 + 128], WRS[:, k, 0:20])
                    p, q = (a, b) if k == 0 else (b, a)
                    yield mm(*p, k == 0, False, 107, *w, *of, th, tl)
                    t = yield mm(*q, False, k == 7, 107, inc=k == 7)
            logits.set((t,))
            rest, wf = yield S

            def busy(n):
                for _ in range(n):
                    t = yield mm(rest[:, 0:256], tri, TRO[:, :], True, True, 110, *wf, tro)
                return t

            yield from busy(28)
            LG = wk(80).rearrange("p (t c) -> p t c", t=4)
            o3 = o[:, 0:160].rearrange("p (t c) -> p t c", t=4)
            t = yield cp(LG, o3[:, :, 0:20], 80, t, *zone)
            t = yield tt(LG, LG, o3[:, :, 20:40], ALU.add, 80, t)
            OP.put(o, t)
            tr_ = yield AllOf(rsf)
            t = yield tt(LG, LG, RS_.unsqueeze(2).broadcast_to([128, 4, 20]), ALU.mult, 80, t, *tr_)
            t = yield tt(LG, LG, BI[:, 0:20].unsqueeze(1).broadcast_to([128, 4, 20]), ALU.add, 80, t, *t3)
            gm, gs, gv, g2 = wk(4), wk(4), wk(4), wk(4)
            oh = wk(16).rearrange("p (t c) -> p t c", t=4)
            lg = LG[:, :, 0:4]
            t = yield vop(lambda e: e.tensor_reduce(gm, lg, AX.X, ALU.max), 16, t)
            tgm = t
            t = yield tt(oh, lg, gm.unsqueeze(2).broadcast_to([128, 4, 4]), ALU.is_ge, 16, t)
            t = yield tt(oh, oh, first4.unsqueeze(1).broadcast_to([128, 4, 4]), ALU.mult, 16, t, t0)
            t = yield vop(lambda e: e.tensor_reduce(g2, oh, AX.X, ALU.max), 16, t)
            t = yield tt(oh, oh, g2.unsqueeze(2).broadcast_to([128, 4, 4]), ALU.is_lt, 16, t)
            t = yield ts(oh, oh, -BIG, None, ALU.mult, None, 16, t)
            EM = wk(64)
            em4 = EM.rearrange("p (t a c) -> p t a c", t=4, a=4)
            t = yield tt(em4, LG[:, :, 4:20].rearrange("p t (a c) -> p t a c", a=4),
                         oh.unsqueeze(3).broadcast_to([128, 4, 4, 4]), ALU.add, 64, t)
            tem = t
            w8, j8 = wk(32), wk(32, U32)
            for T in range(4):
                c, d = slice(8 * T, 8 * T + 8), slice(16 * T, 16 * T + 16)
                ta = yield vop(lambda e, c=c, d=d: e.max(w8[:, c], EM[:, d]), 16, tem)
                tb = yield vop(lambda e, c=c, d=d: e.max_index(j8[:, c], w8[:, c], EM[:, d]), 16, ta)
            ID = wk(8)
            tid_ = yield cp(ID.rearrange("p (t k) -> p t k", t=4), j8.rearrange("p (t c) -> p t c", t=4)[:, :, 0:2], 8, tb)
            O = RF[:, 0:128]
            Of = O.bitcast(F32)
            o_eb = O.rearrange("p (e b) -> p e b", e=16)
            to = yield tt(o_eb, rev.unsqueeze(2).broadcast_to([128, 16, 8]), ID.unsqueeze(1).broadcast_to([128, 16, 8]),
                          ALU.is_equal, 128, tid_)
            INC, EXC = RF[:, 128:256], RF[:, 256:384]
            ti = yield vop(lambda e: e.tensor_tensor_scan(INC, reset8, Of, 0.0, ALU.mult, ALU.add), 128, to)
            te = yield tt(EXC, INC.bitcast(F32), Of, ALU.subtract, 128, ti)
            bank, bf = yield OP
            cnt, cf = yield S
            n_e = cnt[:, 0:16]
            tb_ = yield mm(n_e, ones, INC.rearrange("p (e b) -> p e b", e=16)[:, :, 7], True, True, 60, ti, tro, *cf)
            yield mm(bank[:, 0:128], tri, O, True, False, 219, to, *bf, inc=False)
            t = yield mm(bank[:, 0:128], ones, EXC, False, True, 219, te)
            yield from busy(56)
            w83 = w8.rearrange("p (t c) -> p t c", t=4)
            e2, r2, ge = wk(4), wk(4), wk(16)
            ge3 = ge.rearrange("p (t c) -> p t c", t=4)
            u = yield tt(e2, w83[:, :, 1], w83[:, :, 0], ALU.subtract, 4, tb)
            ue = yield act(e2, e2, AF.Exp, 4, u)
            u = yield tt(ge3, lg, gm.unsqueeze(2).broadcast_to([128, 4, 4]), ALU.subtract, 16, tgm)
            tge = yield act(ge3, ge3, AF.Exp, 16, u)
            big, chs, wa, wb = wk(16), wk(16), wk(16), wk(16)
            LK = wk(32).rearrange("p (f e) -> p f e", f=2)
            place, step = LK[:, 0, :], LK[:, 1, :]
            c = yield stt(big, n_e, 128.0, after2, ALU.is_gt, ALU.mult, 16, tb_)
            c = yield vop(lambda e: e.tensor_tensor_scan(GE[:, 1:17], big, two, 0.0, ALU.add, ALU.min), 16, c, tz)
            c = yield tt(chs, GE[:, 1:17], GE[:, 0:16], ALU.subtract, 16, c)
            c = yield stt(wa, GE[:, 0:16], 2.0, down, ALU.mult, ALU.add, 16)
            c = yield tt(wb, iota16, GE[:, 0:16], ALU.subtract, 16)
            c = yield stt(wa, wa, GE[:, 16:17], chs, ALU.subtract, ALU.mult, 16, c)
            tpl = yield tt(place, wa, wb, ALU.add, 16, c)
            no3, nov = wk(48).rearrange("p (e j) -> p e j", e=16), wk(16)
            c = yield tt(no3, n_e.unsqueeze(2).broadcast_to([128, 16, 3]), lim.unsqueeze(1).broadcast_to([128, 16, 3]),
                         ALU.is_gt, 48)
            S.put(cnt, c)
            c = yield vop(lambda e: e.tensor_reduce(nov, no3, AX.X, ALU.add), 48, c)
            c = yield tt(nov, nov, chs, ALU.subtract, 16, c)
            til = yield vop(lambda e: e.tensor_tensor_scan(OE[:, 1:17], ones16, nov, 0.0, ALU.mult, ALU.add), 16, c)
            c = yield stt(step, OE[:, 0:16], 17.0, chs, ALU.add, ALU.subtract, 16, til)
            tstep = yield tt(step, step, place, ALU.subtract, 16, c)
            LT = wk(256)
            lt4 = LT.rearrange("p (f b e) -> p f b e", f=2, b=8)
            pl = wk(16).rearrange("p (f b) -> p f b", f=2)
            c = yield tt(lt4, Of.rearrange("p (e b) -> p b e", e=16).unsqueeze(1).broadcast_to([128, 2, 8, 16]),
                         LK.unsqueeze(2).broadcast_to([128, 2, 8, 16]), ALU.mult, 256, tstep)
            tlk = yield vop(lambda e: e.tensor_reduce(pl, lt4, AX.X, ALU.add), 256, c)
            RK, r = EXC.bitcast(F32), wk(8)
            tr_ = yield tt(EXC, bank[:, 0:128], Of, ALU.mult, 128, t)
            OP.put(bank, tr_)
            tr_ = yield vop(lambda e: e.tensor_reduce(r, RK.rearrange("p (e b) -> p b e", e=16), AX.X, ALU.add), 128, tr_)
            obb, q, c1 = wk(8), wk(8), wk(8)
            q3 = wk(24).rearrange("p (b j) -> p b j", b=8)
            a = yield tt(q3, r.unsqueeze(2).broadcast_to([128, 8, 3]), lim.unsqueeze(1).broadcast_to([128, 8, 3]),
                         ALU.is_ge, 24, tr_)
            a = yield vop(lambda e: e.tensor_reduce(q, q3, AX.X, ALU.add), 24, a)
            rm = wk(8)
            tq = yield stt(rm, q, -128.0, r, ALU.mult, ALU.add, 8, a)
            c = yield stt(c1, pl[:, 0, :], 13.5, q, ALU.is_ge, ALU.is_lt, 8, tlk)
            d = yield tt(pl[:, 1, :], pl[:, 1, :], q, ALU.subtract, 8)
            a = yield stt(obb, q, 2.0, pl[:, 0, :], ALU.mult, ALU.add, 8, c)
            d = yield tt(pl[:, 1, :], pl[:, 1, :], c1, ALU.mult, 8, d)
            t = yield tt(obb, obb, pl[:, 1, :], ALU.add, 8, d, a)
            ot3 = RF[:, 384:576].rearrange("p (b t) -> p b t", b=8)
            u = yield tt(ot3, iota[:, 0:24].unsqueeze(1).broadcast_to([128, 8, 24]),
                         obb.unsqueeze(2).broadcast_to([128, 8, 24]), ALU.is_equal, 192, t)
            u = yield tt(ot3, ot3.bitcast(F32), tokid.unsqueeze(2).broadcast_to([128, 8, 24]), ALU.mult, 192, u)
            z = yield later
            bank, bf = yield OP
            for h in range(2):
                c = slice(4 * h, 4 * h + 4)
                t8 = yield tt(R8[:, c, :], iota.unsqueeze(1).broadcast_to([128, 4, 128]),
                              rm[:, c].unsqueeze(2).broadcast_to([128, 4, 128]), ALU.is_equal, 512, tq, *z)
                for b in range(4 * h, 4 * h + 4):
                    ti_ = yield mm(bank[:, 0:24], R8[:, b, :], ot3[:, b, :], b == 0, b == 7, 60, u, t8, *bf)
            S.put(rest, (yield from busy(34)))
            ti_ = yield ts(IDX[:, :], bank[:, 0:24], 1000.0, None, ALU.add, None, 24, ti_, *zone)
            idx.set((ti_, *hd))
            pf_ = wk(24)
            tp_ = yield ts(pf_, bank[:, 0:24], 1000.0, None, ALU.add, None, 24, ti_)
            tf_ = []
            for T in range(4):
                tf_.append((yield ts(ROWT[:, :, T], pf_[:, 13:24], -128.0 * T, None, ALU.add, None, 11, tp_, *zone)))
            OP.put(bank, tp_)
            ti2 = yield cp(IOTA[:, :], iota, 128)
            tse = yield tt(SEL[:, :].rearrange("p (a c) -> p a c", a=4), iota.unsqueeze(1).broadcast_to([128, 4, 128]),
                           ROWT[:, 0, :].unsqueeze(2).broadcast_to([128, 4, 128]), ALU.is_equal, 512, *tf_, *zone)
            g["iota"], g["sel"] = (ti2, *tf_), (tse,)
            em, pt = wk(24), wk(24)
            a = yield stt(em, pf_, 1000.0, RT_[:, 543:544].broadcast_to([128, 24]), ALU.is_ge, ALU.mult, 24, tp_)
            tput = yield tt(PUT[:, :], em, pf_, ALU.add, 24, a, *zone)
            CW = wk(8)
            cw3 = CW.rearrange("p (t k) -> p t k", t=4)
            u = yield ts(r2, e2, 1.0, None, ALU.add, None, 4, ue)
            u = yield vop(lambda e: e.reciprocal(r2, r2), 24, u)
            a = yield vop(lambda e: e.tensor_reduce(gs, ge3, AX.X, ALU.add), 16, tge)
            a = yield vop(lambda e: e.reciprocal(gv, gs), 24, a)
            u = yield tt(cw3[:, :, 0], r2, gv, ALU.mult, 4, a, u, *zone)
            u = yield tt(cw3[:, :, 1], cw3[:, :, 0], e2, ALU.mult, 4, u)
            w3 = LT[:, 0:192].rearrange("p (b t) -> p b t", b=8)
            l3 = RF[:, 128:320].rearrange("p (b t) -> p b t", b=8)
            a = yield tt(w3, iota[:, 0:24].unsqueeze(1).broadcast_to([128, 8, 24]),
                         obb.unsqueeze(2).broadcast_to([128, 8, 24]), ALU.is_equal, 192, tlk)
            a = yield tt(w3, w3, CW.unsqueeze(2).broadcast_to([128, 8, 24]), ALU.mult, 192, a, u)
            u = yield act(ot3, w3, AF.Copy, 192, a, ti_)
            a = yield tt(l3, w3, ot3.bitcast(F32), ALU.subtract, 192, u)
            bank, bf = yield OP
            for b in range(8):
                yield mm(bank[:, 0:24], R8[:, b, :], ot3[:, b, :], b == 0, False, 60, a, *bf)
                t = yield mm(bank[:, 0:24], R8[:, b, :], l3[:, b, :], False, b == 7, 60)
            t = yield cp(ROWW[:, :], bank[:, 0:24], 24, t, *zone)
            OP.put(bank, t)
            g["roww"].set((t, tput))
            pe = LT.rearrange("p (j e) -> p j e", j=16)
            of_ = wk(24)
            t = yield tt(pe, place.unsqueeze(1).broadcast_to([128, 16, 16]), iota16.unsqueeze(2).broadcast_to([128, 16, 16]),
                         ALU.is_equal, 256, tpl, a)
            t = yield tt(pe, pe, rev.unsqueeze(1).broadcast_to([128, 16, 16]), ALU.mult, 256, t)
            t = yield vop(lambda e: e.tensor_reduce(of_[:, 8:24], pe, AX.X, ALU.add), 256, t)
            t = yield tt(pe[:, 0:8, :], OE[:, 1:17].unsqueeze(1).broadcast_to([128, 8, 16]),
                         iota8.unsqueeze(2).broadcast_to([128, 8, 16]), ALU.is_le, 128, til, t)
            t = yield vop(lambda e: e.tensor_reduce(of_[:, 1:8], pe[:, 0:7, :], AX.X, ALU.add), 128, t)
            t = yield ts(of_[:, 1:8], of_[:, 1:8], 15.0, None, ALU.min, None, 7, t)
            t = yield ts(of_[:, 1:8], of_[:, 1:8], -1.0, 15.0, ALU.mult, ALU.add, 7, t)
            t = yield cp(of_[:, 0:1], OE[:, 16:17], 1, t)
            t = yield cp(OVF[:, :], of_, 24, t, *zone)
            g["ovf"].set((t,))
            assert pos[0] <= 960

        class Tiles:

            def __init__(self):
                at = lambda name, off, shape, dt=F32: at_(name, off - D0, shape, dt)
                self.XG = Pool([at(f"XG{i}", 16 + 4 * i, [128, 1024]) for i in range(2)])
                self.EX = Pool([at(f"EX{i}", 24 + 8 * i, [128, 16, 128], F32R) for i in range(2)])
                self.SG = Pool([at(f"ES{i}", 40 + 2 * i, [128, 512]) for i in range(2)])
                self.EH = Pool([at("EH0", 44, [128, 8, 128], F32R), at_("EH1", 28, [128, 8, 128], F32R)])
                self.Y = Pool([(at_(f"EY{i}", o, [128, 1024]), at_(f"EZ{i}", o, [128, 1024], F32R))
                               for i, o in enumerate((36, 40, 24))])
                self.EX2 = Pool([])
                self.ex2 = at_("EX2", -D0, [128, 16, 128], F32R)
                self.got = {}

        def experts(board, strm, groups, ahead, src, R, idx, zone, IQ, TP, sums, acc):
            sp = board.spawn
            tiles = [i for gr in groups for i in gr]
            ex = {i: Fut() for i in tiles}
            eh = {i: Fut() for i in tiles}
            ss = {}

            def turn8(get, K, h, l, free, w):
                r = []
                for k0 in range(0, K, 4):
                    bank, bf = yield TP
                    for j in range(4):
                        t = yield tr(bank[:, j * 128:j * 128 + 128], get(k0 + j), *w, *bf, inc=j == 3)
                    b3 = bank[:, :].rearrange("p (a c) -> p a c", a=4)
                    th = yield act(h[:, k0:k0 + 4, :], b3, AF.Copy, 512, t, *free)
                    tl = yield tt(l[:, k0:k0 + 4, :], b3, h[:, k0:k0 + 4, :].bitcast(F32), ALU.subtract, 512, th, *free)
                    TP.put(bank, tl)
                    r += [th, tl]
                return t, tuple(r)

            def fetch(i):
                x, xf = yield R.XG
                w = yield idx
                sem, toks = yield IQ
                t = yield Op("G", 1000.0, lambda e: e.indirect_dma_start(
                    x[:, :], None, HD[:, :], bass.IndirectOffsetOnAxis(IDX[:, i:i + 1], axis=0), bounds_check=511,
                    oob_is_err=False), (*toks, *w, *xf, *zone), 1, sem, 262144)
                IQ.put(sem, t)
                R.got[i] = (x, t)

            def preps():
                for i in tiles:
                    yield lambda: i in R.got
                    x, t = R.got[i]
                    e, ef = yield (R.EX2 if i in (16, 17) else R.EX)
                    t, r = yield from turn8(lambda k: x[:, k * 128:k * 128 + 128], 8, e[:, 0:8, :], e[:, 8:16, :],
                                            ef + zone, (t,))
                    R.XG.put(x, t)
                    ex[i].set((e, r))

            def fetches():
                for i in ahead:
                    yield from fetch(i)

            def ev_gate(gr):
                def ev(nh, T, bank, tok):
                    i = gr[T]
                    s_, sf = yield R.SG
                    t = yield act(s_[:, :], bank[:, :], AF.Silu, 512, tok, *sf, *zone)
                    G.put(bank, t)
                    ss[i] = (s_, t)
                return ev

            def ev_up(gr):
                def ev(nh, T, bank, tok):
                    i = gr[T]
                    yield lambda: i in ss
                    s_, t = ss[i]
                    t = yield tt(s_[:, :], s_[:, :], bank[:, :], ALU.mult, 512, tok, t)
                    G.put(bank, t)
                    h, hf = yield R.EH
                    t, r = yield from turn8(lambda k: s_[:, k * 128:k * 128 + 128], 4, h[:, 0:4, :], h[:, 4:8, :],
                                            hf + zone, (t,))
                    R.SG.put(s_, t)
                    eh[i].set((h, r))
                return ev

            ys = {}

            def ev_split(i):
                def ev(nh, bank, tok):
                    w = yield g["roww"]
                    if nh == 0:
                        ys[i] = ((yield R.Y), (yield R.Y), [])
                    else:
                        yield lambda: i in ys
                    (yh, fh), (yl, fl), ts_ = ys[i]
                    c = slice(nh * 512, nh * 512 + 512)
                    h, l = yh[1][:, c], yl[1][:, c]
                    th = yield act(h, bank[:, :], AF.Copy, 512, tok, *fh, *fl, *w, *zone, scale=ROWW[:, i:i + 1])
                    tl = yield stt(l, bank[:, :], ROWW[:, i:i + 1], h.bitcast(F32), ALU.mult, ALU.subtract, 512, th, *fh, *fl,
                                   *zone)
                    G.put(bank, tl)
                    sp(spread(i, nh, yh, yl, (th, tl), ts_), 1, "spread")
                return ev

            def spread(i, h, yh, yl, w, ends):
                j = max(i - 17, 0)
                if j and h == 0:
                    t = yield tt(SEL[:, :].rearrange("p (a c) -> p a c", a=4), IOTA[:, :].unsqueeze(1).broadcast_to(
                        [128, 4, 128]), ROWT[:, i - 13, :].unsqueeze(2).broadcast_to([128, 4, 128]), ALU.is_equal, 512,
                        *g["iota"], *g["sel"])
                    g["sel"] = (t,)
                    g["for"] = j
                if j:
                    yield lambda: g["for"] == j
                sel = g["sel"]
                for T in range(4):
                    bank, free = yield S
                    c, d = slice(T * 128, T * 128 + 128), slice(h * 512, h * 512 + 512)
                    yield mm(bank[:, :], SEL[:, c], yh[1][:, d], True, False, 216, *w, *sel, *free)
                    t = yield mm(bank[:, :], SEL[:, c], yl[1][:, d], False, True, 216)
                    sp(spread_ev(j, T, h, bank, t), 1, "spread_ev")
                ends.append(t)
                if len(ends) == 2:
                    g["sel"] = tuple(ends)
                    R.Y.put(yh, *ends)
                    R.Y.put(yl, *ends)

            def spread_ev(j, T, h, bank, t):
                w = yield acc[j][(T, h)]
                x = X[:, T, h * 512:h * 512 + 512]
                t = yield tt(x, bank[:, :], x, ALU.add, 512, t, *w)
                S.put(bank, t)
                acc[j + 1][(T, h)].set((t,))

            def ev_down1(i):
                if i >= 18 or i == 13:
                    return ev_split(i)

                def ev(nh, bank, tok):
                    rw = yield g["roww"]
                    if nh == 0:
                        ys[i] = yield R.Y
                        y, yf = ys[i]
                    else:
                        yield lambda: i in ys
                        y, yf = ys[i]
                    t = yield act(y[0][:, nh * 512:nh * 512 + 512], bank[:, :], AF.Copy, 512, tok, *yf, *rw, *zone,
                                  scale=ROWW[:, i:i + 1])
                    G.put(bank, t)
                    if nh == 1:
                        before = yield sums[tiles.index(i)]
                        sem, toks = yield IQ
                        t = yield Op("G", 1000.0, lambda e: e.indirect_dma_start(
                            SUM[:, :], bass.IndirectOffsetOnAxis(PUT[:, i:i + 1], axis=0), y[0][:, :], None,
                            bounds_check=639, oob_is_err=True, compute_op=ALU.add), (*toks, t, *rw, *before), 1, sem,
                            524288)
                        IQ.put(sem, t)
                        R.Y.put(y, t)
                        sums[tiles.index(i) + 1].set((t,))
                return ev

            def ev_down(gr):
                evs = [ev_down1(i) for i in gr]
                return lambda nh, T, bank, tok: evs[T](nh, bank, tok)

            def take(eng):
                w = yield g["ovf"]

                def fn(e):
                    regs[eng] = e.value_load(OVF[0:1, 0:1], min_val=0, max_val=7)
                yield Op(eng, 60.0, fn, w, 0)

            def ready(rs):
                fs = [Fut() for _ in rs]
                for f, r in zip(fs, rs):
                    f.set(r)
                return lambda k, T: fs[T]

            def parts(bufs, K):
                return dict(H=0, L=K, tile=lambda H, k, T: bufs[T][:, H + k, :])

            def up_or_gate(gr, name, ev):
                er = []
                for i in gr:
                    er.append((yield ex[i]))
                yield from gemmB(lambda nh, k: src(gr[0], name, k, 0), 1, 8, ready=ready([r for _, r in er]), evac=ev,
                                 TN=len(gr), strm=strm, spawn=sp, **parts([e for e, _ in er], 8))
                if name == "w_up_2":
                    for i, (e, _) in zip(gr, er):
                        (R.EX2 if i in (16, 17) else R.EX).put(e, g["last"])
                        if i == 17:
                            g["ex2_last"].set((g["last"],))

            def down(gr):
                hr = []
                for i in gr:
                    hr.append((yield eh[i]))
                yield from gemmB(lambda nh, k: src(gr[0], "w_down_2", k, nh * 512), 2, 4, ready=ready([r for _, r in hr]),
                                 evac=ev_down(gr), TN=len(gr), strm=strm, spawn=sp, **parts([h for h, _ in hr], 4))
                for h, _ in hr:
                    R.EH.put(h, g["last"])

            sp(fetches(), 4, "fetches")
            sp(preps(), 4, "preps")
            for n, gr in enumerate(groups):
                if n == 4:
                    for e in "TAVGS":
                        sp(take(e), 8, "take")
                yield from up_or_gate(gr, "w_gate_2", ev_gate(gr))
                if n:
                    yield from down(groups[n - 1])
                yield from up_or_gate(gr, "w_up_2", ev_up(gr))
            yield from down(groups[-1])

        def chosen(name, k, n, j):
            def src():
                w = A[name][0, bass.ds(regs["e"], 1), k * 128:(k + 2) * 128, n:n + 512]
                return w.rearrange("o (a p) c -> p (o a) c", p=128)
            src.j = j
            return src

        def read_expert(j):
            def fn(e):
                regs["e"] = e.value_load(OVF[0:1, j:j + 1], min_val=0, max_val=15)
            return fn

        def reload(w, x_out):
            w = (yield w) + (yield g["ex2_last"])
            for T in range(4):
                r = yield g["x_read"][T]
                t = yield from load(X[:, T, :], SUM[T * 128:T * 128 + 128, :], 524288, *w, *r)
                for h in range(2):
                    x_out[(T, h)].set((t,))

        def moe(x_in, zone):
            idx, logits = g["idx"], g["logits"]
            R = Tiles()

            def src(i, name, k, n):
                if i < 2:
                    return wB(A[name][0, 15 - i], k, n)
                return chosen(name, k, n, 8 + i), "B"

            def more_raw():
                for i in range(13, 15):
                    raw.put(i, *zone)
                w = yield from gather(g["moe_rms"])
                for i in range(6, 9):
                    raw.put(i, *w)
                st = []
                for _ in range(2):
                    st += list((yield STG)[1])
                raw.put(16, *st)
                w += (yield g["sum0"])
                for i in range(17, 21):
                    raw.put(i, *w, *zone)

            def xg():
                w = []
                for x, _ in R.XG.free:
                    w.append((yield Op("G", 1200.0, lambda e, x=x: e.memset(x[:, :], 0.0), zone)))
                R.XG.free = [(x, (t,)) for (x, _), t in zip(R.XG.free, w)]
                FG = ST[0]
                f = yield from load(FG[:, :], A["g_final_2"].rearrange("(o c) -> o c", o=1).broadcast_to([128, 1024]),
                                    524288, *zone)
                g["fg"] = f

            zone = zone + (yield logits)
            yield from xg()
            spawn(more_raw(), 2, "more_raw")
            acc = [xfuts() for _ in range(8)]
            sums = [g["sum0"]] + [Fut() for _ in range(17)]
            g["ex2_last"] = Fut()

            def second():
                w = (yield g["x_read"][0]) + (yield g["x_read"][1])
                R.EX2.put(R.ex2, *w)

            spawn(second(), 2, "second")
            spawn(reload(sums[17], acc[0]), 1, "reload")
            groups = [(i,) for i in range(14)]
            groups.insert(6, (14, 16))
            groups.insert(9, (15, 17))
            yield from experts(bd, strm, groups, sum(groups, ()), src, R, idx, zone, IQ, TP, sums, acc)
            yield from gather(acc[1].values())
            g["moe"] = (R, idx, acc, dict(raw.free))

        def further(zone):
            R, idx, acc, _ = g["moe"]
            b2 = Board("2")
            for n, q in b2.q.items():
                q.t = bd.q[n].t
            order2 = []
            for j in range(6):
                for name, K, H in (("w_gate_2", 8, 1), ("w_up_2", 8, 1), ("w_down_2", 4, 2)):
                    for nh in range(H):
                        for k in range(0, K, 2):
                            order2.append((chosen(name, k, nh * 512, j + 1), "B"))

            def rel0(c):
                d = [strm.rel[m].v for m in strm.rel if m % 8 == c % 8]
                return tuple(t for v in d[-1:] for t in v)

            s2 = Stream(b2, order2, raw, RS2, rel0, False)
            IQ2 = Pool(IS2)
            parts = {n: [] for n in b2.q}
            for j in range(6):
                mark = {n: len(q.items) for n, q in b2.q.items()}
                s2.go(12 * j, 12 * j + 12)

                def src(i, name, k, n):
                    return None, "B"

                b2.spawn(experts(b2, s2, [(18 + j,)], [18 + j], src, R, idx, zone, IQ2, TP, None, acc), 10, "extra")
                b2.run()
                ends = [(q.name, q.n) for q in b2.q.values() if q.n]
                for n, q in b2.q.items():
                    q.items.append((ends, None, None, 0))
                    parts[n].append(q.items[mark[n]:])
            return parts

        def final(zone):
            _, _, acc, free = g["moe"]

            def one(T):
                tmp = RAW[T]
                x = acc[1]
                yield from rms_rows(T, X[:, T, :], (x[(T, 0)], x[(T, 1)]), tmp, free[T], ST[0], (g["fg"],), None, 1e-6, None,
                                    None, each=lambda h, u: spawn(store(T, h, tmp, u), 1, "store"))

            def store(T, h, tmp, u):
                c = slice(h * 512, h * 512 + 512)
                yield from load(out[0, T * 128:T * 128 + 128, c], tmp[:, c], 262144, u)

            for T in range(4):
                spawn(one(T), 2 + T, f"final{T}")

        def spare():
            t = yield from load(SUM[512:640, :].rearrange("p (a c) -> p a c", a=8),
                                ident[:, :].unsqueeze(1).broadcast_to([128, 8, 128]), 524288, g["ident"])
            g["spare"] = (t,)

        def split_out(k, o, t, h, l, rdy, w):
            th = yield act(h, o[:, :], AF.Copy, 512, t, *w)
            tl = yield tt(l, o[:, :], h.bitcast(F32), ALU.subtract, 512, th, *w)
            OP.put(o, tl)
            g["oa_last"] = tl
            for T in range(4):
                rdy.f[(k, T)].set((th, tl))

        def ax_tables(z, g):
            AXT = at_("AXT", 16, [128, 2, 4, 128])

            def th():
                stage, sf = yield STG
                gv = stage[:, 0:128]
                t0 = yield from load(gv[:, 0:64], A["g_q_2"].broadcast_to([128, 64]), 32768, *sf)
                t1 = yield from load(gv[:, 64:128], A["g_k_2"].broadcast_to([128, 64]), 32768, *sf)
                ax = stage[:, 128:640].rearrange("p (t c) -> p t c", t=4)
                t2 = yield from load(ax, A["axial"], 262144, *sf)
                gsw = stage[:, 640:768]
                g4 = gv.rearrange("p (c s) -> p c s", s=2)
                s4 = gsw.rearrange("p (c s) -> p c s", s=2)
                u0 = yield cp(s4[:, :, 0], g4[:, :, 1], 64, t0, t1)
                u1 = yield cp(s4[:, :, 1], g4[:, :, 0], 64)
                r = []
                for w_ in range(2):
                    r.append((yield tt(AXT[:, w_, :, 0:64], ax[:, :, 0:64],
                                       gv[:, w_ * 64:w_ * 64 + 64].unsqueeze(1).broadcast_to([128, 4, 64]), ALU.mult, 256,
                                       t2, t0, t1, *z)))
                    r.append((yield tt(AXT[:, w_, :, 64:128], ax[:, :, 64:128],
                                       gsw[:, w_ * 64:w_ * 64 + 64].unsqueeze(1).broadcast_to([128, 4, 64]), ALU.mult, 256,
                                       u0, u1)))
                STG.put(stage, *r)
                g["axt"] = tuple(r)
            spawn(th(), 2, "axt")
            return AXT

        def root():
            x6, zone, nxt = yield from layer0(pre1)
            x6, zone, nxt = yield from layer1(x6, zone, nxt, pre2)
            x6, zone = yield from block2(x6, zone, nxt)
            yield from moe(x6, zone)
            g["fin"] = (x6, zone)
            strm.over = True
        def wait_all():
            for s in DS:
                if s in bd.dsem:
                    bd.q["S"].items.append(([(s, bd.dsem[s])], None, None, 0))

        for T in range(4):
            g["x", T] = Fut()
        spawn(start(), 0, "start")
        spawn(root(), 10, "spine")
        bd.run()
        bd.parts = {n: [q.items, [], []] for n, q in bd.q.items()}
        if "fin" in g:
            x6, zone = g["fin"]
            extra = further(zone)
            for n, q in bd.q.items():
                q.items = []
                bd.parts[n][1:] = [extra[n], q.items]
            final(zone)
            bd.run()
        wait_all()
        return bd

    emission(True)
    bd = emission(False)
    play(bd)
    ctx.close()
    return bd


_INS = ["x", "p", "ev_w_in", "ev_w_out", "da_lambda", "da_subln_g", "hg_lb_logits", "hg_norm_g", "od_w_in", "od_w_out",
        "ln1_g", "ln1_b", "ffn_w1", "ffn_w2", "ln2_g", "ln2_b", "ple_w_proj", "ple_w_gate", "ple_norm_g", "mem_2",
        "g_mix_2", "w_in_2", "g_q_2", "g_k_2", "w_att_out_2", "sgu_ln_g_2", "sgu_ln_b_2", "w_s_2", "b_s_2",
        "w_sgu_out_2", "w_out_2", "g_cross_2", "g_mem_2", "w_cq_2", "w_ckv_2", "w_co_2", "g_moe_2", "w_rg_2", "b_rg_2",
        "w_re_2", "b_re_2", "w_gate_2", "w_up_2", "w_down_2", "g_final_2"]


def kernel(**inputs):
    import numpy as _np
    import concourse.bacc as _bacc
    from concourse import mybir as _mybir
    from concourse.bass_utils import run_bass_kernel_spmd as _run

    nc = _bacc.Bacc("TRN2", target_bir_lowering=False, num_devices=1)
    arrays, A = {}, {}
    given = [(name, inputs[name]) for name in _INS] + list(constants().items())
    for name, value in given:
        a = _np.ascontiguousarray(value)
        arrays[f"in_{name}_dram"] = a
        A[name] = nc.dram_tensor(f"in_{name}_dram", a.shape, _mybir.dt.from_np(a.dtype), kind="ExternalInput").ap()
    out = nc.dram_tensor("out_0_dram", (1, 512, 1024), _mybir.dt.from_np(_np.dtype("float32")),
                         kind="ExternalOutput").ap()
    build(nc, A, out)
    r = _run(nc, [arrays], core_ids=[0])
    return r.results[0]["out_0_dram"]
```
